# Optimizing a Trainium2 kernel written in Bass

```python
import jax, jax.numpy as jnp
from jax import lax
import numpy as np
import jax
import jax.numpy as jnp

D_MODEL = 1024
BATCH = 1
SEQ = 512
DEPTH = 1

CHUNK = 64
N_META = 16
Q_BLOCK = 128
EPS = 1e-6
ROPE_THETA = 10000.0
CONV_W = 256
CONV_K = 3
MLA_HEADS = 8
QK_NOPE = 64
QK_ROPE = 32
QK_HEAD = QK_NOPE + QK_ROPE
V_HEAD = 64
MLA_W = MLA_HEADS * V_HEAD
Q_RANK = 256
KV_RANK = 128
RET_HEADS = 4
RET_HEAD = 64
RET_W = RET_HEADS * RET_HEAD
D_MIX = CONV_W + MLA_W + RET_W
IN_SPLITS = (CONV_W, CONV_W, CONV_W, CONV_W, Q_RANK, KV_RANK, QK_ROPE, MLA_W, RET_W, RET_W, RET_W, RET_W)
D_IN = int(np.sum(IN_SPLITS))
IN_OFFSETS = tuple(int(o) for o in np.cumsum(IN_SPLITS)[:-1])


def rms_norm(x, w):
    xf = x.astype(jnp.float32)
    y = xf * lax.rsqrt(jnp.mean(xf * xf, axis=-1, keepdims=True) + EPS)
    return (y * w.astype(jnp.float32)).astype(x.dtype)

def rope_tables(n_pos, dim, dtype):
    inv = 1.0 / (ROPE_THETA ** (jnp.arange(0, dim, 2, dtype=jnp.float32) / dim))
    ang = jnp.arange(n_pos, dtype=jnp.float32)[:, None] * inv[None, :]
    return jnp.cos(ang).astype(dtype), jnp.sin(ang).astype(dtype)

def apply_rope(x, cos, sin):
    x1, x2 = jnp.split(x, 2, axis=-1)
    c = cos[:, None, :]
    s = sin[:, None, :]
    return jnp.concatenate([x1 * c - x2 * s, x1 * s + x2 * c], axis=-1)

def chunk_ids(n):
    pos = jnp.arange(n)
    return jnp.where(pos < N_META, 0, 1 + (pos - N_META) // CHUNK)

def short_conv_mixer(xin, b, c, z, conv_w, conv_b):
    L = xin.shape[1]
    u = jnp.pad(c * xin, ((0, 0), (CONV_K - 1, 0), (0, 0)))
    y = conv_b
    for j in range(CONV_K):
        y = y + u[:, j:j + L] * conv_w[j]
    return b * y * jax.nn.silu(z)

def mla_mixer(c_q, c_kv, k_rope, z, q_a_norm, w_uq, kv_a_norm, w_ukv, q_norm, k_norm, cos, sin):
    B, L, _ = c_q.shape
    q = (rms_norm(c_q, q_a_norm) @ w_uq).reshape(B, L, MLA_HEADS, QK_HEAD)
    kv = (rms_norm(c_kv, kv_a_norm) @ w_ukv).reshape(B, L, MLA_HEADS, QK_NOPE + V_HEAD)
    k_nope, v = kv[..., :QK_NOPE], kv[..., QK_NOPE:]
    k_r = jnp.broadcast_to(k_rope[:, :, None, :], (B, L, MLA_HEADS, QK_ROPE))
    k = jnp.concatenate([k_nope, k_r], axis=-1)
    q = rms_norm(q, q_norm)
    k = rms_norm(k, k_norm)
    q = jnp.concatenate([q[..., :QK_NOPE], apply_rope(q[..., QK_NOPE:], cos, sin)], axis=-1)
    k = jnp.concatenate([k[..., :QK_NOPE], apply_rope(k[..., QK_NOPE:], cos, sin)], axis=-1)
    Lp = -(-L // Q_BLOCK) * Q_BLOCK
    pad = ((0, 0), (0, Lp - L), (0, 0), (0, 0))
    q = jnp.pad(q, pad)
    k = jnp.pad(k, pad)
    v = jnp.pad(v, pad)
    cid = chunk_ids(Lp)
    n_blk = Lp // Q_BLOCK
    q_blocks = q.reshape(B, n_blk, Q_BLOCK, MLA_HEADS, QK_HEAD).transpose(1, 0, 2, 3, 4)
    cid_blocks = cid.reshape(n_blk, Q_BLOCK)
    scale = QK_HEAD ** -0.5
    neg = jnp.finfo(jnp.float32).min

    def attend(args):
        qb, qc = args
        s = jnp.einsum('bqhd,bkhd->bhqk', qb, k).astype(jnp.float32) * scale
        mask = cid[None, :] <= qc[:, None]
        s = jnp.where(mask[None, None], s, neg)
        p = jax.nn.softmax(s, axis=-1).astype(v.dtype)
        return jnp.einsum('bhqk,bkhd->bqhd', p, v)

    o = lax.map(attend, (q_blocks, cid_blocks))
    o = o.transpose(1, 0, 2, 3, 4).reshape(B, Lp, MLA_W)[:, :L]
    return o * jax.nn.silu(z)

def retention_mixer(q, k, v, z, ret_norm, cos, sin):
    B, L, _ = q.shape
    dt = q.dtype
    q = apply_rope(q.reshape(B, L, RET_HEADS, RET_HEAD), cos, sin)
    k = apply_rope(k.reshape(B, L, RET_HEADS, RET_HEAD), cos, sin) * (RET_HEAD ** -0.5)
    v = v.reshape(B, L, RET_HEADS, RET_HEAD)
    front = CHUNK - N_META
    back = (-(front + L)) % CHUNK
    pad = ((0, 0), (front, back), (0, 0), (0, 0))
    n_chk = (front + L + back) // CHUNK
    qc = jnp.pad(q, pad).reshape(B, n_chk, CHUNK, RET_HEADS, RET_HEAD)
    kc = jnp.pad(k, pad).reshape(B, n_chk, CHUNK, RET_HEADS, RET_HEAD)
    vc = jnp.pad(v, pad).reshape(B, n_chk, CHUNK, RET_HEADS, RET_HEAD)
    log_g = jnp.log1p(-jnp.exp2(-5.0 - jnp.arange(RET_HEADS, dtype=jnp.float32)))
    idx = jnp.arange(CHUNK, dtype=jnp.float32)
    intra_decay = jnp.exp(log_g[:, None, None] * jnp.abs(idx[:, None] - idx[None, :])).astype(dt)
    kv_decay = jnp.exp(log_g[:, None] * (CHUNK - 1.0 - idx)[None, :]).astype(dt)
    q_decay = jnp.exp(log_g[:, None] * (idx + 1.0)[None, :]).astype(dt)
    chunk_decay = jnp.exp(log_g * CHUNK).astype(dt)
    s = jnp.einsum('bnchd,bnmhd->bnhcm', qc, kc) * intra_decay
    o_intra = jnp.einsum('bnhcm,bnmhd->bnchd', s, vc)
    kv = jnp.einsum('bnmhd,hm,bnmhe->nbhde', kc, kv_decay, vc)

    def step(state, kv_n):
        return state * chunk_decay[None, :, None, None] + kv_n, state

    _, prev = lax.scan(step, jnp.zeros_like(kv[0]), kv)
    o_cross = jnp.einsum('bnchd,nbhde->bnche', qc, prev) * q_decay.T[None, None, :, :, None]
    o = (o_intra + o_cross).reshape(B, n_chk * CHUNK, RET_HEADS, RET_HEAD)[:, front:front + L]
    o = rms_norm(o, ret_norm).reshape(B, L, RET_W)
    return o * jax.nn.silu(z)

def first_inputs(seed: int = 0) -> dict:
    key = jax.random.key(seed)
    ks = jax.random.split(key, 16)
    f32 = jnp.float32

    def nrm(k, shape, scale):
        return jax.random.normal(k, shape, f32) * scale

    def gain(k, shape):
        return 1.0 + 0.05 * jax.random.normal(k, shape, f32)

    return {
        "x": jax.random.normal(ks[0], (BATCH, SEQ, D_MODEL), f32),
        "meta_tokens": nrm(ks[1], (N_META, D_MODEL), 1.0),
        "ln_w": gain(ks[2], (DEPTH, D_MODEL)),
        "w_in": nrm(ks[3], (DEPTH, D_MODEL, D_IN), D_MODEL ** -0.5),
        "w_out": nrm(ks[4], (DEPTH, D_MIX, D_MODEL), D_MIX ** -0.5),
        "conv_w": nrm(ks[5], (DEPTH, CONV_K, CONV_W), CONV_K ** -0.5),
        "conv_b": nrm(ks[6], (DEPTH, CONV_W), 0.02),
        "q_a_norm": gain(ks[7], (DEPTH, Q_RANK)),
        "w_uq": nrm(ks[8], (DEPTH, Q_RANK, MLA_HEADS * QK_HEAD), Q_RANK ** -0.5),
        "kv_a_norm": gain(ks[9], (DEPTH, KV_RANK)),
        "w_ukv": nrm(ks[10], (DEPTH, KV_RANK, MLA_HEADS * (QK_NOPE + V_HEAD)), KV_RANK ** -0.5),
        "q_norm": gain(ks[11], (DEPTH, QK_HEAD)),
        "k_norm": gain(ks[12], (DEPTH, QK_HEAD)),
        "ret_norm": gain(ks[13], (DEPTH, RET_HEAD)),
    }

def first_block(x, meta_tokens, ln_w, w_in, w_out, conv_w, conv_b, q_a_norm, w_uq, kv_a_norm, w_ukv,
              q_norm, k_norm, ret_norm):
    B = x.shape[0]
    meta = jnp.broadcast_to(meta_tokens[None].astype(x.dtype), (B, N_META, D_MODEL))
    h = jnp.concatenate([meta, x], axis=1)
    L = h.shape[1]
    cos_m, sin_m = rope_tables(L, QK_ROPE, h.dtype)
    cos_r, sin_r = rope_tables(L, RET_HEAD, h.dtype)
    for l in range(DEPTH):
        u = rms_norm(h, ln_w[l])
        (cx, cb, cc, cz, cq, ckv, krope, mz, rq, rk, rv, rz) = jnp.split(u @ w_in[l], IN_OFFSETS, axis=-1)
        y_conv = short_conv_mixer(cx, cb, cc, cz, conv_w[l], conv_b[l])
        y_mla = mla_mixer(cq, ckv, krope, mz, q_a_norm[l], w_uq[l], kv_a_norm[l], w_ukv[l],
                          q_norm[l], k_norm[l], cos_m, sin_m)
        y_ret = retention_mixer(rq, rk, rv, rz, ret_norm[l], cos_r, sin_r)
        y = jnp.concatenate([y_conv, y_mla, y_ret], axis=-1)
        h = h + y @ w_out[l]
    return h[:, N_META:]


MEM_LEN = 256

GLA_HEADS = 4
GLA_DK = D_MODEL // 8
GLA_DV = D_MODEL // 4
GLA_GATE_RANK = 16
GLA_GATE_TEMP = 16.0
GLA_CHUNK = 64

DSA_HEADS = 8
DSA_KV_HEADS = 2
DSA_HEAD_DIM = 128
IDX_HEADS = 8
IDX_DIM = 64
IDX_TOPK_MAX = 256

MEM_HEADS = 4
MEM_HEAD_DIM = D_MODEL // 4

N_GROUPS = 4
EXPERTS_PER_GROUP = 4
N_EXPERTS = N_GROUPS * EXPERTS_PER_GROUP
EXPERT_TOPK = 2
D_EXPERT = D_MODEL // 4

N_BRANCH = 3
IN_SPLITS_2 = (
    GLA_HEADS * GLA_DK,
    GLA_HEADS * GLA_DK,
    GLA_HEADS * GLA_DV,
    GLA_HEADS * GLA_DV,
    GLA_GATE_RANK,
    DSA_HEADS * DSA_HEAD_DIM,
    DSA_KV_HEADS * DSA_HEAD_DIM,
    DSA_KV_HEADS * DSA_HEAD_DIM,
    IDX_HEADS * IDX_DIM,
    IDX_DIM,
    IDX_HEADS,
    MEM_HEADS * MEM_HEAD_DIM,
    N_BRANCH * D_MODEL,
)
D_IN_2 = sum(IN_SPLITS_2)


def _rmsnorm(x, g):
    xf = x.astype(jnp.float32)
    y = xf * lax.rsqrt(jnp.mean(xf * xf, axis=-1, keepdims=True) + EPS)
    return y.astype(x.dtype) * g

def _split_in(z):
    offs = []
    acc = 0
    for w in IN_SPLITS_2[:-1]:
        acc += w
        offs.append(acc)
    return jnp.split(z, offs, axis=-1)

def _gla(q, k, v, g_out, a_low, w_a2, b_a2, norm_g):
    B, T = q.shape[:2]
    C = GLA_CHUNK
    N = T // C
    shp_k = (B, N, C, GLA_HEADS, GLA_DK)
    qf = q.astype(jnp.float32).reshape(shp_k) * GLA_DK ** -0.5
    kf = k.astype(jnp.float32).reshape(shp_k)
    vf = v.astype(jnp.float32).reshape(B, N, C, GLA_HEADS, GLA_DV)
    log_a = jax.nn.log_sigmoid((a_low @ w_a2 + b_a2).astype(jnp.float32)) / GLA_GATE_TEMP
    cum = jnp.cumsum(log_a.reshape(shp_k), axis=2)
    last = cum[:, :, -1:]
    q_dec = qf * jnp.exp(cum)
    k_inv = kf * jnp.exp(-cum)
    k_end = kf * jnp.exp(last - cum)
    causal = jnp.tril(jnp.ones((C, C), dtype=bool))
    att = jnp.where(causal, jnp.einsum('bnihd,bnjhd->bnhij', q_dec, k_inv), 0.0)
    o_intra = jnp.einsum('bnhij,bnjhv->bnihv', att, vf)
    upd = jnp.einsum('bnjhd,bnjhv->nbhdv', k_end, vf)
    decay = jnp.exp(last[:, :, 0]).transpose(1, 0, 2, 3)

    def step(state, inp):
        dec, u = inp
        return dec[..., None] * state + u, state

    s0 = jnp.zeros((B, GLA_HEADS, GLA_DK, GLA_DV), jnp.float32)
    _, s_prev = lax.scan(step, s0, (decay, upd))
    o_inter = jnp.einsum('bnihd,nbhdv->bnihv', q_dec, s_prev)
    o = (o_intra + o_inter).reshape(B, T, GLA_HEADS, GLA_DV)
    o = _rmsnorm(o, norm_g.astype(jnp.float32)).reshape(B, T, GLA_HEADS * GLA_DV)
    return (o * jax.nn.silu(g_out.astype(jnp.float32))).astype(q.dtype)

def _dsa(q, k, v, q_idx, k_idx, w_idx, q_gain, k_gain, kidx_gain):
    B, T = q.shape[:2]
    topk = min(IDX_TOPK_MAX, T // 4)
    grp = DSA_HEADS // DSA_KV_HEADS
    q = _rmsnorm(q.reshape(B, T, DSA_HEADS, DSA_HEAD_DIM), q_gain) * DSA_HEAD_DIM ** -0.5
    k = _rmsnorm(k.reshape(B, T, DSA_KV_HEADS, DSA_HEAD_DIM), k_gain)
    v = v.reshape(B, T, DSA_KV_HEADS, DSA_HEAD_DIM)
    q_idx = q_idx.reshape(B, T, IDX_HEADS, IDX_DIM)
    k_idx = _rmsnorm(k_idx, kidx_gain)
    w_idx = w_idx * (IDX_HEADS ** -0.5 * IDX_DIM ** -0.5)
    key_pos = jnp.arange(T)

    def block(i):
        start = i * Q_BLOCK
        qb = lax.dynamic_slice_in_dim(q, start, Q_BLOCK, axis=1)
        qib = lax.dynamic_slice_in_dim(q_idx, start, Q_BLOCK, axis=1)
        wb = lax.dynamic_slice_in_dim(w_idx, start, Q_BLOCK, axis=1)
        qpos = start + jnp.arange(Q_BLOCK)
        rel = jax.nn.relu(jnp.einsum('bqhd,bsd->bqhs', qib, k_idx).astype(jnp.float32))
        score = jnp.einsum('bqh,bqhs->bqs', wb.astype(jnp.float32), rel)
        allowed = key_pos[None, :] <= qpos[:, None]
        score = jnp.where(allowed, score, -jnp.inf)
        _, idx = lax.top_k(score, topk)
        valid = idx <= qpos[None, :, None]
        kg = jax.vmap(lambda kk, ii: kk[ii])(k, idx)
        vg = jax.vmap(lambda vv, ii: vv[ii])(v, idx)
        qg = qb.reshape(B, Q_BLOCK, DSA_KV_HEADS, grp, DSA_HEAD_DIM)
        logits = jnp.einsum('bqgrd,bqkgd->bqgrk', qg, kg).astype(jnp.float32)
        logits = jnp.where(valid[:, :, None, None, :], logits, -jnp.inf)
        p = jax.nn.softmax(logits, axis=-1).astype(v.dtype)
        o = jnp.einsum('bqgrk,bqkgd->bqgrd', p, vg)
        return o.reshape(B, Q_BLOCK, DSA_HEADS * DSA_HEAD_DIM)

    out = lax.map(block, jnp.arange(T // Q_BLOCK))
    return out.transpose(1, 0, 2, 3).reshape(B, T, DSA_HEADS * DSA_HEAD_DIM)

def _memory_attn(q, mem_h, w_kv, q_gain, k_gain):
    B, T = q.shape[:2]
    M = mem_h.shape[1]
    q = _rmsnorm(q.reshape(B, T, MEM_HEADS, MEM_HEAD_DIM), q_gain) * MEM_HEAD_DIM ** -0.5
    kv = (mem_h @ w_kv).reshape(B, M, 2, MEM_HEADS, MEM_HEAD_DIM)
    k = _rmsnorm(kv[:, :, 0], k_gain)
    v = kv[:, :, 1]
    logits = jnp.einsum('bthd,bmhd->bhtm', q, k).astype(jnp.float32)
    p = jax.nn.softmax(logits, axis=-1).astype(v.dtype)
    o = jnp.einsum('bhtm,bmhd->bthd', p, v)
    return o.reshape(B, T, MEM_HEADS * MEM_HEAD_DIM)

def _hier_moe(h, w_r1, b_r1, w_r2, b_r2, w_gate, w_up, w_down):
    B, T, D = h.shape
    hf = h.reshape(B * T, D)
    g_logits = (hf @ w_r1 + b_r1).astype(jnp.float32)
    g_prob = jax.nn.softmax(g_logits, axis=-1)
    g_sel = jnp.argmax(g_logits, axis=-1)
    g_w = jnp.take_along_axis(g_prob, g_sel[:, None], axis=-1)
    e_logits = (hf @ w_r2 + b_r2).astype(jnp.float32).reshape(-1, N_GROUPS, EXPERTS_PER_GROUP)
    e_logits = jnp.take_along_axis(e_logits, g_sel[:, None, None], axis=1)[:, 0]
    e_prob = jax.nn.softmax(e_logits, axis=-1)
    top_p, top_i = lax.top_k(e_prob, EXPERT_TOPK)
    top_p = top_p / jnp.sum(top_p, axis=-1, keepdims=True)
    expert_id = g_sel[:, None] * EXPERTS_PER_GROUP + top_i
    combine = jnp.sum(jax.nn.one_hot(expert_id, N_EXPERTS, dtype=jnp.float32)
                      * (g_w * top_p)[..., None], axis=1)
    hid = jax.nn.silu(jnp.einsum('nd,edf->nef', hf, w_gate)) * jnp.einsum('nd,edf->nef', hf, w_up)
    hid = hid * combine[..., None].astype(hid.dtype)
    out = jnp.einsum('nef,efd->nd', hid, w_down)
    return out.reshape(B, T, D)

def second_inputs(seed: int = 0) -> dict:
    key = jax.random.key(seed)
    ks = iter(jax.random.split(key, 40))
    L = DEPTH

    def w(shape, fan_in):
        return jax.random.normal(next(ks), shape, jnp.float32) * fan_in ** -0.5

    def gain(shape):
        return 1.0 + 0.02 * jax.random.normal(next(ks), shape, jnp.float32)

    def bias(shape, s=0.01):
        return s * jax.random.normal(next(ks), shape, jnp.float32)

    return {
        'x': jax.random.normal(next(ks), (BATCH, SEQ, D_MODEL), jnp.float32),
        'mem': jax.random.normal(next(ks), (BATCH, MEM_LEN, D_MODEL), jnp.float32),
        'g_mix': gain((L, D_MODEL)),
        'g_mem': gain((L, D_MODEL)),
        'w_in': w((L, D_MODEL, D_IN_2), D_MODEL),
        'w_gla_a2': w((L, GLA_GATE_RANK, GLA_HEADS * GLA_DK), GLA_GATE_RANK),
        'b_gla_a2': bias((L, GLA_HEADS * GLA_DK), 0.1),
        'gla_norm': gain((L, GLA_DV)),
        'w_mem_kv': w((L, D_MODEL, 2 * MEM_HEADS * MEM_HEAD_DIM), D_MODEL),
        'dsa_q_norm': gain((L, DSA_HEAD_DIM)),
        'dsa_k_norm': gain((L, DSA_HEAD_DIM)),
        'idx_k_norm': gain((L, IDX_DIM)),
        'mem_q_norm': gain((L, MEM_HEAD_DIM)),
        'mem_k_norm': gain((L, MEM_HEAD_DIM)),
        'b_gate': bias((L, N_BRANCH * D_MODEL), 0.1),
        'w_o_gla': w((L, GLA_HEADS * GLA_DV, D_MODEL), GLA_HEADS * GLA_DV),
        'w_o_dsa': w((L, DSA_HEADS * DSA_HEAD_DIM, D_MODEL), DSA_HEADS * DSA_HEAD_DIM),
        'w_o_mem': w((L, MEM_HEADS * MEM_HEAD_DIM, D_MODEL), MEM_HEADS * MEM_HEAD_DIM),
        'w_out': w((L, D_MODEL, D_MODEL), D_MODEL),
        'g_ffn': gain((L, D_MODEL)),
        'w_r1': w((L, D_MODEL, N_GROUPS), D_MODEL),
        'b_r1': bias((L, N_GROUPS)),
        'w_r2': w((L, D_MODEL, N_EXPERTS), D_MODEL),
        'b_r2': bias((L, N_EXPERTS)),
        'w_gate': w((L, N_EXPERTS, D_MODEL, D_EXPERT), D_MODEL),
        'w_up': w((L, N_EXPERTS, D_MODEL, D_EXPERT), D_MODEL),
        'w_down': w((L, N_EXPERTS, D_EXPERT, D_MODEL), D_EXPERT),
    }

def second_block(x, mem, g_mix, g_mem, w_in, w_gla_a2, b_gla_a2, gla_norm, w_mem_kv,
              dsa_q_norm, dsa_k_norm, idx_k_norm, mem_q_norm, mem_k_norm, b_gate,
              w_o_gla, w_o_dsa, w_o_mem, w_out, g_ffn, w_r1, b_r1, w_r2, b_r2,
              w_gate, w_up, w_down):
    B, T, D = x.shape
    for l in range(DEPTH):
        h = _rmsnorm(x, g_mix[l])
        (gq, gk, gv, gg, ga, dq, dk, dv, iq, ik, iw, mq, gates) = _split_in(h @ w_in[l])
        o_gla = _gla(gq, gk, gv, gg, ga, w_gla_a2[l], b_gla_a2[l], gla_norm[l])
        o_dsa = _dsa(dq, dk, dv, iq, ik, iw, dsa_q_norm[l], dsa_k_norm[l], idx_k_norm[l])
        mem_h = _rmsnorm(mem, g_mem[l])
        o_mem = _memory_attn(mq, mem_h, w_mem_kv[l], mem_q_norm[l], mem_k_norm[l])
        gate = jax.nn.sigmoid((gates + b_gate[l]).astype(jnp.float32)).astype(x.dtype)
        gate = gate.reshape(B, T, N_BRANCH, D)
        merged = (gate[:, :, 0] * (o_gla @ w_o_gla[l])
                  + gate[:, :, 1] * (o_dsa @ w_o_dsa[l])
                  + gate[:, :, 2] * (o_mem @ w_o_mem[l]))
        x = x + merged @ w_out[l]
        x = x + _hier_moe(_rmsnorm(x, g_ffn[l]), w_r1[l], b_r1[l], w_r2[l], b_r2[l],
                          w_gate[l], w_up[l], w_down[l])
    return x


def setup_inputs(seed=0):
    out = dict(first_inputs(seed))
    for name, value in second_inputs(seed + 1).items():
        if name != "x":
            out[name + "_2"] = value
    return out


def reference(
    x, meta_tokens, ln_w, w_in, w_out, conv_w, conv_b, q_a_norm, w_uq, kv_a_norm, w_ukv, q_norm,
    k_norm, ret_norm, mem_2, g_mix_2, g_mem_2, w_in_2, w_gla_a2_2, b_gla_a2_2, gla_norm_2,
    w_mem_kv_2, dsa_q_norm_2, dsa_k_norm_2, idx_k_norm_2, mem_q_norm_2, mem_k_norm_2, b_gate_2,
    w_o_gla_2, w_o_dsa_2, w_o_mem_2, w_out_2, g_ffn_2, w_r1_2, b_r1_2, w_r2_2, b_r2_2, w_gate_2,
    w_up_2, w_down_2,
):
    x = first_block(
        x, meta_tokens, ln_w, w_in, w_out, conv_w, conv_b, q_a_norm, w_uq, kv_a_norm, w_ukv,
        q_norm, k_norm, ret_norm,
    )
    return second_block(
        x, mem_2, g_mix_2, g_mem_2, w_in_2, w_gla_a2_2, b_gla_a2_2, gla_norm_2, w_mem_kv_2,
        dsa_q_norm_2, dsa_k_norm_2, idx_k_norm_2, mem_q_norm_2, mem_k_norm_2, b_gate_2,
        w_o_gla_2, w_o_dsa_2, w_o_mem_2, w_out_2, g_ffn_2, w_r1_2, b_r1_2, w_r2_2, b_r2_2,
        w_gate_2, w_up_2, w_down_2,
    )


_drawn_inputs = setup_inputs


def setup_inputs(seed=0):
    import zlib

    import numpy as np

    out = dict(_drawn_inputs(seed))
    spreads = {}
    factors = {'conv_b': 3.946,
     'q_a_norm': 5.877,
     'kv_a_norm': 3.555,
     'q_norm': 8.0,
     'k_norm': 4.273,
     'g_mem_2': 6.32,
     'gla_norm_2': 31.957,
     'dsa_q_norm_2': 28.918,
     'dsa_k_norm_2': 26.239,
     'idx_k_norm_2': 14.692,
     'mem_q_norm_2': 8.0,
     'mem_k_norm_2': 7.805,
     'b_r1_2': 61.921,
     'b_r2_2': 56.877,
     'b_gla_a2_2': 3.387,
     'g_ffn_2': 8.0}
    for name, (base, spread) in spreads.items():
        noise = np.random.default_rng([zlib.crc32(name.encode()), seed]).standard_normal(out[name].shape)
        drawn = base * np.exp(spread * noise) if base else spread * noise
        out[name] = jnp.asarray(drawn.astype(out[name].dtype))
    for name, factor in factors.items():
        out[name] = (out[name] * factor).astype(out[name].dtype)
    return out
```

```python
from contextlib import ExitStack

import numpy as np
import concourse.bass as bass
from concourse import mybir

F32 = mybir.dt.float32
F32R = mybir.dt.float32r
ALU = mybir.AluOpType
ACTF = mybir.ActivationFunctionType
X = mybir.AxisListType.X

P = 128
D = 1024
KC = D // P
SEQ = 512
NT = SEQ // P
N_META = 16
L = SEQ + N_META
EPS = 1e-6
CHUNK = 64
QKN, QKR, VH = 64, 32, 64
QKH = QKN + QKR
MLA_H = 8
RET_H, RET_D = 4, 64
MEM = 256
GLA_H, GLA_DV = 4, 256
DSA_H, DSA_G = 8, 4
IDX_H, IDX_D = 8, 64
TOPK = SEQ // 4
MEM_H = 4
N_EXP = 16
D_EXP = 256
MASKED = -1e30
PICKED = -3e38

RAW_SLOTS = 4
SPLIT_SLOTS = 4
UNIT = 1024

C_CX, C_CC, C_CQ, C_KR, C_MZ, C_RQ, C_RV = 0, 512, 1024, 1408, 1440, 1952, 2464
C_GQ, C_GK, C_GV, C_GG, C_GA, C_DQ, C_DK, C_IQ, C_IK, C_MQ, C_GATE = (
    0, 512, 1024, 2048, 3072, 3088, 4112, 4624, 5136, 5208, 6232)

GAINS, _row = {}, 0
for _name, _n in (("ln_w", 8), ("g_mix_2", 8), ("g_mem_2", 8), ("g_ffn_2", 8), ("q_a_norm", 2),
                  ("kv_a_norm", 1), ("conv_w", 6), ("conv_b", 2), ("dsa_q_norm_2", 1),
                  ("dsa_k_norm_2", 1), ("mem_q_norm_2", 2), ("mem_k_norm_2", 2), ("b_gla_a2_2", 4),
                  ("gla_norm_2", 2), ("ret_norm", 1), ("idx_k_norm_2", 1)):
    GAINS[_name] = _row
    _row += _n
N_GAINS = _row


class Progress:

    def __init__(self, nc, ctx, engine, sections, known):
        self.sems = {s: ctx.enter_context(nc.semaphore(f"{engine}_done_{s}")) for s in sections}
        self.count = dict.fromkeys(sections, 0)
        self.section = sections[0]
        self.at = {}
        self.known = known.setdefault(engine, {})
        self.ends = known.setdefault(engine + " ends", {})

    def done(self, *keys):
        self.count[self.section] += 1
        for key in keys:
            assert key not in self.at, key
            self.at[key] = (self.section, self.count[self.section])
        return self.sems[self.section], 1

    def after(self, *key):
        section, value = self.known.get(key, (self.section, 1)) if not self.ends else self.known[key]
        return self.sems[section], value

    def end_of(self, section):
        return self.sems[section], self.ends.get(section, 1)


def weight_items(w):
    items = {}

    def add(name, src, cols, chunks=KC, per=2):
        n = sum(b - a for a, b in cols)
        units = []
        for k0 in range(0, chunks, per):
            pieces, at = [], 0
            for a, b in cols:
                pieces.append((at, at + b - a, src[P * k0:P * (k0 + per), a:b].rearrange("(k p) n -> p k n", p=P)))
                at += b - a
            units.append((list(range(k0, k0 + per)), n, pieces))
        items[name] = units

    w_in, w_in2 = w["w_in"][0], w["w_in_2"][0]
    add("conv_a", w_in, [(C_CX, C_CC)])
    add("conv_b", w_in, [(C_CC, C_CQ)])
    add("latent", w_in, [(C_CQ, C_KR)])
    add("k_rope", w_in, [(C_KR, C_MZ)], per=8)
    add("ret_qk", w_in, [(C_RQ, C_RV)])
    add("ret_vz", w_in, [(C_RV, C_RV + 512)])
    add("mla_z", w_in, [(C_MZ, C_RQ)])
    for n in range(2):
        add(f"w_uq{n}", w["w_uq"][0], [(384 * n, 384 * n + 384)], chunks=2)
    for n in range(2):
        add(f"w_ukv{n}", w["w_ukv"][0], [(512 * n, 512 * n + 512)], chunks=1, per=1)
    for n in range(2):
        add(f"w_out{n}", w["w_out"][0], [(512 * n, 512 * n + 512)])
    add("small2", w_in2, [(C_GA, C_DQ), (C_IK, C_MQ)], per=8)
    add("gla_q", w_in2, [(C_GQ, C_GK)])
    add("gla_k", w_in2, [(C_GK, C_GV)])
    for n in range(2):
        add(f"gla_v{n}", w_in2, [(C_GV + 512 * n, C_GV + 512 * n + 512)])
    for n in range(2):
        add(f"gla_g{n}", w_in2, [(C_GG + 512 * n, C_GG + 512 * n + 512)])

    def branch(b, w_o):
        for n in range(2):
            c = C_GATE + D * b + 512 * n
            add(f"gate{b}{n}", w_in2, [(c, c + 512)])
            add(f"w_o{b}{n}", w_o[0], [(512 * n, 512 * n + 512)])

    branch(0, w["w_o_gla_2"])
    add("idx_q", w_in2, [(C_IQ, C_IK)])
    for n in range(2):
        add(f"dsa_q{n}", w_in2, [(C_DQ + 512 * n, C_DQ + 512 * n + 512)])
    add("dsa_kv", w_in2, [(C_DK, C_IQ)])
    branch(1, w["w_o_dsa_2"])
    for n in range(4):
        add(f"mem_kv{n}", w["w_mem_kv_2"][0], [(512 * n, 512 * n + 512)])
    for n in range(2):
        add(f"mem_q{n}", w_in2, [(C_MQ + 512 * n, C_MQ + 512 * n + 512)])
    branch(2, w["w_o_mem_2"])
    for n in range(2):
        add(f"w_out2{n}", w["w_out_2"][0], [(512 * n, 512 * n + 512)])
    items["router"] = [(list(range(KC)), 20, [
        (0, 4, w["w_r1_2"][0].rearrange("(k p) n -> p k n", p=P)),
        (4, 20, w["w_r2_2"][0].rearrange("(k p) n -> p k n", p=P))])]
    for e in range(N_EXP):
        units = []
        for k0 in range(0, KC, 2):
            rows = slice(P * k0, P * (k0 + 2))
            units.append(([k0, k0 + 1], 512, [
                (0, 256, w["w_gate_2"][0, e, rows, :].rearrange("(k p) n -> p k n", p=P)),
                (256, 512, w["w_up_2"][0, e, rows, :].rearrange("(k p) n -> p k n", p=P))]))
        items[f"expert{e}"] = units
    for e in range(N_EXP):
        for n in range(2):
            add(f"down{e}{n}", w["w_down_2"][0, e], [(512 * n, 512 * n + 512)], chunks=2)
    return items


def make_order():
    order = [("constants",), ("norm", "h")]
    order += [("item", n) for n in ("conv_a", "conv_b", "latent")]
    order += [("conv",), ("latent_sums",), ("item", "k_rope")]
    order += [("item", n) for n in ("w_uq0", "w_uq1", "w_ukv0", "w_ukv1", "mla_z", "ret_qk", "ret_vz")]
    order += [("mla_prepare",), ("barrier", "mla")]
    order += [("mla_head", h) for h in range(MLA_H)]
    order += [("barrier", "ret")]
    order += [("ret_head", h) for h in range(RET_H)]
    order += [("ret_norm",), ("mix_one",), ("item", "w_out0"), ("item", "w_out1"), ("barrier", "gla")]
    order += [("norm", "h2")]
    order += [("item", n) for n in ("small2", "gla_q", "gla_k", "gla_v0", "gla_v1")]
    order += [("gla_low",)] + [("gla_head", h) for h in range(GLA_H)] + [("gla_rstd",)]
    order += [("item", "gla_g0"), ("item", "gla_g1"), ("mix", "gla")]
    order += [("item", n) for n in ("gate00", "w_o00", "gate01", "w_o01")]
    order += [("barrier", "dsa"), ("idx_key",), ("item", "idx_q")]
    order += [("idx_scores", t) for t in range(1, NT)]
    order += [("item", n) for n in ("dsa_q0", "dsa_q1", "dsa_kv")]
    order += [("dsa_prepare",), ("barrier", "dsa2")] + [("dsa_head", h) for h in range(DSA_H)]
    order += [("item", n) for n in ("gate10", "w_o10", "gate11", "w_o11")]
    order += [("barrier", "mem"), ("norm", "mem")]
    order += [("item", n) for n in ("mem_kv0", "mem_kv1", "mem_kv2", "mem_kv3", "mem_q0", "mem_q1")]
    order += [("mem_prepare",), ("barrier", "mem2")] + [("mem_head", h) for h in range(MEM_H)]
    order += [("item", n) for n in ("gate20", "w_o20", "gate21", "w_o21")]
    order += [("mix", "merged"), ("item", "w_out20"), ("item", "w_out21")]
    order += [("barrier", "experts"), ("norm", "ffn"), ("item", "router"), ("route",), ("item", "expert0")]
    for e in range(N_EXP):
        if e + 1 < N_EXP:
            order += [("item", f"expert{e + 1}")]
        order += [("item", f"down{e}0"), ("item", f"down{e}1")]
    return order


def sections_of(order):
    return ["start"] + [step[1] for step in order if step[0] == "barrier"]


NORMS = {"h": "ln_w", "h2": "g_mix_2", "ffn": "g_ffn_2", "mem": "g_mem_2"}


def program(nc, w, out, known):
    order = make_order()
    items = weight_items(w)
    units, first_unit = [], {}
    for step in order:
        if step[0] == "item":
            first_unit[step[1]] = len(units)
            units += items[step[1]]

    with ExitStack() as ctx:
        base = 16512

        def sb(name, shape, at_kb, dt=F32):
            assert base + at_kb * 1024 + 4 * int(np.prod(shape[1:])) <= nc.sbuf_usable_end, name
            return nc.alloc_sbuf_tensor_at(name, shape, dt, offset=base + round(at_kb * 32) * 32)

        def semaphore(name):
            return ctx.enter_context(nc.semaphore(name))

        ps = ctx.enter_context(nc.psum_tensor("ps", [P, 8, 512], F32))
        psf = ps[:, :, :].rearrange("p b n -> p (b n)")

        raw = sb("raw", [P, RAW_SLOTS, UNIT], 0)
        w_hi = sb("w_hi", [P, SPLIT_SLOTS, UNIT], 16, F32R)
        w_lo = sb("w_lo", [P, SPLIT_SLOTS, UNIT], 32, F32R)
        act_hi = sb("act_hi", [P, KC, L], 48, F32R)
        act_lo = sb("act_lo", [P, KC, L], 64.5, F32R)
        mix_hi = sb("mix_hi", [P, KC, SEQ], 81, F32R)
        mix_lo = sb("mix_lo", [P, KC, SEQ], 97, F32R)
        x1 = sb("x1", [P, NT, D], 113)
        gains = sb("gains", [P, 64], 129)
        ident = sb("ident", [P, P], 129.25)
        gla_mask = sb("gla_mask", [P, P], 129.75)
        dsa_mask = sb("dsa_mask", [P, P], 130.25)
        mask_q = sb("mask_q", [1, P], 130.75)
        mask_k = sb("mask_k", [1, CHUNK], 131.25)
        ones = sb("ones", [P, 2], 131.5)
        ss = sb("ss", [P, 8, 72], 131.75)
        sm = sb("sm", [P, 4, 32], 134)
        SC = 134.5
        xs = sb("xs", [P, NT, D], 81)
        meta = sb("meta", [N_META, D], 97)
        metas = sb("metas", [N_META, D], 101)
        g_rows = sb("g_rows", [64, P], 105)
        meta_t = sb("meta_t", [P, KC, N_META], 106)
        cx = sb("cx", [P, 2, L], SC)
        cb = sb("cb", [P, 2, SEQ], SC + 4.25)
        cu = sb("cu", [P, 2, L], SC + 8.25)
        cz = sb("cz", [P, 2, SEQ], SC + 12.5)
        cy = sb("cy", [P, 2, SEQ], SC + 16.5)
        q_sb = sb("q_sb", [P, NT, MLA_H * QKH], SC)
        k_sb = sb("k_sb", [P, NT + 1, MLA_H * QKH], SC + 12)
        v_sb = sb("v_sb", [P, NT + 1, MLA_H * VH], SC + 27)
        z_mla = sb("z_mla", [P, NT, MLA_H * VH], SC + 37)
        rqk = sb("rqk", [P, NT + 1, 512], SC + 45)
        rv = sb("rv", [P, NT + 1, 256], SC + 55)
        z_ret = sb("z_ret", [P, NT, 256], SC + 60)
        rope = sb("rope", [P, 5 * 96], SC + 64)
        kr = sb("kr", [P, NT + 1, QKR], SC + 66)
        qk_gain = sb("qk_gain", [P, 2, QKH], SC + 66.75)
        t0 = sb("t0", [P, 256], SC + 67.75)
        t1 = sb("t1", [P, 256], SC + 68.75)
        t2 = sb("t2", [P, 256], SC + 69.75)
        t3 = sb("t3", [P, 256], SC + 70.75)
        cos_m = rope[:, 0:80].rearrange("p (t n) -> p t n", t=5)
        sin_m = rope[:, 80:160].rearrange("p (t n) -> p t n", t=5)
        cos_r = rope[:, 160:320].rearrange("p (t n) -> p t n", t=5)
        sin_r = rope[:, 320:480].rearrange("p (t n) -> p t n", t=5)
        cq_sq = sb("cq_sq", [P, 2, SEQ], SC + 37)
        ckv_sq = sb("ckv_sq", [P, L], SC + 41)
        cq_hi = sb("cq_hi", [P, 2, SEQ], SC + 45, F32R)
        cq_lo = sb("cq_lo", [P, 2, SEQ], SC + 49, F32R)
        ckv_hi = sb("ckv_hi", [P, L], SC + 53, F32R)
        ckv_lo = sb("ckv_lo", [P, L], SC + 55.25, F32R)
        sq = sb("sq", [P, MLA_H * QKH], 81 + 8)
        qT = sb("qT", [P, 2, SEQ], 48)
        kT = sb("kT", [P, 2, L], 52)
        prob = sb("prob", [P, 2, L], 56.25)
        probT = sb("probT", [P, 2, SEQ], 60.5)
        probT_m = sb("probT_m", [N_META, 2, P], 64.5)
        y_mla = sb("y_mla", [P, NT, MLA_H * VH], 65.5)
        y_ret = sb("y_ret", [P, NT, 256], 73.5)
        ysq = sb("ysq", [P, NT, 256], SC)
        decay = sb("decay", [P, 2, SEQ], SC + 12)
        decay_m = sb("decay_m", [N_META, 2, SEQ], SC + 16)
        sd = sb("sd", [P, NT, SEQ], SC)
        sd_m = sb("sd_m", [N_META, SEQ], SC + 8)

        merged = sb("merged", [P, NT, D], SC)
        sm2 = sb("sm2", [P, NT, 88], SC + 16)
        gate = sb("gate", [P, NT, 512], SC + 17.5)
        gate_bias = sb("gate_bias", [P, 2, 512], SC + 25.5)
        gv = sb("gv", [P, NT, D], SC)
        gq = sb("gq", [P, GLA_H, SEQ], SC + 17.5)
        gk = sb("gk", [P, GLA_H, SEQ], SC + 25.5)
        go = sb("go", [P, NT, D], SC + 33.5)
        state = sb("state", [P, 8, GLA_DV], SC + 49.5)
        g_silu = sb("g_silu", [P, 2, 512], SC + 57.5)
        low_t = sb("low_t", [16, SEQ], SC + 61.5)
        w_a2 = sb("w_a2", [16, 512], SC + 63.5)
        scan_mask = sb("scan_mask", [P, SEQ], SC + 65.5)
        g_dec = sb("g_dec", [P, 2, 8], SC + 67.5)
        gz = sb("gz", [P, SEQ], 81)
        gab = sb("gab", [P, SEQ], 83)
        gex = sb("gex", [P, SEQ], 85)
        glc = sb("glc", [P, SEQ], 87)
        gsq = sb("gsq", [P, GLA_DV], 89)
        g_qd = sb("g_qd", [P, 2, SEQ], 90)
        g_ki = sb("g_ki", [P, 2, SEQ], 94)
        g_ke = sb("g_ke", [P, 2, SEQ], 98)
        g_keT = sb("g_keT", [P, 2, SEQ], 102)
        g_att = sb("g_att", [P, 2, SEQ], 106)
        dq = sb("dq", [P, NT, D], 81)
        dk = sb("dk", [P, NT, 256], 101)
        d_sq = sb("d_sq", [P, 2, 512], 97)
        ik2 = sb("ik2", [P, NT, P], 105)
        dqT = sb("dqT", [P, DSA_H, SEQ], SC + 17.5)
        iqT = sb("iqT", [P, 4, SEQ], SC + 33.5)
        dkT = sb("dkT", [P, 2, SEQ], SC + 41.5)
        dv = sb("dv", [P, NT, 256], SC + 45.5)
        ikT = sb("ikT", [P, SEQ], SC + 49.5)
        d_mask = sb("d_mask", [P, 1280], SC + 51.5)
        work = sb("work", [P, 3, SEQ], SC + 56.5)
        rel = sb("rel", [P, 2, SEQ], SC + 62.5)
        d_probT = sb("d_probT", [P, 2, SEQ], SC + 62.5)
        d_prob = sb("d_prob", [P, 2, SEQ], SC + 66.5)
        best8 = sb("best8", [P, 8], SC + 70.5)
        mem_in = sb("mem_in", [P, 2, D], 81)
        mem_sc = sb("mem_sc", [P, 2, D], 89)
        mk = sb("mk", [P, 2, D], SC + 17.5)
        mv = sb("mv", [P, 2, D], SC + 25.5)
        mkT = sb("mkT", [P, 8, MEM], SC + 33.5)
        mem_hi = sb("mem_hi", [P, KC, MEM], SC + 41.5, F32R)
        mem_lo = sb("mem_lo", [P, KC, MEM], SC + 49.5, F32R)
        mqT = sb("mqT", [P, 8, SEQ], SC + 41.5)
        m_prob = sb("m_prob", [P, 2, MEM], SC + 57.5)
        m_probT = sb("m_probT", [P, 2, MEM], SC + 59.5)
        hid_hi = sb("hid_hi", [P, 2, 2, SEQ], SC, F32R)
        hid_lo = sb("hid_lo", [P, 2, 2, SEQ], SC + 8, F32R)
        hid = sb("hid", [P, 2, SEQ], SC + 16)
        e_silu = sb("e_silu", [P, 2, SEQ], SC + 20)
        rl = sb("rl", [P, NT, 20], SC + 24)
        r_bias = sb("r_bias", [P, 20], SC + 24.5)
        rank = sb("rank", [P, 4], SC + 24.625)
        rt = sb("rt", [P, 16, 16], SC + 24.75)
        combine = sb("combine", [P, NT, N_EXP], SC + 26)

        bias_in = [semaphore(f"bias_in{i}") for i in range(2)]
        gla_in = semaphore("gla_in")
        mem_landed = semaphore("mem_landed")
        route_in = semaphore("route_in")
        w_landed = [semaphore(f"w_landed{i}") for i in range(RAW_SLOTS)]
        landed, total = [], [0] * RAW_SLOTS
        for g, (_, _, pieces) in enumerate(units):
            total[g % RAW_SLOTS] += 16 * len(pieces)
            landed.append(total[g % RAW_SLOTS])
        const_in = semaphore("const_in")
        gains_in = semaphore("gains_in")
        zeroed = semaphore("zeroed")
        x_in = semaphore("x_in")
        rope_in = semaphore("rope_in")
        decay_in = [semaphore(f"decay_in{i}") for i in range(2)]
        stored = semaphore("stored")

        LAST = order[-1][1]
        sections = sections_of(order)
        PE = Progress(nc, ctx, "tensor", sections, known)
        ACT = Progress(nc, ctx, "scalar", sections, known)
        DVE = Progress(nc, ctx, "vector", sections, known)
        POOL = Progress(nc, ctx, "gpsimd", sections, known)

        def col(gain, n=0):
            return gains[:, GAINS[gain] + n:GAINS[gain] + n + 1]

        NORM_TILES = {"h": [(x1[:, t, :], xs[:, t, :], P) for t in range(NT)] + [(meta[:, :], metas[:, :], N_META)],
                      "h2": [(x1[:, t, :], xs[:, t, :], P) for t in range(NT)],
                      "ffn": [(x1[:, t, :], xs[:, t, :], P) for t in range(NT)],
                      "mem": [(mem_in[:, t, :], mem_sc[:, t, :], P) for t in range(2)]}

        def barrier(eng, section):
            before = sections[sections.index(section) - 1]
            for other in (PE, ACT, DVE, POOL):
                if other.ends.get(before, 1):
                    eng.wait_ge(*other.end_of(before))


        def last_scores(tag, h):
            return ("S", "mla", NT * h + NT - 1) if tag == "mla" else ("rS", h, NT - 1)

        def idx_of(i):
            return 1 + i // IDX_H, i % IDX_H

        def state_bank(n):
            return 2 * (n % 2) + n // 4, slice(GLA_DV * (n // 2 % 2), GLA_DV * (n // 2 % 2 + 1))

        def norm_dest(name):
            return (mem_hi, 0) if name == "mem" else (act_hi, N_META)

        def norm_lo(name):
            return mem_lo

        def MIX_NEEDS(tag, c, t):
            return DVE.after("go", c // 4, t, c // 2 % 2) if tag == "gla" else DVE.after("merged", 2, c // 4, t)

        def NORM_NEEDS(name, i):
            return []

        def ITEM_NEEDS(name):
            if name in ("conv_a", "conv_b", "latent", "k_rope", "mla_z", "ret_qk", "ret_vz"):
                return [(DVE, ("lo", "h", KC - 1)), (DVE, ("meta_lo", "h"))]
            if name.startswith("w_uq"):
                return [(DVE, ("cq_lo", 1))]
            if name.startswith("w_ukv"):
                return [(DVE, ("ckv_lo", "meta"))]
            if name in ("w_out0", "w_out1"):
                return [(DVE, ("conv_lo", 1)), (DVE, ("mix_lo", KC - 1))]
            if name.startswith(("small2", "gla", "gate", "idx", "dsa", "mem_q")):
                return [(DVE, ("lo", "h2", KC - 1))]
            if name.startswith("mem_kv"):
                return [(DVE, ("lo", "mem", KC - 1))]
            if name.startswith("w_o0"):
                return [(DVE, ("mix_lo", "gla", KC - 1))]
            if name.startswith("w_o1"):
                return [(DVE, ("mix_lo", "dsa", KC - 1))]
            if name.startswith("w_out2"):
                return [(DVE, ("mix_lo", "merged", KC - 1))]
            if name.startswith("w_o2"):
                return [(DVE, ("mix_lo", "mem", KC - 1))]
            if name.startswith(("router", "expert")):
                return [(DVE, ("lo", "ffn", KC - 1))]
            if name.startswith("down"):
                return [(DVE, ("hid_lo", int(name[4:-1]), 1))]
            raise KeyError(name)

        def item_readers(name, b):
            n = int(name[-1]) if name[-1].isdigit() else 0
            if name == "conv_a":
                return [(ACT, ("cx", "meta"))] if b == "meta" else [(ACT, ("cx", b) if b < 2 else ("cb", b - 2))]
            if name == "conv_b":
                return [(DVE, ("cu", "meta"))] if b == "meta" else [(DVE, ("cu", b)) if b < 2 else (ACT, ("cz", b - 2))]
            if name == "latent":
                return [(DVE, ("ckv_lo", "meta"))] if b == "meta" else [(DVE, ("cq_lo", b) if b < 2 else ("ckv_lo",))]
            if name == "k_rope":
                return [(ACT, ("kr",))]
            if name.startswith("w_uq"):
                return [(ACT, ("q_raw", n, b))]
            if name.startswith("w_ukv"):
                return [(DVE, ("v_raw", n, b))]
            if name == "mla_z":
                return [(ACT, ("z_mla", b))]
            if name == "ret_qk":
                return [(DVE, ("rope_r", b, 3))]
            if name == "ret_vz":
                return [(ACT, ("z_ret", b) if b < NT else ("rv", b))]
            if name in ("w_out0", "w_out1"):
                return [(DVE, ("x", name, b))]
            if name.startswith("w_out2"):
                return [(DVE, ("x", name, b))]
            if name == "small2":
                return [(ACT, ("sm2",))]
            if name in ("gla_q", "gla_k"):
                return [(ACT, (name, b))]
            if name.startswith("gla_v"):
                return [(ACT, ("gv", n, b))]
            if name.startswith("gla_g"):
                return [(ACT, ("g_silu", n, b))]
            if name.startswith("gate"):
                return [(DVE, ("gate_sum", int(name[4]), n, b))]
            if name.startswith("w_o"):
                return [(DVE, ("gated", int(name[3]), n, b))]
            if name == "idx_q":
                return [(ACT, ("iqT", b))]
            if name.startswith("dsa_q"):
                return [(ACT, ("dq", n, b))]
            if name == "dsa_kv":
                return [(ACT, ("dv", b))]
            if name.startswith("mem_kv"):
                return [(ACT, ("mkv", n, b))]
            if name.startswith("mem_q"):
                return [(ACT, ("mq", n, b))]
            if name == "router":
                return [(DVE, ("rl",))]
            if name.startswith("expert"):
                e = int(name[6:])
                return [(ACT, ("e_silu", e, b)) if b < 2 else (DVE, ("hid", e, b - 2))]
            if name.startswith("down"):
                return [(DVE, ("x", name, b))]
            raise KeyError(name)

        block = ctx.enter_context(nc.Block())

        @block.sync
        def _(sp):
            for t in range(NT):
                sp.dma_start(x1[:, t, :], w["x"][0, P * t:P * (t + 1), :]).then_inc(x_in, 16)
            sp.dma_start(meta[:, :], w["meta_tokens"]).then_inc(x_in, 16)
            sp.dma_start(ident[:, :], w["c_ident"]).then_inc(const_in, 16)
            sp.dma_start(gla_mask[:, :], w["c_gla_mask"]).then_inc(const_in, 16)
            sp.dma_start(dsa_mask[:, :], w["c_dsa_mask"]).then_inc(const_in, 16)
            sp.dma_start(mask_q[:, :], w["c_mask_q"]).then_inc(const_in, 16)
            sp.dma_start(mask_k[:, :], w["c_mask_k"]).then_inc(const_in, 16)
            sp.dma_start(rope[:, :], w["c_rope"]).then_inc(rope_in, 16)
            sp.dma_start(qk_gain[:, 0, :], w["q_norm"][0].partition_broadcast(P)).then_inc(rope_in, 16)
            sp.dma_start(qk_gain[:, 1, :], w["k_norm"][0].partition_broadcast(P)).then_inc(rope_in, 16)
            for g, (chunks, n, pieces) in enumerate(units):
                if g >= RAW_SLOTS:
                    sp.wait_ge(*POOL.after("w_lo", g - RAW_SLOTS))
                slot = raw[:, g % RAW_SLOTS, 0:len(chunks) * n].rearrange("p (k n) -> p k n", n=n)
                for a, b, src in pieces:
                    sp.dma_start(slot[:, :, a:b], src).then_inc(w_landed[g % RAW_SLOTS], 16)
            for t in range(NT):
                sp.wait_ge(*DVE.after("x", LAST, t))
                sp.dma_start(out[0, P * t:P * (t + 1), :], x1[:, t, :]).then_inc(stored, 16)
            sp.wait_ge(stored, 16 * NT)

        @block.gpsimd
        def _(pool):
            pool.memset(g_rows[:, :], 0.0).then_inc(zeroed, 1)
            pool.memset(ones[:, :], 1.0).then_inc(zeroed, 1)
            pool.wait_ge(zeroed, 2)
            for name, row in GAINS.items():
                src = w[name]
                src = src if name == "conv_w" else src[0]
                if name in ("ret_norm", "idx_k_norm_2"):
                    for half in range(2):
                        pool.dma_start(g_rows[row:row + 1, 64 * half:64 * half + 64], w[name]).then_inc(gains_in, 16)
                elif name == "conv_w":
                    pool.dma_start(g_rows[row:row + 6, :], src[0].rearrange("j (c p) -> (j c) p", p=P)).then_inc(gains_in, 16)
                else:
                    n = src.shape[0] // P
                    pool.dma_start(g_rows[row:row + n, :], src.rearrange("(c p) -> c p", p=P)).then_inc(gains_in, 16)
            fill = [0]

            def split_low(upto):
                for g in range(fill[0], upto):
                    chunks, n, _ = units[g]
                    a = len(chunks) * n
                    pool.wait_ge(*ACT.after("w_hi", g))
                    pool.tensor_tensor(w_lo[:, g % SPLIT_SLOTS, 0:a], raw[:, g % RAW_SLOTS, 0:a],
                                       w_hi[:, g % SPLIT_SLOTS, 0:a].bitcast(F32),
                                       ALU.subtract).then_inc(*POOL.done(("w_lo", g)))
                fill[0] = max(fill[0], upto)

            for step, *a in order:
                if step == "barrier":
                    barrier(pool, a[0])
                    POOL.section = a[0]
                elif step == "item":
                    split_low(min(len(units), first_unit[a[0]] + len(items[a[0]]) + 2))

        n_gain_dmas = len(GAINS) + 2

        @block.tensor
        def _(pe):
            readers = {b: [] for b in range(8)}

            def claim(bank, *who):
                for engine, key in readers[bank]:
                    pe.wait_ge(*engine.after(*key))
                readers[bank] = list(who)

            def product(dst, l_hi, l_lo, r_hi, r_lo, start, stop, skip=False):
                pe.matmul(dst, l_hi, r_hi, start=start, stop=False, skip_group_check=skip)
                pe.matmul(dst, l_hi, r_lo, start=False, stop=False, skip_group_check=skip)
                return pe.matmul(dst, l_lo, r_hi, start=False, stop=stop, skip_group_check=skip)

            def item(name):
                its = items[name]
                g0 = first_unit[name]
                meta_blocks = {"conv_a": 2, "conv_b": 2, "latent": 1}.get(name, 0)
                n_acc = {"latent": 3, "mem_kv0": 2, "mem_kv1": 2, "mem_kv2": 2, "mem_kv3": 2}.get(name, NT)
                by_feature = name in ("conv_a", "conv_b", "latent", "gla_q", "gla_k", "idx_q") or name.startswith("expert")
                small = name in ("k_rope", "small2", "router")
                meta_row = name in ("k_rope", "w_ukv0", "w_ukv1", "ret_qk", "ret_vz")
                if name.startswith("w_uq"):
                    a_hi, a_lo, off = cq_hi, cq_lo, 0
                elif name.startswith("w_ukv"):
                    a_hi, a_lo, off = ckv_hi[:, :].unsqueeze(1), ckv_lo[:, :].unsqueeze(1), N_META
                elif name.startswith("w_o"):
                    a_hi, a_lo, off = mix_hi, mix_lo, 0
                elif name.startswith("mem_kv"):
                    a_hi, a_lo, off = mem_hi, mem_lo, 0
                elif name.startswith("down"):
                    e = int(name[4:-1])
                    a_hi, a_lo, off = hid_hi[:, e % 2, :, :], hid_lo[:, e % 2, :, :], 0
                else:
                    a_hi, a_lo, off = act_hi, act_lo, N_META
                for key in ITEM_NEEDS(name):
                    pe.wait_ge(*key[0].after(*key[1]))
                last_u = len(its) - 1
                for u, (chunks, n, _) in enumerate(its):
                    g = g0 + u
                    pe.wait_ge(*POOL.after("w_lo", g))
                    wh = w_hi[:, g % SPLIT_SLOTS, 0:len(chunks) * n].rearrange("p (k n) -> p k n", n=n)
                    wl = w_lo[:, g % SPLIT_SLOTS, 0:len(chunks) * n].rearrange("p (k n) -> p k n", n=n)
                    n_all = n_acc + meta_row
                    for b in range(n_all):
                        bank = 5 if small else (4 + b if name.startswith("down") else b)
                        if u == 0 and (b == 0 or not small):
                            claim(bank, *item_readers(name, b))
                        for j, k in enumerate(chunks):
                            first = u == 0 and j == 0 and (b == 0 or not small)
                            last = u == last_u and j == len(chunks) - 1
                            if by_feature:
                                cols = slice(P * b, P * b + P)
                                mm = product(ps[:, bank, :], wh[:, j, cols], wl[:, j, cols],
                                             a_hi[:, k, off:off + SEQ], a_lo[:, k, off:off + SEQ], first, last)
                            else:
                                rows = slice(off + P * b, off + P * b + P) if b < NT else slice(0, P)
                                dst = ps[:, bank, n * b:n * b + n] if small else ps[:, bank, 0:n]
                                mm = product(dst, a_hi[:, k, rows], a_lo[:, k, rows], wh[:, j, :], wl[:, j, :],
                                             first, last, skip=small)
                        keys = [("unit", g)] if b == n_all - 1 and not meta_blocks else []
                        if u == last_u:
                            keys.append(("acc", name, b))
                        if keys:
                            mm.then_inc(*PE.done(*keys))
                    for b in range(meta_blocks):
                        if u == 0 and b == 0:
                            claim(4, *item_readers(name, "meta"))
                        for j, k in enumerate(chunks):
                            at = P * (b + (2 if name == "latent" else 0))
                            cols = slice(at, at + P)
                            mm = product(ps[:, 4, N_META * b:N_META * (b + 1)], wh[:, j, cols], wl[:, j, cols],
                                         a_hi[:, k, 0:N_META], a_lo[:, k, 0:N_META],
                                         u == 0 and j == 0 and b == 0, u == last_u and j == len(chunks) - 1, skip=True)
                    if meta_blocks:
                        mm.then_inc(*PE.done(("unit", g), *([("acc", name, "meta")] if u == last_u else [])))

            def norm(name):
                tiles = NORM_TILES[name]
                full = [t for t in tiles if t[2] == P]
                for k in range(KC):
                    bank = 4 + k % 4
                    claim(bank, (DVE, ("lo", name, k)))
                    for i, (_, scaled, _) in enumerate(full):
                        pe.wait_ge(*DVE.after("scaled", name, i))
                        tr = pe.transpose(ps[:, bank, P * i:P * i + P], scaled[:, P * k:P * k + P], ident[:, :])
                    tr.then_inc(*PE.done(("T", name, k)))
                if len(full) < len(tiles):
                    claim(3, (DVE, ("meta_t", name)))
                    pe.wait_ge(*DVE.after("scaled", name, len(full)))
                    for k in range(KC):
                        tr = pe.transpose(ps[:, 3, N_META * k:N_META * (k + 1)], tiles[-1][1][:, P * k:P * k + P],
                                          ident[0:N_META, 0:N_META])
                    tr.then_inc(*PE.done(("T", name, "meta")))

            def attention_transposes(tag, h, width, q_src, k_src):
                claim(6, (ACT, ("qT", tag, h)))
                for t in range(NT):
                    tr = pe.transpose(ps[0:width, 6, P * t:P * t + P], q_src(t), ident[:, :])
                tr.then_inc(*PE.done(("qT", tag, h)))
                claim(4, (DVE, ("kT", tag, h)))
                claim(5, (DVE, ("kT", tag, h)))
                pe.transpose(ps[0:width, 4, SEQ - N_META:SEQ], k_src(NT)[0:N_META, :], ident[0:N_META, 0:N_META])
                for t in range(NT):
                    tr = pe.transpose(ps[0:width, 5, P * t:P * t + P], k_src(t), ident[:, :])
                tr.then_inc(*PE.done(("kT", tag, h)))

            def mla_scores(j):
                h, t = divmod(j, NT)
                n = P * (t + 1)
                if t == 0:
                    pe.wait_ge(*ACT.after("qT", "mla", h))
                    pe.wait_ge(*DVE.after("kT", "mla", h))
                claim(4, (ACT, ("exp", "mla", j)))
                claim(5, (ACT, ("exp", "mla", j)))
                q = qT[0:QKH, h % 2, P * t:P * t + P]
                pe.matmul(ps[:, 4, SEQ - N_META:SEQ], q, kT[0:QKH, h % 2, 0:N_META], start=True, stop=True)
                pe.matmul(ps[:, 5, 0:n], q, kT[0:QKH, h % 2, N_META:N_META + n], start=True, stop=False)
                pe.matmul(ps[:, 5, n - CHUNK:n], mask_q[:, :], mask_k[:, :], start=False,
                          stop=True).then_inc(*PE.done(("S", "mla", j)))

            def mla_prob_transposes(j):
                h, t = divmod(j, NT)
                pe.wait_ge(*ACT.after("exp", "mla", j))
                claim(7, (DVE, ("PTm", "mla", j)))
                pe.transpose(ps[0:N_META, 7, 0:P], prob[:, j % 2, 0:N_META], ident[:, :]).then_inc(*PE.done(("PTm", "mla", j)))
                claim(6, (ACT, ("PT", "mla", j)))
                for b in range(t + 1):
                    tr = pe.transpose(ps[:, 6, P * b:P * b + P], prob[:, j % 2, N_META + P * b:N_META + P * (b + 1)], ident[:, :])
                tr.then_inc(*PE.done(("PT", "mla", j)))

            def mla_values(j):
                h, t = divmod(j, NT)
                pe.wait_ge(*ACT.after("PT", "mla", j))
                claim(7, (DVE, ("y", "mla", j)))
                pe.matmul(ps[:, 7, P:P + VH], probT_m[:, j % 2, :], v_sb[0:N_META, NT, VH * h:VH * (h + 1)], start=True, stop=False)
                for b in range(t + 1):
                    mm = pe.matmul(ps[:, 7, P:P + VH], probT[:, j % 2, P * b:P * b + P], v_sb[:, b, VH * h:VH * (h + 1)],
                                   start=False, stop=(b == t))
                mm.then_inc(*PE.done(("O", "mla", j)))

            def mla_head(h):
                attention_transposes("mla", h, QKH, lambda t: q_sb[:, t, QKH * h:QKH * (h + 1)],
                                     lambda t: k_sb[:, t, QKH * h:QKH * (h + 1)])
                for j in range(NT * h, NT * (h + 1)):
                    mla_scores(j)
                    mla_prob_transposes(j)
                    mla_values(j)

            def ret_head(h):
                attention_transposes("ret", h, RET_D, lambda t: rqk[:, t, RET_D * h:RET_D * (h + 1)],
                                     lambda t: rqk[:, t, 256 + RET_D * h:256 + RET_D * (h + 1)])
                pe.wait_ge(*ACT.after("qT", "ret", h))
                pe.wait_ge(*DVE.after("kT", "ret", h))
                claim(7, (DVE, ("sd", h, "meta")))
                pe.matmul(ps[0:N_META, 7, :], kT[0:RET_D, h % 2, 0:N_META], qT[0:RET_D, h % 2, :],
                          start=True, stop=True).then_inc(*PE.done(("rS", h, "meta")))
                for b in range(NT):
                    claim(b, (DVE, ("sd", h, b)))
                    pe.matmul(ps[:, b, P * b:SEQ], kT[0:RET_D, h % 2, N_META + P * b:N_META + P * (b + 1)],
                              qT[0:RET_D, h % 2, P * b:SEQ], start=True, stop=True).then_inc(*PE.done(("rS", h, b)))
                pe.wait_ge(*DVE.after("sd", h, "meta"))
                claim(5, (ACT, ("rO", h)))
                for t in range(NT):
                    dst = ps[:, 5, RET_D * t:RET_D * (t + 1)]
                    pe.matmul(dst, sd_m[:, P * t:P * t + P], rv[0:N_META, NT, RET_D * h:RET_D * (h + 1)], start=True, stop=False)
                    for b in range(t + 1):
                        pe.wait_ge(*DVE.after("sd", h, b))
                        mm = pe.matmul(dst, sd[:, b, P * t:P * t + P], rv[:, b, RET_D * h:RET_D * (h + 1)],
                                       start=False, stop=(b == t))
                mm.then_inc(*PE.done(("rO", h)))

            def gla_low():
                pe.wait_ge(*ACT.after("sm2"))
                claim(6, (ACT, ("low_t",)))
                for t in range(NT):
                    tr = pe.transpose(ps[0:16, 6, P * t:P * t + P], sm2[:, t, 0:16], ident[:, :])
                tr.then_inc(*PE.done(("low_t",)))

            def gla_head(h):
                if h == 0:
                    pe.wait_ge(gla_in, 32)
                    pe.wait_ge(*ACT.after("low_t"))
                    for t in range(NT):
                        pe.wait_ge(*ACT.after("gv", 0, t))
                        pe.wait_ge(*ACT.after("gv", 1, t))
                s = h % 2
                claim(7, (ACT, ("g_z", h)))
                pe.matmul(ps[:, 7, :], w_a2[:, P * h:P * h + P], low_t[:, :], start=True,
                          stop=True).then_inc(*PE.done(("g_z", h)))
                claim(6, (ACT, ("g_keT", h)))
                pe.wait_ge(*DVE.after("g_ke", h))
                for t in range(NT):
                    tr = pe.transpose(ps[:, 6, P * t:P * t + P], g_ke[:, s, P * t:P * t + P], ident[:, :])
                tr.then_inc(*PE.done(("g_keT", h)))
                claim(7, (DVE, ("g_att", h)))
                for t in range(NT):
                    mm = pe.matmul(ps[:, 7, P * t:P * t + P], g_ki[:, s, P * t:P * t + P], g_qd[:, s, P * t:P * t + P],
                                   start=True, stop=True)
                mm.then_inc(*PE.done(("g_att", h)))
                pe.wait_ge(*ACT.after("g_keT", h))
                for pair in ((0, 2), (1, 3), (4, 6), (5,)):
                    bank = state_bank(pair[0])[0]
                    claim(bank, (DVE, ("g_state", h, pair[-1])))
                    for n in pair:
                        rows = slice(CHUNK * (n % 2), CHUNK * (n % 2) + CHUNK)
                        mm = pe.matmul(ps[:, bank, state_bank(n)[1]], g_keT[rows, s, P * (n // 2):P * (n // 2) + P],
                                       gv[rows, n // 2, GLA_DV * h:GLA_DV * (h + 1)], start=True, stop=True)
                    mm.then_inc(*PE.done(("g_upd", h, bank)))
                pe.wait_ge(*DVE.after("g_att", h))
                for t in range(NT):
                    bank = 4 + t % 2
                    claim(bank, (ACT, ("g_oss", h, t)))
                    dst = ps[:, bank, 0:GLA_DV]
                    v = gv[:, t, GLA_DV * h:GLA_DV * (h + 1)]
                    if t == 0:
                        pe.matmul(ps[0:CHUNK, bank, 0:GLA_DV], g_att[:, s, 0:CHUNK], v, start=True, stop=True)
                        pe.matmul(ps[CHUNK:P, bank, 0:GLA_DV], g_att[:, s, CHUNK:P], v, start=True, stop=False)
                    else:
                        pe.matmul(dst, g_att[:, s, P * t:P * t + P], v, start=True, stop=False)
                    for half in range(2):
                        n = 2 * t + half
                        if n == 0:
                            continue
                        pe.wait_ge(*DVE.after("g_state", h, n - 1))
                        rows = slice(CHUNK * half, CHUNK * half + CHUNK)
                        mm = pe.matmul(ps[rows, bank, 0:GLA_DV], g_qd[:, s, CHUNK * n:CHUNK * (n + 1)], state[:, n, :],
                                       start=False, stop=True)
                    mm.then_inc(*PE.done(("g_o", h, t)))

            def mix(tag):
                for c in range(KC):
                    bank = 4 + c % 4
                    claim(bank, (DVE, ("mix_lo", tag, c)))
                    for t in range(NT):
                        pe.wait_ge(*MIX_NEEDS(tag, c, t))
                        src = go if tag == "gla" else merged
                        tr = pe.transpose(ps[:, bank, P * t:P * t + P], src[:, t, P * c:P * c + P], ident[:, :])
                    tr.then_inc(*PE.done(("mixT", tag, c)))

            def idx_key():
                claim(6, (ACT, ("ikT",)))
                for t in range(NT):
                    pe.wait_ge(*DVE.after("ik2", t))
                    tr = pe.transpose(ps[:, 6, P * t:P * t + P], ik2[:, t, :], ident[:, :])
                tr.then_inc(*PE.done(("ikT",)))

            def idx_scores(t):
                n = P * (t + 1)
                pe.wait_ge(*ACT.after("ikT"))
                for h in range(IDX_H):
                    bank = 4 + h % 4
                    pe.wait_ge(*ACT.after("iqT", h // 2))
                    claim(bank, (ACT, ("rel", t, h)))
                    rows = slice(IDX_D * (h % 2), IDX_D * (h % 2) + IDX_D)
                    pe.matmul(ps[:, bank, 0:n], iqT[rows, h // 2, P * t:P * t + P], ikT[rows, 0:n], start=True,
                              stop=True).then_inc(*PE.done(("rel", t, h)))

            def head_transposes(tag, c, src, last_needed):
                bank = 4 + c % 4
                claim(bank, (ACT, (tag, c)))
                for t in range(len(src)):
                    pe.wait_ge(*DVE.after(*last_needed[t]))
                    tr = pe.transpose(ps[:, bank, P * t:P * t + P], src[t], ident[:, :])
                tr.then_inc(*PE.done((tag, c)))

            def dsa_prepare():
                for c in range(DSA_H):
                    head_transposes("dqT", c, [dq[:, t, P * c:P * c + P] for t in range(NT)],
                                    [("dqn", t) for t in range(NT)])
                for c in range(2):
                    head_transposes("dkT", c, [dk[:, t, P * c:P * c + P] for t in range(NT)],
                                    [("dkn", t) for t in range(NT)])

            def dsa_scores(j):
                h, t = divmod(j, NT)
                n = P * (t + 1)
                claim(4 + j % 2, (DVE, ("d_max", j)))
                pe.matmul(ps[:, 4 + j % 2, 0:n], dqT[:, h, P * t:P * t + P], dkT[:, h // DSA_G, 0:n], start=True,
                          stop=True).then_inc(*PE.done(("d_S", j)))

            def dsa_transposes(j):
                pe.wait_ge(*DVE.after("d_norm", j))
                claim(6, (ACT, ("d_PT", j)))
                for b in range(j % NT + 1):
                    tr = pe.transpose(ps[:, 6, P * b:P * b + P], d_prob[:, j % 2, P * b:P * b + P], ident[:, :])
                tr.then_inc(*PE.done(("d_PT", j)))

            def dsa_values(j):
                h, t = divmod(j, NT)
                g = h // DSA_G
                pe.wait_ge(*ACT.after("d_PT", j))
                if t == 0:
                    claim(7, (DVE, ("mix_lo", "dsa", h)))
                for b in range(t + 1):
                    mm = pe.matmul(ps[:, 7, P * t:P * t + P], dv[:, b, P * g:P * g + P], d_probT[:, j % 2, P * b:P * b + P],
                                   start=(b == 0), stop=(b == t))
                mm.then_inc(*PE.done(("d_O", j)))

            def dsa_head(h):
                for j in range(NT * h, NT * (h + 1)):
                    if j == 0:
                        dsa_scores(0)
                    if j + 1 < NT * DSA_H:
                        dsa_scores(j + 1)
                    dsa_transposes(j)
                    dsa_values(j)

            def mem_prepare():
                for c in range(KC):
                    head_transposes("mkT", c, [mk[:, t, P * c:P * c + P] for t in range(2)], [("mkn", t) for t in range(2)])
                for c in range(KC):
                    head_transposes("mqT", c, [dq[:, t, P * c:P * c + P] for t in range(NT)], [("mqn", t) for t in range(NT)])

            def mem_scores(j):
                h, t = divmod(j, NT)
                claim(4 + j % 2, (ACT, ("m_exp", j)))
                for c in range(2):
                    mm = pe.matmul(ps[:, 4 + j % 2, 0:MEM], mqT[:, 2 * h + c, P * t:P * t + P], mkT[:, 2 * h + c, :],
                                   start=(c == 0), stop=(c == 1))
                mm.then_inc(*PE.done(("m_S", j)))

            def mem_head(h):
                for j in range(NT * h, NT * (h + 1)):
                    t = j % NT
                    if j == 0:
                        mem_scores(0)
                    if j + 1 < NT * MEM_H:
                        mem_scores(j + 1)
                    pe.wait_ge(*DVE.after("m_norm", j))
                    claim(6, (ACT, ("m_PT", j)))
                    for b in range(2):
                        tr = pe.transpose(ps[:, 6, P * b:P * b + P], m_prob[:, j % 2, P * b:P * b + P], ident[:, :])
                    tr.then_inc(*PE.done(("m_PT", j)))
                    pe.wait_ge(*ACT.after("m_PT", j))
                    for c in range(2):
                        bank = 7 if c == 0 else 3
                        if t == 0:
                            claim(bank, (DVE, ("mix_lo", "mem", 2 * h + c)))
                        for b in range(2):
                            mm = pe.matmul(ps[:, bank, P * t:P * t + P], mv[:, b, 2 * P * h + P * c:2 * P * h + P * (c + 1)],
                                           m_probT[:, j % 2, P * b:P * b + P], start=(b == 0), stop=(b == 1))
                    mm.then_inc(*PE.done(("m_O", j)))

            def latent_sums():
                pe.wait_ge(zeroed, 2)
                pe.wait_ge(*ACT.after("latent_sq", "meta"))
                claim(6, (DVE, ("lat_v",)))
                for t in range(NT):
                    for c in range(2):
                        pe.matmul(ps[:, 6, t:t + 1], cq_sq[:, c, P * t:P * t + P], ones[:, 0:1], start=(c == 0), stop=(c == 1))
                for t in range(NT):
                    pe.matmul(ps[:, 6, NT + t:NT + t + 1], ckv_sq[:, N_META + P * t:N_META + P * (t + 1)], ones[:, 0:1],
                              start=True, stop=True)
                pe.matmul(ps[0:N_META, 6, 8:9], ckv_sq[:, 0:N_META], ones[:, 0:1], start=True,
                          stop=True).then_inc(*PE.done(("lat_ss",)))

            def mix_one():
                for c in range(6):
                    bank = 6 + c % 2
                    claim(bank, (DVE, ("mix_lo", 2 + c)))
                    for t in range(NT):
                        if c < 4:
                            src = y_mla[:, t, P * c:P * c + P]
                        else:
                            pe.wait_ge(*DVE.after("y_ret", t))
                            src = y_ret[:, t, P * (c - 4):P * (c - 3)]
                        tr = pe.transpose(ps[:, bank, P * t:P * t + P], src, ident[:, :])
                    tr.then_inc(*PE.done(("mixT", 2 + c)))

            pe.wait_ge(const_in, 80)
            for step, *a in order:
                if step == "constants":
                    pe.wait_ge(gains_in, 16 * n_gain_dmas)
                    claim(7, (DVE, ("gains",)))
                    pe.transpose(ps[:, 7, 0:64], g_rows[:, :], ident[0:64, 0:64]).then_inc(*PE.done(("gains",)))
                elif step == "item":
                    item(*a)
                elif step == "norm":
                    norm(*a)
                elif step == "latent_sums":
                    latent_sums()
                elif step == "mla_head":
                    mla_head(*a)
                elif step == "ret_head":
                    ret_head(*a)
                elif step == "mix_one":
                    mix_one()
                elif step == "gla_low":
                    gla_low(*a)
                elif step == "gla_head":
                    gla_head(*a)
                elif step == "mix":
                    mix(*a)
                elif step == "idx_key":
                    idx_key(*a)
                elif step == "idx_scores":
                    idx_scores(*a)
                elif step == "dsa_prepare":
                    dsa_prepare(*a)
                elif step == "dsa_head":
                    dsa_head(*a)
                elif step == "mem_prepare":
                    mem_prepare(*a)
                elif step == "mem_head":
                    mem_head(*a)
                elif step == "barrier":
                    barrier(pe, a[0])
                    PE.section = a[0]

        @block.scalar
        def _(act):
            fill = [0]

            def split_high(upto):
                for g in range(fill[0], upto):
                    chunks, n, _ = units[g]
                    a = len(chunks) * n
                    act.wait_ge(w_landed[g % RAW_SLOTS], landed[g])
                    if g >= SPLIT_SLOTS:
                        act.wait_ge(*PE.after("unit", g - SPLIT_SLOTS))
                    nc.scalar.activation(w_hi[:, g % SPLIT_SLOTS, 0:a], raw[:, g % RAW_SLOTS, 0:a],
                                         ACTF.Copy).then_inc(*ACT.done(("w_hi", g)))
                fill[0] = max(fill[0], upto)

            def rsqrt_start(key, v):
                act.wait_ge(*DVE.after("v", *key))
                nc.scalar.activation(v[1], v[0], ACTF.Ln).then_inc(*ACT.done(("ln", *key)))
                act.wait_ge(*ACT.after("ln", *key))
                nc.scalar.activation(v[1], v[1], ACTF.Exp, scale=-0.5).then_inc(*ACT.done(("y0", *key)))

            def norm(name):
                tiles = NORM_TILES[name]
                if name == "h":
                    act.wait_ge(x_in, 80)
                if name == "mem":
                    act.wait_ge(mem_landed, 32)
                act.wait_ge(*DVE.after("ss0", name))
                for i, (src, scaled, rows) in enumerate(tiles):
                    for key in NORM_NEEDS(name, i):
                        act.wait_ge(*key[0].after(*key[1]))
                    nc.scalar.activation(scaled, src, ACTF.Square,
                                         accum_out=ss[0:rows, 0, i:i + 1]).then_inc(*ACT.done(("ss", name, i)))
                n = len(tiles)
                rsqrt_start((name,), (ss[:, 1, 0:n], ss[:, 2, 0:n]))
                n = sum(t[2] == P for t in tiles) * P
                hi, off = norm_dest(name)
                for k in range(KC):
                    act.wait_ge(*PE.after("T", name, k))
                    nc.scalar.activation(hi[:, k, off:off + n], ps[:, 4 + k % 4, 0:n], ACTF.Copy,
                                         scale=col(NORMS[name], k)).then_inc(*ACT.done(("hi", name, k)))
                if name == "h":
                    act.wait_ge(*DVE.after("meta_t", name))
                    nc.scalar.activation(act_hi[:, :, 0:N_META], meta_t[:, :, :], ACTF.Copy).then_inc(*ACT.done(("meta_hi", name)))

            def copy(key, dst, src, func=ACTF.Copy, scale=1.0):
                return nc.scalar.activation(dst, src, func, scale=scale)

            def item(name):
                if name == "conv_a":
                    for b in range(2):
                        act.wait_ge(*PE.after("acc", name, b))
                        nc.scalar.activation(cx[:, b, N_META:], ps[:, b, :], ACTF.Copy).then_inc(*ACT.done(("cx", b)))
                    for b in range(2):
                        act.wait_ge(*PE.after("acc", name, 2 + b))
                        nc.scalar.activation(cb[:, b, :], ps[:, 2 + b, :], ACTF.Copy).then_inc(*ACT.done(("cb", b)))
                    act.wait_ge(*PE.after("acc", name, "meta"))
                    nc.scalar.activation(cx[:, :, 0:N_META], ps[:, 4, 0:2 * N_META].rearrange("p (b n) -> p b n", b=2),
                                         ACTF.Copy).then_inc(*ACT.done(("cx", "meta")))
                elif name == "conv_b":
                    for b in range(2):
                        act.wait_ge(*PE.after("acc", name, 2 + b))
                        nc.scalar.activation(cz[:, b, :], ps[:, 2 + b, :], ACTF.Silu).then_inc(*ACT.done(("cz", b)))
                elif name == "latent":
                    for b in range(2):
                        act.wait_ge(*PE.after("acc", name, b))
                        nc.scalar.activation(cq_sq[:, b, :], ps[:, b, :], ACTF.Square).then_inc(*ACT.done(("latent_sq", b)))
                        nc.scalar.activation(cq_hi[:, b, :], ps[:, b, :], ACTF.Copy,
                                             scale=col("q_a_norm", b)).then_inc(*ACT.done(("cq_hi", b)))
                    act.wait_ge(*PE.after("acc", name, 2))
                    nc.scalar.activation(ckv_sq[:, N_META:], ps[:, 2, :], ACTF.Square).then_inc(*ACT.done(("latent_sq", 2)))
                    nc.scalar.activation(ckv_hi[:, N_META:], ps[:, 2, :], ACTF.Copy,
                                         scale=col("kv_a_norm")).then_inc(*ACT.done(("ckv_hi",)))
                    act.wait_ge(*PE.after("acc", name, "meta"))
                    nc.scalar.activation(ckv_hi[:, 0:N_META], ps[:, 4, 0:N_META], ACTF.Copy,
                                         scale=col("kv_a_norm")).then_inc(*ACT.done(("ckv_hi", "meta")))
                    nc.scalar.activation(ckv_sq[:, 0:N_META], ps[:, 4, 0:N_META],
                                         ACTF.Square).then_inc(*ACT.done(("latent_sq", "meta")))
                elif name == "k_rope":
                    act.wait_ge(*PE.after("acc", name, NT))
                    nc.scalar.activation(kr[:, :, :], ps[:, 5, 0:(NT + 1) * QKR].rearrange("p (t n) -> p t n", n=QKR),
                                         ACTF.Copy).then_inc(*ACT.done(("kr",)))
                elif name.startswith("w_uq"):
                    n = int(name[-1])
                    act.wait_ge(*DVE.after("r", "lat"))
                    act.wait_ge(*DVE.after("conv_lo", 1))
                    for t in range(NT):
                        act.wait_ge(*PE.after("acc", name, t))
                        nc.scalar.activation(q_sb[:, t, 384 * n:384 * n + 384], ps[:, t, 0:384], ACTF.Copy,
                                             scale=ss[:, 2, t:t + 1]).then_inc(*ACT.done(("q_raw", n, t)))
                elif name.startswith("w_ukv"):
                    n = int(name[-1])
                    for t in range(NT + 1):
                        rows = P if t < NT else N_META
                        act.wait_ge(*PE.after("acc", name, t))
                        src = ps[0:rows, t, :].rearrange("p (h n) -> p h n", h=4)
                        dst = k_sb[0:rows, t, 384 * n:384 * n + 384].rearrange("p (h n) -> p h n", h=4)
                        nc.scalar.activation(dst[:, :, 0:QKN], src[:, :, 0:QKN], ACTF.Copy,
                                             scale=ss[0:rows, 2, NT + t:NT + t + 1]).then_inc(*ACT.done(("k_raw", n, t)))
                elif name == "mla_z":
                    for t in range(NT):
                        act.wait_ge(*PE.after("acc", name, t))
                        nc.scalar.activation(z_mla[:, t, :], ps[:, t, :], ACTF.Silu).then_inc(*ACT.done(("z_mla", t)))
                elif name == "ret_vz":
                    for t in range(NT + 1):
                        rows = P if t < NT else N_META
                        act.wait_ge(*PE.after("acc", name, t))
                        nc.scalar.activation(rv[0:rows, t, :], ps[0:rows, t, 0:256], ACTF.Copy).then_inc(*ACT.done(("rv", t)))
                        if t < NT:
                            nc.scalar.activation(z_ret[:, t, :], ps[:, t, 256:512], ACTF.Silu).then_inc(*ACT.done(("z_ret", t)))

                elif name == "small2":
                    act.wait_ge(*PE.after("acc", name, NT - 1))
                    nc.scalar.activation(sm2[:, :, :], ps[:, 5, 0:NT * 88].rearrange("p (t n) -> p t n", n=88),
                                         ACTF.Copy).then_inc(*ACT.done(("sm2",)))
                elif name in ("gla_q", "gla_k"):
                    dst = gq if name == "gla_q" else gk
                    for b in range(GLA_H):
                        act.wait_ge(*PE.after("acc", name, b))
                        nc.scalar.activation(dst[:, b, :], ps[:, b, :], ACTF.Copy).then_inc(*ACT.done((name, b)))
                elif name.startswith(("gla_v", "gla_g")):
                    n = int(name[-1])
                    for t in range(NT):
                        act.wait_ge(*PE.after("acc", name, t))
                        if name.startswith("gla_v"):
                            nc.scalar.activation(gv[:, t, 512 * n:512 * n + 512], ps[:, t, :],
                                                 ACTF.Copy).then_inc(*ACT.done(("gv", n, t)))
                        else:
                            if n or t >= 2:
                                act.wait_ge(*DVE.after("go", *divmod(NT * n + t - 2, NT), 1))
                            nc.scalar.activation(g_silu[:, t % 2, :], ps[:, t, :], ACTF.Silu).then_inc(*ACT.done(("g_silu", n, t)))
                elif name.startswith("gate"):
                    for t in range(NT):
                        act.wait_ge(*DVE.after("gate_sum", int(name[4]), int(name[5]), t))
                        nc.scalar.activation(gate[:, t, :], gate[:, t, :], ACTF.Sigmoid).then_inc(*ACT.done(("gate", int(name[4]), int(name[5]), t)))
                elif name == "idx_q":
                    for b in range(4):
                        act.wait_ge(*PE.after("acc", name, b))
                        nc.scalar.activation(iqT[:, b, :], ps[:, b, :], ACTF.Copy).then_inc(*ACT.done(("iqT", b)))
                elif name.startswith("dsa_q") or name.startswith("mem_q"):
                    n = int(name[-1])
                    tag = name[0:1]
                    for t in range(NT):
                        act.wait_ge(*PE.after("acc", name, t))
                        i = NT * n + t
                        if i >= 2:
                            act.wait_ge(*DVE.after(tag + "q_ss", i - 2))
                        elif tag == "m":
                            act.wait_ge(*DVE.after("mk_ss", 2 + i))
                        nc.scalar.activation(d_sq[:, i % 2, :], ps[:, t, :], ACTF.Square).then_inc(*ACT.done((tag + "q_sq", i)))
                        nc.scalar.activation(dq[:, t, 512 * n:512 * n + 512], ps[:, t, :],
                                             ACTF.Copy).then_inc(*ACT.done(("dq" if tag == "d" else "mq", n, t)))
                elif name == "dsa_kv":
                    for t in range(NT):
                        act.wait_ge(*PE.after("acc", name, t))
                        act.wait_ge(*DVE.after(*(("dk_ss", t - 2) if t >= 2 else ("dq_ss", 6 + t))))
                        nc.scalar.activation(d_sq[:, t % 2, 0:256], ps[:, t, 0:256], ACTF.Square).then_inc(*ACT.done(("dk_sq", t)))
                        nc.scalar.activation(dk[:, t, :], ps[:, t, 0:256], ACTF.Copy).then_inc(*ACT.done(("dk", t)))
                        nc.scalar.activation(dv[:, t, :], ps[:, t, 256:512], ACTF.Copy).then_inc(*ACT.done(("dv", t)))
                elif name.startswith("mem_kv"):
                    n = int(name[-1])
                    for t in range(2):
                        act.wait_ge(*PE.after("acc", name, t))
                        if n < 2:
                            if n:
                                act.wait_ge(*DVE.after("mk_ss", t))
                            nc.scalar.activation(d_sq[:, t, :], ps[:, t, :], ACTF.Square).then_inc(*ACT.done(("mk_sq", 2 * n + t)))
                        dst = (mk if n < 2 else mv)[:, t, 512 * (n % 2):512 * (n % 2) + 512]
                        nc.scalar.activation(dst, ps[:, t, :], ACTF.Copy).then_inc(*ACT.done(("mkv", n, t)))
                elif name.startswith("expert"):
                    e = int(name[6:])
                    for b in range(2):
                        act.wait_ge(*PE.after("acc", name, b))
                        if e:
                            act.wait_ge(*DVE.after("hid", e - 1, b))
                        nc.scalar.activation(e_silu[:, b, :], ps[:, b, :], ACTF.Silu).then_inc(*ACT.done(("e_silu", e, b)))
                    for b in range(2):
                        act.wait_ge(*DVE.after("hid", e, b))
                        if e >= 2:
                            act.wait_ge(*PE.after("acc", f"down{e - 2}1", NT - 1))
                        nc.scalar.activation(hid_hi[:, e % 2, b, :], hid[:, b, :], ACTF.Copy).then_inc(*ACT.done(("hid_hi", e, b)))

            def gla_low():
                act.wait_ge(*PE.after("low_t"))
                nc.scalar.activation(low_t[:, :], ps[0:16, 6, :], ACTF.Copy).then_inc(*ACT.done(("low_t",)))

            def gla_head(h):
                s = h % 2
                act.wait_ge(*PE.after("g_z", h))
                if h:
                    act.wait_ge(*DVE.after("g_la", h - 1))
                nc.scalar.activation(gz[:, :], ps[:, 7, :], ACTF.Identity, bias=col("b_gla_a2_2", h)).then_inc(*ACT.done(("g_z", h)))
                act.wait_ge(*ACT.after("g_z", h))
                if h:
                    act.wait_ge(*ACT.after("g_dec", h - 1))
                nc.scalar.activation(gab[:, :], gz[:, :], ACTF.Abs).then_inc(*ACT.done(("g_ab", h)))
                act.wait_ge(*ACT.after("g_ab", h))
                nc.scalar.activation(gex[:, :], gab[:, :], ACTF.Exp, scale=-1.0).then_inc(*ACT.done(("g_ex", h)))
                act.wait_ge(*ACT.after("g_ex", h))
                nc.scalar.activation(gex[:, :], gex[:, :], ACTF.Ln, bias=1.0).then_inc(*ACT.done(("g_ln", h)))
                act.wait_ge(*DVE.after("g_lc", h))
                if h >= 2:
                    act.wait_ge(*PE.after("g_o", h - 2, NT - 1))
                k = 1.0 / 16
                nc.scalar.activation(g_qd[:, s, :], gab[:, :], ACTF.Exp, scale=k).then_inc(*ACT.done(("g_e1", h)))
                nc.scalar.activation(g_ki[:, s, :], gab[:, :], ACTF.Exp, scale=-k).then_inc(*ACT.done(("g_e2", h)))
                nc.scalar.activation(g_ke[:, s, :], glc[:, :], ACTF.Exp, scale=k).then_inc(*ACT.done(("g_e3", h)))
                nc.scalar.activation(g_dec[:, s, :], gab[:, CHUNK - 1::CHUNK], ACTF.Exp, scale=k).then_inc(*ACT.done(("g_dec", h)))
                act.wait_ge(*PE.after("g_keT", h))
                nc.scalar.activation(g_keT[:, s, :], ps[:, 6, :], ACTF.Copy).then_inc(*ACT.done(("g_keT", h)))
                for t in range(NT):
                    act.wait_ge(*PE.after("g_o", h, t))
                    src = ps[:, 4 + t % 2, 0:GLA_DV]
                    nc.scalar.activation(go[:, t, GLA_DV * h:GLA_DV * (h + 1)], src, ACTF.Copy).then_inc(*ACT.done(("g_oc", h, t)))
                    if h or t:
                        act.wait_ge(*ACT.after("g_oss", *divmod(NT * h + t - 1, NT)))
                    nc.scalar.activation(gsq[:, :], src, ACTF.Square,
                                         accum_out=ss[:, 5, NT * t + h:NT * t + h + 1]).then_inc(*ACT.done(("g_oss", h, t)))

            def mix(tag):
                for c in range(KC):
                    act.wait_ge(*PE.after("mixT", tag, c))
                    nc.scalar.activation(mix_hi[:, c, :], ps[:, 4 + c % 4, :], ACTF.Copy,
                                         scale=col("gla_norm_2", c % 2) if tag == "gla" else 1.0
                                         ).then_inc(*ACT.done(("mix_hi", tag, c)))

            def idx_key():
                act.wait_ge(*DVE.after("ss0", "idx"))
                for t in range(NT):
                    if t:
                        act.wait_ge(*ACT.after("ik_ss", t - 1))
                    nc.scalar.activation(d_sq[:, 0, 0:IDX_D], sm2[:, t, 16:80], ACTF.Square,
                                         accum_out=ss[:, 0, t:t + 1]).then_inc(*ACT.done(("ik_ss", t)))
                rsqrt_start(("ik",), (ss[:, 1, 0:4], ss[:, 2, 0:4]))
                act.wait_ge(*PE.after("ikT"))
                nc.scalar.activation(ikT[:, :], ps[:, 6, :], ACTF.Copy, scale=col("idx_k_norm_2")).then_inc(*ACT.done(("ikT",)))

            def idx_scores(t):
                n = P * (t + 1)
                for h in range(IDX_H):
                    act.wait_ge(*PE.after("rel", t, h))
                    i = IDX_H * (t - 1) + h
                    if i >= 2:
                        act.wait_ge(*DVE.after("score", *idx_of(i - 2)))
                    nc.scalar.activation(rel[:, h % 2, 0:n], ps[:, 4 + h % 4, 0:n], ACTF.Relu).then_inc(*ACT.done(("rel", t, h)))

            def head_transposed(tag, c, dst, n, gain):
                act.wait_ge(*PE.after(tag, c))
                nc.scalar.activation(dst, ps[:, 4 + c % 4, 0:n], ACTF.Copy, scale=gain).then_inc(*ACT.done((tag, c)))

            def dsa_prepare():
                rsqrt_start(("dsa",), (ss[:, 3, 0:40], ss[:, 4, 0:40]))
                for c in range(DSA_H):
                    head_transposed("dqT", c, dqT[:, c, :], SEQ, col("dsa_q_norm_2"))
                for c in range(2):
                    head_transposed("dkT", c, dkT[:, c, :], SEQ, col("dsa_k_norm_2"))

            def mix_high(tag, c, bank):
                nc.scalar.activation(mix_hi[:, c, :], ps[:, bank, :], ACTF.Copy).then_inc(*ACT.done(("mix_hi", tag, c)))

            def dsa_exp(j):
                n = P * (j % NT + 1)
                act.wait_ge(*DVE.after("d_nmax", j))
                nc.scalar.activation(d_prob[:, j % 2, 0:n], d_prob[:, j % 2, 0:n], ACTF.Exp, bias=sm[:, 1, j:j + 1],
                                     scale=float(P) ** -0.5, accum_out=sm[:, 2, j:j + 1]).then_inc(*ACT.done(("d_exp", j)))

            def dsa_head(h):
                for j in range(NT * h, NT * (h + 1)):
                    n = P * (j % NT + 1)
                    if j == 0:
                        dsa_exp(0)
                    if j + 1 < NT * DSA_H:
                        dsa_exp(j + 1)
                    act.wait_ge(*PE.after("d_PT", j))
                    if j >= 2:
                        act.wait_ge(*PE.after("d_O", j - 2))
                    nc.scalar.activation(d_probT[:, j % 2, 0:n], ps[:, 6, 0:n], ACTF.Copy).then_inc(*ACT.done(("d_PT", j)))
                act.wait_ge(*PE.after("d_O", NT * h + NT - 1))
                mix_high("dsa", h, 7)

            def mem_prepare():
                rsqrt_start(("mem_heads",), (ss[:, 3, 0:24], ss[:, 4, 0:24]))
                for c in range(KC):
                    head_transposed("mkT", c, mkT[:, c, :], MEM, col("mem_k_norm_2", c % 2))
                for c in range(KC):
                    head_transposed("mqT", c, mqT[:, c, :], SEQ, col("mem_q_norm_2", c % 2))

            def mem_exp(j):
                act.wait_ge(*DVE.after("m_nmax", j))
                if j >= 2:
                    act.wait_ge(*PE.after("m_PT", j - 2))
                nc.scalar.activation(m_prob[:, j % 2, :], ps[:, 4 + j % 2, 0:MEM], ACTF.Exp, bias=sm[:, 1, j:j + 1],
                                     scale=float(MEM) ** -0.5, accum_out=sm[:, 2, j:j + 1]).then_inc(*ACT.done(("m_exp", j)))

            def mem_head(h):
                for j in range(NT * h, NT * (h + 1)):
                    if j == 0:
                        mem_exp(0)
                    if j + 1 < NT * MEM_H:
                        mem_exp(j + 1)
                    act.wait_ge(*PE.after("m_PT", j))
                    if j >= 2:
                        act.wait_ge(*PE.after("m_O", j - 2))
                    nc.scalar.activation(m_probT[:, j % 2, :], ps[:, 6, 0:MEM], ACTF.Copy).then_inc(*ACT.done(("m_PT", j)))
                act.wait_ge(*PE.after("m_O", NT * h + NT - 1))
                mix_high("mem", 2 * h, 7)
                mix_high("mem", 2 * h + 1, 3)

            def route():
                act.wait_ge(*DVE.after("r_g"))
                nc.scalar.activation(rt[:, 2, :], rt[:, 2, :], ACTF.Exp).then_inc(*ACT.done(("r_eg",)))
                act.wait_ge(*DVE.after("r_d"))
                nc.scalar.activation(rt[:, 9, 0:4], rt[:, 9, 0:4], ACTF.Exp).then_inc(*ACT.done(("r_ed",)))

            def loads(section):
                if section == "gla":
                    act.dma_start(w_a2[:, :], w["w_gla_a2_2"][0]).then_inc(gla_in, 16)
                    act.dma_start(scan_mask[:, :], w["c_scan"]).then_inc(gla_in, 16)
                elif section == "mem":
                    for t in range(2):
                        act.dma_start(mem_in[:, t, :], w["mem_2"][0, P * t:P * t + P, :]).then_inc(mem_landed, 16)
                elif section == "experts":
                    act.dma_start(r_bias[:, 0:4], w["b_r1_2"][0].partition_broadcast(P)).then_inc(route_in, 16)
                    act.dma_start(r_bias[:, 4:20], w["b_r2_2"][0].partition_broadcast(P)).then_inc(route_in, 16)

            def mla_prepare():
                for t in range(NT + 1):
                    for kind, x in (("q", q_sb), ("k", k_sb)):
                        if kind == "q" and t == NT:
                            continue
                        rows = P if t < NT else N_META
                        if kind == "k":
                            act.wait_ge(*DVE.after("kr_in", t))
                        else:
                            act.wait_ge(*ACT.after("q_raw", 1, t))
                        if (kind, t) != ("q", 0):
                            act.wait_ge(*DVE.after("hss", *(("k", t - 1) if kind == "q" else (("q", t) if t < NT else ("k", t - 1)))))
                        nc.scalar.activation(sq[0:rows, :], x[0:rows, t, :], ACTF.Square).then_inc(*ACT.done(("hsq", kind, t)))
                rsqrt_start(("head",), (ss[:, 3, 0:72], ss[:, 4, 0:72]))

            def q_transposed(tag, h, width):
                act.wait_ge(*PE.after("qT", tag, h))
                if h >= 2:
                    act.wait_ge(*PE.after(*last_scores(tag, h - 2)))
                nc.scalar.activation(qT[0:width, h % 2, :], ps[0:width, 6, :], ACTF.Copy).then_inc(*ACT.done(("qT", tag, h)))

            def mla_head(h):
                q_transposed("mla", h, QKH)
                for j in range(NT * h, NT * (h + 1)):
                    n = P * (j % NT + 1)
                    act.wait_ge(*DVE.after("nmax", "mla", j))
                    if j >= 2:
                        act.wait_ge(*PE.after("PT", "mla", j - 2))
                    nc.scalar.activation(prob[:, j % 2, 0:N_META + n], psf[:, 5 * SEQ - N_META:5 * SEQ + n], ACTF.Exp,
                                         bias=sm[:, 1, j:j + 1], scale=float(QKH) ** -0.5,
                                         accum_out=sm[:, 2, j:j + 1]).then_inc(*ACT.done(("exp", "mla", j)))
                    act.wait_ge(*PE.after("PT", "mla", j))
                    if j >= 2:
                        act.wait_ge(*PE.after("O", "mla", j - 2))
                    nc.scalar.activation(probT[:, j % 2, 0:n], ps[:, 6, 0:n], ACTF.Copy).then_inc(*ACT.done(("PT", "mla", j)))

            def load_decay(h):
                act.dma_start(decay[:, h % 2, :], w["c_decay"][h]).then_inc(decay_in[h % 2], 16)
                act.dma_start(decay_m[:, h % 2, :], w["c_decay_m"][h]).then_inc(decay_in[h % 2], 16)

            def ret_head(h):
                if h == 0:
                    load_decay(0)
                    load_decay(1)
                q_transposed("ret", h, RET_D)
                act.wait_ge(*PE.after("rO", h))
                if h + 2 < RET_H:
                    load_decay(h + 2)
                nc.scalar.activation(y_ret[:, :, RET_D * h:RET_D * (h + 1)],
                                     ps[:, 5, 0:NT * RET_D].rearrange("p (t n) -> p t n", t=NT),
                                     ACTF.Copy).then_inc(*ACT.done(("rO", h)))

            def ret_norm():
                act.wait_ge(*ACT.after("rO", RET_H - 1))
                act.wait_ge(*PE.after("rO", RET_H - 1))
                nc.scalar.activation(ysq[:, :, :], y_ret[:, :, :], ACTF.Square).then_inc(*ACT.done(("ysq",)))
                rsqrt_start(("ret",), (ss[:, 3, 0:16], ss[:, 4, 0:16]))

            def mix_one():
                for c in range(6):
                    act.wait_ge(*PE.after("mixT", 2 + c))
                    nc.scalar.activation(mix_hi[:, 2 + c, :], ps[:, 6 + c % 2, :], ACTF.Copy,
                                         scale=1.0 if c < 4 else col("ret_norm")).then_inc(*ACT.done(("mix_hi", 2 + c)))

            for step, *a in order:
                if step == "item" and a[0].startswith("gate"):
                    b, n = int(a[0][4]), int(a[0][5])
                    if b:
                        act.wait_ge(*DVE.after("gate_sum", b - 1, n, NT - 1))
                    else:
                        act.wait_ge(*DVE.after("g_ke", GLA_H - 1))
                    c = D * b + 512 * n
                    act.dma_start(gate_bias[:, n, :], w["b_gate_2"][0, c:c + 512].partition_broadcast(P)).then_inc(bias_in[n], 16)
                if step == "item":
                    split_high(min(len(units), first_unit[a[0]] + len(items[a[0]]) + 2))
                    item(*a)
                elif step == "norm":
                    norm(*a)
                elif step == "conv":
                    for b in range(2):
                        act.wait_ge(*DVE.after("cy", b))
                        nc.scalar.activation(mix_hi[:, b, :], cy[:, b, :], ACTF.Copy).then_inc(*ACT.done(("conv_hi", b)))
                elif step == "latent_sums":
                    rsqrt_start(("lat",), (ss[:, 1, 0:9], ss[:, 2, 0:9]))
                elif step == "mla_prepare":
                    mla_prepare()
                elif step == "mla_head":
                    mla_head(*a)
                elif step == "ret_head":
                    ret_head(*a)
                elif step == "ret_norm":
                    ret_norm()
                elif step == "mix_one":
                    mix_one()
                elif step == "gla_low":
                    gla_low()
                elif step == "gla_head":
                    gla_head(*a)
                elif step == "gla_rstd":
                    rsqrt_start(("gla",), (ss[:, 3, 0:16], ss[:, 4, 0:16]))
                elif step == "mix":
                    mix(*a)
                elif step == "idx_key":
                    idx_key()
                elif step == "idx_scores":
                    idx_scores(*a)
                elif step == "dsa_prepare":
                    dsa_prepare()
                elif step == "dsa_head":
                    dsa_head(*a)
                elif step == "mem_prepare":
                    mem_prepare()
                elif step == "mem_head":
                    mem_head(*a)
                elif step == "route":
                    route()
                elif step == "barrier":
                    barrier(act, a[0])
                    ACT.section = a[0]
                    loads(a[0])

        @block.vector
        def _(dve):
            def mean(key, v, total, width):
                return dve.tensor_scalar(v, total, 1.0 / width, EPS, ALU.mult, ALU.add).then_inc(*DVE.done(("v", *key)))

            def rsqrt_finish(key, v, y, t):
                dve.wait_ge(*ACT.after("y0", *key))
                dve.scalar_tensor_tensor(t, y, -0.5, y, ALU.mult, ALU.mult).then_inc(*DVE.done(("r1", *key)))
                dve.wait_ge(*DVE.after("r1", *key))
                dve.tensor_tensor(t, t, v, ALU.mult).then_inc(*DVE.done(("r2", *key)))
                dve.wait_ge(*DVE.after("r2", *key))
                dve.scalar_tensor_tensor(y, t, 1.5, y, ALU.add, ALU.mult).then_inc(*DVE.done(("r", *key)))
                dve.wait_ge(*DVE.after("r", *key))

            def norm(name):
                tiles = NORM_TILES[name]
                n = len(tiles)
                dve.memset(ss[:, 0:3, 0:n], 1.0).then_inc(*DVE.done(("ss0", name)))
                for i in range(n):
                    dve.wait_ge(*ACT.after("ss", name, i))
                mean((name,), ss[:, 1, 0:n], ss[:, 0, 0:n], D)
                rsqrt_finish((name,), ss[:, 1, 0:n], ss[:, 2, 0:n], ss[:, 0, 0:n])
                for i, (src, scaled, rows) in enumerate(tiles):
                    dve.tensor_scalar(scaled, src, ss[0:rows, 2, i:i + 1], None, ALU.mult).then_inc(*DVE.done(("scaled", name, i)))
                n = sum(t[2] == P for t in tiles) * P
                hi, off = norm_dest(name)
                lo = act_lo if hi is act_hi else norm_lo(name)
                for k in range(KC):
                    dve.wait_ge(*ACT.after("hi", name, k))
                    dve.scalar_tensor_tensor(lo[:, k, off:off + n], ps[:, 4 + k % 4, 0:n], col(NORMS[name], k),
                                             hi[:, k, off:off + n].bitcast(F32), ALU.mult,
                                             ALU.subtract).then_inc(*DVE.done(("lo", name, k)))
                if name == "h":
                    dve.wait_ge(*PE.after("T", name, "meta"))
                    g = gains[:, GAINS["ln_w"]:GAINS["ln_w"] + KC].unsqueeze(2).to_broadcast([P, KC, N_META])
                    dve.tensor_tensor(meta_t[:, :, :], ps[:, 3, 0:KC * N_META].rearrange("p (k n) -> p k n", k=KC), g,
                                      ALU.mult).then_inc(*DVE.done(("meta_t", name)))
                    dve.wait_ge(*ACT.after("meta_hi", name))
                    dve.tensor_tensor(act_lo[:, :, 0:N_META], meta_t[:, :, :], act_hi[:, :, 0:N_META].bitcast(F32),
                                      ALU.subtract).then_inc(*DVE.done(("meta_lo", name)))

            def low_part(key, lo, src, hi, gain=1.0):
                return dve.scalar_tensor_tensor(lo, src, gain, hi.bitcast(F32), ALU.mult,
                                                ALU.subtract).then_inc(*DVE.done(key))

            def rope_turn(key, x, out, rows, heads, half, t, cos, sin):
                n = heads * half
                tmp = [b[0:rows, 0:n].rearrange("p (h n) -> p h n", h=heads) for b in (t0, t1, t2, t3)]
                c = cos[0:rows, t, :].unsqueeze(1).to_broadcast([rows, heads, half])
                s = sin[0:rows, t, :].unsqueeze(1).to_broadcast([rows, heads, half])
                a, b = x[:, :, 0:half], x[:, :, half:2 * half]
                dve.tensor_tensor(tmp[0], a, c, ALU.mult).then_inc(*DVE.done((*key, 0)))
                dve.tensor_tensor(tmp[1], b, s, ALU.mult).then_inc(*DVE.done((*key, 1)))
                dve.tensor_tensor(tmp[2], a, s, ALU.mult).then_inc(*DVE.done((*key, 2)))
                dve.tensor_tensor(tmp[3], b, c, ALU.mult).then_inc(*DVE.done((*key, 3)))
                dve.wait_ge(*DVE.after(*key, 3))
                dve.tensor_tensor(out[:, :, 0:half], tmp[0], tmp[1], ALU.subtract).then_inc(*DVE.done((*key, 4)))
                dve.tensor_tensor(out[:, :, half:2 * half], tmp[2], tmp[3], ALU.add).then_inc(*DVE.done((*key, 5)))

            def item(name):
                if name == "conv_b":
                    for b in range(2):
                        dve.wait_ge(*PE.after("acc", name, b))
                        dve.wait_ge(*ACT.after("cx", b))
                        dve.tensor_tensor(cu[:, b, N_META:], ps[:, b, :], cx[:, b, N_META:], ALU.mult).then_inc(*DVE.done(("cu", b)))
                    dve.wait_ge(*PE.after("acc", name, "meta"))
                    dve.wait_ge(*ACT.after("cx", "meta"))
                    dve.tensor_tensor(cu[:, :, 0:N_META], ps[:, 4, 0:2 * N_META].rearrange("p (b n) -> p b n", b=2),
                                      cx[:, :, 0:N_META], ALU.mult).then_inc(*DVE.done(("cu", "meta")))
                elif name == "latent":
                    for b in range(2):
                        dve.wait_ge(*ACT.after("cq_hi", b))
                        low_part(("cq_lo", b), cq_lo[:, b, :], ps[:, b, :], cq_hi[:, b, :], col("q_a_norm", b))
                    dve.wait_ge(*ACT.after("ckv_hi"))
                    low_part(("ckv_lo",), ckv_lo[:, N_META:], ps[:, 2, :], ckv_hi[:, N_META:], col("kv_a_norm"))
                    dve.wait_ge(*ACT.after("latent_sq", "meta"))
                    low_part(("ckv_lo", "meta"), ckv_lo[:, 0:N_META], ps[:, 4, 0:N_META], ckv_hi[:, 0:N_META], col("kv_a_norm"))
                elif name.startswith("w_ukv"):
                    n = int(name[-1])
                    for t in range(NT + 1):
                        rows = P if t < NT else N_META
                        dve.wait_ge(*ACT.after("k_raw", n, t))
                        src = ps[0:rows, t, :].rearrange("p (h n) -> p h n", h=4)
                        dst = v_sb[0:rows, t, 256 * n:256 * n + 256].rearrange("p (h n) -> p h n", h=4)
                        dve.tensor_scalar(dst, src[:, :, QKN:P], ss[0:rows, 2, NT + t:NT + t + 1], None,
                                          ALU.mult).then_inc(*DVE.done(("v_raw", n, t)))
                elif name == "ret_qk":
                    dve.wait_ge(rope_in, 48)
                    for t in range(NT + 1):
                        rows = P if t < NT else N_META
                        dve.wait_ge(*PE.after("acc", name, t))
                        if t:
                            dve.wait_ge(*DVE.after("rope_r", t - 1, 5))
                        rope_turn(("rope_r", t), ps[0:rows, t, :].rearrange("p (h n) -> p h n", h=8),
                                  rqk[0:rows, t, :].rearrange("p (h n) -> p h n", h=8), rows, 8, 32, t, cos_r, sin_r)
                elif name.startswith("w_out"):
                    n = int(name[-1])
                    for t in range(NT):
                        dve.wait_ge(*PE.after("acc", name, t))
                        x = x1[:, t, 512 * n:512 * n + 512]
                        dve.tensor_tensor(x, ps[:, t, :], x, ALU.add).then_inc(*DVE.done(("x", name, t)))

                elif name.startswith("gla_g"):
                    n = int(name[-1])
                    for t in range(NT):
                        dve.wait_ge(*ACT.after("g_silu", n, t))
                        for i in range(2):
                            h = 2 * n + i
                            o = go[:, t, GLA_DV * h:GLA_DV * (h + 1)]
                            dve.scalar_tensor_tensor(o, o, ss[:, 4, NT * t + h:NT * t + h + 1],
                                                     g_silu[:, t % 2, GLA_DV * i:GLA_DV * (i + 1)], ALU.mult,
                                                     ALU.mult).then_inc(*DVE.done(("go", n, t, i)))
                elif name.startswith("gate"):
                    b, n = int(name[4]), int(name[5])
                    dve.wait_ge(bias_in[n], 16 * (b + 1))
                    for t in range(NT):
                        dve.wait_ge(*PE.after("acc", name, t))
                        if (b, n) != (0, 0):
                            dve.wait_ge(*DVE.after("merged", *((b, 0) if n else (b - 1, 1)), t))
                        dve.tensor_tensor(gate[:, t, :], ps[:, t, :], gate_bias[:, n, :],
                                          ALU.add).then_inc(*DVE.done(("gate_sum", b, n, t)))
                elif name.startswith("w_o"):
                    b, n = int(name[3]), int(name[4])
                    for t in range(NT):
                        dve.wait_ge(*PE.after("acc", name, t))
                        dve.wait_ge(*ACT.after("gate", b, n, t))
                        m = merged[:, t, 512 * n:512 * n + 512]
                        if b == 0:
                            dve.tensor_tensor(m, ps[:, t, :], gate[:, t, :],
                                              ALU.mult).then_inc(*DVE.done(("gated", b, n, t), ("merged", b, n, t)))
                        else:
                            dve.tensor_tensor(gate[:, t, :], ps[:, t, :], gate[:, t, :],
                                              ALU.mult).then_inc(*DVE.done(("gated", b, n, t)))
                            dve.wait_ge(*DVE.after("gated", b, n, t))
                            dve.tensor_tensor(m, m, gate[:, t, :], ALU.add).then_inc(*DVE.done(("merged", b, n, t)))
                elif name.startswith(("dsa_q", "mem_q")):
                    tag, n = name[0:1], int(name[-1])
                    for t in range(NT):
                        i = NT * n + t
                        dve.wait_ge(*ACT.after(tag + "q_sq", i))
                        heads = 4 if tag == "d" else 2
                        at = 8 * t + 4 * n if tag == "d" else 8 + 4 * t + 2 * n
                        dve.tensor_reduce(ss[:, 5, at:at + heads], d_sq[:, i % 2, :].rearrange("p (h n) -> p h n", h=heads), X,
                                          ALU.add).then_inc(*DVE.done((tag + "q_ss", i)))
                elif name == "dsa_kv":
                    for t in range(NT):
                        dve.wait_ge(*ACT.after("dk_sq", t))
                        dve.tensor_reduce(ss[:, 5, 32 + 2 * t:34 + 2 * t],
                                          d_sq[:, t % 2, 0:256].rearrange("p (h n) -> p h n", h=2), X,
                                          ALU.add).then_inc(*DVE.done(("dk_ss", t)))
                elif name in ("mem_kv0", "mem_kv1"):
                    n = int(name[-1])
                    for t in range(2):
                        dve.wait_ge(*ACT.after("mk_sq", 2 * n + t))
                        dve.tensor_reduce(ss[:, 5, 4 * t + 2 * n:4 * t + 2 * n + 2],
                                          d_sq[:, t, :].rearrange("p (h n) -> p h n", h=2), X,
                                          ALU.add).then_inc(*DVE.done(("mk_ss", 2 * n + t)))
                elif name.startswith("expert"):
                    e = int(name[6:])
                    for b in range(2):
                        dve.wait_ge(*ACT.after("e_silu", e, b))
                        dve.wait_ge(*PE.after("acc", name, 2 + b))
                        if e:
                            dve.wait_ge(*ACT.after("hid_hi", e - 1, b))
                            dve.wait_ge(*DVE.after("hid_lo", e - 1, b))
                        dve.tensor_tensor(hid[:, b, :], ps[:, 2 + b, :], e_silu[:, b, :], ALU.mult).then_inc(*DVE.done(("hid", e, b)))
                    for b in range(2):
                        dve.wait_ge(*ACT.after("hid_hi", e, b))
                        dve.tensor_tensor(hid_lo[:, e % 2, b, :], hid[:, b, :], hid_hi[:, e % 2, b, :].bitcast(F32),
                                          ALU.subtract).then_inc(*DVE.done(("hid_lo", e, b)))
                elif name.startswith("down"):
                    e, n = int(name[4:-1]), int(name[-1])
                    for t in range(NT):
                        dve.wait_ge(*PE.after("acc", name, t))
                        if e:
                            dve.wait_ge(*DVE.after("x", f"down{e - 1}{n}", t))
                        x = x1[:, t, 512 * n:512 * n + 512]
                        dve.scalar_tensor_tensor(x, ps[:, 4 + t, :], combine[:, t, e:e + 1], x, ALU.mult,
                                                 ALU.add).then_inc(*DVE.done(("x", name, t)))
                elif name == "router":
                    dve.wait_ge(route_in, 32)
                    dve.wait_ge(*PE.after("acc", name, NT - 1))
                    dve.tensor_tensor(rl[:, :, :], ps[:, 5, 0:NT * 20].rearrange("p (t n) -> p t n", n=20),
                                      r_bias[:, :].unsqueeze(1).to_broadcast([P, NT, 20]), ALU.add).then_inc(*DVE.done(("rl",)))

            def gla_head(h):
                s = h % 2
                if h == 0:
                    dve.wait_ge(gla_in, 32)
                    for b in range(GLA_H):
                        dve.wait_ge(*ACT.after("gla_q", b))
                        dve.wait_ge(*ACT.after("gla_k", b))
                dve.wait_ge(*ACT.after("g_z", h))
                dve.wait_ge(*ACT.after("g_ln", h))
                dve.scalar_tensor_tensor(gz[:, :], gz[:, :], 0.0, gex[:, :], ALU.min, ALU.subtract).then_inc(*DVE.done(("g_la0", h)))
                dve.wait_ge(*DVE.after("g_la0", h))
                dve.tensor_tensor_scan(gab[:, :], scan_mask[:, :], gz[:, :], 0.0, ALU.mult, ALU.add).then_inc(*DVE.done(("g_la", h)))
                dve.wait_ge(*DVE.after("g_la", h))
                cum = gab[:, :].rearrange("p (c n) -> p c n", n=CHUNK)
                dve.tensor_tensor(glc[:, :].rearrange("p (c n) -> p c n", n=CHUNK),
                                  cum[:, :, CHUNK - 1:CHUNK].to_broadcast([P, 8, CHUNK]), cum,
                                  ALU.subtract).then_inc(*DVE.done(("g_lc", h)))
                dve.wait_ge(*ACT.after("g_e1", h))
                dve.scalar_tensor_tensor(g_qd[:, s, :], gq[:, h, :], float(P) ** -0.5, g_qd[:, s, :], ALU.mult,
                                         ALU.mult).then_inc(*DVE.done(("g_qd", h)))
                dve.wait_ge(*ACT.after("g_e2", h))
                dve.tensor_tensor(g_ki[:, s, :], gk[:, h, :], g_ki[:, s, :], ALU.mult).then_inc(*DVE.done(("g_ki", h)))
                dve.wait_ge(*ACT.after("g_e3", h))
                dve.tensor_tensor(g_ke[:, s, :], gk[:, h, :], g_ke[:, s, :], ALU.mult).then_inc(*DVE.done(("g_ke", h)))
                dve.wait_ge(*PE.after("g_att", h))
                dve.tensor_tensor(g_att[:, s, :].rearrange("p (t n) -> p t n", n=P), ps[:, 7, :].rearrange("p (t n) -> p t n", n=P),
                                  gla_mask[:, :].unsqueeze(1).to_broadcast([P, NT, P]), ALU.mult).then_inc(*DVE.done(("g_att", h)))
                for n in range(7):
                    bank, cols = state_bank(n)
                    dve.wait_ge(*PE.after("g_upd", h, bank))
                    if n == 0 and h:
                        dve.wait_ge(*PE.after("g_o", h - 1, NT - 1))
                    upd = ps[:, bank, cols]
                    if n == 0:
                        dve.tensor_copy(state[:, 1, :], upd).then_inc(*DVE.done(("g_state", h, 0)))
                    else:
                        dve.wait_ge(*ACT.after("g_dec", h))
                        dve.wait_ge(*DVE.after("g_state", h, n - 1))
                        dve.scalar_tensor_tensor(state[:, n + 1, :], state[:, n, :], g_dec[:, s, n:n + 1], upd, ALU.mult,
                                                 ALU.add).then_inc(*DVE.done(("g_state", h, n)))

            def gla_rstd():
                dve.wait_ge(*ACT.after("g_oss", GLA_H - 1, NT - 1))
                mean(("gla",), ss[:, 3, 0:16], ss[:, 5, 0:16], GLA_DV)
                rsqrt_finish(("gla",), ss[:, 3, 0:16], ss[:, 4, 0:16], ss[:, 0, 0:16])

            def mix(tag):
                for c in range(KC):
                    dve.wait_ge(*ACT.after("mix_hi", tag, c))
                    low_part(("mix_lo", tag, c), mix_lo[:, c, :], ps[:, 4 + c % 4, :], mix_hi[:, c, :],
                             col("gla_norm_2", c % 2) if tag == "gla" else 1.0)

            def idx_key():
                dve.memset(ss[:, 0:6, :], 1.0).then_inc(*DVE.done(("ss0", "idx")))
                dve.wait_ge(*ACT.after("ik_ss", NT - 1))
                mean(("ik",), ss[:, 1, 0:4], ss[:, 0, 0:4], IDX_D)
                rsqrt_finish(("ik",), ss[:, 1, 0:4], ss[:, 2, 0:4], ss[:, 0, 0:4])
                for t in range(NT):
                    dve.tensor_scalar(ik2[:, t, 0:IDX_D], sm2[:, t, 16:80], ss[:, 2, t:t + 1], None,
                                      ALU.mult).then_inc(*DVE.done(("ik1", t)))
                    dve.tensor_scalar(ik2[:, t, IDX_D:P], sm2[:, t, 16:80], ss[:, 2, t:t + 1], None,
                                      ALU.mult).then_inc(*DVE.done(("ik2", t)))
                dve.tensor_scalar(sm2[:, :, 80:88], sm2[:, :, 80:88], float(IDX_H * IDX_D) ** -0.5, None,
                                  ALU.mult).then_inc(*DVE.done(("iw",)))
                dve.tensor_copy(d_mask[:, 0:P], dsa_mask[:, :]).then_inc(*DVE.done(("d_mask", 0)))
                dve.wait_ge(*DVE.after("iw"))

            def idx_scores(t):
                n = P * (t + 1)
                acc = work[:, t - 1, 0:n]
                for h in range(IDX_H):
                    dve.wait_ge(*ACT.after("rel", t, h))
                    wt = sm2[:, t, 80 + h:81 + h]
                    if h == 0:
                        dve.tensor_scalar(acc, rel[:, 0, 0:n], wt, None, ALU.mult).then_inc(*DVE.done(("score", t, 0)))
                    else:
                        dve.wait_ge(*DVE.after("score", t, h - 1))
                        dve.scalar_tensor_tensor(acc, rel[:, h % 2, 0:n], wt, acc, ALU.mult, ALU.add).then_inc(*DVE.done(("score", t, h)))
                dve.wait_ge(*DVE.after("score", t, IDX_H - 1))
                dve.tensor_tensor(acc[:, n - P:n], acc[:, n - P:n], dsa_mask[:, :], ALU.add).then_inc(*DVE.done(("picked", t, 0)))

            def top_keys(t):
                n = P * (t + 1)
                acc = work[:, t - 1, 0:n]
                for i in range(TOPK // 8):
                    dve.wait_ge(*DVE.after("picked", t, i))
                    if i == 0 and t > 1:
                        dve.wait_ge(*DVE.after("picked", t - 1, TOPK // 8))
                    dve.max(best8[:, :], acc).then_inc(*DVE.done(("best", t, i)))
                    dve.wait_ge(*DVE.after("best", t, i))
                    dve.match_replace(acc, best8[:, :], acc, PICKED).then_inc(*DVE.done(("picked", t, i + 1)))
                dve.wait_ge(*DVE.after("picked", t, TOPK // 8))
                at = P * (t * (t + 1) // 2)
                dve.tensor_scalar(d_mask[:, at:at + n], acc, 2 * MASKED, MASKED, ALU.is_gt, ALU.mult).then_inc(*DVE.done(("d_mask", t)))

            def scaled_heads(key, x, r, heads):
                x3 = x.rearrange("p (h n) -> p h n", h=heads)
                dve.tensor_tensor(x3, x3, r.unsqueeze(2).to_broadcast([P, heads, x3.shape[2]]),
                                  ALU.mult).then_inc(*DVE.done(key))

            def dsa_prepare():
                dve.wait_ge(*DVE.after("dk_ss", NT - 1))
                mean(("dsa",), ss[:, 3, 0:40], ss[:, 5, 0:40], P)
                rsqrt_finish(("dsa",), ss[:, 3, 0:40], ss[:, 4, 0:40], ss[:, 5, 0:40])
                for t in range(NT):
                    dve.wait_ge(*ACT.after("dq", 1, t))
                    scaled_heads(("dqn", t), dq[:, t, :], ss[:, 4, 8 * t:8 * t + 8], 8)
                for t in range(NT):
                    dve.wait_ge(*ACT.after("dk", t))
                    scaled_heads(("dkn", t), dk[:, t, :], ss[:, 4, 32 + 2 * t:34 + 2 * t], 2)

            def dsa_max(j):
                t = j % NT
                n, at = P * (t + 1), P * (t * (t + 1) // 2)
                dve.wait_ge(*PE.after("d_S", j))
                if j >= 2:
                    dve.wait_ge(*PE.after("d_PT", j - 2))
                dve.tensor_tensor_reduce(d_prob[:, j % 2, 0:n], ps[:, 4 + j % 2, 0:n], d_mask[:, at:at + n], 1.0, PICKED, ALU.add,
                                         ALU.max, sm[:, 0, j:j + 1]).then_inc(*DVE.done(("d_max", j)))
                dve.wait_ge(*DVE.after("d_max", j))
                dve.tensor_scalar(sm[:, 1, j:j + 1], sm[:, 0, j:j + 1], -float(P) ** -0.5, None,
                                  ALU.mult).then_inc(*DVE.done(("d_nmax", j)))

            def normalise(tag, j, x):
                dve.wait_ge(*ACT.after(tag + "_exp", j))
                dve.reciprocal(sm[:, 3, j:j + 1], sm[:, 2, j:j + 1]).then_inc(*DVE.done((tag + "_rsum", j)))
                dve.wait_ge(*DVE.after(tag + "_rsum", j))
                dve.tensor_scalar(x, x, sm[:, 3, j:j + 1], None, ALU.mult).then_inc(*DVE.done((tag + "_norm", j)))

            def dsa_head(h):
                for j in range(NT * h, NT * (h + 1)):
                    if j == 0:
                        dsa_max(0)
                    if j + 1 < NT * DSA_H:
                        dsa_max(j + 1)
                    normalise("d", j, d_prob[:, j % 2, 0:P * (j % NT + 1)])
                dve.wait_ge(*ACT.after("mix_hi", "dsa", h))
                low_part(("mix_lo", "dsa", h), mix_lo[:, h, :], ps[:, 7, :], mix_hi[:, h, :])

            def mem_prepare():
                dve.wait_ge(*DVE.after("mq_ss", 2 * NT - 1))
                mean(("mem_heads",), ss[:, 3, 0:24], ss[:, 5, 0:24], MEM)
                rsqrt_finish(("mem_heads",), ss[:, 3, 0:24], ss[:, 4, 0:24], ss[:, 5, 0:24])
                for t in range(2):
                    dve.wait_ge(*ACT.after("mkv", 1, t))
                    scaled_heads(("mkn", t), mk[:, t, :], ss[:, 4, 4 * t:4 * t + 4], 4)
                for t in range(NT):
                    dve.wait_ge(*ACT.after("mq", 1, t))
                    scaled_heads(("mqn", t), dq[:, t, :], ss[:, 4, 8 + 4 * t:12 + 4 * t], 4)

            def mem_max(j):
                dve.wait_ge(*PE.after("m_S", j))
                dve.tensor_reduce(sm[:, 0, j:j + 1], ps[:, 4 + j % 2, 0:MEM], X, ALU.max).then_inc(*DVE.done(("m_max", j)))
                dve.wait_ge(*DVE.after("m_max", j))
                dve.tensor_scalar(sm[:, 1, j:j + 1], sm[:, 0, j:j + 1], -float(MEM) ** -0.5, None,
                                  ALU.mult).then_inc(*DVE.done(("m_nmax", j)))

            def mem_head(h):
                for j in range(NT * h, NT * (h + 1)):
                    if j == 0:
                        mem_max(0)
                    if j + 1 < NT * MEM_H:
                        mem_max(j + 1)
                    normalise("m", j, m_prob[:, j % 2, :])
                for c in range(2):
                    dve.wait_ge(*ACT.after("mix_hi", "mem", 2 * h + c))
                    low_part(("mix_lo", "mem", 2 * h + c), mix_lo[:, 2 * h + c, :], ps[:, 7 if c == 0 else 3, :],
                             mix_hi[:, 2 * h + c, :])

            def route():
                step_at = [0]

                def link(ins):
                    step_at[0] += 1
                    ins.then_inc(*DVE.done(("route", step_at[0])))
                    dve.wait_ge(*DVE.after("route", step_at[0]))

                def four(row):
                    return rt[:, row, :].rearrange("p (t n) -> p t n", n=4)

                def one(row):
                    return rt[:, row, 0:4].unsqueeze(2).to_broadcast([P, NT, 4])

                def first_best(x, best, key, hot):
                    link(dve.tensor_reduce(rt[:, best, 0:4], x, X, ALU.max))
                    link(dve.tensor_tensor(four(key), x, one(best), ALU.is_equal))
                    link(dve.tensor_tensor(four(key), four(key), rank[:, :].unsqueeze(1).to_broadcast([P, NT, 4]), ALU.mult))
                    link(dve.tensor_reduce(rt[:, 15, 0:4], four(key), X, ALU.max))
                    link(dve.tensor_tensor(four(hot), four(key), one(15), ALU.is_equal))

                for i in range(4):
                    link(dve.memset(rank[:, i:i + 1], 4.0 - i))
                dve.wait_ge(*DVE.after("rl"))
                g = rl[:, :, 0:4]
                first_best(g, 0, 1, 3)
                dve.tensor_tensor(four(2), g, one(0), ALU.subtract).then_inc(*DVE.done(("r_g",)))
                e4 = rl[:, :, 4:20].rearrange("p t (g e) -> p t e g", g=4)
                c4 = combine[:, :, :].rearrange("p t (g e) -> p t e g", g=4)
                hot_g = four(3).unsqueeze(2).to_broadcast([P, NT, 4, 4])
                link(dve.tensor_tensor(c4, e4, hot_g, ALU.mult))
                link(dve.tensor_reduce(four(4), c4, X, ALU.add))
                first_best(four(4), 5, 6, 7)
                link(dve.scalar_tensor_tensor(four(8), four(7), MASKED, four(4), ALU.mult, ALU.add))
                first_best(four(8), 10, 6, 11)
                dve.tensor_tensor(rt[:, 9, 0:4], rt[:, 10, 0:4], rt[:, 5, 0:4], ALU.subtract).then_inc(*DVE.done(("r_d",)))
                dve.wait_ge(*ACT.after("r_ed"))
                link(dve.tensor_scalar(rt[:, 12, 0:4], rt[:, 9, 0:4], 1.0, None, ALU.add))
                dve.wait_ge(*ACT.after("r_eg"))
                link(dve.tensor_reduce(rt[:, 13, 0:4], four(2), X, ALU.add))
                link(dve.tensor_tensor(rt[:, 12, 0:4], rt[:, 12, 0:4], rt[:, 13, 0:4], ALU.mult))
                link(dve.reciprocal(rt[:, 12, 0:4], rt[:, 12, 0:4]))
                link(dve.tensor_tensor(four(11), four(11), one(9), ALU.mult))
                link(dve.tensor_tensor(four(7), four(7), four(11), ALU.add))
                link(dve.tensor_tensor(four(7), four(7), one(12), ALU.mult))
                link(dve.tensor_tensor(c4, hot_g, four(7).unsqueeze(3).to_broadcast([P, NT, 4, 4]), ALU.mult))

            def conv():
                for b in range(2):
                    y = cy[:, b, :]
                    dve.wait_ge(*DVE.after("cu", b))
                    dve.wait_ge(*DVE.after("cu", "meta"))
                    dve.tensor_scalar(y, cu[:, b, N_META:], col("conv_w", 4 + b), col("conv_b", b), ALU.mult,
                                      ALU.add).then_inc(*DVE.done(("cy2", b)))
                    for j in (1, 0):
                        dve.wait_ge(*DVE.after(f"cy{j + 1}", b))
                        at = N_META - 2 + j
                        dve.scalar_tensor_tensor(y, cu[:, b, at:at + SEQ], col("conv_w", 2 * j + b), y, ALU.mult,
                                                 ALU.add).then_inc(*DVE.done((f"cy{j}", b)))
                    dve.wait_ge(*DVE.after("cy0", b))
                    dve.wait_ge(*ACT.after("cb", b))
                    dve.tensor_tensor(y, y, cb[:, b, :], ALU.mult).then_inc(*DVE.done(("cyb", b)))
                    dve.wait_ge(*DVE.after("cyb", b))
                    dve.wait_ge(*ACT.after("cz", b))
                    dve.tensor_tensor(y, y, cz[:, b, :], ALU.mult).then_inc(*DVE.done(("cy", b)))
                    dve.wait_ge(*ACT.after("conv_hi", b))
                    low_part(("conv_lo", b), mix_lo[:, b, :], y, mix_hi[:, b, :])

            def latent_sums():
                dve.memset(ss[:, 1:3, 0:9], 1.0).then_inc(*DVE.done(("lat0",)))
                dve.wait_ge(*DVE.after("lat0"))
                dve.wait_ge(*PE.after("lat_ss"))
                dve.tensor_scalar(ss[:, 1, 0:4], ps[:, 6, 0:4], 1.0 / 256, EPS, ALU.mult, ALU.add).then_inc(*DVE.done(("lat_q",)))
                dve.tensor_scalar(ss[:, 1, 4:8], ps[:, 6, 4:8], 1.0 / 128, EPS, ALU.mult, ALU.add).then_inc(*DVE.done(("lat_kv",)))
                dve.tensor_scalar(ss[0:N_META, 1, 8:9], ps[0:N_META, 6, 8:9], 1.0 / 128, EPS, ALU.mult,
                                  ALU.add).then_inc(*DVE.done(("lat_v",), ("v", "lat")))
                rsqrt_finish(("lat",), ss[:, 1, 0:9], ss[:, 2, 0:9], ss[:, 0, 0:9])

            def mla_prepare():
                dve.memset(ss[:, 3:6, 0:72], 1.0).then_inc(*DVE.done(("head0",)))
                dve.wait_ge(*DVE.after("head0"))
                dve.wait_ge(rope_in, 48)
                dve.wait_ge(*ACT.after("kr"))
                for t in range(NT + 1):
                    rows = P if t < NT else N_META
                    for n in range(2):
                        dve.wait_ge(*ACT.after("k_raw", n, t))
                    k3 = k_sb[0:rows, t, :].rearrange("p (h n) -> p h n", h=MLA_H)
                    dve.tensor_copy(k3[:, :, QKN:QKH], kr[0:rows, t, :].unsqueeze(1).to_broadcast([rows, MLA_H, QKR])
                                    ).then_inc(*DVE.done(("kr_in", t)))
                    for kind, base_col in (("q", 0), ("k", 32)):
                        if kind == "q" and t == NT:
                            continue
                        dve.wait_ge(*ACT.after("hsq", kind, t))
                        at = base_col + 8 * t
                        dve.tensor_reduce(ss[0:rows, 5, at:at + 8], sq[0:rows, :].rearrange("p (h n) -> p h n", h=MLA_H), X,
                                          ALU.add).then_inc(*DVE.done(("hss", kind, t)))
                dve.wait_ge(*DVE.after("hss", "k", NT))
                mean(("head",), ss[:, 3, 0:72], ss[:, 5, 0:72], QKH)
                rsqrt_finish(("head",), ss[:, 3, 0:72], ss[:, 4, 0:72], ss[:, 5, 0:72])
                before = None
                for t in range(NT + 1):
                    rows = P if t < NT else N_META
                    for g, (kind, x, base_col) in enumerate((("q", q_sb, 0), ("k", k_sb, 32))):
                        if kind == "q" and t == NT:
                            continue
                        at = base_col + 8 * t
                        x3 = x[0:rows, t, :].rearrange("p (h n) -> p h n", h=MLA_H)
                        r = ss[0:rows, 4, at:at + 8].unsqueeze(2).to_broadcast([rows, MLA_H, QKH])
                        dve.tensor_tensor(x3, x3, r, ALU.mult).then_inc(*DVE.done(("hn1", kind, t)))
                        dve.wait_ge(*DVE.after("hn1", kind, t))
                        dve.tensor_tensor(x3, x3, qk_gain[0:rows, g, :].unsqueeze(1).to_broadcast([rows, MLA_H, QKH]),
                                          ALU.mult).then_inc(*DVE.done(("hn2", kind, t)))
                        dve.wait_ge(*DVE.after("hn2", kind, t))
                        if before:
                            dve.wait_ge(*DVE.after(*before, 5))
                        before = ("rope_m", kind, t)
                        rope_turn(before, x3[:, :, QKN:QKH], x3[:, :, QKN:QKH], rows, MLA_H, QKR // 2, t, cos_m, sin_m)

            def k_transposed(tag, h, width):
                dve.wait_ge(*PE.after("kT", tag, h))
                if h >= 2:
                    dve.wait_ge(*PE.after(*last_scores(tag, h - 2)))
                dve.tensor_copy(kT[0:width, h % 2, :], psf[0:width, 5 * SEQ - N_META:6 * SEQ]).then_inc(*DVE.done(("kT", tag, h)))

            def mla_head(h):
                k_transposed("mla", h, QKH)
                for j in range(NT * h, NT * (h + 1)):
                    t = j % NT
                    n = P * (t + 1)
                    dve.wait_ge(*PE.after("S", "mla", j))
                    dve.tensor_reduce(sm[:, 0, j:j + 1], psf[:, 5 * SEQ - N_META:5 * SEQ + n], X,
                                      ALU.max).then_inc(*DVE.done(("max", "mla", j)))
                    dve.wait_ge(*DVE.after("max", "mla", j))
                    dve.tensor_scalar(sm[:, 1, j:j + 1], sm[:, 0, j:j + 1], -float(QKH) ** -0.5, None,
                                      ALU.mult).then_inc(*DVE.done(("nmax", "mla", j)))
                    dve.wait_ge(*ACT.after("exp", "mla", j))
                    dve.reciprocal(sm[:, 3, j:j + 1], sm[:, 2, j:j + 1]).then_inc(*DVE.done(("rsum", "mla", j)))
                    dve.wait_ge(*PE.after("PTm", "mla", j))
                    dve.tensor_copy(probT_m[:, j % 2, :], ps[0:N_META, 7, 0:P]).then_inc(*DVE.done(("PTm", "mla", j)))
                    dve.wait_ge(*PE.after("O", "mla", j))
                    dve.wait_ge(*DVE.after("rsum", "mla", j))
                    dve.wait_ge(*ACT.after("z_mla", t))
                    cols = slice(VH * h, VH * (h + 1))
                    dve.scalar_tensor_tensor(y_mla[:, t, cols], ps[:, 7, P:P + VH], sm[:, 3, j:j + 1], z_mla[:, t, cols],
                                             ALU.mult, ALU.mult).then_inc(*DVE.done(("y", "mla", j)))

            def ret_head(h):
                k_transposed("ret", h, RET_D)
                dve.wait_ge(decay_in[h % 2], 32 * (h // 2 + 1))
                dve.wait_ge(*PE.after("rS", h, "meta"))
                if h:
                    dve.wait_ge(*PE.after("rO", h - 1))
                dve.tensor_tensor(sd_m[:, :], ps[0:N_META, 7, :], decay_m[:, h % 2, :], ALU.mult).then_inc(*DVE.done(("sd", h, "meta")))
                for b in range(NT):
                    dve.wait_ge(*PE.after("rS", h, b))
                    dve.tensor_tensor(sd[:, b, P * b:SEQ], ps[:, b, P * b:SEQ], decay[:, h % 2, 0:SEQ - P * b],
                                      ALU.mult).then_inc(*DVE.done(("sd", h, b)))

            def ret_norm():
                dve.wait_ge(*ACT.after("ysq"))
                dve.tensor_reduce(ss[:, 5, 0:16], ysq[:, :, :].rearrange("p t (h n) -> p (t h) n", n=RET_D), X,
                                  ALU.add).then_inc(*DVE.done(("yss",)))
                dve.wait_ge(*DVE.after("yss"))
                mean(("ret",), ss[:, 3, 0:16], ss[:, 5, 0:16], RET_D)
                rsqrt_finish(("ret",), ss[:, 3, 0:16], ss[:, 4, 0:16], ss[:, 5, 0:16])
                for t in range(NT):
                    y = y_ret[:, t, :].rearrange("p (h n) -> p h n", h=RET_H)
                    dve.tensor_tensor(y, y, ss[:, 4, 4 * t:4 * t + 4].unsqueeze(2).to_broadcast([P, RET_H, RET_D]),
                                      ALU.mult).then_inc(*DVE.done(("yn", t)))
                    dve.wait_ge(*DVE.after("yn", t))
                    dve.tensor_tensor(y_ret[:, t, :], y_ret[:, t, :], z_ret[:, t, :], ALU.mult).then_inc(*DVE.done(("y_ret", t)))

            def mix_one():
                for c in range(6):
                    dve.wait_ge(*ACT.after("mix_hi", 2 + c))
                    low_part(("mix_lo", 2 + c), mix_lo[:, 2 + c, :], ps[:, 6 + c % 2, :], mix_hi[:, 2 + c, :],
                             1.0 if c < 4 else col("ret_norm"))

            for step, *a in order:
                if step == "constants":
                    dve.wait_ge(*PE.after("gains"))
                    dve.tensor_copy(gains[:, :], ps[:, 7, 0:64]).then_inc(*DVE.done(("gains",)))
                    dve.wait_ge(*DVE.after("gains"))
                elif step == "item":
                    item(*a)
                elif step == "norm":
                    norm(*a)
                elif step == "conv":
                    conv()
                elif step == "latent_sums":
                    latent_sums()
                elif step == "mla_prepare":
                    mla_prepare()
                elif step == "mla_head":
                    mla_head(*a)
                elif step == "ret_head":
                    ret_head(*a)
                elif step == "ret_norm":
                    ret_norm()
                elif step == "mix_one":
                    mix_one()
                elif step == "gla_head":
                    gla_head(*a)
                elif step == "gla_rstd":
                    gla_rstd()
                elif step == "mix":
                    mix(*a)
                elif step == "idx_key":
                    idx_key()
                elif step == "idx_scores":
                    idx_scores(*a)
                    if a[0] == NT - 1:
                        for t in range(1, NT):
                            top_keys(t)
                elif step == "dsa_prepare":
                    dsa_prepare()
                elif step == "dsa_head":
                    dsa_head(*a)
                elif step == "mem_prepare":
                    mem_prepare()
                elif step == "mem_head":
                    mem_head(*a)
                elif step == "route":
                    route()
                elif step == "barrier":
                    barrier(dve, a[0])
                    DVE.section = a[0]

        for engine, p in (("tensor", PE), ("scalar", ACT), ("vector", DVE), ("gpsimd", POOL)):
            known[engine] = p.at
            known[engine + " ends"] = p.count


def constants():
    f = np.float32
    pos = np.arange(L, dtype=f)

    def tables(dim):
        inv = f(1.0) / (f(10000.0) ** (np.arange(0, dim, 2, dtype=f) / f(dim)))
        ang = pos[:, None] * inv[None, :]
        return np.cos(ang).astype(f), np.sin(ang).astype(f)

    def tiles(table):
        n = table.shape[1]
        t = np.zeros((P, NT + 1, n), f)
        for i in range(NT):
            t[:, i] = table[N_META + P * i:N_META + P * (i + 1)]
        t[:N_META, NT] = table[:N_META]
        return t.reshape(P, -1)

    cm, sm = tables(QKR)
    cr, sr = tables(RET_D)
    rope = np.concatenate([tiles(cm), tiles(sm), tiles(cr), tiles(sr)], axis=1)
    log_g = np.log1p(-np.exp2(-5.0 - np.arange(RET_H)))
    m, c = np.arange(P)[:, None], np.arange(SEQ)[None, :]
    seen = (m // CHUNK) <= (c // CHUNK)
    decay = np.stack([np.where(seen, np.exp(g * np.abs(c - m)), 0.0) for g in log_g]) * RET_D ** -0.5
    mm = np.arange(N_META)[:, None]
    decay_m = np.stack([np.exp(g * (c + N_META - mm)) for g in log_g]) * RET_D ** -0.5
    j, i = np.arange(P)[:, None], np.arange(P)[None, :]
    return {
        "c_ident": np.eye(P, dtype=f),
        "c_gla_mask": ((j // CHUNK == i // CHUNK) & (i >= j)).astype(f),
        "c_dsa_mask": np.where(i <= j, 0.0, MASKED).astype(f),
        "c_mask_q": (np.arange(P) < CHUNK).astype(f)[None, :],
        "c_mask_k": np.full((1, CHUNK), MASKED, f),
        "c_rope": rope.astype(f),
        "c_decay": decay.astype(f),
        "c_decay_m": decay_m.astype(f),
        "c_scan": np.tile((np.arange(SEQ) % CHUNK != 0).astype(f), (P, 1)),
    }


def kernel(**inputs):
    import concourse.bacc as bacc
    from concourse.bass_utils import run_bass_kernel_spmd

    arrays = {name: np.ascontiguousarray(a) for name, a in inputs.items()}
    arrays.update(constants())

    def build(known):
        nc = bacc.Bacc("TRN2", target_bir_lowering=False, num_devices=1)
        w = {name: nc.dram_tensor(f"in_{name}", a.shape, mybir.dt.from_np(a.dtype), kind="ExternalInput").ap()
             for name, a in arrays.items()}
        out = nc.dram_tensor("out_0", (1, SEQ, D), F32, kind="ExternalOutput").ap()
        program(nc, w, out, known)
        return nc

    known = {}
    build(known)
    nc = build(known)
    r = run_bass_kernel_spmd(nc, [{f"in_{name}": a for name, a in arrays.items()}], core_ids=[0])
    return r.results[0]["out_0"]
```

```python
from contextlib import ExitStack

import numpy as np
import concourse.bass as bass
from concourse import mybir

F32 = mybir.dt.float32
F32R = mybir.dt.float32r
ALU = mybir.AluOpType
ACTF = mybir.ActivationFunctionType
X = mybir.AxisListType.X

P = 128
D = 1024
KC = D // P
SEQ = 512
NT = SEQ // P
N_META = 16
L = SEQ + N_META
EPS = 1e-6
CHUNK = 64
QKN, QKR, VH = 64, 32, 64
QKH = QKN + QKR
MLA_H = 8
RET_H, RET_D = 4, 64
MEM = 256
GLA_H, GLA_DV = 4, 256
DSA_H, DSA_G = 8, 4
IDX_H, IDX_D = 8, 64
TOPK = SEQ // 4
MEM_H = 4
N_EXP = 16
D_EXP = 256
MASKED = -1e30
PICKED = -3e38

RAW_SLOTS = 4
SPLIT_SLOTS = 4
UNIT = 1024

C_CX, C_CC, C_CQ, C_KR, C_MZ, C_RQ, C_RV = 0, 512, 1024, 1408, 1440, 1952, 2464
C_GQ, C_GK, C_GV, C_GG, C_GA, C_DQ, C_DK, C_IQ, C_IK, C_MQ, C_GATE = (
    0, 512, 1024, 2048, 3072, 3088, 4112, 4624, 5136, 5208, 6232)

GAINS, _row = {}, 0
for _name, _n in (("ln_w", 8), ("g_mix_2", 8), ("g_mem_2", 8), ("g_ffn_2", 8), ("q_a_norm", 2),
                  ("kv_a_norm", 1), ("conv_w", 6), ("conv_b", 2), ("dsa_q_norm_2", 1),
                  ("dsa_k_norm_2", 1), ("mem_q_norm_2", 2), ("mem_k_norm_2", 2), ("b_gla_a2_2", 4),
                  ("gla_norm_2", 2), ("ret_norm", 1), ("idx_k_norm_2", 1)):
    GAINS[_name] = _row
    _row += _n
N_GAINS = _row


class Progress:

    def __init__(self, nc, ctx, engine, sections, known):
        self.sems = {s: ctx.enter_context(nc.semaphore(f"{engine}_done_{s}")) for s in sections}
        self.count = dict.fromkeys(sections, 0)
        self.section = sections[0]
        self.at = {}
        self.known = known.setdefault(engine, {})
        self.ends = known.setdefault(engine + " ends", {})

    def done(self, *keys):
        self.count[self.section] += 1
        for key in keys:
            assert key not in self.at, key
            self.at[key] = (self.section, self.count[self.section])
        return self.sems[self.section], 1

    def after(self, *key):
        section, value = self.known.get(key, (self.section, 1)) if not self.ends else self.known[key]
        return self.sems[section], value

    def end_of(self, section):
        return self.sems[section], self.ends.get(section, 1)


def weight_items(w):
    items = {}

    def add(name, src, cols, chunks=KC, per=2):
        n = sum(b - a for a, b in cols)
        units = []
        for k0 in range(0, chunks, per):
            pieces, at = [], 0
            for a, b in cols:
                pieces.append((at, at + b - a, src[P * k0:P * (k0 + per), a:b].rearrange("(k p) n -> p k n", p=P)))
                at += b - a
            units.append((list(range(k0, k0 + per)), n, pieces))
        items[name] = units

    w_in, w_in2 = w["w_in"][0], w["w_in_2"][0]
    add("conv_a", w_in, [(C_CX, C_CC)])
    add("conv_b", w_in, [(C_CC, C_CQ)])
    add("latent", w_in, [(C_CQ, C_KR)])
    add("k_rope", w_in, [(C_KR, C_MZ)], per=8)
    add("ret_qk", w_in, [(C_RQ, C_RV)])
    add("ret_vz", w_in, [(C_RV, C_RV + 512)])
    add("mla_z", w_in, [(C_MZ, C_RQ)])
    for n in range(2):
        add(f"w_uq{n}", w["w_uq"][0], [(384 * n, 384 * n + 384)], chunks=2)
    for n in range(2):
        add(f"w_ukv{n}", w["w_ukv"][0], [(512 * n, 512 * n + 512)], chunks=1, per=1)
    for n in range(2):
        add(f"w_out{n}", w["w_out"][0], [(512 * n, 512 * n + 512)])
    add("small2", w_in2, [(C_GA, C_DQ), (C_IK, C_MQ)], per=8)
    add("gla_q", w_in2, [(C_GQ, C_GK)])
    add("gla_k", w_in2, [(C_GK, C_GV)])
    for n in range(2):
        add(f"gla_v{n}", w_in2, [(C_GV + 512 * n, C_GV + 512 * n + 512)])
    for n in range(2):
        add(f"gla_g{n}", w_in2, [(C_GG + 512 * n, C_GG + 512 * n + 512)])

    def branch(b, w_o):
        for n in range(2):
            c = C_GATE + D * b + 512 * n
            add(f"gate{b}{n}", w_in2, [(c, c + 512)])
            add(f"w_o{b}{n}", w_o[0], [(512 * n, 512 * n + 512)])

    branch(0, w["w_o_gla_2"])
    add("idx_q", w_in2, [(C_IQ, C_IK)])
    for n in range(2):
        add(f"dsa_q{n}", w_in2, [(C_DQ + 512 * n, C_DQ + 512 * n + 512)])
    add("dsa_kv", w_in2, [(C_DK, C_IQ)])
    branch(1, w["w_o_dsa_2"])
    for n in range(4):
        add(f"mem_kv{n}", w["w_mem_kv_2"][0], [(512 * n, 512 * n + 512)])
    for n in range(2):
        add(f"mem_q{n}", w_in2, [(C_MQ + 512 * n, C_MQ + 512 * n + 512)])
    branch(2, w["w_o_mem_2"])
    for n in range(2):
        add(f"w_out2{n}", w["w_out_2"][0], [(512 * n, 512 * n + 512)])
    items["router"] = [(list(range(KC)), 20, [
        (0, 4, w["w_r1_2"][0].rearrange("(k p) n -> p k n", p=P)),
        (4, 20, w["w_r2_2"][0].rearrange("(k p) n -> p k n", p=P))])]
    for e in range(N_EXP):
        units = []
        for k0 in range(0, KC, 2):
            rows = slice(P * k0, P * (k0 + 2))
            units.append(([k0, k0 + 1], 512, [
                (0, 256, w["w_gate_2"][0, e, rows, :].rearrange("(k p) n -> p k n", p=P)),
                (256, 512, w["w_up_2"][0, e, rows, :].rearrange("(k p) n -> p k n", p=P))]))
        items[f"expert{e}"] = units
    for e in range(N_EXP):
        for n in range(2):
            add(f"down{e}{n}", w["w_down_2"][0, e], [(512 * n, 512 * n + 512)], chunks=2)
    return items


def make_order():
    order = [("constants",), ("norm", "h")]
    order += [("item", n) for n in ("conv_a", "conv_b", "latent")]
    order += [("conv",), ("latent_sums",), ("item", "k_rope")]
    order += [("item", n) for n in ("w_uq0", "w_uq1", "w_ukv0", "w_ukv1")]
    order += [("mla_sums",), ("item", "mla_z"), ("mla_norm", 0), ("mla_norm", 1), ("item", "ret_qk")]
    order += [("mla_norm", t) for t in range(2, NT + 1)] + [("item", "ret_vz"), ("barrier", "mla")]
    pieces = [(p, h) for h in range(RET_H) for p in ("ret_transposes", "ret_scores", "ret_values")]
    n = NT * MLA_H
    for j in range(n + 3):
        if j >= 3:
            order += [("mla_values", j - 3)]
        if j % 2 == 0 and j >= 4 and pieces:
            order += [pieces.pop(0)]
        if 2 <= j < n + 2:
            order += [("mla_turn", j - 2)]
        if j % NT == 0 and j < n:
            order += [("mla_transposes", j // NT)]
        if j < n:
            order += [("mla_scores", j)]
    order += pieces
    order += [("ret_norm",), ("mix_one",), ("item", "w_out0"), ("item", "w_out1"), ("barrier", "gla")]
    order += [("norm", "h2")]
    order += [("item", n) for n in ("small2", "gla_q", "gla_k")]
    order += [("gla_low",), ("gla_decays", 0), ("item", "gla_v0"), ("gla_decays", 1), ("item", "gla_v1")]
    for h in range(GLA_H):
        order += [("gla_states", h), ("gla_values", h)]
        if h + 2 < GLA_H:
            order += [("gla_decays", h + 2)]
        if h == 1:
            order += [("gla_rstd", 0), ("item", "gla_g0")]
    order += [("gla_rstd", 1), ("item", "gla_g1"), ("item", "gate00"), ("mix", "gla")]
    order += [("item", n) for n in ("w_o00", "gate01", "w_o01")]
    order += [("barrier", "dsa"), ("idx_key",), ("item", "idx_q")]
    order += [("idx_scores", t) for t in range(1, NT)]
    order += [("item", "dsa_kv"), ("item", "dsa_q0"), ("dsa_prepare", "k"), ("item", "dsa_q1"), ("dsa_prepare", "q0")]
    order += [("dsa_prepare", "q1"), ("barrier", "dsa2")]
    n = NT * DSA_H
    for j in range(n + 3):
        order += [("dsa_values", j - 3)] * (j >= 3) + [("dsa_turn", j - 2)] * (2 <= j < n + 2) + [("dsa_scores", j)] * (j < n)
    order += [("item", n) for n in ("gate10", "w_o10", "gate11", "w_o11")]
    order += [("barrier", "mem"), ("norm", "mem")]
    order += [("item", n) for n in ("mem_kv0", "mem_kv1", "mem_kv2", "mem_kv3", "mem_q0")]
    order += [("mem_prepare", "k"), ("item", "mem_q1"), ("mem_prepare", "q0"), ("mem_prepare", "q1"), ("barrier", "mem2")]
    n = NT * MEM_H
    for j in range(n + 3):
        order += [("mem_values", j - 3)] * (j >= 3) + [("mem_turn", j - 2)] * (2 <= j < n + 2) + [("mem_scores", j)] * (j < n)
    order += [("item", n) for n in ("gate20", "w_o20", "gate21", "w_o21")]
    order += [("mix", "merged"), ("item", "w_out20"), ("item", "w_out21")]
    order += [("barrier", "experts"), ("norm", "ffn"), ("item", "router"), ("route",), ("item", "expert0")]
    for e in range(N_EXP):
        if e + 1 < N_EXP:
            order += [("item", f"expert{e + 1}")]
        order += [("item", f"down{e}0"), ("item", f"down{e}1")]
    return order


def sections_of(order):
    return ["start"] + [step[1] for step in order if step[0] == "barrier"]


NORMS = {"h": "ln_w", "h2": "g_mix_2", "ffn": "g_ffn_2", "mem": "g_mem_2"}


def program(nc, w, out, known):
    order = make_order()
    items = weight_items(w)
    units, first_unit = [], {}
    for step in order:
        if step[0] == "item":
            first_unit[step[1]] = len(units)
            units += items[step[1]]

    with ExitStack() as ctx:
        base = 16512

        def sb(name, shape, at_kb, dt=F32):
            assert base + at_kb * 1024 + 4 * int(np.prod(shape[1:])) <= nc.sbuf_usable_end, name
            return nc.alloc_sbuf_tensor_at(name, shape, dt, offset=base + round(at_kb * 32) * 32)

        def semaphore(name):
            return ctx.enter_context(nc.semaphore(name))

        ps = ctx.enter_context(nc.psum_tensor("ps", [P, 8, 512], F32))
        psf = ps[:, :, :].rearrange("p b n -> p (b n)")

        raw = sb("raw", [P, RAW_SLOTS, UNIT], 0)
        w_hi = sb("w_hi", [P, SPLIT_SLOTS, UNIT], 16, F32R)
        w_lo = sb("w_lo", [P, SPLIT_SLOTS, UNIT], 32, F32R)
        act_hi = sb("act_hi", [P, KC, L], 48, F32R)
        act_lo = sb("act_lo", [P, KC, L], 64.5, F32R)
        mix_hi = sb("mix_hi", [P, KC, SEQ], 81, F32R)
        mix_lo = sb("mix_lo", [P, KC, SEQ], 97, F32R)
        x1 = sb("x1", [P, NT, D], 113)
        gains = sb("gains", [P, 64], 129)
        ident = sb("ident", [P, P], 129.25)
        gla_mask = sb("gla_mask", [P, P], 129.75)
        dsa_mask = sb("dsa_mask", [P, P], 130.25)
        mask_q = sb("mask_q", [1, P], 130.75)
        mask_k = sb("mask_k", [1, CHUNK], 131.25)
        ones = sb("ones", [P, 2], 131.5)
        ss = sb("ss", [P, 8, 72], 131.75)
        sm = sb("sm", [P, 4, 32], 134)
        SC = 134.5
        xs = sb("xs", [P, NT, D], 81)
        meta = sb("meta", [N_META, D], 97)
        metas = sb("metas", [N_META, D], 101)
        g_rows = sb("g_rows", [64, P], 105)
        meta_t = sb("meta_t", [P, KC, N_META], 106)
        cx = sb("cx", [P, 2, L], SC)
        cb = sb("cb", [P, 2, SEQ], SC + 4.25)
        cu = sb("cu", [P, 2, L], SC + 8.25)
        cz = sb("cz", [P, 2, SEQ], SC + 12.5)
        cy = sb("cy", [P, 2, SEQ], SC + 16.5)
        q_sb = sb("q_sb", [P, NT, MLA_H * QKH], SC)
        k_sb = sb("k_sb", [P, NT + 1, MLA_H * QKH], SC + 12)
        v_sb = sb("v_sb", [P, NT + 1, MLA_H * VH], SC + 27)
        z_mla = sb("z_mla", [P, NT, MLA_H * VH], SC + 37)
        rqk = sb("rqk", [P, NT + 1, 512], SC + 45)
        rv = sb("rv", [P, NT + 1, 256], SC + 55)
        z_ret = sb("z_ret", [P, NT, 256], SC + 60)
        rope = sb("rope", [P, 5 * 96], SC + 64)
        kr = sb("kr", [P, NT + 1, QKR], SC + 66)
        qk_gain = sb("qk_gain", [P, 2, QKH], SC + 66.75)
        t0 = sb("t0", [P, 256], SC + 67.75)
        t1 = sb("t1", [P, 256], SC + 68.75)
        t2 = sb("t2", [P, 256], SC + 69.75)
        t3 = sb("t3", [P, 256], SC + 70.75)
        cos_m = rope[:, 0:80].rearrange("p (t n) -> p t n", t=5)
        sin_m = rope[:, 80:160].rearrange("p (t n) -> p t n", t=5)
        cos_r = rope[:, 160:320].rearrange("p (t n) -> p t n", t=5)
        sin_r = rope[:, 320:480].rearrange("p (t n) -> p t n", t=5)
        cq_sq = sb("cq_sq", [P, 2, SEQ], SC + 37)
        ckv_sq = sb("ckv_sq", [P, L], SC + 41)
        cq_hi = sb("cq_hi", [P, 2, SEQ], SC + 45, F32R)
        cq_lo = sb("cq_lo", [P, 2, SEQ], SC + 49, F32R)
        ckv_hi = sb("ckv_hi", [P, L], SC + 53, F32R)
        ckv_lo = sb("ckv_lo", [P, L], SC + 55.25, F32R)
        sq = sb("sq", [P, 2, MLA_H * QKH], 81 + 8)
        qT = sb("qT", [P, 2, SEQ], 48)
        kT = sb("kT", [P, 2, L], 52)
        prob = sb("prob", [P, 3, L], 56.25)
        probT = sb("probT", [P, 2, SEQ], 62.5)
        probT_m = sb("probT_m", [N_META, 2, P], 66.5)
        y_mla = sb("y_mla", [P, NT, MLA_H * VH], 67.5)
        y_ret = sb("y_ret", [P, NT, 256], 75.5)
        sd = sb("sd", [P, NT, SEQ], 85)
        ysq = sb("ysq", [P, NT, 256], 85)
        sd_m = sb("sd_m", [N_META, SEQ], 93)
        decay = sb("decay", [P, SEQ], 95)
        rqT = sb("rqT", [P, 2, SEQ], 101)
        rkT = sb("rkT", [P, 2, L], 105)
        decay_m = sb("decay_m", [N_META, SEQ], 109.25)

        merged = sb("merged", [P, NT, D], SC)
        sm2 = sb("sm2", [P, NT, 88], SC + 16)
        gate = sb("gate", [P, NT, 512], SC + 17.5)
        gate_bias = sb("gate_bias", [P, 2, 512], SC + 25.5)
        gv = sb("gv", [P, NT, D], SC)
        gq = sb("gq", [P, GLA_H, SEQ], SC + 17.5)
        gk = sb("gk", [P, GLA_H, SEQ], SC + 25.5)
        go = sb("go", [P, NT, D], SC + 33.5)
        state = sb("state", [P, 8, GLA_DV], SC + 49.5)
        g_silu = sb("g_silu", [P, 2, 512], SC + 57.5)
        low_t = sb("low_t", [16, SEQ], SC + 61.5)
        w_a2 = sb("w_a2", [16, 512], SC + 63.5)
        scan_mask = sb("scan_mask", [P, SEQ], SC + 65.5)
        g_dec = sb("g_dec", [P, 2, 8], SC + 67.5)
        gz = sb("gz", [P, SEQ], 81)
        gab = sb("gab", [P, SEQ], 83)
        gex = sb("gex", [P, SEQ], 85)
        glc = sb("glc", [P, SEQ], 87)
        gsq = sb("gsq", [P, GLA_DV], 89)
        g_qd = sb("g_qd", [P, 2, SEQ], 90)
        g_ki = sb("g_ki", [P, 2, SEQ], 94)
        g_ke = sb("g_ke", [P, 2, SEQ], 98)
        g_keT = sb("g_keT", [P, 2, SEQ], 102)
        g_att = sb("g_att", [P, 2, SEQ], 106)
        dq = sb("dq", [P, NT, D], 81)
        dk = sb("dk", [P, NT, 256], 101)
        d_sq = sb("d_sq", [P, 2, 512], 97)
        ik2 = sb("ik2", [P, NT, P], 105)
        dqT = sb("dqT", [P, DSA_H, SEQ], SC + 17.5)
        iqT = sb("iqT", [P, 4, SEQ], SC + 33.5)
        dkT = sb("dkT", [P, 2, SEQ], SC + 41.5)
        dv = sb("dv", [P, NT, 256], SC + 45.5)
        ikT = sb("ikT", [P, SEQ], SC + 49.5)
        d_mask = sb("d_mask", [P, 1280], SC + 51.5)
        work = sb("work", [P, 3, SEQ], SC + 56.5)
        rel = sb("rel", [P, 2, SEQ], SC + 62.5)
        d_probT = sb("d_probT", [P, 2, SEQ], SC + 62.5)
        d_prob = sb("d_prob", [P, 3, SEQ], SC + 66.5)
        best8 = sb("best8", [P, 8], SC + 73)
        mem_in = sb("mem_in", [P, 2, D], 81)
        mem_sc = sb("mem_sc", [P, 2, D], 89)
        mk = sb("mk", [P, 2, D], SC + 17.5)
        mv = sb("mv", [P, 2, D], SC + 25.5)
        mkT = sb("mkT", [P, 8, MEM], SC + 33.5)
        mem_hi = sb("mem_hi", [P, KC, MEM], SC + 41.5, F32R)
        mem_lo = sb("mem_lo", [P, KC, MEM], SC + 49.5, F32R)
        mqT = sb("mqT", [P, 8, SEQ], SC + 41.5)
        m_prob = sb("m_prob", [P, 3, MEM], SC + 57.5)
        m_probT = sb("m_probT", [P, 2, MEM], SC + 60.5)
        hid_hi = sb("hid_hi", [P, 2, 2, SEQ], SC, F32R)
        hid_lo = sb("hid_lo", [P, 2, 2, SEQ], SC + 8, F32R)
        hid = sb("hid", [P, 2, SEQ], SC + 16)
        e_silu = sb("e_silu", [P, 2, SEQ], SC + 20)
        rl = sb("rl", [P, NT, 20], SC + 24)
        r_bias = sb("r_bias", [P, 20], SC + 24.5)
        rank = sb("rank", [P, 4], SC + 24.625)
        rt = sb("rt", [P, 16, 16], SC + 24.75)
        combine = sb("combine", [P, NT, N_EXP], SC + 26)

        bias_in = [semaphore(f"bias_in{i}") for i in range(2)]
        gla_in = semaphore("gla_in")
        mem_landed = semaphore("mem_landed")
        route_in = semaphore("route_in")
        w_landed = [semaphore(f"w_landed{i}") for i in range(RAW_SLOTS)]
        landed, total = [], [0] * RAW_SLOTS
        for g, (_, _, pieces) in enumerate(units):
            total[g % RAW_SLOTS] += 16 * len(pieces)
            landed.append(total[g % RAW_SLOTS])
        const_in = semaphore("const_in")
        gains_in = semaphore("gains_in")
        zeroed = semaphore("zeroed")
        x_in = semaphore("x_in")
        rope_in = semaphore("rope_in")
        decay_in = semaphore("decay_in")
        stored = semaphore("stored")

        LAST = order[-1][1]
        sections = sections_of(order)
        PE = Progress(nc, ctx, "tensor", sections, known)
        ACT = Progress(nc, ctx, "scalar", sections, known)
        DVE = Progress(nc, ctx, "vector", sections, known)
        POOL = Progress(nc, ctx, "gpsimd", sections, known)

        def col(gain, n=0):
            return gains[:, GAINS[gain] + n:GAINS[gain] + n + 1]

        NORM_TILES = {"h": [(x1[:, t, :], xs[:, t, :], P) for t in range(NT)] + [(meta[:, :], metas[:, :], N_META)],
                      "h2": [(x1[:, t, :], xs[:, t, :], P) for t in range(NT)],
                      "ffn": [(x1[:, t, :], xs[:, t, :], P) for t in range(NT)],
                      "mem": [(mem_in[:, t, :], mem_sc[:, t, :], P) for t in range(2)]}

        def barrier(eng, section):
            before = sections[sections.index(section) - 1]
            for other in (PE, ACT, DVE, POOL):
                if other.ends.get(before, 1):
                    eng.wait_ge(*other.end_of(before))


        def last_scores(tag, h):
            return ("S", "mla", NT * h + NT - 1) if tag == "mla" else ("rS", h, NT - 1)

        def idx_of(i):
            return 1 + i // IDX_H, i % IDX_H

        def state_bank(n):
            return 2 * (n % 2) + n // 4, slice(GLA_DV * (n // 2 % 2), GLA_DV * (n // 2 % 2 + 1))

        MEM_BANKS = (7, 3, 1, 2, 7, 3, 1, 2)

        HEAD_TILES = [(kind, t) for t in range(NT + 1) for kind in ("q", "k") if (kind, t) != ("q", NT)]

        HEAD_STATS = {("dsa", "q0"): (0, 16), ("dsa", "q1"): (16, 32), ("dsa", "k"): (32, 40),
                      ("mem", "k"): (0, 8), ("mem", "q0"): (8, 16), ("mem", "q1"): (16, 24)}

        def gla_stat(h, t):
            return 8 * (h // 2) + 2 * t + h % 2

        def norm_dest(name):
            return (mem_hi, 0) if name == "mem" else (act_hi, N_META)

        def norm_lo(name):
            return mem_lo

        def MIX_NEEDS(tag, c, t):
            return DVE.after("go", c // 4, t, c // 2 % 2) if tag == "gla" else DVE.after("merged", 2, c // 4, t)

        def NORM_NEEDS(name, i):
            return []

        def ITEM_NEEDS(name):
            if name in ("conv_a", "conv_b", "latent", "k_rope", "mla_z", "ret_qk", "ret_vz"):
                return [(DVE, ("lo", "h", KC - 1)), (DVE, ("meta_lo", "h"))]
            if name.startswith("w_uq"):
                return [(DVE, ("cq_lo", 1))]
            if name.startswith("w_ukv"):
                return [(DVE, ("ckv_lo", "meta"))]
            if name in ("w_out0", "w_out1"):
                return [(DVE, ("conv_lo", 1)), (DVE, ("mix_lo", KC - 1))]
            if name.startswith(("small2", "gla", "gate", "idx", "dsa", "mem_q")):
                return [(DVE, ("lo", "h2", KC - 1))]
            if name.startswith("mem_kv"):
                return [(DVE, ("lo", "mem", KC - 1))]
            if name.startswith("w_o0"):
                return [(DVE, ("mix_lo", "gla", KC - 1))]
            if name.startswith("w_o1"):
                return [(DVE, ("mix_lo", "dsa", KC - 1))]
            if name.startswith("w_out2"):
                return [(DVE, ("mix_lo", "merged", KC - 1))]
            if name.startswith("w_o2"):
                return [(DVE, ("mix_lo", "mem", KC - 1))]
            if name.startswith(("router", "expert")):
                return [(DVE, ("lo", "ffn", KC - 1))]
            if name.startswith("down"):
                return [(DVE, ("hid_lo", int(name[4:-1]), 1))]
            raise KeyError(name)

        def item_readers(name, b):
            n = int(name[-1]) if name[-1].isdigit() else 0
            if name == "conv_a":
                return [(ACT, ("cx", "meta"))] if b == "meta" else [(ACT, ("cx", b) if b < 2 else ("cb", b - 2))]
            if name == "conv_b":
                return [(DVE, ("cu", "meta"))] if b == "meta" else [(DVE, ("cu", b)) if b < 2 else (ACT, ("cz", b - 2))]
            if name == "latent":
                return [(DVE, ("ckv_lo", "meta"))] if b == "meta" else [(DVE, ("cq_lo", b) if b < 2 else ("ckv_lo",))]
            if name == "k_rope":
                return [(ACT, ("kr",))]
            if name.startswith("w_uq"):
                return [(ACT, ("q_raw", n, b))]
            if name.startswith("w_ukv"):
                return [(DVE, ("v_raw", n, b))]
            if name == "mla_z":
                return [(ACT, ("z_mla", b))]
            if name == "ret_qk":
                return [(DVE, ("rope_r", b, 3))]
            if name == "ret_vz":
                return [(ACT, ("z_ret", b) if b < NT else ("rv", b))]
            if name in ("w_out0", "w_out1"):
                return [(DVE, ("x", name, b))]
            if name.startswith("w_out2"):
                return [(DVE, ("x", name, b))]
            if name == "small2":
                return [(ACT, ("sm2",))]
            if name in ("gla_q", "gla_k"):
                return [(ACT, (name, b))]
            if name.startswith("gla_v"):
                return [(ACT, ("gv", n, b))]
            if name.startswith("gla_g"):
                return [(ACT, ("g_silu", n, b))]
            if name.startswith("gate"):
                return [(DVE, ("gate_sum", int(name[4]), n, b))]
            if name.startswith("w_o"):
                return [(DVE, ("gated", int(name[3]), n, b))]
            if name == "idx_q":
                return [(ACT, ("iqT", b))]
            if name.startswith("dsa_q"):
                return [(ACT, ("dq", n, b))]
            if name == "dsa_kv":
                return [(ACT, ("dv", b))]
            if name.startswith("mem_kv"):
                return [(ACT, ("mkv", n, b))]
            if name.startswith("mem_q"):
                return [(ACT, ("mq", n, b))]
            if name == "router":
                return [(DVE, ("rl",))]
            if name.startswith("expert"):
                e = int(name[6:])
                return [(ACT, ("e_silu", e, b)) if b < 2 else (DVE, ("hid", e, b - 2))]
            if name.startswith("down"):
                return [(DVE, ("x", name, b))]
            raise KeyError(name)

        block = ctx.enter_context(nc.Block())

        @block.sync
        def _(sp):
            for t in range(NT):
                sp.dma_start(x1[:, t, :], w["x"][0, P * t:P * (t + 1), :]).then_inc(x_in, 16)
            sp.dma_start(meta[:, :], w["meta_tokens"]).then_inc(x_in, 16)
            sp.dma_start(ident[:, :], w["c_ident"]).then_inc(const_in, 16)
            sp.dma_start(gla_mask[:, :], w["c_gla_mask"]).then_inc(const_in, 16)
            sp.dma_start(dsa_mask[:, :], w["c_dsa_mask"]).then_inc(const_in, 16)
            sp.dma_start(mask_q[:, :], w["c_mask_q"]).then_inc(const_in, 16)
            sp.dma_start(mask_k[:, :], w["c_mask_k"]).then_inc(const_in, 16)
            sp.dma_start(rope[:, :], w["c_rope"]).then_inc(rope_in, 16)
            sp.dma_start(qk_gain[:, 0, :], w["q_norm"][0].partition_broadcast(P)).then_inc(rope_in, 16)
            sp.dma_start(qk_gain[:, 1, :], w["k_norm"][0].partition_broadcast(P)).then_inc(rope_in, 16)
            for g, (chunks, n, pieces) in enumerate(units):
                if g >= RAW_SLOTS:
                    sp.wait_ge(*POOL.after("w_lo", g - RAW_SLOTS))
                slot = raw[:, g % RAW_SLOTS, 0:len(chunks) * n].rearrange("p (k n) -> p k n", n=n)
                for a, b, src in pieces:
                    sp.dma_start(slot[:, :, a:b], src).then_inc(w_landed[g % RAW_SLOTS], 16)
            for t in range(NT):
                sp.wait_ge(*DVE.after("x", LAST, t))
                sp.dma_start(out[0, P * t:P * (t + 1), :], x1[:, t, :]).then_inc(stored, 16)
            sp.wait_ge(stored, 16 * NT)

        @block.gpsimd
        def _(pool):
            pool.memset(g_rows[:, :], 0.0).then_inc(zeroed, 1)
            pool.memset(ones[:, :], 1.0).then_inc(zeroed, 1)
            pool.wait_ge(zeroed, 2)
            for name, row in GAINS.items():
                src = w[name]
                src = src if name == "conv_w" else src[0]
                if name in ("ret_norm", "idx_k_norm_2"):
                    for half in range(2):
                        pool.dma_start(g_rows[row:row + 1, 64 * half:64 * half + 64], w[name]).then_inc(gains_in, 16)
                elif name == "conv_w":
                    pool.dma_start(g_rows[row:row + 6, :], src[0].rearrange("j (c p) -> (j c) p", p=P)).then_inc(gains_in, 16)
                else:
                    n = src.shape[0] // P
                    pool.dma_start(g_rows[row:row + n, :], src.rearrange("(c p) -> c p", p=P)).then_inc(gains_in, 16)
            fill = [0]

            def split_low(upto):
                for g in range(fill[0], upto):
                    chunks, n, _ = units[g]
                    a = len(chunks) * n
                    pool.wait_ge(*ACT.after("w_hi", g))
                    pool.tensor_tensor(w_lo[:, g % SPLIT_SLOTS, 0:a], raw[:, g % RAW_SLOTS, 0:a],
                                       w_hi[:, g % SPLIT_SLOTS, 0:a].bitcast(F32),
                                       ALU.subtract).then_inc(*POOL.done(("w_lo", g)))
                fill[0] = max(fill[0], upto)

            def mla_norm_keys(t):
                rows = P if t < NT else N_META
                at = 32 + 8 * t
                x3 = k_sb[0:rows, t, :].rearrange("p (h n) -> p h n", h=MLA_H)
                pool.wait_ge(*DVE.after("r", "head"))
                pool.tensor_tensor(x3, x3, ss[0:rows, 4, at:at + 8].unsqueeze(2).to_broadcast([rows, MLA_H, QKH]),
                                   ALU.mult).then_inc(*POOL.done(("hn1", "k", t)))
                pool.wait_ge(*POOL.after("hn1", "k", t))
                pool.tensor_tensor(x3, x3, qk_gain[0:rows, 1, :].unsqueeze(1).to_broadcast([rows, MLA_H, QKH]),
                                   ALU.mult).then_inc(*POOL.done(("hn2", "k", t)))

            for step, *a in order:
                if step == "mla_norm":
                    mla_norm_keys(a[0])
                elif step == "barrier":
                    barrier(pool, a[0])
                    POOL.section = a[0]
                elif step == "item":
                    split_low(min(len(units), first_unit[a[0]] + len(items[a[0]]) + 2))

        n_gain_dmas = len(GAINS) + 2

        @block.tensor
        def _(pe):
            readers = {b: [] for b in range(8)}

            def claim(bank, *who):
                for engine, key in readers[bank]:
                    pe.wait_ge(*engine.after(*key))
                readers[bank] = list(who)

            def product(dst, l_hi, l_lo, r_hi, r_lo, start, stop, skip=False):
                pe.matmul(dst, l_hi, r_hi, start=start, stop=False, skip_group_check=skip)
                pe.matmul(dst, l_hi, r_lo, start=False, stop=False, skip_group_check=skip)
                return pe.matmul(dst, l_lo, r_hi, start=False, stop=stop, skip_group_check=skip)

            def item(name):
                its = items[name]
                g0 = first_unit[name]
                meta_blocks = {"conv_a": 2, "conv_b": 2, "latent": 1}.get(name, 0)
                n_acc = {"latent": 3, "mem_kv0": 2, "mem_kv1": 2, "mem_kv2": 2, "mem_kv3": 2}.get(name, NT)
                by_feature = name in ("conv_a", "conv_b", "latent", "gla_q", "gla_k", "idx_q") or name.startswith("expert")
                small = name in ("k_rope", "small2", "router")
                meta_row = name in ("k_rope", "w_ukv0", "w_ukv1", "ret_qk", "ret_vz")
                if name.startswith("w_uq"):
                    a_hi, a_lo, off = cq_hi, cq_lo, 0
                elif name.startswith("w_ukv"):
                    a_hi, a_lo, off = ckv_hi[:, :].unsqueeze(1), ckv_lo[:, :].unsqueeze(1), N_META
                elif name.startswith("w_o"):
                    a_hi, a_lo, off = mix_hi, mix_lo, 0
                elif name.startswith("mem_kv"):
                    a_hi, a_lo, off = mem_hi, mem_lo, 0
                elif name.startswith("down"):
                    e = int(name[4:-1])
                    a_hi, a_lo, off = hid_hi[:, e % 2, :, :], hid_lo[:, e % 2, :, :], 0
                else:
                    a_hi, a_lo, off = act_hi, act_lo, N_META
                for key in ITEM_NEEDS(name):
                    pe.wait_ge(*key[0].after(*key[1]))
                last_u = len(its) - 1
                for u, (chunks, n, _) in enumerate(its):
                    g = g0 + u
                    pe.wait_ge(*POOL.after("w_lo", g))
                    wh = w_hi[:, g % SPLIT_SLOTS, 0:len(chunks) * n].rearrange("p (k n) -> p k n", n=n)
                    wl = w_lo[:, g % SPLIT_SLOTS, 0:len(chunks) * n].rearrange("p (k n) -> p k n", n=n)
                    n_all = n_acc + meta_row
                    for b in range(n_all):
                        bank = 5 if small else (4 + b if name.startswith("down") else b)
                        if u == 0 and (b == 0 or not small):
                            claim(bank, *item_readers(name, b))
                        for j, k in enumerate(chunks):
                            first = u == 0 and j == 0 and (b == 0 or not small)
                            last = u == last_u and j == len(chunks) - 1
                            if by_feature:
                                cols = slice(P * b, P * b + P)
                                mm = product(ps[:, bank, :], wh[:, j, cols], wl[:, j, cols],
                                             a_hi[:, k, off:off + SEQ], a_lo[:, k, off:off + SEQ], first, last)
                            else:
                                rows = slice(off + P * b, off + P * b + P) if b < NT else slice(0, P)
                                dst = ps[:, bank, n * b:n * b + n] if small else ps[:, bank, 0:n]
                                mm = product(dst, a_hi[:, k, rows], a_lo[:, k, rows], wh[:, j, :], wl[:, j, :],
                                             first, last, skip=small)
                        keys = [("unit", g)] if b == n_all - 1 and not meta_blocks else []
                        if u == last_u:
                            keys.append(("acc", name, b))
                        if keys:
                            mm.then_inc(*PE.done(*keys))
                    for b in range(meta_blocks):
                        if u == 0 and b == 0:
                            claim(4, *item_readers(name, "meta"))
                        for j, k in enumerate(chunks):
                            at = P * (b + (2 if name == "latent" else 0))
                            cols = slice(at, at + P)
                            mm = product(ps[:, 4, N_META * b:N_META * (b + 1)], wh[:, j, cols], wl[:, j, cols],
                                         a_hi[:, k, 0:N_META], a_lo[:, k, 0:N_META],
                                         u == 0 and j == 0 and b == 0, u == last_u and j == len(chunks) - 1, skip=True)
                    if meta_blocks:
                        mm.then_inc(*PE.done(("unit", g), *([("acc", name, "meta")] if u == last_u else [])))

            def norm(name):
                tiles = NORM_TILES[name]
                full = [t for t in tiles if t[2] == P]
                for k in range(KC):
                    bank = 4 + k % 4
                    claim(bank, (DVE, ("lo", name, k)))
                    for i, (_, scaled, _) in enumerate(full):
                        pe.wait_ge(*DVE.after("scaled", name, i))
                        tr = pe.transpose(ps[:, bank, P * i:P * i + P], scaled[:, P * k:P * k + P], ident[:, :])
                    tr.then_inc(*PE.done(("T", name, k)))
                if len(full) < len(tiles):
                    claim(3, (DVE, ("meta_t", name)))
                    pe.wait_ge(*DVE.after("scaled", name, len(full)))
                    for k in range(KC):
                        tr = pe.transpose(ps[:, 3, N_META * k:N_META * (k + 1)], tiles[-1][1][:, P * k:P * k + P],
                                          ident[0:N_META, 0:N_META])
                    tr.then_inc(*PE.done(("T", name, "meta")))

            def attention_transposes(tag, h, width, q_bank, k_bank, q_src, k_src):
                claim(q_bank, (ACT, ("qT", tag, h)))
                for t in range(NT):
                    tr = pe.transpose(ps[0:width, q_bank, P * t:P * t + P], q_src(t), ident[:, :])
                tr.then_inc(*PE.done(("qT", tag, h)))
                claim(k_bank, (DVE, ("kT", tag, h)))
                claim(k_bank + 1, (DVE, ("kT", tag, h)))
                pe.transpose(ps[0:width, k_bank, SEQ - N_META:SEQ], k_src(NT)[0:N_META, :], ident[0:N_META, 0:N_META])
                for t in range(NT):
                    tr = pe.transpose(ps[0:width, k_bank + 1, P * t:P * t + P], k_src(t), ident[:, :])
                tr.then_inc(*PE.done(("kT", tag, h)))

            def mla_scores(j):
                h, t = divmod(j, NT)
                n = P * (t + 1)
                if t == 0:
                    pe.wait_ge(*ACT.after("qT", "mla", h))
                    pe.wait_ge(*DVE.after("kT", "mla", h))
                claim(4, (ACT, ("exp", "mla", j)))
                claim(5, (ACT, ("exp", "mla", j)))
                q = qT[0:QKH, h % 2, P * t:P * t + P]
                pe.matmul(ps[:, 4, SEQ - N_META:SEQ], q, kT[0:QKH, h % 2, 0:N_META], start=True, stop=True)
                pe.matmul(ps[:, 5, 0:n], q, kT[0:QKH, h % 2, N_META:N_META + n], start=True, stop=False)
                pe.matmul(ps[:, 5, n - CHUNK:n], mask_q[:, :], mask_k[:, :], start=False,
                          stop=True).then_inc(*PE.done(("S", "mla", j)))

            def mla_turn(j):
                h, t = divmod(j, NT)
                pe.wait_ge(*ACT.after("exp", "mla", j))
                claim(7, (DVE, ("PTm", "mla", j)))
                pe.transpose(ps[0:N_META, 7, 0:P], prob[:, j % 3, 0:N_META], ident[:, :]).then_inc(*PE.done(("PTm", "mla", j)))
                claim(6, (ACT, ("PT", "mla", j)))
                for b in range(t + 1):
                    tr = pe.transpose(ps[:, 6, P * b:P * b + P], prob[:, j % 3, N_META + P * b:N_META + P * (b + 1)], ident[:, :])
                tr.then_inc(*PE.done(("PT", "mla", j)))

            def mla_values(j):
                h, t = divmod(j, NT)
                pe.wait_ge(*ACT.after("PT", "mla", j))
                claim(7, (DVE, ("y", "mla", j)))
                pe.matmul(ps[:, 7, P:P + VH], probT_m[:, j % 2, :], v_sb[0:N_META, NT, VH * h:VH * (h + 1)], start=True, stop=False)
                for b in range(t + 1):
                    mm = pe.matmul(ps[:, 7, P:P + VH], probT[:, j % 2, P * b:P * b + P], v_sb[:, b, VH * h:VH * (h + 1)],
                                   start=False, stop=(b == t))
                mm.then_inc(*PE.done(("O", "mla", j)))

            def mla_transposes(h):
                attention_transposes("mla", h, QKH, 6, 4, lambda t: q_sb[:, t, QKH * h:QKH * (h + 1)],
                                     lambda t: k_sb[:, t, QKH * h:QKH * (h + 1)])

            def ret_transposes(h):
                attention_transposes("ret", h, RET_D, 0, 1, lambda t: rqk[:, t, RET_D * h:RET_D * (h + 1)],
                                     lambda t: rqk[:, t, 256 + RET_D * h:256 + RET_D * (h + 1)])

            def ret_scores(h):
                pe.wait_ge(*ACT.after("qT", "ret", h))
                pe.wait_ge(*DVE.after("kT", "ret", h))
                claim(3, (DVE, ("sd", h, "meta")))
                pe.matmul(ps[0:N_META, 3, :], rkT[0:RET_D, h % 2, 0:N_META], rqT[0:RET_D, h % 2, :],
                          start=True, stop=True).then_inc(*PE.done(("rS", h, "meta")))
                for b in range(NT):
                    claim(b, (DVE, ("sd", h, b)))
                    pe.matmul(ps[:, b, P * b:SEQ], rkT[0:RET_D, h % 2, N_META + P * b:N_META + P * (b + 1)],
                              rqT[0:RET_D, h % 2, P * b:SEQ], start=True, stop=True).then_inc(*PE.done(("rS", h, b)))

            def ret_values(h):
                pe.wait_ge(*DVE.after("sd", h, "meta"))
                claim(0, (ACT, ("rO", h)))
                for t in range(NT):
                    dst = ps[:, 0, RET_D * t:RET_D * (t + 1)]
                    pe.matmul(dst, sd_m[:, P * t:P * t + P], rv[0:N_META, NT, RET_D * h:RET_D * (h + 1)], start=True, stop=False)
                    for b in range(t + 1):
                        pe.wait_ge(*DVE.after("sd", h, b))
                        mm = pe.matmul(dst, sd[:, b, P * t:P * t + P], rv[:, b, RET_D * h:RET_D * (h + 1)],
                                       start=False, stop=(b == t))
                mm.then_inc(*PE.done(("rO", h)))

            def gla_low():
                pe.wait_ge(*ACT.after("sm2"))
                claim(6, (ACT, ("low_t",)))
                for t in range(NT):
                    tr = pe.transpose(ps[0:16, 6, P * t:P * t + P], sm2[:, t, 0:16], ident[:, :])
                tr.then_inc(*PE.done(("low_t",)))

            def gla_decays(h):
                if h == 0:
                    pe.wait_ge(gla_in, 32)
                    pe.wait_ge(*ACT.after("low_t"))
                claim(7, (ACT, ("g_z", h)))
                pe.matmul(ps[:, 7, :], w_a2[:, P * h:P * h + P], low_t[:, :], start=True,
                          stop=True).then_inc(*PE.done(("g_z", h)))

            def gla_states(h):
                s = h % 2
                if h == 0:
                    for t in range(NT):
                        pe.wait_ge(*ACT.after("gv", 0, t))
                        pe.wait_ge(*ACT.after("gv", 1, t))
                claim(6, (ACT, ("g_keT", h)))
                pe.wait_ge(*DVE.after("g_ke", h))
                for t in range(NT):
                    tr = pe.transpose(ps[:, 6, P * t:P * t + P], g_ke[:, s, P * t:P * t + P], ident[:, :])
                tr.then_inc(*PE.done(("g_keT", h)))
                claim(7, (DVE, ("g_att", h)))
                for t in range(NT):
                    mm = pe.matmul(ps[:, 7, P * t:P * t + P], g_ki[:, s, P * t:P * t + P], g_qd[:, s, P * t:P * t + P],
                                   start=True, stop=True)
                mm.then_inc(*PE.done(("g_att", h)))
                pe.wait_ge(*ACT.after("g_keT", h))
                for pair in ((0, 2), (1, 3), (4, 6), (5,)):
                    bank = state_bank(pair[0])[0]
                    claim(bank, (DVE, ("g_state", h, pair[-1])))
                    for n in pair:
                        rows = slice(CHUNK * (n % 2), CHUNK * (n % 2) + CHUNK)
                        mm = pe.matmul(ps[:, bank, state_bank(n)[1]], g_keT[rows, s, P * (n // 2):P * (n // 2) + P],
                                       gv[rows, n // 2, GLA_DV * h:GLA_DV * (h + 1)], start=True, stop=True)
                    mm.then_inc(*PE.done(("g_upd", h, bank)))

            def gla_values(h):
                s = h % 2
                pe.wait_ge(*DVE.after("g_att", h))
                for t in range(NT):
                    bank = 4 + t % 2
                    claim(bank, (ACT, ("g_oss", h, t)))
                    v = gv[:, t, GLA_DV * h:GLA_DV * (h + 1)]
                    if t == 0:
                        pe.matmul(ps[0:CHUNK, bank, 0:GLA_DV], g_att[:, s, 0:CHUNK], v, start=True, stop=True)
                        pe.matmul(ps[CHUNK:P, bank, 0:GLA_DV], g_att[:, s, CHUNK:P], v, start=True, stop=False)
                    else:
                        pe.matmul(ps[:, bank, 0:GLA_DV], g_att[:, s, P * t:P * t + P], v, start=True, stop=False)
                    for half in range(2):
                        n = 2 * t + half
                        if n == 0:
                            continue
                        pe.wait_ge(*DVE.after("g_state", h, n - 1))
                        rows = slice(CHUNK * half, CHUNK * half + CHUNK)
                        mm = pe.matmul(ps[rows, bank, 0:GLA_DV], g_qd[:, s, CHUNK * n:CHUNK * (n + 1)], state[:, n, :],
                                       start=False, stop=True)
                    mm.then_inc(*PE.done(("g_o", h, t)))

            def mix(tag):
                for c in range(KC):
                    bank = 4 + c % 4
                    claim(bank, (DVE, ("mix_lo", tag, c)))
                    for t in range(NT):
                        pe.wait_ge(*MIX_NEEDS(tag, c, t))
                        src = go if tag == "gla" else merged
                        tr = pe.transpose(ps[:, bank, P * t:P * t + P], src[:, t, P * c:P * c + P], ident[:, :])
                    tr.then_inc(*PE.done(("mixT", tag, c)))

            def idx_key():
                claim(6, (ACT, ("ikT",)))
                for t in range(NT):
                    pe.wait_ge(*DVE.after("ik2", t))
                    tr = pe.transpose(ps[:, 6, P * t:P * t + P], ik2[:, t, :], ident[:, :])
                tr.then_inc(*PE.done(("ikT",)))

            def idx_scores(t):
                n = P * (t + 1)
                pe.wait_ge(*ACT.after("ikT"))
                for h in range(IDX_H):
                    bank = 4 + h % 4
                    pe.wait_ge(*ACT.after("iqT", h // 2))
                    claim(bank, (ACT, ("rel", t, h)))
                    rows = slice(IDX_D * (h % 2), IDX_D * (h % 2) + IDX_D)
                    pe.matmul(ps[:, bank, 0:n], iqT[rows, h // 2, P * t:P * t + P], ikT[rows, 0:n], start=True,
                              stop=True).then_inc(*PE.done(("rel", t, h)))

            def head_transposes(tag, c, src, last_needed):
                bank = 4 + c % 4
                claim(bank, (ACT, (tag, c)))
                for t in range(len(src)):
                    pe.wait_ge(*DVE.after(*last_needed[t]))
                    tr = pe.transpose(ps[:, bank, P * t:P * t + P], src[t], ident[:, :])
                tr.then_inc(*PE.done((tag, c)))

            def dsa_prepare(part):
                if part == "k":
                    for c in range(2):
                        head_transposes("dkT", c, [dk[:, t, P * c:P * c + P] for t in range(NT)],
                                        [("dkn", t) for t in range(NT)])
                else:
                    n = int(part[1])
                    for c in range(4 * n, 4 * n + 4):
                        head_transposes("dqT", c, [dq[:, t, P * c:P * c + P] for t in range(NT)],
                                        [("dqn", n, t) for t in range(NT)])

            def dsa_scores(j):
                h, t = divmod(j, NT)
                n = P * (t + 1)
                claim(4 + j % 2, (DVE, ("d_max", j)))
                pe.matmul(ps[:, 4 + j % 2, 0:n], dqT[:, h, P * t:P * t + P], dkT[:, h // DSA_G, 0:n], start=True,
                          stop=True).then_inc(*PE.done(("d_S", j)))

            def dsa_turn(j):
                bank = 6 if j % 2 else 2
                pe.wait_ge(*DVE.after("d_norm", j))
                claim(bank, (ACT, ("d_PT", j)))
                for b in range(j % NT + 1):
                    tr = pe.transpose(ps[:, bank, P * b:P * b + P], d_prob[:, j % 3, P * b:P * b + P], ident[:, :])
                tr.then_inc(*PE.done(("d_PT", j)))

            def dsa_values(j):
                h, t = divmod(j, NT)
                g = h // DSA_G
                bank = 7 if h % 2 else 3
                pe.wait_ge(*ACT.after("d_PT", j))
                if t == 0:
                    claim(bank, (DVE, ("mix_lo", "dsa", h)))
                for b in range(t + 1):
                    mm = pe.matmul(ps[:, bank, P * t:P * t + P], dv[:, b, P * g:P * g + P], d_probT[:, j % 2, P * b:P * b + P],
                                   start=(b == 0), stop=(b == t))
                mm.then_inc(*PE.done(("d_O", j)))

            def mem_prepare(part):
                if part == "k":
                    for c in range(KC):
                        head_transposes("mkT", c, [mk[:, t, P * c:P * c + P] for t in range(2)], [("mkn", t) for t in range(2)])
                else:
                    n = int(part[1])
                    for c in range(4 * n, 4 * n + 4):
                        head_transposes("mqT", c, [dq[:, t, P * c:P * c + P] for t in range(NT)],
                                        [("mqn", n, t) for t in range(NT)])

            def mem_scores(j):
                h, t = divmod(j, NT)
                claim(4 + j % 2, (ACT, ("m_exp", j)))
                for c in range(2):
                    mm = pe.matmul(ps[:, 4 + j % 2, 0:MEM], mqT[:, 2 * h + c, P * t:P * t + P], mkT[:, 2 * h + c, :],
                                   start=(c == 0), stop=(c == 1))
                mm.then_inc(*PE.done(("m_S", j)))

            def mem_turn(j):
                pe.wait_ge(*DVE.after("m_norm", j))
                claim(6, (ACT, ("m_PT", j)))
                for b in range(2):
                    tr = pe.transpose(ps[:, 6, P * b:P * b + P], m_prob[:, j % 3, P * b:P * b + P], ident[:, :])
                tr.then_inc(*PE.done(("m_PT", j)))

            def mem_values(j):
                h, t = divmod(j, NT)
                pe.wait_ge(*ACT.after("m_PT", j))
                for c in range(2):
                    bank = MEM_BANKS[2 * h + c]
                    if t == 0:
                        claim(bank, (DVE, ("mix_lo", "mem", 2 * h + c)))
                    for b in range(2):
                        mm = pe.matmul(ps[:, bank, P * t:P * t + P], mv[:, b, 2 * P * h + P * c:2 * P * h + P * (c + 1)],
                                       m_probT[:, j % 2, P * b:P * b + P], start=(b == 0), stop=(b == 1))
                mm.then_inc(*PE.done(("m_O", j)))

            def latent_sums():
                pe.wait_ge(zeroed, 2)
                pe.wait_ge(*ACT.after("latent_sq", "meta"))
                claim(6, (DVE, ("lat_v",)))
                for t in range(NT):
                    for c in range(2):
                        pe.matmul(ps[:, 6, t:t + 1], cq_sq[:, c, P * t:P * t + P], ones[:, 0:1], start=(c == 0), stop=(c == 1))
                for t in range(NT):
                    pe.matmul(ps[:, 6, NT + t:NT + t + 1], ckv_sq[:, N_META + P * t:N_META + P * (t + 1)], ones[:, 0:1],
                              start=True, stop=True)
                pe.matmul(ps[0:N_META, 6, 8:9], ckv_sq[:, 0:N_META], ones[:, 0:1], start=True,
                          stop=True).then_inc(*PE.done(("lat_ss",)))

            def mix_one():
                for c in range(6):
                    bank = 6 + c % 2
                    claim(bank, (DVE, ("mix_lo", 2 + c)))
                    for t in range(NT):
                        if c < 4:
                            src = y_mla[:, t, P * c:P * c + P]
                        else:
                            pe.wait_ge(*DVE.after("y_ret", t))
                            src = y_ret[:, t, P * (c - 4):P * (c - 3)]
                        tr = pe.transpose(ps[:, bank, P * t:P * t + P], src, ident[:, :])
                    tr.then_inc(*PE.done(("mixT", 2 + c)))

            pe.wait_ge(const_in, 80)
            for step, *a in order:
                if step == "constants":
                    pe.wait_ge(gains_in, 16 * n_gain_dmas)
                    claim(7, (DVE, ("gains",)))
                    pe.transpose(ps[:, 7, 0:64], g_rows[:, :], ident[0:64, 0:64]).then_inc(*PE.done(("gains",)))
                elif step == "norm":
                    norm(*a)
                elif step == "item":
                    item(*a)
                elif step == "latent_sums":
                    latent_sums(*a)
                elif step == "mla_transposes":
                    mla_transposes(*a)
                elif step == "mla_scores":
                    mla_scores(*a)
                elif step == "mla_turn":
                    mla_turn(*a)
                elif step == "mla_values":
                    mla_values(*a)
                elif step == "ret_transposes":
                    ret_transposes(*a)
                elif step == "ret_scores":
                    ret_scores(*a)
                elif step == "ret_values":
                    ret_values(*a)
                elif step == "mix_one":
                    mix_one(*a)
                elif step == "gla_low":
                    gla_low(*a)
                elif step == "gla_decays":
                    gla_decays(*a)
                elif step == "gla_states":
                    gla_states(*a)
                elif step == "gla_values":
                    gla_values(*a)
                elif step == "mix":
                    mix(*a)
                elif step == "idx_key":
                    idx_key(*a)
                elif step == "idx_scores":
                    idx_scores(*a)
                elif step == "dsa_prepare":
                    dsa_prepare(*a)
                elif step == "dsa_scores":
                    dsa_scores(*a)
                elif step == "dsa_turn":
                    dsa_turn(*a)
                elif step == "dsa_values":
                    dsa_values(*a)
                elif step == "mem_prepare":
                    mem_prepare(*a)
                elif step == "mem_scores":
                    mem_scores(*a)
                elif step == "mem_turn":
                    mem_turn(*a)
                elif step == "mem_values":
                    mem_values(*a)
                elif step == "barrier":
                    barrier(pe, a[0])
                    PE.section = a[0]

        @block.scalar
        def _(act):
            fill = [0]

            def split_high(upto):
                for g in range(fill[0], upto):
                    chunks, n, _ = units[g]
                    a = len(chunks) * n
                    act.wait_ge(w_landed[g % RAW_SLOTS], landed[g])
                    if g >= SPLIT_SLOTS:
                        act.wait_ge(*PE.after("unit", g - SPLIT_SLOTS))
                    nc.scalar.activation(w_hi[:, g % SPLIT_SLOTS, 0:a], raw[:, g % RAW_SLOTS, 0:a],
                                         ACTF.Copy).then_inc(*ACT.done(("w_hi", g)))
                fill[0] = max(fill[0], upto)

            def rsqrt_start(key, v):
                act.wait_ge(*DVE.after("v", *key))
                nc.scalar.activation(v[1], v[0], ACTF.Ln).then_inc(*ACT.done(("ln", *key)))
                act.wait_ge(*ACT.after("ln", *key))
                nc.scalar.activation(v[1], v[1], ACTF.Exp, scale=-0.5).then_inc(*ACT.done(("y0", *key)))

            def norm(name):
                tiles = NORM_TILES[name]
                if name == "h":
                    act.wait_ge(x_in, 80)
                if name == "mem":
                    act.wait_ge(mem_landed, 32)
                act.wait_ge(*DVE.after("ss0", name))
                for i, (src, scaled, rows) in enumerate(tiles):
                    for key in NORM_NEEDS(name, i):
                        act.wait_ge(*key[0].after(*key[1]))
                    nc.scalar.activation(scaled, src, ACTF.Square,
                                         accum_out=ss[0:rows, 0, i:i + 1]).then_inc(*ACT.done(("ss", name, i)))
                n = len(tiles)
                rsqrt_start((name,), (ss[:, 1, 0:n], ss[:, 2, 0:n]))
                n = sum(t[2] == P for t in tiles) * P
                hi, off = norm_dest(name)
                for k in range(KC):
                    act.wait_ge(*PE.after("T", name, k))
                    nc.scalar.activation(hi[:, k, off:off + n], ps[:, 4 + k % 4, 0:n], ACTF.Copy,
                                         scale=col(NORMS[name], k)).then_inc(*ACT.done(("hi", name, k)))
                if name == "h":
                    act.wait_ge(*DVE.after("meta_t", name))
                    nc.scalar.activation(act_hi[:, :, 0:N_META], meta_t[:, :, :], ACTF.Copy).then_inc(*ACT.done(("meta_hi", name)))

            def copy(key, dst, src, func=ACTF.Copy, scale=1.0):
                return nc.scalar.activation(dst, src, func, scale=scale)

            def item(name):
                if name == "conv_a":
                    for b in range(2):
                        act.wait_ge(*PE.after("acc", name, b))
                        nc.scalar.activation(cx[:, b, N_META:], ps[:, b, :], ACTF.Copy).then_inc(*ACT.done(("cx", b)))
                    for b in range(2):
                        act.wait_ge(*PE.after("acc", name, 2 + b))
                        nc.scalar.activation(cb[:, b, :], ps[:, 2 + b, :], ACTF.Copy).then_inc(*ACT.done(("cb", b)))
                    act.wait_ge(*PE.after("acc", name, "meta"))
                    nc.scalar.activation(cx[:, :, 0:N_META], ps[:, 4, 0:2 * N_META].rearrange("p (b n) -> p b n", b=2),
                                         ACTF.Copy).then_inc(*ACT.done(("cx", "meta")))
                elif name == "conv_b":
                    for b in range(2):
                        act.wait_ge(*PE.after("acc", name, 2 + b))
                        nc.scalar.activation(cz[:, b, :], ps[:, 2 + b, :], ACTF.Silu).then_inc(*ACT.done(("cz", b)))
                elif name == "latent":
                    for b in range(2):
                        act.wait_ge(*PE.after("acc", name, b))
                        nc.scalar.activation(cq_sq[:, b, :], ps[:, b, :], ACTF.Square).then_inc(*ACT.done(("latent_sq", b)))
                        nc.scalar.activation(cq_hi[:, b, :], ps[:, b, :], ACTF.Copy,
                                             scale=col("q_a_norm", b)).then_inc(*ACT.done(("cq_hi", b)))
                    act.wait_ge(*PE.after("acc", name, 2))
                    nc.scalar.activation(ckv_sq[:, N_META:], ps[:, 2, :], ACTF.Square).then_inc(*ACT.done(("latent_sq", 2)))
                    nc.scalar.activation(ckv_hi[:, N_META:], ps[:, 2, :], ACTF.Copy,
                                         scale=col("kv_a_norm")).then_inc(*ACT.done(("ckv_hi",)))
                    act.wait_ge(*PE.after("acc", name, "meta"))
                    nc.scalar.activation(ckv_hi[:, 0:N_META], ps[:, 4, 0:N_META], ACTF.Copy,
                                         scale=col("kv_a_norm")).then_inc(*ACT.done(("ckv_hi", "meta")))
                    nc.scalar.activation(ckv_sq[:, 0:N_META], ps[:, 4, 0:N_META],
                                         ACTF.Square).then_inc(*ACT.done(("latent_sq", "meta")))
                elif name == "k_rope":
                    act.wait_ge(*PE.after("acc", name, NT))
                    nc.scalar.activation(kr[:, :, :], ps[:, 5, 0:(NT + 1) * QKR].rearrange("p (t n) -> p t n", n=QKR),
                                         ACTF.Copy).then_inc(*ACT.done(("kr",)))
                elif name.startswith("w_uq"):
                    n = int(name[-1])
                    act.wait_ge(*DVE.after("r", "lat"))
                    act.wait_ge(*DVE.after("conv_lo", 1))
                    for t in range(NT):
                        act.wait_ge(*PE.after("acc", name, t))
                        nc.scalar.activation(q_sb[:, t, 384 * n:384 * n + 384], ps[:, t, 0:384], ACTF.Copy,
                                             scale=ss[:, 2, t:t + 1]).then_inc(*ACT.done(("q_raw", n, t)))
                elif name.startswith("w_ukv"):
                    n = int(name[-1])
                    for t in range(NT + 1):
                        rows = P if t < NT else N_META
                        act.wait_ge(*PE.after("acc", name, t))
                        src = ps[0:rows, t, :].rearrange("p (h n) -> p h n", h=4)
                        dst = k_sb[0:rows, t, 384 * n:384 * n + 384].rearrange("p (h n) -> p h n", h=4)
                        nc.scalar.activation(dst[:, :, 0:QKN], src[:, :, 0:QKN], ACTF.Copy,
                                             scale=ss[0:rows, 2, NT + t:NT + t + 1]).then_inc(*ACT.done(("k_raw", n, t)))
                elif name == "mla_z":
                    for t in range(NT):
                        act.wait_ge(*PE.after("acc", name, t))
                        nc.scalar.activation(z_mla[:, t, :], ps[:, t, :], ACTF.Silu).then_inc(*ACT.done(("z_mla", t)))
                elif name == "ret_vz":
                    for t in range(NT + 1):
                        rows = P if t < NT else N_META
                        act.wait_ge(*PE.after("acc", name, t))
                        nc.scalar.activation(rv[0:rows, t, :], ps[0:rows, t, 0:256], ACTF.Copy).then_inc(*ACT.done(("rv", t)))
                        if t < NT:
                            nc.scalar.activation(z_ret[:, t, :], ps[:, t, 256:512], ACTF.Silu).then_inc(*ACT.done(("z_ret", t)))

                elif name == "small2":
                    act.wait_ge(*PE.after("acc", name, NT - 1))
                    nc.scalar.activation(sm2[:, :, :], ps[:, 5, 0:NT * 88].rearrange("p (t n) -> p t n", n=88),
                                         ACTF.Copy).then_inc(*ACT.done(("sm2",)))
                elif name in ("gla_q", "gla_k"):
                    dst = gq if name == "gla_q" else gk
                    for b in range(GLA_H):
                        act.wait_ge(*PE.after("acc", name, b))
                        nc.scalar.activation(dst[:, b, :], ps[:, b, :], ACTF.Copy).then_inc(*ACT.done((name, b)))
                elif name.startswith(("gla_v", "gla_g")):
                    n = int(name[-1])
                    for t in range(NT):
                        act.wait_ge(*PE.after("acc", name, t))
                        if name.startswith("gla_v"):
                            nc.scalar.activation(gv[:, t, 512 * n:512 * n + 512], ps[:, t, :],
                                                 ACTF.Copy).then_inc(*ACT.done(("gv", n, t)))
                        else:
                            if n or t >= 2:
                                act.wait_ge(*DVE.after("go", *divmod(NT * n + t - 2, NT), 1))
                            nc.scalar.activation(g_silu[:, t % 2, :], ps[:, t, :], ACTF.Silu).then_inc(*ACT.done(("g_silu", n, t)))
                elif name.startswith("gate"):
                    for t in range(NT):
                        act.wait_ge(*DVE.after("gate_sum", int(name[4]), int(name[5]), t))
                        nc.scalar.activation(gate[:, t, :], gate[:, t, :], ACTF.Sigmoid).then_inc(*ACT.done(("gate", int(name[4]), int(name[5]), t)))
                elif name == "idx_q":
                    for b in range(4):
                        act.wait_ge(*PE.after("acc", name, b))
                        nc.scalar.activation(iqT[:, b, :], ps[:, b, :], ACTF.Copy).then_inc(*ACT.done(("iqT", b)))
                elif name.startswith("dsa_q") or name.startswith("mem_q"):
                    n = int(name[-1])
                    tag = name[0:1]
                    for t in range(NT):
                        act.wait_ge(*PE.after("acc", name, t))
                        i = NT * n + t
                        if i >= 2:
                            act.wait_ge(*DVE.after(tag + "q_ss", i - 2))
                        else:
                            act.wait_ge(*DVE.after(tag + "k_ss", 2 + i))
                        nc.scalar.activation(d_sq[:, i % 2, :], ps[:, t, :], ACTF.Square).then_inc(*ACT.done((tag + "q_sq", i)))
                        nc.scalar.activation(dq[:, t, 512 * n:512 * n + 512], ps[:, t, :],
                                             ACTF.Copy).then_inc(*ACT.done(("dq" if tag == "d" else "mq", n, t)))
                elif name == "dsa_kv":
                    for t in range(NT):
                        act.wait_ge(*PE.after("acc", name, t))
                        if t >= 2:
                            act.wait_ge(*DVE.after("dk_ss", t - 2))
                        nc.scalar.activation(d_sq[:, t % 2, 0:256], ps[:, t, 0:256], ACTF.Square).then_inc(*ACT.done(("dk_sq", t)))
                        nc.scalar.activation(dk[:, t, :], ps[:, t, 0:256], ACTF.Copy).then_inc(*ACT.done(("dk", t)))
                        nc.scalar.activation(dv[:, t, :], ps[:, t, 256:512], ACTF.Copy).then_inc(*ACT.done(("dv", t)))
                elif name.startswith("mem_kv"):
                    n = int(name[-1])
                    for t in range(2):
                        act.wait_ge(*PE.after("acc", name, t))
                        if n < 2:
                            if n:
                                act.wait_ge(*DVE.after("mk_ss", t))
                            nc.scalar.activation(d_sq[:, t, :], ps[:, t, :], ACTF.Square).then_inc(*ACT.done(("mk_sq", 2 * n + t)))
                        dst = (mk if n < 2 else mv)[:, t, 512 * (n % 2):512 * (n % 2) + 512]
                        nc.scalar.activation(dst, ps[:, t, :], ACTF.Copy).then_inc(*ACT.done(("mkv", n, t)))
                elif name.startswith("expert"):
                    e = int(name[6:])
                    for b in range(2):
                        act.wait_ge(*PE.after("acc", name, b))
                        if e:
                            act.wait_ge(*DVE.after("hid", e - 1, b))
                        nc.scalar.activation(e_silu[:, b, :], ps[:, b, :], ACTF.Silu).then_inc(*ACT.done(("e_silu", e, b)))
                    for b in range(2):
                        act.wait_ge(*DVE.after("hid", e, b))
                        if e >= 2:
                            act.wait_ge(*PE.after("acc", f"down{e - 2}1", NT - 1))
                        nc.scalar.activation(hid_hi[:, e % 2, b, :], hid[:, b, :], ACTF.Copy).then_inc(*ACT.done(("hid_hi", e, b)))

            def gla_low():
                act.wait_ge(*PE.after("low_t"))
                nc.scalar.activation(low_t[:, :], ps[0:16, 6, :], ACTF.Copy).then_inc(*ACT.done(("low_t",)))

            def gla_decays(h):
                s = h % 2
                act.wait_ge(*PE.after("g_z", h))
                if h:
                    act.wait_ge(*DVE.after("g_la", h - 1))
                nc.scalar.activation(gz[:, :], ps[:, 7, :], ACTF.Identity, bias=col("b_gla_a2_2", h)).then_inc(*ACT.done(("g_z", h)))
                act.wait_ge(*ACT.after("g_z", h))
                if h:
                    act.wait_ge(*ACT.after("g_dec", h - 1))
                nc.scalar.activation(gab[:, :], gz[:, :], ACTF.Abs).then_inc(*ACT.done(("g_ab", h)))
                act.wait_ge(*ACT.after("g_ab", h))
                nc.scalar.activation(gex[:, :], gab[:, :], ACTF.Exp, scale=-1.0).then_inc(*ACT.done(("g_ex", h)))
                act.wait_ge(*ACT.after("g_ex", h))
                nc.scalar.activation(gex[:, :], gex[:, :], ACTF.Ln, bias=1.0).then_inc(*ACT.done(("g_ln", h)))
                act.wait_ge(*DVE.after("g_lc", h))
                if h >= 2:
                    act.wait_ge(*PE.after("g_o", h - 2, NT - 1))
                k = 1.0 / 16
                nc.scalar.activation(g_ke[:, s, :], glc[:, :], ACTF.Exp, scale=k).then_inc(*ACT.done(("g_e3", h)))
                nc.scalar.activation(g_qd[:, s, :], gab[:, :], ACTF.Exp, scale=k).then_inc(*ACT.done(("g_e1", h)))
                nc.scalar.activation(g_ki[:, s, :], gab[:, :], ACTF.Exp, scale=-k).then_inc(*ACT.done(("g_e2", h)))
                nc.scalar.activation(g_dec[:, s, :], gab[:, CHUNK - 1::CHUNK], ACTF.Exp, scale=k).then_inc(*ACT.done(("g_dec", h)))

            def gla_states(h):
                act.wait_ge(*PE.after("g_keT", h))
                nc.scalar.activation(g_keT[:, h % 2, :], ps[:, 6, :], ACTF.Copy).then_inc(*ACT.done(("g_keT", h)))

            def gla_values(h):
                for t in range(NT):
                    act.wait_ge(*PE.after("g_o", h, t))
                    src = ps[:, 4 + t % 2, 0:GLA_DV]
                    nc.scalar.activation(go[:, t, GLA_DV * h:GLA_DV * (h + 1)], src, ACTF.Copy).then_inc(*ACT.done(("g_oc", h, t)))
                    if h or t:
                        act.wait_ge(*ACT.after("g_oss", *divmod(NT * h + t - 1, NT)))
                    at = gla_stat(h, t)
                    nc.scalar.activation(gsq[:, :], src, ACTF.Square,
                                         accum_out=ss[:, 5, at:at + 1]).then_inc(*ACT.done(("g_oss", h, t)))

            def mix(tag):
                for c in range(KC):
                    act.wait_ge(*PE.after("mixT", tag, c))
                    nc.scalar.activation(mix_hi[:, c, :], ps[:, 4 + c % 4, :], ACTF.Copy,
                                         scale=col("gla_norm_2", c % 2) if tag == "gla" else 1.0
                                         ).then_inc(*ACT.done(("mix_hi", tag, c)))

            def idx_key():
                act.wait_ge(*DVE.after("ss0", "idx"))
                for t in range(NT):
                    if t:
                        act.wait_ge(*ACT.after("ik_ss", t - 1))
                    nc.scalar.activation(d_sq[:, 0, 0:IDX_D], sm2[:, t, 16:80], ACTF.Square,
                                         accum_out=ss[:, 0, t:t + 1]).then_inc(*ACT.done(("ik_ss", t)))
                rsqrt_start(("ik",), (ss[:, 1, 0:4], ss[:, 2, 0:4]))
                act.wait_ge(*PE.after("ikT"))
                nc.scalar.activation(ikT[:, :], ps[:, 6, :], ACTF.Copy, scale=col("idx_k_norm_2")).then_inc(*ACT.done(("ikT",)))

            def idx_scores(t):
                n = P * (t + 1)
                for h in range(IDX_H):
                    act.wait_ge(*PE.after("rel", t, h))
                    i = IDX_H * (t - 1) + h
                    if i >= 2:
                        act.wait_ge(*DVE.after("score", *idx_of(i - 2)))
                    nc.scalar.activation(rel[:, h % 2, 0:n], ps[:, 4 + h % 4, 0:n], ACTF.Relu).then_inc(*ACT.done(("rel", t, h)))

            def head_transposed(tag, c, dst, n, gain):
                act.wait_ge(*PE.after(tag, c))
                nc.scalar.activation(dst, ps[:, 4 + c % 4, 0:n], ACTF.Copy, scale=gain).then_inc(*ACT.done((tag, c)))

            def dsa_prepare(part):
                a, b = HEAD_STATS["dsa", part]
                rsqrt_start(("dsa", part), (ss[:, 3, a:b], ss[:, 4, a:b]))
                if part == "k":
                    for c in range(2):
                        head_transposed("dkT", c, dkT[:, c, :], SEQ, col("dsa_k_norm_2"))
                else:
                    n = int(part[1])
                    for c in range(4 * n, 4 * n + 4):
                        head_transposed("dqT", c, dqT[:, c, :], SEQ, col("dsa_q_norm_2"))

            def mix_high(tag, c, bank):
                nc.scalar.activation(mix_hi[:, c, :], ps[:, bank, :], ACTF.Copy).then_inc(*ACT.done(("mix_hi", tag, c)))

            def dsa_scores(j):
                n = P * (j % NT + 1)
                act.wait_ge(*DVE.after("d_nmax", j))
                nc.scalar.activation(d_prob[:, j % 3, 0:n], d_prob[:, j % 3, 0:n], ACTF.Exp, bias=sm[:, 1, j:j + 1],
                                     scale=float(P) ** -0.5, accum_out=sm[:, 2, j:j + 1]).then_inc(*ACT.done(("d_exp", j)))

            def dsa_turn(j):
                n = P * (j % NT + 1)
                act.wait_ge(*PE.after("d_PT", j))
                if j >= 2:
                    act.wait_ge(*PE.after("d_O", j - 2))
                nc.scalar.activation(d_probT[:, j % 2, 0:n], ps[:, 6 if j % 2 else 2, 0:n], ACTF.Copy).then_inc(*ACT.done(("d_PT", j)))

            def dsa_values(j):
                h, t = divmod(j, NT)
                if t == NT - 1:
                    act.wait_ge(*PE.after("d_O", j))
                    mix_high("dsa", h, 7 if h % 2 else 3)

            def mem_prepare(part):
                a, b = HEAD_STATS["mem", part]
                rsqrt_start(("mem", part), (ss[:, 3, a:b], ss[:, 4, a:b]))
                if part == "k":
                    for c in range(KC):
                        head_transposed("mkT", c, mkT[:, c, :], MEM, col("mem_k_norm_2", c % 2))
                else:
                    n = int(part[1])
                    for c in range(4 * n, 4 * n + 4):
                        head_transposed("mqT", c, mqT[:, c, :], SEQ, col("mem_q_norm_2", c % 2))

            def mem_scores(j):
                act.wait_ge(*DVE.after("m_nmax", j))
                if j >= 3:
                    act.wait_ge(*PE.after("m_PT", j - 3))
                nc.scalar.activation(m_prob[:, j % 3, :], ps[:, 4 + j % 2, 0:MEM], ACTF.Exp, bias=sm[:, 1, j:j + 1],
                                     scale=float(MEM) ** -0.5, accum_out=sm[:, 2, j:j + 1]).then_inc(*ACT.done(("m_exp", j)))

            def mem_turn(j):
                act.wait_ge(*PE.after("m_PT", j))
                if j >= 2:
                    act.wait_ge(*PE.after("m_O", j - 2))
                nc.scalar.activation(m_probT[:, j % 2, :], ps[:, 6, 0:MEM], ACTF.Copy).then_inc(*ACT.done(("m_PT", j)))

            def mem_values(j):
                h, t = divmod(j, NT)
                if t == NT - 1:
                    act.wait_ge(*PE.after("m_O", j))
                    for c in range(2):
                        mix_high("mem", 2 * h + c, MEM_BANKS[2 * h + c])

            def route():
                act.wait_ge(*DVE.after("r_g"))
                nc.scalar.activation(rt[:, 2, :], rt[:, 2, :], ACTF.Exp).then_inc(*ACT.done(("r_eg",)))
                act.wait_ge(*DVE.after("r_d"))
                nc.scalar.activation(rt[:, 9, 0:4], rt[:, 9, 0:4], ACTF.Exp).then_inc(*ACT.done(("r_ed",)))

            def loads(section):
                if section == "mla":
                    load_decay(0)
                elif section == "gla":
                    act.dma_start(w_a2[:, :], w["w_gla_a2_2"][0]).then_inc(gla_in, 16)
                    act.dma_start(scan_mask[:, :], w["c_scan"]).then_inc(gla_in, 16)
                elif section == "mem":
                    for t in range(2):
                        act.dma_start(mem_in[:, t, :], w["mem_2"][0, P * t:P * t + P, :]).then_inc(mem_landed, 16)
                elif section == "experts":
                    act.dma_start(r_bias[:, 0:4], w["b_r1_2"][0].partition_broadcast(P)).then_inc(route_in, 16)
                    act.dma_start(r_bias[:, 4:20], w["b_r2_2"][0].partition_broadcast(P)).then_inc(route_in, 16)

            def mla_sums():
                for i, (kind, t) in enumerate(HEAD_TILES):
                    rows = P if t < NT else N_META
                    x = q_sb if kind == "q" else k_sb
                    act.wait_ge(*(ACT.after("q_raw", 1, t) if kind == "q" else DVE.after("kr_in", t)))
                    if i >= 2:
                        act.wait_ge(*DVE.after("hss", *HEAD_TILES[i - 2]))
                    nc.scalar.activation(sq[0:rows, i % 2, :], x[0:rows, t, :], ACTF.Square).then_inc(*ACT.done(("hsq", kind, t)))
                rsqrt_start(("head",), (ss[:, 3, 0:72], ss[:, 4, 0:72]))

            def q_transposed(tag, h, width, dst, bank):
                act.wait_ge(*PE.after("qT", tag, h))
                if h >= 2:
                    act.wait_ge(*PE.after(*last_scores(tag, h - 2)))
                nc.scalar.activation(dst[0:width, h % 2, :], ps[0:width, bank, :], ACTF.Copy).then_inc(*ACT.done(("qT", tag, h)))

            def mla_scores(j):
                n = P * (j % NT + 1)
                act.wait_ge(*DVE.after("nmax", "mla", j))
                if j >= 3:
                    act.wait_ge(*PE.after("PT", "mla", j - 3))
                nc.scalar.activation(prob[:, j % 3, 0:N_META + n], psf[:, 5 * SEQ - N_META:5 * SEQ + n], ACTF.Exp,
                                     bias=sm[:, 1, j:j + 1], scale=float(QKH) ** -0.5,
                                     accum_out=sm[:, 2, j:j + 1]).then_inc(*ACT.done(("exp", "mla", j)))

            def mla_turn(j):
                n = P * (j % NT + 1)
                act.wait_ge(*PE.after("PT", "mla", j))
                if j >= 2:
                    act.wait_ge(*PE.after("O", "mla", j - 2))
                nc.scalar.activation(probT[:, j % 2, 0:n], ps[:, 6, 0:n], ACTF.Copy).then_inc(*ACT.done(("PT", "mla", j)))

            def load_decay(h):
                act.dma_start(decay[:, :], w["c_decay"][h]).then_inc(decay_in, 16)
                act.dma_start(decay_m[:, :], w["c_decay_m"][h]).then_inc(decay_in, 16)

            def ret_values(h):
                if h + 1 < RET_H:
                    act.wait_ge(*DVE.after("sd", h, NT - 1))
                    load_decay(h + 1)
                act.wait_ge(*PE.after("rO", h))
                nc.scalar.activation(y_ret[:, :, RET_D * h:RET_D * (h + 1)],
                                     ps[:, 0, 0:NT * RET_D].rearrange("p (t n) -> p t n", t=NT),
                                     ACTF.Copy).then_inc(*ACT.done(("rO", h)))

            def ret_norm():
                act.wait_ge(*ACT.after("rO", RET_H - 1))
                act.wait_ge(*PE.after("rO", RET_H - 1))
                nc.scalar.activation(ysq[:, :, :], y_ret[:, :, :], ACTF.Square).then_inc(*ACT.done(("ysq",)))
                rsqrt_start(("ret",), (ss[:, 3, 0:16], ss[:, 4, 0:16]))

            def mix_one():
                for c in range(6):
                    act.wait_ge(*PE.after("mixT", 2 + c))
                    nc.scalar.activation(mix_hi[:, 2 + c, :], ps[:, 6 + c % 2, :], ACTF.Copy,
                                         scale=1.0 if c < 4 else col("ret_norm")).then_inc(*ACT.done(("mix_hi", 2 + c)))

            steps = {"mla_sums": mla_sums, "mla_scores": mla_scores, "mla_turn": mla_turn, "ret_values": ret_values,
                     "ret_norm": ret_norm, "mix_one": mix_one, "gla_low": gla_low, "gla_decays": gla_decays,
                     "gla_states": gla_states, "gla_values": gla_values, "mix": mix, "idx_key": idx_key,
                     "idx_scores": idx_scores, "dsa_prepare": dsa_prepare, "dsa_scores": dsa_scores,
                     "dsa_turn": dsa_turn, "dsa_values": dsa_values, "mem_prepare": mem_prepare,
                     "mem_scores": mem_scores, "mem_turn": mem_turn, "mem_values": mem_values, "route": route}
            for step, *a in order:
                if step == "item" and a[0].startswith("gate"):
                    b, n = int(a[0][4]), int(a[0][5])
                    if b:
                        act.wait_ge(*DVE.after("gate_sum", b - 1, n, NT - 1))
                    else:
                        act.wait_ge(*DVE.after("g_ke", GLA_H - 1))
                    c = D * b + 512 * n
                    act.dma_start(gate_bias[:, n, :], w["b_gate_2"][0, c:c + 512].partition_broadcast(P)).then_inc(bias_in[n], 16)
                if step == "item":
                    split_high(min(len(units), first_unit[a[0]] + len(items[a[0]]) + 2))
                    item(*a)
                elif step == "norm":
                    norm(*a)
                elif step == "conv":
                    for b in range(2):
                        act.wait_ge(*DVE.after("cy", b))
                        nc.scalar.activation(mix_hi[:, b, :], cy[:, b, :], ACTF.Copy).then_inc(*ACT.done(("conv_hi", b)))
                elif step == "latent_sums":
                    rsqrt_start(("lat",), (ss[:, 1, 0:9], ss[:, 2, 0:9]))
                elif step == "mla_transposes":
                    q_transposed("mla", a[0], QKH, qT, 6)
                elif step == "ret_transposes":
                    q_transposed("ret", a[0], RET_D, rqT, 0)
                elif step == "gla_rstd":
                    a, b = 8 * a[0], 8 * a[0] + 8
                    rsqrt_start(("gla", a // 8), (ss[:, 3, a:b], ss[:, 4, a:b]))
                elif step in steps:
                    steps[step](*a)
                elif step == "barrier":
                    barrier(act, a[0])
                    ACT.section = a[0]
                    loads(a[0])

        @block.vector
        def _(dve):
            def mean(key, v, total, width):
                return dve.tensor_scalar(v, total, 1.0 / width, EPS, ALU.mult, ALU.add).then_inc(*DVE.done(("v", *key)))

            def rsqrt_finish(key, v, y, t):
                dve.wait_ge(*ACT.after("y0", *key))
                dve.scalar_tensor_tensor(t, y, -0.5, y, ALU.mult, ALU.mult).then_inc(*DVE.done(("r1", *key)))
                dve.wait_ge(*DVE.after("r1", *key))
                dve.tensor_tensor(t, t, v, ALU.mult).then_inc(*DVE.done(("r2", *key)))
                dve.wait_ge(*DVE.after("r2", *key))
                dve.scalar_tensor_tensor(y, t, 1.5, y, ALU.add, ALU.mult).then_inc(*DVE.done(("r", *key)))
                dve.wait_ge(*DVE.after("r", *key))

            def norm(name):
                tiles = NORM_TILES[name]
                n = len(tiles)
                dve.memset(ss[:, 0:3, 0:n], 1.0).then_inc(*DVE.done(("ss0", name)))
                for i in range(n):
                    dve.wait_ge(*ACT.after("ss", name, i))
                mean((name,), ss[:, 1, 0:n], ss[:, 0, 0:n], D)
                rsqrt_finish((name,), ss[:, 1, 0:n], ss[:, 2, 0:n], ss[:, 0, 0:n])
                for i, (src, scaled, rows) in enumerate(tiles):
                    dve.tensor_scalar(scaled, src, ss[0:rows, 2, i:i + 1], None, ALU.mult).then_inc(*DVE.done(("scaled", name, i)))
                n = sum(t[2] == P for t in tiles) * P
                hi, off = norm_dest(name)
                lo = act_lo if hi is act_hi else norm_lo(name)
                for k in range(KC):
                    dve.wait_ge(*ACT.after("hi", name, k))
                    dve.scalar_tensor_tensor(lo[:, k, off:off + n], ps[:, 4 + k % 4, 0:n], col(NORMS[name], k),
                                             hi[:, k, off:off + n].bitcast(F32), ALU.mult,
                                             ALU.subtract).then_inc(*DVE.done(("lo", name, k)))
                if name == "h":
                    dve.wait_ge(*PE.after("T", name, "meta"))
                    g = gains[:, GAINS["ln_w"]:GAINS["ln_w"] + KC].unsqueeze(2).to_broadcast([P, KC, N_META])
                    dve.tensor_tensor(meta_t[:, :, :], ps[:, 3, 0:KC * N_META].rearrange("p (k n) -> p k n", k=KC), g,
                                      ALU.mult).then_inc(*DVE.done(("meta_t", name)))
                    dve.wait_ge(*ACT.after("meta_hi", name))
                    dve.tensor_tensor(act_lo[:, :, 0:N_META], meta_t[:, :, :], act_hi[:, :, 0:N_META].bitcast(F32),
                                      ALU.subtract).then_inc(*DVE.done(("meta_lo", name)))

            def low_part(key, lo, src, hi, gain=1.0):
                return dve.scalar_tensor_tensor(lo, src, gain, hi.bitcast(F32), ALU.mult,
                                                ALU.subtract).then_inc(*DVE.done(key))

            turned = []

            def rope_turn(key, x, out, rows, heads, half, t, cos, sin):
                n = heads * half
                if turned:
                    dve.wait_ge(*DVE.after(*turned[-1], 5))
                turned.append(key)
                tmp = [b[0:rows, 0:n].rearrange("p (h n) -> p h n", h=heads) for b in (t0, t1, t2, t3)]
                c = cos[0:rows, t, :].unsqueeze(1).to_broadcast([rows, heads, half])
                s = sin[0:rows, t, :].unsqueeze(1).to_broadcast([rows, heads, half])
                a, b = x[:, :, 0:half], x[:, :, half:2 * half]
                dve.tensor_tensor(tmp[0], a, c, ALU.mult).then_inc(*DVE.done((*key, 0)))
                dve.tensor_tensor(tmp[1], b, s, ALU.mult).then_inc(*DVE.done((*key, 1)))
                dve.tensor_tensor(tmp[2], a, s, ALU.mult).then_inc(*DVE.done((*key, 2)))
                dve.tensor_tensor(tmp[3], b, c, ALU.mult).then_inc(*DVE.done((*key, 3)))
                dve.wait_ge(*DVE.after(*key, 3))
                dve.tensor_tensor(out[:, :, 0:half], tmp[0], tmp[1], ALU.subtract).then_inc(*DVE.done((*key, 4)))
                dve.tensor_tensor(out[:, :, half:2 * half], tmp[2], tmp[3], ALU.add).then_inc(*DVE.done((*key, 5)))

            def item(name):
                if name == "conv_b":
                    for b in range(2):
                        dve.wait_ge(*PE.after("acc", name, b))
                        dve.wait_ge(*ACT.after("cx", b))
                        dve.tensor_tensor(cu[:, b, N_META:], ps[:, b, :], cx[:, b, N_META:], ALU.mult).then_inc(*DVE.done(("cu", b)))
                    dve.wait_ge(*PE.after("acc", name, "meta"))
                    dve.wait_ge(*ACT.after("cx", "meta"))
                    dve.tensor_tensor(cu[:, :, 0:N_META], ps[:, 4, 0:2 * N_META].rearrange("p (b n) -> p b n", b=2),
                                      cx[:, :, 0:N_META], ALU.mult).then_inc(*DVE.done(("cu", "meta")))
                elif name == "latent":
                    for b in range(2):
                        dve.wait_ge(*ACT.after("cq_hi", b))
                        low_part(("cq_lo", b), cq_lo[:, b, :], ps[:, b, :], cq_hi[:, b, :], col("q_a_norm", b))
                    dve.wait_ge(*ACT.after("ckv_hi"))
                    low_part(("ckv_lo",), ckv_lo[:, N_META:], ps[:, 2, :], ckv_hi[:, N_META:], col("kv_a_norm"))
                    dve.wait_ge(*ACT.after("latent_sq", "meta"))
                    low_part(("ckv_lo", "meta"), ckv_lo[:, 0:N_META], ps[:, 4, 0:N_META], ckv_hi[:, 0:N_META], col("kv_a_norm"))
                elif name.startswith("w_ukv"):
                    n = int(name[-1])
                    for t in range(NT + 1):
                        rows = P if t < NT else N_META
                        dve.wait_ge(*ACT.after("k_raw", n, t))
                        src = ps[0:rows, t, :].rearrange("p (h n) -> p h n", h=4)
                        dst = v_sb[0:rows, t, 256 * n:256 * n + 256].rearrange("p (h n) -> p h n", h=4)
                        dve.tensor_scalar(dst, src[:, :, QKN:P], ss[0:rows, 2, NT + t:NT + t + 1], None,
                                          ALU.mult).then_inc(*DVE.done(("v_raw", n, t)))
                elif name == "ret_qk":
                    dve.wait_ge(rope_in, 48)
                    for t in range(NT + 1):
                        rows = P if t < NT else N_META
                        dve.wait_ge(*PE.after("acc", name, t))
                        rope_turn(("rope_r", t), ps[0:rows, t, :].rearrange("p (h n) -> p h n", h=8),
                                  rqk[0:rows, t, :].rearrange("p (h n) -> p h n", h=8), rows, 8, 32, t, cos_r, sin_r)
                elif name.startswith("w_out"):
                    n = int(name[-1])
                    for t in range(NT):
                        dve.wait_ge(*PE.after("acc", name, t))
                        x = x1[:, t, 512 * n:512 * n + 512]
                        dve.tensor_tensor(x, ps[:, t, :], x, ALU.add).then_inc(*DVE.done(("x", name, t)))

                elif name.startswith("gla_g"):
                    n = int(name[-1])
                    for t in range(NT):
                        dve.wait_ge(*ACT.after("g_silu", n, t))
                        for i in range(2):
                            h = 2 * n + i
                            o = go[:, t, GLA_DV * h:GLA_DV * (h + 1)]
                            dve.scalar_tensor_tensor(o, o, ss[:, 4, gla_stat(h, t):gla_stat(h, t) + 1],
                                                     g_silu[:, t % 2, GLA_DV * i:GLA_DV * (i + 1)], ALU.mult,
                                                     ALU.mult).then_inc(*DVE.done(("go", n, t, i)))
                elif name.startswith("gate"):
                    b, n = int(name[4]), int(name[5])
                    dve.wait_ge(bias_in[n], 16 * (b + 1))
                    for t in range(NT):
                        dve.wait_ge(*PE.after("acc", name, t))
                        if (b, n) != (0, 0):
                            dve.wait_ge(*DVE.after("merged", *((b, 0) if n else (b - 1, 1)), t))
                        dve.tensor_tensor(gate[:, t, :], ps[:, t, :], gate_bias[:, n, :],
                                          ALU.add).then_inc(*DVE.done(("gate_sum", b, n, t)))
                elif name.startswith("w_o"):
                    b, n = int(name[3]), int(name[4])
                    for t in range(NT):
                        dve.wait_ge(*PE.after("acc", name, t))
                        dve.wait_ge(*ACT.after("gate", b, n, t))
                        m = merged[:, t, 512 * n:512 * n + 512]
                        if b == 0:
                            dve.tensor_tensor(m, ps[:, t, :], gate[:, t, :],
                                              ALU.mult).then_inc(*DVE.done(("gated", b, n, t), ("merged", b, n, t)))
                        else:
                            dve.tensor_tensor(gate[:, t, :], ps[:, t, :], gate[:, t, :],
                                              ALU.mult).then_inc(*DVE.done(("gated", b, n, t)))
                            dve.wait_ge(*DVE.after("gated", b, n, t))
                            dve.tensor_tensor(m, m, gate[:, t, :], ALU.add).then_inc(*DVE.done(("merged", b, n, t)))
                elif name.startswith(("dsa_q", "mem_q")):
                    tag, n = name[0:1], int(name[-1])
                    if tag == "d":
                        top_keys(2 + n)
                    for t in range(NT):
                        i = NT * n + t
                        dve.wait_ge(*ACT.after(tag + "q_sq", i))
                        heads = 4 if tag == "d" else 2
                        at = HEAD_STATS["dsa" if tag == "d" else "mem", f"q{n}"][0] + heads * t
                        dve.tensor_reduce(ss[:, 5, at:at + heads], d_sq[:, i % 2, :].rearrange("p (h n) -> p h n", h=heads), X,
                                          ALU.add).then_inc(*DVE.done((tag + "q_ss", i)))
                elif name == "dsa_kv":
                    top_keys(1)
                    for t in range(NT):
                        dve.wait_ge(*ACT.after("dk_sq", t))
                        dve.tensor_reduce(ss[:, 5, 32 + 2 * t:34 + 2 * t],
                                          d_sq[:, t % 2, 0:256].rearrange("p (h n) -> p h n", h=2), X,
                                          ALU.add).then_inc(*DVE.done(("dk_ss", t)))
                elif name in ("mem_kv0", "mem_kv1"):
                    n = int(name[-1])
                    for t in range(2):
                        dve.wait_ge(*ACT.after("mk_sq", 2 * n + t))
                        dve.tensor_reduce(ss[:, 5, 4 * t + 2 * n:4 * t + 2 * n + 2],
                                          d_sq[:, t, :].rearrange("p (h n) -> p h n", h=2), X,
                                          ALU.add).then_inc(*DVE.done(("mk_ss", 2 * n + t)))
                elif name.startswith("expert"):
                    e = int(name[6:])
                    for b in range(2):
                        dve.wait_ge(*ACT.after("e_silu", e, b))
                        dve.wait_ge(*PE.after("acc", name, 2 + b))
                        if e:
                            dve.wait_ge(*ACT.after("hid_hi", e - 1, b))
                            dve.wait_ge(*DVE.after("hid_lo", e - 1, b))
                        dve.tensor_tensor(hid[:, b, :], ps[:, 2 + b, :], e_silu[:, b, :], ALU.mult).then_inc(*DVE.done(("hid", e, b)))
                    for b in range(2):
                        dve.wait_ge(*ACT.after("hid_hi", e, b))
                        dve.tensor_tensor(hid_lo[:, e % 2, b, :], hid[:, b, :], hid_hi[:, e % 2, b, :].bitcast(F32),
                                          ALU.subtract).then_inc(*DVE.done(("hid_lo", e, b)))
                elif name.startswith("down"):
                    e, n = int(name[4:-1]), int(name[-1])
                    for t in range(NT):
                        dve.wait_ge(*PE.after("acc", name, t))
                        if e:
                            dve.wait_ge(*DVE.after("x", f"down{e - 1}{n}", t))
                        x = x1[:, t, 512 * n:512 * n + 512]
                        dve.scalar_tensor_tensor(x, ps[:, 4 + t, :], combine[:, t, e:e + 1], x, ALU.mult,
                                                 ALU.add).then_inc(*DVE.done(("x", name, t)))
                elif name == "router":
                    dve.wait_ge(route_in, 32)
                    dve.wait_ge(*PE.after("acc", name, NT - 1))
                    dve.tensor_tensor(rl[:, :, :], ps[:, 5, 0:NT * 20].rearrange("p (t n) -> p t n", n=20),
                                      r_bias[:, :].unsqueeze(1).to_broadcast([P, NT, 20]), ALU.add).then_inc(*DVE.done(("rl",)))

            def gla_decays(h):
                s = h % 2
                if h == 0:
                    dve.wait_ge(gla_in, 32)
                    for b in range(GLA_H):
                        dve.wait_ge(*ACT.after("gla_q", b))
                        dve.wait_ge(*ACT.after("gla_k", b))
                dve.wait_ge(*ACT.after("g_z", h))
                dve.wait_ge(*ACT.after("g_ln", h))
                dve.scalar_tensor_tensor(gz[:, :], gz[:, :], 0.0, gex[:, :], ALU.min, ALU.subtract).then_inc(*DVE.done(("g_la0", h)))
                dve.wait_ge(*DVE.after("g_la0", h))
                dve.tensor_tensor_scan(gab[:, :], scan_mask[:, :], gz[:, :], 0.0, ALU.mult, ALU.add).then_inc(*DVE.done(("g_la", h)))
                dve.wait_ge(*DVE.after("g_la", h))
                cum = gab[:, :].rearrange("p (c n) -> p c n", n=CHUNK)
                dve.tensor_tensor(glc[:, :].rearrange("p (c n) -> p c n", n=CHUNK),
                                  cum[:, :, CHUNK - 1:CHUNK].to_broadcast([P, 8, CHUNK]), cum,
                                  ALU.subtract).then_inc(*DVE.done(("g_lc", h)))
                dve.wait_ge(*ACT.after("g_e3", h))
                dve.tensor_tensor(g_ke[:, s, :], gk[:, h, :], g_ke[:, s, :], ALU.mult).then_inc(*DVE.done(("g_ke", h)))
                dve.wait_ge(*ACT.after("g_e1", h))
                dve.scalar_tensor_tensor(g_qd[:, s, :], gq[:, h, :], float(P) ** -0.5, g_qd[:, s, :], ALU.mult,
                                         ALU.mult).then_inc(*DVE.done(("g_qd", h)))
                dve.wait_ge(*ACT.after("g_e2", h))
                dve.tensor_tensor(g_ki[:, s, :], gk[:, h, :], g_ki[:, s, :], ALU.mult).then_inc(*DVE.done(("g_ki", h)))

            def gla_states(h):
                s = h % 2
                dve.wait_ge(*PE.after("g_att", h))
                dve.tensor_tensor(g_att[:, s, :].rearrange("p (t n) -> p t n", n=P), ps[:, 7, :].rearrange("p (t n) -> p t n", n=P),
                                  gla_mask[:, :].unsqueeze(1).to_broadcast([P, NT, P]), ALU.mult).then_inc(*DVE.done(("g_att", h)))
                for n in range(7):
                    bank, cols = state_bank(n)
                    dve.wait_ge(*PE.after("g_upd", h, bank))
                    if n == 0 and h:
                        dve.wait_ge(*PE.after("g_o", h - 1, NT - 1))
                    upd = ps[:, bank, cols]
                    if n == 0:
                        dve.tensor_copy(state[:, 1, :], upd).then_inc(*DVE.done(("g_state", h, 0)))
                    else:
                        dve.wait_ge(*ACT.after("g_dec", h))
                        dve.wait_ge(*DVE.after("g_state", h, n - 1))
                        dve.scalar_tensor_tensor(state[:, n + 1, :], state[:, n, :], g_dec[:, s, n:n + 1], upd, ALU.mult,
                                                 ALU.add).then_inc(*DVE.done(("g_state", h, n)))

            def gla_rstd(n):
                dve.wait_ge(*ACT.after("g_oss", 2 * n + 1, NT - 1))
                a, b = 8 * n, 8 * n + 8
                mean(("gla", n), ss[:, 3, a:b], ss[:, 5, a:b], GLA_DV)
                rsqrt_finish(("gla", n), ss[:, 3, a:b], ss[:, 4, a:b], ss[:, 0, a:b])

            def mix(tag):
                for c in range(KC):
                    dve.wait_ge(*ACT.after("mix_hi", tag, c))
                    low_part(("mix_lo", tag, c), mix_lo[:, c, :], ps[:, 4 + c % 4, :], mix_hi[:, c, :],
                             col("gla_norm_2", c % 2) if tag == "gla" else 1.0)

            def idx_key():
                dve.memset(ss[:, 0:6, :], 1.0).then_inc(*DVE.done(("ss0", "idx")))
                dve.wait_ge(*ACT.after("ik_ss", NT - 1))
                mean(("ik",), ss[:, 1, 0:4], ss[:, 0, 0:4], IDX_D)
                rsqrt_finish(("ik",), ss[:, 1, 0:4], ss[:, 2, 0:4], ss[:, 0, 0:4])
                for t in range(NT):
                    dve.tensor_scalar(ik2[:, t, 0:IDX_D], sm2[:, t, 16:80], ss[:, 2, t:t + 1], None,
                                      ALU.mult).then_inc(*DVE.done(("ik1", t)))
                    dve.tensor_scalar(ik2[:, t, IDX_D:P], sm2[:, t, 16:80], ss[:, 2, t:t + 1], None,
                                      ALU.mult).then_inc(*DVE.done(("ik2", t)))
                dve.tensor_scalar(sm2[:, :, 80:88], sm2[:, :, 80:88], float(IDX_H * IDX_D) ** -0.5, None,
                                  ALU.mult).then_inc(*DVE.done(("iw",)))
                dve.tensor_copy(d_mask[:, 0:P], dsa_mask[:, :]).then_inc(*DVE.done(("d_mask", 0)))
                dve.wait_ge(*DVE.after("iw"))

            def idx_scores(t):
                n = P * (t + 1)
                acc = work[:, t - 1, 0:n]
                for h in range(IDX_H):
                    dve.wait_ge(*ACT.after("rel", t, h))
                    wt = sm2[:, t, 80 + h:81 + h]
                    if h == 0:
                        dve.tensor_scalar(acc, rel[:, 0, 0:n], wt, None, ALU.mult).then_inc(*DVE.done(("score", t, 0)))
                    else:
                        dve.wait_ge(*DVE.after("score", t, h - 1))
                        dve.scalar_tensor_tensor(acc, rel[:, h % 2, 0:n], wt, acc, ALU.mult, ALU.add).then_inc(*DVE.done(("score", t, h)))
                dve.wait_ge(*DVE.after("score", t, IDX_H - 1))
                dve.tensor_tensor(acc[:, n - P:n], acc[:, n - P:n], dsa_mask[:, :], ALU.add).then_inc(*DVE.done(("picked", t, 0)))

            def top_keys(t):
                n = P * (t + 1)
                acc = work[:, t - 1, 0:n]
                for i in range(TOPK // 8):
                    dve.wait_ge(*DVE.after("picked", t, i))
                    if i == 0 and t > 1:
                        dve.wait_ge(*DVE.after("picked", t - 1, TOPK // 8))
                    dve.max(best8[:, :], acc).then_inc(*DVE.done(("best", t, i)))
                    dve.wait_ge(*DVE.after("best", t, i))
                    dve.match_replace(acc, best8[:, :], acc, PICKED).then_inc(*DVE.done(("picked", t, i + 1)))
                dve.wait_ge(*DVE.after("picked", t, TOPK // 8))
                at = P * (t * (t + 1) // 2)
                dve.tensor_scalar(d_mask[:, at:at + n], acc, 2 * MASKED, MASKED, ALU.is_gt, ALU.mult).then_inc(*DVE.done(("d_mask", t)))

            def scaled_heads(key, x, r, heads):
                x3 = x.rearrange("p (h n) -> p h n", h=heads)
                dve.tensor_tensor(x3, x3, r.unsqueeze(2).to_broadcast([P, heads, x3.shape[2]]),
                                  ALU.mult).then_inc(*DVE.done(key))

            def dsa_prepare(part):
                a, b = HEAD_STATS["dsa", part]
                dve.wait_ge(*DVE.after(*(("dk_ss", NT - 1) if part == "k" else ("dq_ss", NT * int(part[1]) + NT - 1))))
                mean(("dsa", part), ss[:, 3, a:b], ss[:, 5, a:b], P)
                rsqrt_finish(("dsa", part), ss[:, 3, a:b], ss[:, 4, a:b], ss[:, 5, a:b])
                for t in range(NT):
                    if part == "k":
                        dve.wait_ge(*ACT.after("dk", t))
                        scaled_heads(("dkn", t), dk[:, t, :], ss[:, 4, a + 2 * t:a + 2 * t + 2], 2)
                    else:
                        n = int(part[1])
                        dve.wait_ge(*ACT.after("dq", n, t))
                        scaled_heads(("dqn", n, t), dq[:, t, 512 * n:512 * n + 512], ss[:, 4, a + 4 * t:a + 4 * t + 4], 4)

            def dsa_max(j):
                t = j % NT
                n, at = P * (t + 1), P * (t * (t + 1) // 2)
                dve.wait_ge(*PE.after("d_S", j))
                if j >= 3:
                    dve.wait_ge(*PE.after("d_PT", j - 3))
                dve.tensor_tensor_reduce(d_prob[:, j % 3, 0:n], ps[:, 4 + j % 2, 0:n], d_mask[:, at:at + n], 1.0, PICKED, ALU.add,
                                         ALU.max, sm[:, 0, j:j + 1]).then_inc(*DVE.done(("d_max", j)))

            def mem_max(j):
                dve.wait_ge(*PE.after("m_S", j))
                dve.tensor_reduce(sm[:, 0, j:j + 1], ps[:, 4 + j % 2, 0:MEM], X, ALU.max).then_inc(*DVE.done(("m_max", j)))

            def softmax_step(tag, j, count, largest, probs, scale):
                if j < count:
                    largest(j)
                if j:
                    dve.wait_ge(*ACT.after(tag + "_exp", j - 1))
                    dve.reciprocal(sm[:, 3, j - 1:j], sm[:, 2, j - 1:j]).then_inc(*DVE.done((tag + "_rsum", j - 1)))
                if j < count:
                    dve.wait_ge(*DVE.after(tag + "_max", j))
                    dve.tensor_scalar(sm[:, 1, j:j + 1], sm[:, 0, j:j + 1], scale, None,
                                      ALU.mult).then_inc(*DVE.done((tag + "_nmax", j)))
                if j:
                    dve.wait_ge(*DVE.after(tag + "_rsum", j - 1))
                    x = probs(j - 1)
                    dve.tensor_scalar(x, x, sm[:, 3, j - 1:j], None, ALU.mult).then_inc(*DVE.done((tag + "_norm", j - 1)))

            def dsa_scores(j):
                softmax_step("d", j, NT * DSA_H, dsa_max, lambda i: d_prob[:, i % 3, 0:P * (i % NT + 1)], -float(P) ** -0.5)

            def dsa_values(j):
                h, t = divmod(j, NT)
                if t == NT - 1:
                    dve.wait_ge(*ACT.after("mix_hi", "dsa", h))
                    low_part(("mix_lo", "dsa", h), mix_lo[:, h, :], ps[:, 7 if h % 2 else 3, :], mix_hi[:, h, :])

            def mem_prepare(part):
                a, b = HEAD_STATS["mem", part]
                dve.wait_ge(*DVE.after(*(("mk_ss", 3) if part == "k" else ("mq_ss", NT * int(part[1]) + NT - 1))))
                mean(("mem", part), ss[:, 3, a:b], ss[:, 5, a:b], MEM)
                rsqrt_finish(("mem", part), ss[:, 3, a:b], ss[:, 4, a:b], ss[:, 5, a:b])
                if part == "k":
                    for t in range(2):
                        dve.wait_ge(*ACT.after("mkv", 1, t))
                        scaled_heads(("mkn", t), mk[:, t, :], ss[:, 4, 4 * t:4 * t + 4], 4)
                else:
                    n = int(part[1])
                    for t in range(NT):
                        dve.wait_ge(*ACT.after("mq", n, t))
                        scaled_heads(("mqn", n, t), dq[:, t, 512 * n:512 * n + 512], ss[:, 4, a + 2 * t:a + 2 * t + 2], 2)

            def mem_scores(j):
                softmax_step("m", j, NT * MEM_H, mem_max, lambda i: m_prob[:, i % 3, :], -float(MEM) ** -0.5)

            def mem_values(j):
                h, t = divmod(j, NT)
                if t == NT - 1:
                    for c in range(2):
                        dve.wait_ge(*ACT.after("mix_hi", "mem", 2 * h + c))
                        low_part(("mix_lo", "mem", 2 * h + c), mix_lo[:, 2 * h + c, :], ps[:, MEM_BANKS[2 * h + c], :],
                                 mix_hi[:, 2 * h + c, :])

            def route():
                step_at = [0]

                def link(ins):
                    step_at[0] += 1
                    ins.then_inc(*DVE.done(("route", step_at[0])))
                    dve.wait_ge(*DVE.after("route", step_at[0]))

                def four(row):
                    return rt[:, row, :].rearrange("p (t n) -> p t n", n=4)

                def one(row):
                    return rt[:, row, 0:4].unsqueeze(2).to_broadcast([P, NT, 4])

                def first_best(x, best, key, hot):
                    link(dve.tensor_reduce(rt[:, best, 0:4], x, X, ALU.max))
                    link(dve.tensor_tensor(four(key), x, one(best), ALU.is_equal))
                    link(dve.tensor_tensor(four(key), four(key), rank[:, :].unsqueeze(1).to_broadcast([P, NT, 4]), ALU.mult))
                    link(dve.tensor_reduce(rt[:, 15, 0:4], four(key), X, ALU.max))
                    link(dve.tensor_tensor(four(hot), four(key), one(15), ALU.is_equal))

                for i in range(4):
                    link(dve.memset(rank[:, i:i + 1], 4.0 - i))
                dve.wait_ge(*DVE.after("rl"))
                g = rl[:, :, 0:4]
                first_best(g, 0, 1, 3)
                dve.tensor_tensor(four(2), g, one(0), ALU.subtract).then_inc(*DVE.done(("r_g",)))
                e4 = rl[:, :, 4:20].rearrange("p t (g e) -> p t e g", g=4)
                c4 = combine[:, :, :].rearrange("p t (g e) -> p t e g", g=4)
                hot_g = four(3).unsqueeze(2).to_broadcast([P, NT, 4, 4])
                link(dve.tensor_tensor(c4, e4, hot_g, ALU.mult))
                link(dve.tensor_reduce(four(4), c4, X, ALU.add))
                first_best(four(4), 5, 6, 7)
                link(dve.scalar_tensor_tensor(four(8), four(7), MASKED, four(4), ALU.mult, ALU.add))
                first_best(four(8), 10, 6, 11)
                dve.tensor_tensor(rt[:, 9, 0:4], rt[:, 10, 0:4], rt[:, 5, 0:4], ALU.subtract).then_inc(*DVE.done(("r_d",)))
                dve.wait_ge(*ACT.after("r_ed"))
                link(dve.tensor_scalar(rt[:, 12, 0:4], rt[:, 9, 0:4], 1.0, None, ALU.add))
                dve.wait_ge(*ACT.after("r_eg"))
                link(dve.tensor_reduce(rt[:, 13, 0:4], four(2), X, ALU.add))
                link(dve.tensor_tensor(rt[:, 12, 0:4], rt[:, 12, 0:4], rt[:, 13, 0:4], ALU.mult))
                link(dve.reciprocal(rt[:, 12, 0:4], rt[:, 12, 0:4]))
                link(dve.tensor_tensor(four(11), four(11), one(9), ALU.mult))
                link(dve.tensor_tensor(four(7), four(7), four(11), ALU.add))
                link(dve.tensor_tensor(four(7), four(7), one(12), ALU.mult))
                link(dve.tensor_tensor(c4, hot_g, four(7).unsqueeze(3).to_broadcast([P, NT, 4, 4]), ALU.mult))

            def conv():
                for b in range(2):
                    y = cy[:, b, :]
                    dve.wait_ge(*DVE.after("cu", b))
                    dve.wait_ge(*DVE.after("cu", "meta"))
                    dve.tensor_scalar(y, cu[:, b, N_META:], col("conv_w", 4 + b), col("conv_b", b), ALU.mult,
                                      ALU.add).then_inc(*DVE.done(("cy2", b)))
                    for j in (1, 0):
                        dve.wait_ge(*DVE.after(f"cy{j + 1}", b))
                        at = N_META - 2 + j
                        dve.scalar_tensor_tensor(y, cu[:, b, at:at + SEQ], col("conv_w", 2 * j + b), y, ALU.mult,
                                                 ALU.add).then_inc(*DVE.done((f"cy{j}", b)))
                    dve.wait_ge(*DVE.after("cy0", b))
                    dve.wait_ge(*ACT.after("cb", b))
                    dve.tensor_tensor(y, y, cb[:, b, :], ALU.mult).then_inc(*DVE.done(("cyb", b)))
                    dve.wait_ge(*DVE.after("cyb", b))
                    dve.wait_ge(*ACT.after("cz", b))
                    dve.tensor_tensor(y, y, cz[:, b, :], ALU.mult).then_inc(*DVE.done(("cy", b)))
                    dve.wait_ge(*ACT.after("conv_hi", b))
                    low_part(("conv_lo", b), mix_lo[:, b, :], y, mix_hi[:, b, :])

            def latent_sums():
                dve.memset(ss[:, 1:3, 0:9], 1.0).then_inc(*DVE.done(("lat0",)))
                dve.wait_ge(*DVE.after("lat0"))
                dve.wait_ge(*PE.after("lat_ss"))
                dve.tensor_scalar(ss[:, 1, 0:4], ps[:, 6, 0:4], 1.0 / 256, EPS, ALU.mult, ALU.add).then_inc(*DVE.done(("lat_q",)))
                dve.tensor_scalar(ss[:, 1, 4:8], ps[:, 6, 4:8], 1.0 / 128, EPS, ALU.mult, ALU.add).then_inc(*DVE.done(("lat_kv",)))
                dve.tensor_scalar(ss[0:N_META, 1, 8:9], ps[0:N_META, 6, 8:9], 1.0 / 128, EPS, ALU.mult,
                                  ALU.add).then_inc(*DVE.done(("lat_v",), ("v", "lat")))
                rsqrt_finish(("lat",), ss[:, 1, 0:9], ss[:, 2, 0:9], ss[:, 0, 0:9])

            def mla_sums():
                dve.memset(ss[:, 3:6, 0:72], 1.0).then_inc(*DVE.done(("head0",)))
                dve.wait_ge(*DVE.after("head0"))
                dve.wait_ge(rope_in, 48)
                dve.wait_ge(*ACT.after("kr"))
                for t in range(NT + 1):
                    rows = P if t < NT else N_META
                    for n in range(2):
                        dve.wait_ge(*ACT.after("k_raw", n, t))
                    k3 = k_sb[0:rows, t, :].rearrange("p (h n) -> p h n", h=MLA_H)
                    dve.tensor_copy(k3[:, :, QKN:QKH], kr[0:rows, t, :].unsqueeze(1).to_broadcast([rows, MLA_H, QKR])
                                    ).then_inc(*DVE.done(("kr_in", t)))
                for i, (kind, t) in enumerate(HEAD_TILES):
                    rows = P if t < NT else N_META
                    dve.wait_ge(*ACT.after("hsq", kind, t))
                    at = (0 if kind == "q" else 32) + 8 * t
                    dve.tensor_reduce(ss[0:rows, 5, at:at + 8], sq[0:rows, i % 2, :].rearrange("p (h n) -> p h n", h=MLA_H), X,
                                      ALU.add).then_inc(*DVE.done(("hss", kind, t)))
                dve.wait_ge(*DVE.after("hss", "k", NT))
                mean(("head",), ss[:, 3, 0:72], ss[:, 5, 0:72], QKH)
                rsqrt_finish(("head",), ss[:, 3, 0:72], ss[:, 4, 0:72], ss[:, 5, 0:72])

            def mla_norm(t):
                rows = P if t < NT else N_META
                for kind, x in (("q", q_sb), ("k", k_sb)):
                    if kind == "q" and t == NT:
                        continue
                    x3 = x[0:rows, t, :].rearrange("p (h n) -> p h n", h=MLA_H)
                    if kind == "q":
                        r = ss[0:rows, 4, 8 * t:8 * t + 8].unsqueeze(2).to_broadcast([rows, MLA_H, QKH])
                        dve.tensor_tensor(x3, x3, r, ALU.mult).then_inc(*DVE.done(("hn1", "q", t)))
                        dve.wait_ge(*DVE.after("hn1", "q", t))
                        dve.tensor_tensor(x3, x3, qk_gain[0:rows, 0, :].unsqueeze(1).to_broadcast([rows, MLA_H, QKH]),
                                          ALU.mult).then_inc(*DVE.done(("hn2", "q", t)))
                        dve.wait_ge(*DVE.after("hn2", "q", t))
                    else:
                        dve.wait_ge(*POOL.after("hn2", "k", t))
                    rope_turn(("rope_m", kind, t), x3[:, :, QKN:QKH], x3[:, :, QKN:QKH], rows, MLA_H, QKR // 2, t, cos_m, sin_m)

            def k_transposed(tag, h, width, dst, bank):
                dve.wait_ge(*PE.after("kT", tag, h))
                if h >= 2:
                    dve.wait_ge(*PE.after(*last_scores(tag, h - 2)))
                dve.tensor_copy(dst[0:width, h % 2, :],
                                psf[0:width, (bank + 1) * SEQ - N_META:(bank + 2) * SEQ]).then_inc(*DVE.done(("kT", tag, h)))

            def mla_scores(j):
                n = P * (j % NT + 1)
                dve.wait_ge(*PE.after("S", "mla", j))
                dve.tensor_reduce(sm[:, 0, j:j + 1], psf[:, 5 * SEQ - N_META:5 * SEQ + n], X,
                                  ALU.max).then_inc(*DVE.done(("max", "mla", j)))
                dve.wait_ge(*DVE.after("max", "mla", j))
                dve.tensor_scalar(sm[:, 1, j:j + 1], sm[:, 0, j:j + 1], -float(QKH) ** -0.5, None,
                                  ALU.mult).then_inc(*DVE.done(("nmax", "mla", j)))

            def mla_turn(j):
                dve.wait_ge(*ACT.after("exp", "mla", j))
                dve.reciprocal(sm[:, 3, j:j + 1], sm[:, 2, j:j + 1]).then_inc(*DVE.done(("rsum", "mla", j)))
                dve.wait_ge(*PE.after("PTm", "mla", j))
                dve.tensor_copy(probT_m[:, j % 2, :], ps[0:N_META, 7, 0:P]).then_inc(*DVE.done(("PTm", "mla", j)))

            def mla_values(j):
                h, t = divmod(j, NT)
                dve.wait_ge(*PE.after("O", "mla", j))
                dve.wait_ge(*DVE.after("rsum", "mla", j))
                dve.wait_ge(*ACT.after("z_mla", t))
                cols = slice(VH * h, VH * (h + 1))
                dve.scalar_tensor_tensor(y_mla[:, t, cols], ps[:, 7, P:P + VH], sm[:, 3, j:j + 1], z_mla[:, t, cols],
                                         ALU.mult, ALU.mult).then_inc(*DVE.done(("y", "mla", j)))

            def ret_scores(h):
                dve.wait_ge(decay_in, 32 * (h + 1))
                dve.wait_ge(*PE.after("rS", h, "meta"))
                if h:
                    dve.wait_ge(*PE.after("rO", h - 1))
                dve.tensor_tensor(sd_m[:, :], ps[0:N_META, 3, :], decay_m[:, :], ALU.mult).then_inc(*DVE.done(("sd", h, "meta")))
                for b in range(NT):
                    dve.wait_ge(*PE.after("rS", h, b))
                    dve.tensor_tensor(sd[:, b, P * b:SEQ], ps[:, b, P * b:SEQ], decay[:, 0:SEQ - P * b],
                                      ALU.mult).then_inc(*DVE.done(("sd", h, b)))

            def ret_norm():
                dve.wait_ge(*ACT.after("ysq"))
                dve.tensor_reduce(ss[:, 5, 0:16], ysq[:, :, :].rearrange("p t (h n) -> p (t h) n", n=RET_D), X,
                                  ALU.add).then_inc(*DVE.done(("yss",)))
                dve.wait_ge(*DVE.after("yss"))
                mean(("ret",), ss[:, 3, 0:16], ss[:, 5, 0:16], RET_D)
                rsqrt_finish(("ret",), ss[:, 3, 0:16], ss[:, 4, 0:16], ss[:, 5, 0:16])
                for t in range(NT):
                    y = y_ret[:, t, :].rearrange("p (h n) -> p h n", h=RET_H)
                    dve.tensor_tensor(y, y, ss[:, 4, 4 * t:4 * t + 4].unsqueeze(2).to_broadcast([P, RET_H, RET_D]),
                                      ALU.mult).then_inc(*DVE.done(("yn", t)))
                    dve.wait_ge(*DVE.after("yn", t))
                    dve.tensor_tensor(y_ret[:, t, :], y_ret[:, t, :], z_ret[:, t, :], ALU.mult).then_inc(*DVE.done(("y_ret", t)))

            def mix_one():
                for c in range(6):
                    dve.wait_ge(*ACT.after("mix_hi", 2 + c))
                    low_part(("mix_lo", 2 + c), mix_lo[:, 2 + c, :], ps[:, 6 + c % 2, :], mix_hi[:, 2 + c, :],
                             1.0 if c < 4 else col("ret_norm"))

            steps = {"item": item, "norm": norm, "conv": conv, "latent_sums": latent_sums, "mla_sums": mla_sums,
                     "mla_norm": mla_norm, "mla_scores": mla_scores, "mla_turn": mla_turn, "mla_values": mla_values,
                     "ret_scores": ret_scores, "ret_norm": ret_norm, "mix_one": mix_one, "gla_decays": gla_decays,
                     "gla_states": gla_states, "gla_rstd": gla_rstd, "mix": mix, "idx_key": idx_key,
                     "idx_scores": idx_scores, "dsa_prepare": dsa_prepare, "dsa_scores": dsa_scores,
                     "dsa_values": dsa_values, "mem_prepare": mem_prepare, "mem_scores": mem_scores,
                     "mem_values": mem_values, "route": route}
            for step, *a in order:
                if step == "constants":
                    dve.wait_ge(*PE.after("gains"))
                    dve.tensor_copy(gains[:, :], ps[:, 7, 0:64]).then_inc(*DVE.done(("gains",)))
                    dve.wait_ge(*DVE.after("gains"))
                elif step == "mla_transposes":
                    k_transposed("mla", a[0], QKH, kT, 4)
                elif step == "ret_transposes":
                    k_transposed("ret", a[0], RET_D, rkT, 1)
                elif step == "dsa_turn":
                    if a[0] == NT * DSA_H - 1:
                        dsa_scores(a[0] + 1)
                elif step == "mem_turn":
                    if a[0] == NT * MEM_H - 1:
                        mem_scores(a[0] + 1)
                elif step in steps:
                    steps[step](*a)
                elif step == "barrier":
                    barrier(dve, a[0])
                    DVE.section = a[0]

        for engine, p in (("tensor", PE), ("scalar", ACT), ("vector", DVE), ("gpsimd", POOL)):
            known[engine] = p.at
            known[engine + " ends"] = p.count


def constants():
    f = np.float32
    pos = np.arange(L, dtype=f)

    def tables(dim):
        inv = f(1.0) / (f(10000.0) ** (np.arange(0, dim, 2, dtype=f) / f(dim)))
        ang = pos[:, None] * inv[None, :]
        return np.cos(ang).astype(f), np.sin(ang).astype(f)

    def tiles(table):
        n = table.shape[1]
        t = np.zeros((P, NT + 1, n), f)
        for i in range(NT):
            t[:, i] = table[N_META + P * i:N_META + P * (i + 1)]
        t[:N_META, NT] = table[:N_META]
        return t.reshape(P, -1)

    cm, sm = tables(QKR)
    cr, sr = tables(RET_D)
    rope = np.concatenate([tiles(cm), tiles(sm), tiles(cr), tiles(sr)], axis=1)
    log_g = np.log1p(-np.exp2(-5.0 - np.arange(RET_H)))
    m, c = np.arange(P)[:, None], np.arange(SEQ)[None, :]
    seen = (m // CHUNK) <= (c // CHUNK)
    decay = np.stack([np.where(seen, np.exp(g * np.abs(c - m)), 0.0) for g in log_g]) * RET_D ** -0.5
    mm = np.arange(N_META)[:, None]
    decay_m = np.stack([np.exp(g * (c + N_META - mm)) for g in log_g]) * RET_D ** -0.5
    j, i = np.arange(P)[:, None], np.arange(P)[None, :]
    return {
        "c_ident": np.eye(P, dtype=f),
        "c_gla_mask": ((j // CHUNK == i // CHUNK) & (i >= j)).astype(f),
        "c_dsa_mask": np.where(i <= j, 0.0, MASKED).astype(f),
        "c_mask_q": (np.arange(P) < CHUNK).astype(f)[None, :],
        "c_mask_k": np.full((1, CHUNK), MASKED, f),
        "c_rope": rope.astype(f),
        "c_decay": decay.astype(f),
        "c_decay_m": decay_m.astype(f),
        "c_scan": np.tile((np.arange(SEQ) % CHUNK != 0).astype(f), (P, 1)),
    }


def kernel(**inputs):
    import concourse.bacc as bacc
    from concourse.bass_utils import run_bass_kernel_spmd

    arrays = {name: np.ascontiguousarray(a) for name, a in inputs.items()}
    arrays.update(constants())

    def build(known):
        nc = bacc.Bacc("TRN2", target_bir_lowering=False, num_devices=1)
        w = {name: nc.dram_tensor(f"in_{name}", a.shape, mybir.dt.from_np(a.dtype), kind="ExternalInput").ap()
             for name, a in arrays.items()}
        out = nc.dram_tensor("out_0", (1, SEQ, D), F32, kind="ExternalOutput").ap()
        program(nc, w, out, known)
        return nc

    known = {}
    build(known)
    nc = build(known)
    r = run_bass_kernel_spmd(nc, [{f"in_{name}": a for name, a in arrays.items()}], core_ids=[0])
    return r.results[0]["out_0"]
```

```python
from contextlib import ExitStack

import numpy as np
import concourse.bass as bass
from concourse import mybir

F32 = mybir.dt.float32
F32R = mybir.dt.float32r
ALU = mybir.AluOpType
ACTF = mybir.ActivationFunctionType
X = mybir.AxisListType.X

P = 128
D = 1024
KC = D // P
SEQ = 512
NT = SEQ // P
N_META = 16
L = SEQ + N_META
EPS = 1e-6
CHUNK = 64
QKN, QKR, VH = 64, 32, 64
QKH = QKN + QKR
MLA_H = 8
RET_H, RET_D = 4, 64
MEM = 256
GLA_H, GLA_DV = 4, 256
DSA_H, DSA_G = 8, 4
IDX_H, IDX_D = 8, 64
TOPK = SEQ // 4
MEM_H = 4
N_EXP = 16
D_EXP = 256
MASKED = -1e30
PICKED = -3e38

RAW_SLOTS = 4
SPLIT_SLOTS = 4
UNIT = 1024

C_CX, C_CC, C_CQ, C_KR, C_MZ, C_RQ, C_RV = 0, 512, 1024, 1408, 1440, 1952, 2464
C_GQ, C_GK, C_GV, C_GG, C_GA, C_DQ, C_DK, C_IQ, C_IK, C_MQ, C_GATE = (
    0, 512, 1024, 2048, 3072, 3088, 4112, 4624, 5136, 5208, 6232)

GAINS, _row = {}, 0
for _name, _n in (("ln_w", 8), ("g_mix_2", 8), ("g_mem_2", 8), ("g_ffn_2", 8), ("q_a_norm", 2),
                  ("kv_a_norm", 1), ("conv_w", 6), ("conv_b", 2), ("dsa_q_norm_2", 1),
                  ("dsa_k_norm_2", 1), ("mem_q_norm_2", 2), ("mem_k_norm_2", 2), ("b_gla_a2_2", 4),
                  ("gla_norm_2", 2), ("ret_norm", 1), ("idx_k_norm_2", 1)):
    GAINS[_name] = _row
    _row += _n
N_GAINS = _row


class Progress:

    def __init__(self, nc, ctx, engine, sections, known):
        self.sems = {s: ctx.enter_context(nc.semaphore(f"{engine}_done_{s}")) for s in sections}
        self.count = dict.fromkeys(sections, 0)
        self.section = sections[0]
        self.at = {}
        self.known = known.setdefault(engine, {})
        self.ends = known.setdefault(engine + " ends", {})

    def done(self, *keys):
        self.count[self.section] += 1
        for key in keys:
            assert key not in self.at, key
            self.at[key] = (self.section, self.count[self.section])
        return self.sems[self.section], 1

    def after(self, *key):
        section, value = self.known.get(key, (self.section, 1)) if not self.ends else self.known[key]
        return self.sems[section], value

    def end_of(self, section):
        return self.sems[section], self.ends.get(section, 1)


def weight_items(w):
    items = {}

    def add(name, src, cols, chunks=KC, per=2):
        n = sum(b - a for a, b in cols)
        units = []
        for k0 in range(0, chunks, per):
            pieces, at = [], 0
            for a, b in cols:
                pieces.append((at, at + b - a, src[P * k0:P * (k0 + per), a:b].rearrange("(k p) n -> p k n", p=P)))
                at += b - a
            units.append((list(range(k0, k0 + per)), n, pieces))
        items[name] = units

    w_in, w_in2 = w["w_in"][0], w["w_in_2"][0]
    add("conv_a", w_in, [(C_CX, C_CC)])
    add("conv_b", w_in, [(C_CC, C_CQ)])
    add("latent", w_in, [(C_CQ, C_KR)])
    add("k_rope", w_in, [(C_KR, C_MZ)], per=8)
    add("ret_qk", w_in, [(C_RQ, C_RV)])
    add("ret_vz", w_in, [(C_RV, C_RV + 512)])
    add("mla_z", w_in, [(C_MZ, C_RQ)])
    for n in range(2):
        add(f"w_uq{n}", w["w_uq"][0], [(384 * n, 384 * n + 384)], chunks=2)
    for n in range(2):
        add(f"w_ukv{n}", w["w_ukv"][0], [(512 * n, 512 * n + 512)], chunks=1, per=1)
    for n in range(2):
        add(f"w_out{n}", w["w_out"][0], [(512 * n, 512 * n + 512)])
    add("small2", w_in2, [(C_GA, C_DQ), (C_IK, C_MQ)], per=8)
    add("gla_q", w_in2, [(C_GQ, C_GK)])
    add("gla_k", w_in2, [(C_GK, C_GV)])
    for n in range(2):
        add(f"gla_v{n}", w_in2, [(C_GV + 512 * n, C_GV + 512 * n + 512)])
    for n in range(2):
        add(f"gla_g{n}", w_in2, [(C_GG + 512 * n, C_GG + 512 * n + 512)])

    def branch(b, w_o):
        for n in range(2):
            c = C_GATE + D * b + 512 * n
            add(f"gate{b}{n}", w_in2, [(c, c + 512)])
            add(f"w_o{b}{n}", w_o[0], [(512 * n, 512 * n + 512)])

    branch(0, w["w_o_gla_2"])
    add("idx_q", w_in2, [(C_IQ, C_IK)])
    for n in range(2):
        add(f"dsa_q{n}", w_in2, [(C_DQ + 512 * n, C_DQ + 512 * n + 512)])
    add("dsa_kv", w_in2, [(C_DK, C_IQ)])
    branch(1, w["w_o_dsa_2"])
    for n in range(4):
        add(f"mem_kv{n}", w["w_mem_kv_2"][0], [(512 * n, 512 * n + 512)])
    for n in range(2):
        add(f"mem_q{n}", w_in2, [(C_MQ + 512 * n, C_MQ + 512 * n + 512)])
    branch(2, w["w_o_mem_2"])
    for n in range(2):
        add(f"w_out2{n}", w["w_out_2"][0], [(512 * n, 512 * n + 512)])
    items["router"] = [(list(range(KC)), 20, [
        (0, 4, w["w_r1_2"][0].rearrange("(k p) n -> p k n", p=P)),
        (4, 20, w["w_r2_2"][0].rearrange("(k p) n -> p k n", p=P))])]
    for e in range(N_EXP):
        units = []
        for k0 in range(0, KC, 2):
            rows = slice(P * k0, P * (k0 + 2))
            units.append(([k0, k0 + 1], 512, [
                (0, 256, w["w_gate_2"][0, e, rows, :].rearrange("(k p) n -> p k n", p=P)),
                (256, 512, w["w_up_2"][0, e, rows, :].rearrange("(k p) n -> p k n", p=P))]))
        items[f"expert{e}"] = units
    for e in range(N_EXP):
        for n in range(2):
            add(f"down{e}{n}", w["w_down_2"][0, e], [(512 * n, 512 * n + 512)], chunks=2)
    return items


E_UNITS = 6
E_SLOTS = 12


def make_order():
    order = [("constants",), ("norm", "h")]
    order += [("item", n) for n in ("conv_a", "conv_b", "latent")]
    order += [("latent_sums",), ("item", "k_rope"), ("conv",)]
    order += [("item", n) for n in ("w_uq0", "w_uq1", "w_ukv0", "w_ukv1")]
    order += [("mla_sums",), ("item", "mla_z"), ("mla_norm", 0), ("mla_norm", 1), ("item", "ret_qk")]
    order += [("mla_norm", t) for t in range(2, NT + 1)] + [("item", "ret_vz"), ("barrier", "mla")]
    pieces = [(p, h) for h in range(RET_H) for p in ("ret_transposes", "ret_scores", "ret_values")]
    n = NT * MLA_H
    for j in range(n + 3):
        if j >= 3:
            order += [("mla_values", j - 3)]
        if j % 2 == 0 and j >= 4 and pieces:
            order += [pieces.pop(0)]
        if 2 <= j < n + 2:
            order += [("mla_turn", j - 2)]
        if j % NT == 0 and j < n:
            order += [("mla_transposes", j // NT)]
        if j < n:
            order += [("mla_scores", j)]
    order += pieces
    order += [("ret_norm",), ("mix_one",), ("item", "w_out0"), ("item", "w_out1"), ("barrier", "gla")]
    order += [("norm", "h2")]
    order += [("item", n) for n in ("small2", "gla_q", "gla_k")]
    order += [("gla_low",), ("gla_decays", 0), ("item", "gla_v0"), ("gla_decays", 1), ("item", "gla_v1")]
    for h in range(GLA_H):
        order += [("gla_states", h), ("gla_values", h)]
        if h + 2 < GLA_H:
            order += [("gla_decays", h + 2)]
        if h == 1:
            order += [("gla_rstd", 0), ("item", "gla_g0")]
    order += [("gla_rstd", 1), ("item", "gla_g1"), ("item", "gate00"), ("mix", "gla")]
    order += [("item", n) for n in ("w_o00", "gate01", "w_o01")]
    order += [("barrier", "dsa"), ("idx_key",), ("item", "idx_q")]
    order += [("idx_scores", t) for t in range(1, NT)]
    order += [("item", "dsa_kv"), ("dsa_scale", "k"), ("item", "dsa_q0"), ("dsa_prepare", "k"), ("dsa_scale", "q0")]
    order += [("item", "dsa_q1"), ("dsa_prepare", "q0"), ("dsa_scale", "q1"), ("dsa_prepare", "q1"), ("barrier", "dsa2")]
    n = NT * DSA_H
    for j in range(n + 3):
        order += [("dsa_values", j - 3)] * (j >= 3) + [("dsa_turn", j - 2)] * (2 <= j < n + 2) + [("dsa_scores", j)] * (j < n)
    order += [("barrier", "mem"), ("norm_scale", "mem"), ("item", "gate10"), ("norm", "mem")]
    order += [("item", n) for n in ("w_o10", "gate11", "w_o11")]
    order += [("item", "mem_kv0"), ("item", "mem_kv1"), ("mem_scale", "k")]
    order += [("item", n) for n in ("mem_kv2", "mem_kv3", "mem_q0")]
    order += [("mem_prepare", "k"), ("mem_scale", "q0"), ("item", "mem_q1"), ("mem_prepare", "q0"), ("mem_scale", "q1")]
    order += [("mem_prepare", "q1"), ("barrier", "mem2")]
    n = NT * MEM_H
    for j in range(n + 3):
        order += [("mem_values", j - 3)] * (j >= 3) + [("mem_turn", j - 2)] * (2 <= j < n + 2) + [("mem_scores", j)] * (j < n)
    order += [("item", n) for n in ("gate20", "w_o20", "gate21", "w_o21")]
    order += [("mix", "merged"), ("item", "w_out20"), ("item", "w_out21")]
    order += [("barrier", "experts"), ("norm", "ffn"), ("split_x",), ("item", "router"), ("weights", 3), ("route", 0)]
    order += [("sort",), ("weights", 4), ("resort",), ("weights", E_UNITS)]
    for v in range(NT * N_EXP):
        if v >= NT and v // NT % 4 == 0:
            order += [("finish", v - NT)]
        if v % NT < 2:
            order += [("weights", E_UNITS * (v // NT + 1) + 3 + v % NT)]
        order += [("visit", v)]
        if v == 0:
            order += [("route", 1)]
        if v == NT - 1:
            order += [("combine_s",)]
        if v % NT == NT - 1:
            order += [("weights", E_UNITS * (v // NT + 2))]
    order += [("finish", NT * (N_EXP - 1) + s) for s in range(NT)]
    order += [("unsort",)]
    return order


def sections_of(order):
    return ["start"] + [step[1] for step in order if step[0] == "barrier"]


NORMS = {"h": "ln_w", "h2": "g_mix_2", "ffn": "g_ffn_2", "mem": "g_mem_2"}


def program(nc, w, out, known):
    order = make_order()
    items = weight_items(w)
    units, first_unit = [], {}
    for step in order:
        if step[0] == "item":
            first_unit[step[1]] = len(units)
            units += items[step[1]]
    expert_unit = len(units)
    for e in range(N_EXP):
        units += items[f"expert{e}"] + items[f"down{e}0"] + items[f"down{e}1"]

    with ExitStack() as ctx:
        base = 16512

        def sb(name, shape, at_kb, dt=F32):
            assert base + at_kb * 1024 + 4 * int(np.prod(shape[1:])) <= nc.sbuf_usable_end, name
            return nc.alloc_sbuf_tensor_at(name, shape, dt, offset=base + round(at_kb * 32) * 32)

        def semaphore(name):
            return ctx.enter_context(nc.semaphore(name))

        ps = ctx.enter_context(nc.psum_tensor("ps", [P, 8, 512], F32))
        psf = ps[:, :, :].rearrange("p b n -> p (b n)")

        raw = sb("raw", [P, RAW_SLOTS, UNIT], 0)
        w_hi = sb("w_hi", [P, SPLIT_SLOTS, UNIT], 16, F32R)
        w_lo = sb("w_lo", [P, SPLIT_SLOTS, UNIT], 32, F32R)
        act_hi = sb("act_hi", [P, KC, L], 48, F32R)
        act_lo = sb("act_lo", [P, KC, L], 64.5, F32R)
        mix_hi = sb("mix_hi", [P, KC, SEQ], 81, F32R)
        mix_lo = sb("mix_lo", [P, KC, SEQ], 97, F32R)
        x1 = sb("x1", [P, NT, D], 113)
        gains = sb("gains", [P, 64], 129)
        ident = sb("ident", [P, P], 129.25)
        gla_mask = sb("gla_mask", [P, P], 129.75)
        dsa_mask = sb("dsa_mask", [P, P], 130.25)
        mask_q = sb("mask_q", [1, P], 130.75)
        mask_k = sb("mask_k", [1, CHUNK], 131.25)
        ones = sb("ones", [P, 2], 131.5)
        ss = sb("ss", [P, 8, 72], 131.75)
        sm = sb("sm", [P, 4, 32], 134)
        SC = 134.5
        xs = sb("xs", [P, NT, D], 81)
        meta = sb("meta", [N_META, D], 97)
        metas = sb("metas", [N_META, D], 101)
        g_rows = sb("g_rows", [64, P], 105)
        meta_t = sb("meta_t", [P, KC, N_META], 106)
        cx = sb("cx", [P, 2, L], SC)
        cb = sb("cb", [P, 2, SEQ], SC + 4.25)
        cu = sb("cu", [P, 2, L], SC + 8.25)
        cz = sb("cz", [P, 2, SEQ], SC + 12.5)
        cy = sb("cy", [P, 2, SEQ], SC + 16.5)
        q_sb = sb("q_sb", [P, NT, MLA_H * QKH], SC)
        k_sb = sb("k_sb", [P, NT + 1, MLA_H * QKH], SC + 12)
        v_sb = sb("v_sb", [P, NT + 1, MLA_H * VH], SC + 27)
        z_mla = sb("z_mla", [P, NT, MLA_H * VH], SC + 37)
        rqk = sb("rqk", [P, NT + 1, 512], SC + 45)
        rv = sb("rv", [P, NT + 1, 256], SC + 55)
        z_ret = sb("z_ret", [P, NT, 256], SC + 60)
        rope = sb("rope", [P, 5 * 96], SC + 64)
        kr = sb("kr", [P, NT + 1, QKR], SC + 66)
        qk_gain = sb("qk_gain", [P, 2, QKH], SC + 66.75)
        t0 = sb("t0", [P, 256], SC + 67.75)
        t1 = sb("t1", [P, 256], SC + 68.75)
        t2 = sb("t2", [P, 256], SC + 69.75)
        t3 = sb("t3", [P, 256], SC + 70.75)
        small_t = sb("small_t", [P, L], SC + 60)
        cos_m = rope[:, 0:80].rearrange("p (t n) -> p t n", t=5)
        sin_m = rope[:, 80:160].rearrange("p (t n) -> p t n", t=5)
        cos_r = rope[:, 160:320].rearrange("p (t n) -> p t n", t=5)
        sin_r = rope[:, 320:480].rearrange("p (t n) -> p t n", t=5)
        cq_sq = sb("cq_sq", [P, 2, SEQ], SC + 37)
        ckv_sq = sb("ckv_sq", [P, L], SC + 41)
        cq_hi = sb("cq_hi", [P, 2, SEQ], SC + 45, F32R)
        cq_lo = sb("cq_lo", [P, 2, SEQ], SC + 49, F32R)
        ckv_hi = sb("ckv_hi", [P, L], SC + 53, F32R)
        ckv_lo = sb("ckv_lo", [P, L], SC + 55.25, F32R)
        sq = sb("sq", [P, 2, MLA_H * QKH], 81 + 8)
        qT = sb("qT", [P, 2, SEQ], 48)
        kT = sb("kT", [P, 2, L], 52)
        prob = sb("prob", [P, 3, L], 56.25)
        probT = sb("probT", [P, 2, SEQ], 62.5)
        probT_m = sb("probT_m", [N_META, 2, P], 66.5)
        y_mla = sb("y_mla", [P, NT, MLA_H * VH], 67.5)
        y_ret = sb("y_ret", [P, NT, 256], 75.5)
        sd = sb("sd", [P, NT, SEQ], 85)
        ysq = sb("ysq", [P, NT, 256], 85)
        sd_m = sb("sd_m", [N_META, SEQ], 93)
        decay = sb("decay", [P, SEQ], 95)
        rqT = sb("rqT", [P, 2, SEQ], 101)
        rkT = sb("rkT", [P, 2, L], 105)
        decay_m = sb("decay_m", [N_META, SEQ], 109.25)

        merged = sb("merged", [P, NT, D], SC)
        sm2 = sb("sm2", [P, NT, 88], SC + 16)
        gate = sb("gate", [P, NT, 512], SC + 17.5)
        gate_bias = sb("gate_bias", [P, 2, 512], SC + 25.5)
        gv = sb("gv", [P, NT, D], SC)
        gq = sb("gq", [P, GLA_H, SEQ], SC + 17.5)
        gk = sb("gk", [P, GLA_H, SEQ], SC + 25.5)
        go = sb("go", [P, NT, D], SC + 33.5)
        state = sb("state", [P, 8, GLA_DV], SC + 49.5)
        g_silu = sb("g_silu", [P, 2, 512], SC + 57.5)
        low_t = sb("low_t", [16, SEQ], SC + 61.5)
        w_a2 = sb("w_a2", [16, 512], SC + 63.5)
        scan_mask = sb("scan_mask", [P, SEQ], SC + 65.5)
        g_dec = sb("g_dec", [P, 2, 8], SC + 67.5)
        gz = sb("gz", [P, SEQ], 81)
        gab = sb("gab", [P, SEQ], 83)
        gex = sb("gex", [P, SEQ], 85)
        glc = sb("glc", [P, SEQ], 87)
        gsq = sb("gsq", [P, GLA_DV], 89)
        g_qd = sb("g_qd", [P, 2, SEQ], 90)
        g_ki = sb("g_ki", [P, 2, SEQ], 94)
        g_ke = sb("g_ke", [P, 2, SEQ], 98)
        g_keT = sb("g_keT", [P, 2, SEQ], 102)
        g_att = sb("g_att", [P, 2, SEQ], 106)
        dq = sb("dq", [P, NT, D], 81)
        dk = sb("dk", [P, NT, 256], 101)
        d_sq = sb("d_sq", [P, 2, 512], 97)
        ik2 = sb("ik2", [P, NT, P], 105)
        dqT = sb("dqT", [P, DSA_H, SEQ], SC + 17.5)
        iqT = sb("iqT", [P, 4, SEQ], SC + 33.5)
        dkT = sb("dkT", [P, 2, SEQ], SC + 41.5)
        dv = sb("dv", [P, NT, 256], SC + 45.5)
        ikT = sb("ikT", [P, SEQ], SC + 49.5)
        d_mask = sb("d_mask", [P, 1280], SC + 51.5)
        work = sb("work", [P, 3, SEQ], SC + 56.5)
        rel = sb("rel", [P, 2, SEQ], SC + 62.5)
        d_probT = sb("d_probT", [P, 2, SEQ], SC + 62.5)
        d_prob = sb("d_prob", [P, 3, SEQ], SC + 66.5)
        best8 = sb("best8", [P, 8], SC + 73)
        mem_in = sb("mem_in", [P, 2, D], SC + 33.5)
        mem_sc = sb("mem_sc", [P, 2, D], SC + 57.5)
        mk = sb("mk", [P, 2, D], SC + 17.5)
        mv = sb("mv", [P, 2, D], SC + 25.5)
        mkT = sb("mkT", [P, 8, MEM], SC + 33.5)
        mem_hi = sb("mem_hi", [P, KC, MEM], SC + 41.5, F32R)
        mem_lo = sb("mem_lo", [P, KC, MEM], SC + 49.5, F32R)
        mqT = sb("mqT", [P, 8, SEQ], SC + 41.5)
        m_prob = sb("m_prob", [P, 3, MEM], SC + 57.5)
        m_probT = sb("m_probT", [P, 2, MEM], SC + 60.5)
        xs_hi = sb("xs_hi", [P, NT, D], SC, F32R)
        xs_lo = sb("xs_lo", [P, NT, D], SC + 16, F32R)
        y_exp = sb("y_exp", [P, NT, D], SC)
        perm = sb("perm", [P, NT, SEQ], SC + 32, F32R)
        hid_hi = sb("hid_hi", [P, NT, D_EXP], SC + 48, F32R)
        hid_lo = sb("hid_lo", [P, NT, D_EXP], SC + 52, F32R)
        rl = sb("rl", [P, NT, 20], SC + 57)
        r_bias = sb("r_bias", [P, 20], SC + 57.5)
        rank = sb("rank", [P, 4], SC + 57.625)
        rt = sb("rt", [P, 16, 16], SC + 57.75)
        combine = sb("combine", [P, NT, N_EXP], SC + 58.75)
        combine_s = sb("combine_s", [P, NT, N_EXP], SC + 59)
        so = sb("so", [P, 8, 16], SC + 59.25)
        flags = sb("flags", [P, 16], SC + 59.75, mybir.dt.int32)
        hid = sb("hid", [P, 2, D_EXP], SC + 60)
        e_silu = sb("e_silu", [P, 2, D_EXP], SC + 62)
        skipped = sb("skipped", [1, 2, NT * N_EXP], SC + 72)
        iota = sb("iota", [P, SEQ], SC + 48)
        before_t = sb("before_t", [P, P], SC + 50)
        all_ones = sb("all_ones", [P, P], SC + 50.5)
        permT = sb("permT", [P, NT, SEQ], 48, F32R)
        more_hi = sb("more_hi", [P, 4, UNIT], 48, F32R)
        more_lo = sb("more_lo", [P, 4, UNIT], 64, F32R)
        far_hi = sb("far_hi", [P, 2, UNIT], SC + 16, F32R)
        far_lo = sb("far_lo", [P, 2, UNIT], SC + 24, F32R)
        gap_w = sb("gap_w", [P, 2, UNIT], SC + 40, F32R)
        end_w = sb("end_w", [P, 2, UNIT], SC + 64, F32R)

        bias_in = [semaphore(f"bias_in{i}") for i in range(2)]
        gla_in = semaphore("gla_in")
        mem_landed = semaphore("mem_landed")
        route_in = semaphore("route_in")
        sort_in = semaphore("sort_in")
        w_landed = [semaphore(f"w_landed{i}") for i in range(RAW_SLOTS)]
        landed, total = [], [0] * RAW_SLOTS
        for g, (_, _, pieces) in enumerate(units):
            total[g % RAW_SLOTS] += 16 * len(pieces)
            landed.append(total[g % RAW_SLOTS])
        const_in = semaphore("const_in")
        gains_in = [semaphore(f"gains_in{i}") for i in range(2)]
        zeroed = semaphore("zeroed")
        x_in = semaphore("x_in")
        rope_in = semaphore("rope_in")
        decay_in = semaphore("decay_in")
        stored = semaphore("stored")

        LAST = "unsort"
        sections = sections_of(order)
        PE = Progress(nc, ctx, "tensor", sections, known)
        ACT = Progress(nc, ctx, "scalar", sections, known)
        DVE = Progress(nc, ctx, "vector", sections, known)
        POOL = Progress(nc, ctx, "gpsimd", sections, known)

        def col(gain, n=0):
            return gains[:, GAINS[gain] + n:GAINS[gain] + n + 1]

        NORM_TILES = {"h": [(x1[:, t, :], xs[:, t, :], P) for t in range(NT)] + [(meta[:, :], metas[:, :], N_META)],
                      "h2": [(x1[:, t, :], xs[:, t, :], P) for t in range(NT)],
                      "ffn": [(x1[:, t, :], xs[:, t, :], P) for t in range(NT)],
                      "mem": [(mem_in[:, t, :], mem_sc[:, t, :], P) for t in range(2)]}

        def barrier(eng, section):
            before = sections[sections.index(section) - 1]
            for other in (PE, ACT, DVE, POOL):
                if other.ends.get(before, 1):
                    eng.wait_ge(*other.end_of(before))


        def last_scores(tag, h):
            return ("S", "mla", NT * h + NT - 1) if tag == "mla" else ("rS", h, NT - 1)

        def idx_of(i):
            return 1 + i // IDX_H, i % IDX_H

        def state_bank(n):
            return 2 * (n % 2) + n // 4, slice(GLA_DV * (n // 2 % 2), GLA_DV * (n // 2 % 2 + 1))

        MEM_BANKS = (7, 3, 1, 2, 7, 3, 1, 2)

        HEAD_TILES = [(kind, t) for t in range(NT + 1) for kind in ("q", "k") if (kind, t) != ("q", NT)]

        HEAD_STATS = {("dsa", "q0"): (0, 16), ("dsa", "q1"): (16, 32), ("dsa", "k"): (32, 40),
                      ("mem", "k"): (0, 8), ("mem", "q0"): (8, 16), ("mem", "q1"): (16, 24)}

        def gla_stat(h, t):
            return 8 * (h // 2) + 2 * t + h % 2

        def load_gains(eng, part):
            for name, row in list(GAINS.items())[part::2]:
                src = w[name][0]
                if name in ("ret_norm", "idx_k_norm_2"):
                    for half in range(2):
                        eng.dma_start(g_rows[row:row + 1, 64 * half:64 * half + 64], w[name]).then_inc(gains_in[part], 16)
                elif name == "conv_w":
                    eng.dma_start(g_rows[row:row + 6, :], src.rearrange("j (c p) -> (j c) p", p=P)).then_inc(gains_in[part], 16)
                else:
                    n = src.shape[0] // P
                    eng.dma_start(g_rows[row:row + n, :], src.rearrange("(c p) -> c p", p=P)).then_inc(gains_in[part], 16)

        def load_flags(eng, name):
            registers = [eng.alloc_register(f"{name}_active{i}") for i in range(16)]
            eng.wait_ge(*DVE.after("flags"))
            eng.load(registers, flags[0:1, 0:16])
            return registers

        def split_slot(g):
            if g < expert_unit:
                return w_hi[:, g % SPLIT_SLOTS, :], w_lo[:, g % SPLIT_SLOTS, :]
            i = (g - expert_unit) % E_SLOTS
            if i < 8:
                hi, lo = (w_hi, w_lo) if i < 4 else (more_hi, more_lo)
                return hi[:, i % 4, :], lo[:, i % 4, :]
            if i < 10:
                return far_hi[:, i - 8, :], far_lo[:, i - 8, :]
            both = gap_w if i == 10 else end_w
            return both[:, 0, :], both[:, 1, :]

        def low_by(g):
            return DVE if g >= expert_unit and (g - expert_unit) % E_UNITS >= 4 else POOL

        def slot_free(g):
            if g < expert_unit:
                return ("unit", g - SPLIT_SLOTS) if g >= SPLIT_SLOTS else None
            i = g - expert_unit
            if i >= E_SLOTS:
                return "unit", g - E_SLOTS
            return ("unit", expert_unit - 1) if i < 8 else ("resorted", KC - 1)

        y_hi = mix_hi[:, :, :].rearrange("p (t a) n -> p t (a n)", t=NT)
        y_lo = mix_lo[:, :, :].rearrange("p (t a) n -> p t (a n)", t=NT)

        def norm_dest(name):
            return (mem_hi, 0) if name == "mem" else (act_hi, N_META)

        def norm_lo(name):
            return mem_lo

        def MIX_NEEDS(tag, c, t):
            return DVE.after("go", c // 4, t, c // 2 % 2) if tag == "gla" else DVE.after("merged", 2, c // 4, t)

        def NORM_NEEDS(name, i):
            return []

        def ITEM_NEEDS(name):
            if name in ("conv_a", "conv_b", "latent", "k_rope", "mla_z", "ret_qk", "ret_vz"):
                return [(DVE, ("lo", "h", KC - 1)), (DVE, ("meta_lo", "h"))]
            if name.startswith("w_uq"):
                return [(DVE, ("cq_lo", 1))]
            if name.startswith("w_ukv"):
                return [(DVE, ("ckv_lo", "meta"))]
            if name in ("w_out0", "w_out1"):
                return [(DVE, ("conv_lo", 1)), (DVE, ("mix_lo", KC - 1))]
            if name.startswith(("small2", "gla", "gate", "idx", "dsa", "mem_q")):
                return [(DVE, ("lo", "h2", KC - 1))]
            if name.startswith("mem_kv"):
                return [(DVE, ("lo", "mem", KC - 1))]
            if name.startswith("w_o0"):
                return [(DVE, ("mix_lo", "gla", KC - 1))]
            if name.startswith("w_o1"):
                return [(DVE, ("mix_lo", "dsa", KC - 1))]
            if name.startswith("w_out2"):
                return [(DVE, ("mix_lo", "merged", KC - 1))]
            if name.startswith("w_o2"):
                return [(DVE, ("mix_lo", "mem", KC - 1))]
            if name == "router":
                return [(DVE, ("lo", "ffn", KC - 1))]
            raise KeyError(name)

        def item_readers(name, b):
            n = int(name[-1]) if name[-1].isdigit() else 0
            if name == "conv_a":
                return [(ACT, ("cx", "meta"))] if b == "meta" else [(ACT, ("cx", b) if b < 2 else ("cb", b - 2))]
            if name == "conv_b":
                return [(DVE, ("cu", "meta"))] if b == "meta" else [(DVE, ("cu", b)) if b < 2 else (ACT, ("cz", b - 2))]
            if name == "latent":
                return [(DVE, ("ckv_lo", "meta"))] if b == "meta" else [(DVE, ("cq_lo", b) if b < 2 else ("ckv_lo",))]
            if name == "k_rope":
                return [(ACT, ("kr",))]
            if name.startswith("w_uq"):
                return [(ACT, ("q_raw", n, b))]
            if name.startswith("w_ukv"):
                return [(DVE, ("v_raw", n, b))]
            if name == "mla_z":
                return [(ACT, ("z_mla", b))]
            if name == "ret_qk":
                return [(DVE, ("rope_r", b, 3))]
            if name == "ret_vz":
                return [(ACT, ("z_ret", b) if b < NT else ("rv", b))]
            if name in ("w_out0", "w_out1"):
                return [(DVE, ("x", name, b))]
            if name.startswith("w_out2"):
                return [(DVE, ("x", name, b))]
            if name == "small2":
                return [(ACT, ("sm2",))]
            if name in ("gla_q", "gla_k"):
                return [(ACT, (name, b))]
            if name.startswith("gla_v"):
                return [(ACT, ("gv", n, b))]
            if name.startswith("gla_g"):
                return [(ACT, ("g_silu", n, b))]
            if name.startswith("gate"):
                return [(DVE, ("gate_sum", int(name[4]), n, b))]
            if name.startswith("w_o"):
                return [(DVE, ("gated", int(name[3]), n, b))]
            if name == "idx_q":
                return [(ACT, ("iqT", b))]
            if name.startswith("dsa_q"):
                return [(ACT, ("dq", n, b))]
            if name == "dsa_kv":
                return [(ACT, ("dv", b))]
            if name.startswith("mem_kv"):
                return [(ACT, ("mkv", n, b))]
            if name.startswith("mem_q"):
                return [(ACT, ("mq", n, b))]
            if name == "router":
                return [(DVE, ("rl",))]
            raise KeyError(name)

        block = ctx.enter_context(nc.Block())

        @block.sync
        def _(sp):
            for t in range(NT):
                sp.dma_start(x1[:, t, :], w["x"][0, P * t:P * (t + 1), :]).then_inc(x_in, 16)
            sp.dma_start(meta[:, :], w["meta_tokens"]).then_inc(x_in, 16)
            sp.dma_start(ident[:, :], w["c_ident"]).then_inc(const_in, 16)
            sp.dma_start(gla_mask[:, :], w["c_gla_mask"]).then_inc(const_in, 16)
            sp.dma_start(dsa_mask[:, :], w["c_dsa_mask"]).then_inc(const_in, 16)
            sp.dma_start(mask_q[:, :], w["c_mask_q"]).then_inc(const_in, 16)
            sp.dma_start(mask_k[:, :], w["c_mask_k"]).then_inc(const_in, 16)
            sp.dma_start(rope[:, :], w["c_rope"]).then_inc(rope_in, 16)
            sp.dma_start(qk_gain[:, 0, :], w["q_norm"][0].partition_broadcast(P)).then_inc(rope_in, 16)
            sp.dma_start(qk_gain[:, 1, :], w["k_norm"][0].partition_broadcast(P)).then_inc(rope_in, 16)
            for g, (chunks, n, pieces) in enumerate(units):
                if g >= RAW_SLOTS:
                    sp.wait_ge(*low_by(g - RAW_SLOTS).after("w_lo", g - RAW_SLOTS))
                slot = raw[:, g % RAW_SLOTS, 0:len(chunks) * n].rearrange("p (k n) -> p k n", n=n)
                for a, b, src in pieces:
                    sp.dma_start(slot[:, :, a:b], src).then_inc(w_landed[g % RAW_SLOTS], 16)
            for t in range(NT):
                sp.wait_ge(*DVE.after("x", LAST, t))
                sp.dma_start(out[0, P * t:P * (t + 1), :], x1[:, t, :]).then_inc(stored, 16)
            sp.wait_ge(stored, 16 * NT)

        @block.gpsimd
        def _(pool):
            pool.memset(g_rows[:, :], 0.0).then_inc(zeroed, 1)
            pool.memset(ones[:, :], 1.0).then_inc(zeroed, 1)
            pool.wait_ge(zeroed, 2)
            load_gains(pool, 0)
            fill = [0]

            def split_low(upto):
                for g in range(fill[0], upto):
                    chunks, n, _ = units[g]
                    a = len(chunks) * n
                    if low_by(g) is DVE:
                        continue
                    pool.wait_ge(*ACT.after("w_hi", g))
                    hi, lo = split_slot(g)
                    pool.tensor_tensor(lo[:, 0:a], raw[:, g % RAW_SLOTS, 0:a], hi[:, 0:a].bitcast(F32),
                                       ALU.subtract).then_inc(*POOL.done(("w_lo", g)))
                fill[0] = max(fill[0], upto)

            def mla_norm_keys(t):
                rows = P if t < NT else N_META
                at = 32 + 8 * t
                x3 = k_sb[0:rows, t, :].rearrange("p (h n) -> p h n", h=MLA_H)
                pool.wait_ge(*DVE.after("r", "head"))
                pool.tensor_tensor(x3, x3, ss[0:rows, 4, at:at + 8].unsqueeze(2).to_broadcast([rows, MLA_H, QKH]),
                                   ALU.mult).then_inc(*POOL.done(("hn1", "k", t)))
                pool.wait_ge(*POOL.after("hn1", "k", t))
                pool.tensor_tensor(x3, x3, qk_gain[0:rows, 1, :].unsqueeze(1).to_broadcast([rows, MLA_H, QKH]),
                                   ALU.mult).then_inc(*POOL.done(("hn2", "k", t)))

            for step, *a in order:
                if step == "mla_norm":
                    mla_norm_keys(a[0])
                elif step == "barrier":
                    barrier(pool, a[0])
                    POOL.section = a[0]
                    if a[0] == "experts":
                        pool.memset(all_ones[:, :], 1.0).then_inc(*POOL.done(("all_ones",)))
                elif step == "item":
                    split_low(min(expert_unit, first_unit[a[0]] + len(items[a[0]]) + 2))
                elif step == "weights":
                    split_low(min(len(units), expert_unit + a[0]))
                elif step == "split_x":
                    for t in range(NT):
                        pool.wait_ge(*ACT.after("xs_hi", t))
                        pool.tensor_tensor(xs_lo[:, t, :], xs[:, t, :], xs_hi[:, t, :].bitcast(F32),
                                           ALU.subtract).then_inc(*POOL.done(("xs_lo", t)))

        n_gain_dmas = len(GAINS) // 2 + 1

        @block.tensor
        def _(pe):
            readers = {b: [] for b in range(8)}

            def claim(bank, *who):
                for engine, key in readers[bank]:
                    pe.wait_ge(*engine.after(*key))
                readers[bank] = list(who)

            def product(dst, l_hi, l_lo, r_hi, r_lo, start, stop, skip=False):
                pe.matmul(dst, l_hi, r_hi, start=start, stop=False, skip_group_check=skip)
                pe.matmul(dst, l_hi, r_lo, start=False, stop=False, skip_group_check=skip)
                return pe.matmul(dst, l_lo, r_hi, start=False, stop=stop, skip_group_check=skip)

            def small_item(name):
                (chunks, n, _), = items[name]
                g = first_unit[name]
                meta = name == "k_rope"
                for key in ITEM_NEEDS(name):
                    pe.wait_ge(*key[0].after(*key[1]))
                pe.wait_ge(*POOL.after("w_lo", g))
                wh, wl = [x[:, 0:KC * n].rearrange("p (k n) -> p k n", n=n) for x in split_slot(g)]
                claim(5, (ACT, ("small", name)))
                if meta:
                    claim(6, (ACT, ("small", name)))
                for k in range(KC):
                    mm = product(ps[0:n, 5, :], wh[:, k, :], wl[:, k, :], act_hi[:, k, N_META:L], act_lo[:, k, N_META:L],
                                 k == 0, k == KC - 1)
                if meta:
                    for k in range(KC):
                        mm = product(ps[0:n, 6, 0:N_META], wh[:, k, :], wl[:, k, :], act_hi[:, k, 0:N_META],
                                     act_lo[:, k, 0:N_META], k == 0, k == KC - 1)
                mm.then_inc(*PE.done(("unit", g), ("small", name)))
                pe.wait_ge(*ACT.after("small", name))
                claim(5, *item_readers(name, 0))
                for t in range(NT + meta):
                    rows = P if t < NT else N_META
                    tr = pe.transpose(ps[0:rows, 5, n * t:n * t + n], small_t[0:n, P * t:P * t + rows], ident[0:n, 0:n])
                tr.then_inc(*PE.done(("acc", name, NT - 1 + meta)))

            def item(name):
                if name in ("k_rope", "small2", "router"):
                    return small_item(name)
                its = items[name]
                g0 = first_unit[name]
                meta_blocks = {"conv_a": 2, "conv_b": 2, "latent": 1}.get(name, 0)
                n_acc = {"latent": 3, "mem_kv0": 2, "mem_kv1": 2, "mem_kv2": 2, "mem_kv3": 2}.get(name, NT)
                by_feature = name in ("conv_a", "conv_b", "latent", "gla_q", "gla_k", "idx_q")
                meta_row = name in ("w_ukv0", "w_ukv1", "ret_qk", "ret_vz")
                if name.startswith("w_uq"):
                    a_hi, a_lo, off = cq_hi, cq_lo, 0
                elif name.startswith("w_ukv"):
                    a_hi, a_lo, off = ckv_hi[:, :].unsqueeze(1), ckv_lo[:, :].unsqueeze(1), N_META
                elif name.startswith("w_o"):
                    a_hi, a_lo, off = mix_hi, mix_lo, 0
                elif name.startswith("mem_kv"):
                    a_hi, a_lo, off = mem_hi, mem_lo, 0
                else:
                    a_hi, a_lo, off = act_hi, act_lo, N_META
                for key in ITEM_NEEDS(name):
                    pe.wait_ge(*key[0].after(*key[1]))
                last_u = len(its) - 1
                for u, (chunks, n, _) in enumerate(its):
                    g = g0 + u
                    pe.wait_ge(*POOL.after("w_lo", g))
                    wh = w_hi[:, g % SPLIT_SLOTS, 0:len(chunks) * n].rearrange("p (k n) -> p k n", n=n)
                    wl = w_lo[:, g % SPLIT_SLOTS, 0:len(chunks) * n].rearrange("p (k n) -> p k n", n=n)
                    n_all = n_acc + meta_row
                    for b in range(n_all):
                        bank = b
                        if u == 0:
                            claim(bank, *item_readers(name, b))
                        for j, k in enumerate(chunks):
                            first = u == 0 and j == 0
                            last = u == last_u and j == len(chunks) - 1
                            if by_feature:
                                cols = slice(P * b, P * b + P)
                                mm = product(ps[:, bank, :], wh[:, j, cols], wl[:, j, cols],
                                             a_hi[:, k, off:off + SEQ], a_lo[:, k, off:off + SEQ], first, last)
                            else:
                                rows = slice(off + P * b, off + P * b + P) if b < NT else slice(0, P)
                                mm = product(ps[:, bank, 0:n], a_hi[:, k, rows], a_lo[:, k, rows], wh[:, j, :], wl[:, j, :],
                                             first, last)
                        keys = [("unit", g)] if b == n_all - 1 and not meta_blocks else []
                        if u == last_u:
                            keys.append(("acc", name, b))
                        if keys:
                            mm.then_inc(*PE.done(*keys))
                    for b in range(meta_blocks):
                        if u == 0 and b == 0:
                            claim(4, *item_readers(name, "meta"))
                        for j, k in enumerate(chunks):
                            at = P * (b + (2 if name == "latent" else 0))
                            cols = slice(at, at + P)
                            mm = product(ps[:, 4, N_META * b:N_META * (b + 1)], wh[:, j, cols], wl[:, j, cols],
                                         a_hi[:, k, 0:N_META], a_lo[:, k, 0:N_META],
                                         u == 0 and j == 0 and b == 0, u == last_u and j == len(chunks) - 1, skip=True)
                    if meta_blocks:
                        mm.then_inc(*PE.done(("unit", g), *([("acc", name, "meta")] if u == last_u else [])))

            def norm(name):
                tiles = NORM_TILES[name]
                full = [t for t in tiles if t[2] == P]
                for k in range(KC):
                    bank = 4 + k % 4
                    claim(bank, (DVE, ("lo", name, k)))
                    for i, (_, scaled, _) in enumerate(full):
                        pe.wait_ge(*DVE.after("scaled", name, i))
                        tr = pe.transpose(ps[:, bank, P * i:P * i + P], scaled[:, P * k:P * k + P], ident[:, :])
                    tr.then_inc(*PE.done(("T", name, k)))
                if len(full) < len(tiles):
                    claim(3, (DVE, ("meta_t", name)))
                    pe.wait_ge(*DVE.after("scaled", name, len(full)))
                    for k in range(KC):
                        tr = pe.transpose(ps[:, 3, N_META * k:N_META * (k + 1)], tiles[-1][1][:, P * k:P * k + P],
                                          ident[0:N_META, 0:N_META])
                    tr.then_inc(*PE.done(("T", name, "meta")))

            def attention_transposes(tag, h, width, q_bank, k_bank, q_src, k_src):
                claim(q_bank, (ACT, ("qT", tag, h)))
                for t in range(NT):
                    tr = pe.transpose(ps[0:width, q_bank, P * t:P * t + P], q_src(t), ident[:, :])
                tr.then_inc(*PE.done(("qT", tag, h)))
                claim(k_bank, (DVE, ("kT", tag, h)))
                claim(k_bank + 1, (DVE, ("kT", tag, h)))
                pe.transpose(ps[0:width, k_bank, SEQ - N_META:SEQ], k_src(NT)[0:N_META, :], ident[0:N_META, 0:N_META])
                for t in range(NT):
                    tr = pe.transpose(ps[0:width, k_bank + 1, P * t:P * t + P], k_src(t), ident[:, :])
                tr.then_inc(*PE.done(("kT", tag, h)))

            def mla_scores(j):
                h, t = divmod(j, NT)
                n = P * (t + 1)
                if t == 0:
                    pe.wait_ge(*ACT.after("qT", "mla", h))
                    pe.wait_ge(*DVE.after("kT", "mla", h))
                claim(4, (ACT, ("exp", "mla", j)))
                claim(5, (ACT, ("exp", "mla", j)))
                q = qT[0:QKH, h % 2, P * t:P * t + P]
                pe.matmul(ps[:, 4, SEQ - N_META:SEQ], q, kT[0:QKH, h % 2, 0:N_META], start=True, stop=True)
                pe.matmul(ps[:, 5, 0:n], q, kT[0:QKH, h % 2, N_META:N_META + n], start=True, stop=False)
                pe.matmul(ps[:, 5, n - CHUNK:n], mask_q[:, :], mask_k[:, :], start=False,
                          stop=True).then_inc(*PE.done(("S", "mla", j)))

            def mla_turn(j):
                h, t = divmod(j, NT)
                pe.wait_ge(*ACT.after("exp", "mla", j))
                claim(7, (DVE, ("PTm", "mla", j)))
                pe.transpose(ps[0:N_META, 7, 0:P], prob[:, j % 3, 0:N_META], ident[:, :]).then_inc(*PE.done(("PTm", "mla", j)))
                claim(6, (ACT, ("PT", "mla", j)))
                for b in range(t + 1):
                    tr = pe.transpose(ps[:, 6, P * b:P * b + P], prob[:, j % 3, N_META + P * b:N_META + P * (b + 1)], ident[:, :])
                tr.then_inc(*PE.done(("PT", "mla", j)))

            def mla_values(j):
                h, t = divmod(j, NT)
                pe.wait_ge(*ACT.after("PT", "mla", j))
                claim(7, (DVE, ("y", "mla", j)))
                pe.matmul(ps[:, 7, P:P + VH], probT_m[:, j % 2, :], v_sb[0:N_META, NT, VH * h:VH * (h + 1)], start=True, stop=False)
                for b in range(t + 1):
                    mm = pe.matmul(ps[:, 7, P:P + VH], probT[:, j % 2, P * b:P * b + P], v_sb[:, b, VH * h:VH * (h + 1)],
                                   start=False, stop=(b == t))
                mm.then_inc(*PE.done(("O", "mla", j)))

            def mla_transposes(h):
                attention_transposes("mla", h, QKH, 6, 4, lambda t: q_sb[:, t, QKH * h:QKH * (h + 1)],
                                     lambda t: k_sb[:, t, QKH * h:QKH * (h + 1)])

            def ret_transposes(h):
                attention_transposes("ret", h, RET_D, 0, 1, lambda t: rqk[:, t, RET_D * h:RET_D * (h + 1)],
                                     lambda t: rqk[:, t, 256 + RET_D * h:256 + RET_D * (h + 1)])

            def ret_scores(h):
                pe.wait_ge(*ACT.after("qT", "ret", h))
                pe.wait_ge(*DVE.after("kT", "ret", h))
                claim(3, (DVE, ("sd", h, "meta")))
                pe.matmul(ps[0:N_META, 3, :], rkT[0:RET_D, h % 2, 0:N_META], rqT[0:RET_D, h % 2, :],
                          start=True, stop=True).then_inc(*PE.done(("rS", h, "meta")))
                for b in range(NT):
                    claim(b, (DVE, ("sd", h, b)))
                    pe.matmul(ps[:, b, P * b:SEQ], rkT[0:RET_D, h % 2, N_META + P * b:N_META + P * (b + 1)],
                              rqT[0:RET_D, h % 2, P * b:SEQ], start=True, stop=True).then_inc(*PE.done(("rS", h, b)))

            def ret_values(h):
                pe.wait_ge(*DVE.after("sd", h, "meta"))
                claim(0, (ACT, ("rO", h)))
                for t in range(NT):
                    dst = ps[:, 0, RET_D * t:RET_D * (t + 1)]
                    pe.matmul(dst, sd_m[:, P * t:P * t + P], rv[0:N_META, NT, RET_D * h:RET_D * (h + 1)], start=True, stop=False)
                    for b in range(t + 1):
                        pe.wait_ge(*DVE.after("sd", h, b))
                        mm = pe.matmul(dst, sd[:, b, P * t:P * t + P], rv[:, b, RET_D * h:RET_D * (h + 1)],
                                       start=False, stop=(b == t))
                mm.then_inc(*PE.done(("rO", h)))

            def gla_low():
                pe.wait_ge(*ACT.after("sm2"))
                claim(6, (ACT, ("low_t",)))
                for t in range(NT):
                    tr = pe.transpose(ps[0:16, 6, P * t:P * t + P], sm2[:, t, 0:16], ident[:, :])
                tr.then_inc(*PE.done(("low_t",)))

            def gla_decays(h):
                if h == 0:
                    pe.wait_ge(gla_in, 32)
                    pe.wait_ge(*ACT.after("low_t"))
                claim(7, (ACT, ("g_z", h)))
                pe.matmul(ps[:, 7, :], w_a2[:, P * h:P * h + P], low_t[:, :], start=True,
                          stop=True).then_inc(*PE.done(("g_z", h)))

            def gla_states(h):
                s = h % 2
                if h == 0:
                    for t in range(NT):
                        pe.wait_ge(*ACT.after("gv", 0, t))
                        pe.wait_ge(*ACT.after("gv", 1, t))
                claim(6, (ACT, ("g_keT", h)))
                pe.wait_ge(*DVE.after("g_ke", h))
                for t in range(NT):
                    tr = pe.transpose(ps[:, 6, P * t:P * t + P], g_ke[:, s, P * t:P * t + P], ident[:, :])
                tr.then_inc(*PE.done(("g_keT", h)))
                claim(7, (DVE, ("g_att", h)))
                for t in range(NT):
                    mm = pe.matmul(ps[:, 7, P * t:P * t + P], g_ki[:, s, P * t:P * t + P], g_qd[:, s, P * t:P * t + P],
                                   start=True, stop=True)
                mm.then_inc(*PE.done(("g_att", h)))
                pe.wait_ge(*ACT.after("g_keT", h))
                for pair in ((0, 2), (1, 3), (4, 6), (5,)):
                    bank = state_bank(pair[0])[0]
                    claim(bank, (DVE, ("g_state", h, pair[-1])))
                    for n in pair:
                        rows = slice(CHUNK * (n % 2), CHUNK * (n % 2) + CHUNK)
                        mm = pe.matmul(ps[:, bank, state_bank(n)[1]], g_keT[rows, s, P * (n // 2):P * (n // 2) + P],
                                       gv[rows, n // 2, GLA_DV * h:GLA_DV * (h + 1)], start=True, stop=True)
                    mm.then_inc(*PE.done(("g_upd", h, bank)))

            def gla_values(h):
                s = h % 2
                pe.wait_ge(*DVE.after("g_att", h))
                for t in range(NT):
                    bank = 4 + t % 2
                    claim(bank, (ACT, ("g_oss", h, t)))
                    v = gv[:, t, GLA_DV * h:GLA_DV * (h + 1)]
                    if t == 0:
                        pe.matmul(ps[0:CHUNK, bank, 0:GLA_DV], g_att[:, s, 0:CHUNK], v, start=True, stop=True)
                        pe.matmul(ps[CHUNK:P, bank, 0:GLA_DV], g_att[:, s, CHUNK:P], v, start=True, stop=False)
                    else:
                        pe.matmul(ps[:, bank, 0:GLA_DV], g_att[:, s, P * t:P * t + P], v, start=True, stop=False)
                    for half in range(2):
                        n = 2 * t + half
                        if n == 0:
                            continue
                        pe.wait_ge(*DVE.after("g_state", h, n - 1))
                        rows = slice(CHUNK * half, CHUNK * half + CHUNK)
                        mm = pe.matmul(ps[rows, bank, 0:GLA_DV], g_qd[:, s, CHUNK * n:CHUNK * (n + 1)], state[:, n, :],
                                       start=False, stop=True)
                    mm.then_inc(*PE.done(("g_o", h, t)))

            def mix(tag):
                for c in range(KC):
                    bank = 4 + c % 4
                    claim(bank, (DVE, ("mix_lo", tag, c)))
                    for t in range(NT):
                        pe.wait_ge(*MIX_NEEDS(tag, c, t))
                        src = go if tag == "gla" else merged
                        tr = pe.transpose(ps[:, bank, P * t:P * t + P], src[:, t, P * c:P * c + P], ident[:, :])
                    tr.then_inc(*PE.done(("mixT", tag, c)))

            def idx_key():
                claim(6, (ACT, ("ikT",)))
                for t in range(NT):
                    pe.wait_ge(*DVE.after("ik2", t))
                    tr = pe.transpose(ps[:, 6, P * t:P * t + P], ik2[:, t, :], ident[:, :])
                tr.then_inc(*PE.done(("ikT",)))

            def idx_scores(t):
                n = P * (t + 1)
                pe.wait_ge(*ACT.after("ikT"))
                for h in range(IDX_H):
                    bank = 4 + h % 4
                    pe.wait_ge(*ACT.after("iqT", h // 2))
                    claim(bank, (ACT, ("rel", t, h)))
                    rows = slice(IDX_D * (h % 2), IDX_D * (h % 2) + IDX_D)
                    pe.matmul(ps[:, bank, 0:n], iqT[rows, h // 2, P * t:P * t + P], ikT[rows, 0:n], start=True,
                              stop=True).then_inc(*PE.done(("rel", t, h)))

            def head_transposes(tag, c, src, last_needed):
                bank = 4 + c % 4
                claim(bank, (ACT, (tag, c)))
                for t in range(len(src)):
                    pe.wait_ge(*DVE.after(*last_needed[t]))
                    tr = pe.transpose(ps[:, bank, P * t:P * t + P], src[t], ident[:, :])
                tr.then_inc(*PE.done((tag, c)))

            def dsa_prepare(part):
                if part == "k":
                    for c in range(2):
                        head_transposes("dkT", c, [dk[:, t, P * c:P * c + P] for t in range(NT)],
                                        [("dkn", t) for t in range(NT)])
                else:
                    n = int(part[1])
                    for c in range(4 * n, 4 * n + 4):
                        head_transposes("dqT", c, [dq[:, t, P * c:P * c + P] for t in range(NT)],
                                        [("dqn", n, t) for t in range(NT)])

            def dsa_scores(j):
                h, t = divmod(j, NT)
                n = P * (t + 1)
                claim(4 + j % 2, (DVE, ("d_max", j)))
                pe.matmul(ps[:, 4 + j % 2, 0:n], dqT[:, h, P * t:P * t + P], dkT[:, h // DSA_G, 0:n], start=True,
                          stop=True).then_inc(*PE.done(("d_S", j)))

            def dsa_turn(j):
                bank = 6 if j % 2 else 2
                pe.wait_ge(*DVE.after("d_norm", j))
                claim(bank, (ACT, ("d_PT", j)))
                for b in range(j % NT + 1):
                    tr = pe.transpose(ps[:, bank, P * b:P * b + P], d_prob[:, j % 3, P * b:P * b + P], ident[:, :])
                tr.then_inc(*PE.done(("d_PT", j)))

            def dsa_values(j):
                h, t = divmod(j, NT)
                g = h // DSA_G
                bank = 7 if h % 2 else 3
                pe.wait_ge(*ACT.after("d_PT", j))
                if t == 0:
                    claim(bank, (DVE, ("mix_lo", "dsa", h)))
                for b in range(t + 1):
                    mm = pe.matmul(ps[:, bank, P * t:P * t + P], dv[:, b, P * g:P * g + P], d_probT[:, j % 2, P * b:P * b + P],
                                   start=(b == 0), stop=(b == t))
                mm.then_inc(*PE.done(("d_O", j)))

            def mem_prepare(part):
                if part == "k":
                    for c in range(KC):
                        head_transposes("mkT", c, [mk[:, t, P * c:P * c + P] for t in range(2)], [("mkn", t) for t in range(2)])
                else:
                    n = int(part[1])
                    for c in range(4 * n, 4 * n + 4):
                        head_transposes("mqT", c, [dq[:, t, P * c:P * c + P] for t in range(NT)],
                                        [("mqn", n, t) for t in range(NT)])

            def mem_scores(j):
                h, t = divmod(j, NT)
                claim(4 + j % 2, (ACT, ("m_exp", j)))
                for c in range(2):
                    mm = pe.matmul(ps[:, 4 + j % 2, 0:MEM], mqT[:, 2 * h + c, P * t:P * t + P], mkT[:, 2 * h + c, :],
                                   start=(c == 0), stop=(c == 1))
                mm.then_inc(*PE.done(("m_S", j)))

            def mem_turn(j):
                pe.wait_ge(*DVE.after("m_norm", j))
                claim(6, (ACT, ("m_PT", j)))
                for b in range(2):
                    tr = pe.transpose(ps[:, 6, P * b:P * b + P], m_prob[:, j % 3, P * b:P * b + P], ident[:, :])
                tr.then_inc(*PE.done(("m_PT", j)))

            def mem_values(j):
                h, t = divmod(j, NT)
                pe.wait_ge(*ACT.after("m_PT", j))
                for c in range(2):
                    bank = MEM_BANKS[2 * h + c]
                    if t == 0:
                        claim(bank, (DVE, ("mix_lo", "mem", 2 * h + c)))
                    for b in range(2):
                        mm = pe.matmul(ps[:, bank, P * t:P * t + P], mv[:, b, 2 * P * h + P * c:2 * P * h + P * (c + 1)],
                                       m_probT[:, j % 2, P * b:P * b + P], start=(b == 0), stop=(b == 1))
                mm.then_inc(*PE.done(("m_O", j)))

            def sort():
                pe.wait_ge(*DVE.after("hot"))
                pe.wait_ge(*POOL.after("all_ones"))
                pe.wait_ge(sort_in, 32)
                claim(6, (DVE, ("counts",)))
                pe.matmul(ps[:, 6, 0:16], before_t[:, :], rt[:, 3, :], start=True, stop=True, skip_group_check=True)
                pe.matmul(ps[:, 6, 16:32], all_ones[:, :], rt[:, 3, :], start=True, stop=True,
                          skip_group_check=True).then_inc(*PE.done(("counts",)))

            def combine_sorted():
                pe.wait_ge(*DVE.after("combine"))
                claim(6, (DVE, ("combine_s",)))
                for s in range(NT):
                    for t in range(NT):
                        mm = pe.matmul(ps[:, 6, N_EXP * s:N_EXP * (s + 1)], perm[:, t, P * s:P * s + P].bitcast(F32),
                                       combine[:, t, :], start=(t == 0), stop=(t == NT - 1), skip_group_check=True)
                mm.then_inc(*PE.done(("combine_s",)))

            def resort():
                for t in range(NT):
                    pe.wait_ge(*POOL.after("xs_lo", t))
                    pe.wait_ge(*DVE.after("perm", t))
                for k in range(KC):
                    bank = k % 4
                    claim(bank, (DVE, ("s_lo", k)))
                    for t in range(NT):
                        for i, x in enumerate((xs_hi, xs_lo)):
                            mm = pe.matmul(ps[:, bank, :], x[:, t, P * k:P * k + P], perm[:, t, :], start=(t + i == 0),
                                           stop=(t == NT - 1 and i == 1))
                    mm.then_inc(*PE.done(("resorted", k)))

            def flag(v):
                return active[NT * (v // NT // 4) + v % NT]

            def skip(done, steps):
                pe.matmul(ps[0:1, 7, 0:1], ones[:, 0:1], ones[:, 0:1], start=True, stop=True).then_inc(done[0], steps)

            def down(v):
                e, s = divmod(v, NT)
                g0 = expert_unit + E_UNITS * e + 4
                b0 = 5
                pe.wait_ge(*DVE.after("w_lo", g0 + 1))
                pe.wait_ge(*DVE.after("hid_lo", v))
                claim(b0, (DVE, ("y", v)))
                claim(b0 + 1, (DVE, ("y", v)))
                for n in range(2):
                    wh, wl = split_slot(g0 + n)
                    for c in range(2):
                        mm = product(ps[:, b0 + n, :], hid_hi[:, s, P * c:P * c + P], hid_lo[:, s, P * c:P * c + P],
                                     wh[:, 512 * c:512 * c + 512], wl[:, 512 * c:512 * c + 512], c == 0, c == 1)
                done = PE.done(("down", v), *([("unit", g0 + i) for i in range(2)] if s == NT - 1 else []))
                mm.then_inc(*done)
                return done

            def visit(v):
                e, s = divmod(v, NT)
                g0 = expert_unit + E_UNITS * e
                bank = s
                with pe.If_ne(flag(v), 0):
                    pe.wait_ge(*POOL.after("w_lo", g0 + 3))
                    claim(bank, (ACT, ("e_silu", v)), (DVE, ("hid", v)))
                    for k in range(KC):
                        wh, wl = [x[:, 512 * (k % 2):512 * (k % 2) + 512] for x in split_slot(g0 + k // 2)]
                        rows = slice(P * s, P * s + P)
                        mm = product(ps[:, bank, :], mix_hi[:, k, rows], mix_lo[:, k, rows], wh, wl, k == 0, k == KC - 1)
                    mm.then_inc(*PE.done(("up", v), *([("unit", g0 + i) for i in range(4)] if s == NT - 1 else [])))
                    if e % 4:
                        down(v - NT)
                    pe.wait_ge(*DVE.after("hid", v))
                    claim(4, (ACT, ("hid_hi", v)), (DVE, ("hid_lo", v)))
                    for c in range(2):
                        tr = pe.transpose(ps[:, 4, P * c:P * c + P], hid[:, v % 2, P * c:P * c + P], ident[:, :])
                    done = PE.done(("turn", v))
                    tr.then_inc(*done)
                with pe.Else():
                    skip(done, 3 if e % 4 else 2)

            def finish(v):
                with pe.If_ne(flag(v), 0):
                    done = down(v)
                with pe.Else():
                    skip(done, 1)

            def unsort():
                for s in range(NT):
                    bank = s % 2
                    claim(bank, (ACT, ("permT", s)))
                    for t in range(NT):
                        tr = pe.transpose(ps[:, bank, P * t:P * t + P], perm[:, t, P * s:P * s + P].bitcast(F32), ident[:, :])
                    tr.then_inc(*PE.done(("permT", s)))
                for t in range(NT):
                    for n in range(2):
                        bank = (2 + 2 * t + n) % 8
                        claim(bank, (DVE, ("x", LAST, t)))
                        for s in range(NT):
                            pe.wait_ge(*ACT.after("permT", s))
                            pe.wait_ge(*DVE.after("y_lo", s))
                            p = permT[:, s, P * t:P * t + P]
                            pe.matmul(ps[:, bank, :], p, y_hi[:, s, 512 * n:512 * n + 512], start=(s == 0), stop=False)
                            mm = pe.matmul(ps[:, bank, :], p, y_lo[:, s, 512 * n:512 * n + 512], start=False, stop=(s == NT - 1))
                        mm.then_inc(*PE.done(("unsorted", t, n)))

            def latent_sums():
                pe.wait_ge(zeroed, 2)
                pe.wait_ge(*ACT.after("latent_sq", "meta"))
                claim(6, (DVE, ("lat_v",)))
                for t in range(NT):
                    for c in range(2):
                        pe.matmul(ps[:, 6, t:t + 1], cq_sq[:, c, P * t:P * t + P], ones[:, 0:1], start=(c == 0), stop=(c == 1))
                for t in range(NT):
                    pe.matmul(ps[:, 6, NT + t:NT + t + 1], ckv_sq[:, N_META + P * t:N_META + P * (t + 1)], ones[:, 0:1],
                              start=True, stop=True)
                pe.matmul(ps[0:N_META, 6, 8:9], ckv_sq[:, 0:N_META], ones[:, 0:1], start=True,
                          stop=True).then_inc(*PE.done(("lat_ss",)))

            def mix_one():
                for c in range(6):
                    bank = 6 + c % 2
                    claim(bank, (DVE, ("mix_lo", 2 + c)))
                    for t in range(NT):
                        if c < 4:
                            src = y_mla[:, t, P * c:P * c + P]
                        else:
                            pe.wait_ge(*DVE.after("y_ret", t))
                            src = y_ret[:, t, P * (c - 4):P * (c - 3)]
                        tr = pe.transpose(ps[:, bank, P * t:P * t + P], src, ident[:, :])
                    tr.then_inc(*PE.done(("mixT", 2 + c)))

            active = []
            pe.wait_ge(const_in, 80)
            for step, *a in order:
                if step == "constants":
                    for part in range(2):
                        pe.wait_ge(gains_in[part], 16 * n_gain_dmas)
                    claim(7, (DVE, ("gains",)))
                    pe.transpose(ps[:, 7, 0:64], g_rows[:, :], ident[0:64, 0:64]).then_inc(*PE.done(("gains",)))
                elif step == "norm":
                    norm(*a)
                elif step == "item":
                    item(*a)
                elif step == "latent_sums":
                    latent_sums(*a)
                elif step == "mla_transposes":
                    mla_transposes(*a)
                elif step == "mla_scores":
                    mla_scores(*a)
                elif step == "mla_turn":
                    mla_turn(*a)
                elif step == "mla_values":
                    mla_values(*a)
                elif step == "ret_transposes":
                    ret_transposes(*a)
                elif step == "ret_scores":
                    ret_scores(*a)
                elif step == "ret_values":
                    ret_values(*a)
                elif step == "mix_one":
                    mix_one(*a)
                elif step == "gla_low":
                    gla_low(*a)
                elif step == "gla_decays":
                    gla_decays(*a)
                elif step == "gla_states":
                    gla_states(*a)
                elif step == "gla_values":
                    gla_values(*a)
                elif step == "mix":
                    mix(*a)
                elif step == "idx_key":
                    idx_key(*a)
                elif step == "idx_scores":
                    idx_scores(*a)
                elif step == "dsa_prepare":
                    dsa_prepare(*a)
                elif step == "dsa_scores":
                    dsa_scores(*a)
                elif step == "dsa_turn":
                    dsa_turn(*a)
                elif step == "dsa_values":
                    dsa_values(*a)
                elif step == "mem_prepare":
                    mem_prepare(*a)
                elif step == "mem_scores":
                    mem_scores(*a)
                elif step == "mem_turn":
                    mem_turn(*a)
                elif step == "mem_values":
                    mem_values(*a)
                elif step == "sort":
                    sort()
                elif step == "combine_s":
                    combine_sorted()
                elif step == "resort":
                    active = load_flags(pe, "pe")
                    resort()
                    pe.wait_ge(*DVE.after("s_lo", KC - 1))
                elif step == "visit":
                    visit(*a)
                elif step == "finish":
                    finish(*a)
                elif step == "unsort":
                    unsort()
                elif step == "barrier":
                    barrier(pe, a[0])
                    PE.section = a[0]

        @block.scalar
        def _(act):
            fill = [0]

            def split_high(upto):
                for g in range(fill[0], upto):
                    chunks, n, _ = units[g]
                    a = len(chunks) * n
                    act.wait_ge(w_landed[g % RAW_SLOTS], landed[g])
                    if slot_free(g):
                        act.wait_ge(*PE.after(*slot_free(g)))
                    nc.scalar.activation(split_slot(g)[0][:, 0:a], raw[:, g % RAW_SLOTS, 0:a], ACTF.Copy).then_inc(*ACT.done(("w_hi", g)))
                fill[0] = max(fill[0], upto)

            def rsqrt_start(key, v):
                act.wait_ge(*DVE.after("v", *key))
                nc.scalar.activation(v[1], v[0], ACTF.Ln).then_inc(*ACT.done(("ln", *key)))
                act.wait_ge(*ACT.after("ln", *key))
                nc.scalar.activation(v[1], v[1], ACTF.Exp, scale=-0.5).then_inc(*ACT.done(("y0", *key)))

            def norm_scale(name):
                tiles = NORM_TILES[name]
                if name == "h":
                    act.wait_ge(x_in, 80)
                if name == "mem":
                    act.wait_ge(mem_landed, 32)
                act.wait_ge(*DVE.after("ss0", name))
                for i, (src, scaled, rows) in enumerate(tiles):
                    for key in NORM_NEEDS(name, i):
                        act.wait_ge(*key[0].after(*key[1]))
                    nc.scalar.activation(scaled, src, ACTF.Square,
                                         accum_out=ss[0:rows, 0, i:i + 1]).then_inc(*ACT.done(("ss", name, i)))
                n = len(tiles)
                rsqrt_start((name,), (ss[:, 1, 0:n], ss[:, 2, 0:n]))

            def norm(name):
                tiles = NORM_TILES[name]
                if ("norm_scale", name) not in order:
                    norm_scale(name)
                n = sum(t[2] == P for t in tiles) * P
                hi, off = norm_dest(name)
                for k in range(KC):
                    act.wait_ge(*PE.after("T", name, k))
                    nc.scalar.activation(hi[:, k, off:off + n], ps[:, 4 + k % 4, 0:n], ACTF.Copy,
                                         scale=col(NORMS[name], k)).then_inc(*ACT.done(("hi", name, k)))
                if name == "h":
                    act.wait_ge(*DVE.after("meta_t", name))
                    nc.scalar.activation(act_hi[:, :, 0:N_META], meta_t[:, :, :], ACTF.Copy).then_inc(*ACT.done(("meta_hi", name)))

            def copy(key, dst, src, func=ACTF.Copy, scale=1.0):
                return nc.scalar.activation(dst, src, func, scale=scale)

            def item(name):
                if name in ("k_rope", "small2", "router"):
                    n = items[name][0][1]
                    act.wait_ge(*PE.after("small", name))
                    if name == "k_rope":
                        nc.scalar.activation(small_t[0:n, SEQ:L], ps[0:n, 6, 0:N_META], ACTF.Copy
                                             ).then_inc(*ACT.done(("small_meta", name)))
                    nc.scalar.activation(small_t[0:n, 0:SEQ], ps[0:n, 5, :], ACTF.Copy).then_inc(*ACT.done(("small", name)))
                if name == "conv_a":
                    for b in range(2):
                        act.wait_ge(*PE.after("acc", name, b))
                        nc.scalar.activation(cx[:, b, N_META:], ps[:, b, :], ACTF.Copy).then_inc(*ACT.done(("cx", b)))
                    for b in range(2):
                        act.wait_ge(*PE.after("acc", name, 2 + b))
                        nc.scalar.activation(cb[:, b, :], ps[:, 2 + b, :], ACTF.Copy).then_inc(*ACT.done(("cb", b)))
                    act.wait_ge(*PE.after("acc", name, "meta"))
                    nc.scalar.activation(cx[:, :, 0:N_META], ps[:, 4, 0:2 * N_META].rearrange("p (b n) -> p b n", b=2),
                                         ACTF.Copy).then_inc(*ACT.done(("cx", "meta")))
                elif name == "conv_b":
                    for b in range(2):
                        act.wait_ge(*PE.after("acc", name, 2 + b))
                        nc.scalar.activation(cz[:, b, :], ps[:, 2 + b, :], ACTF.Silu).then_inc(*ACT.done(("cz", b)))
                elif name == "latent":
                    for b in range(2):
                        act.wait_ge(*PE.after("acc", name, b))
                        nc.scalar.activation(cq_sq[:, b, :], ps[:, b, :], ACTF.Square).then_inc(*ACT.done(("latent_sq", b)))
                        nc.scalar.activation(cq_hi[:, b, :], ps[:, b, :], ACTF.Copy,
                                             scale=col("q_a_norm", b)).then_inc(*ACT.done(("cq_hi", b)))
                    act.wait_ge(*PE.after("acc", name, 2))
                    nc.scalar.activation(ckv_sq[:, N_META:], ps[:, 2, :], ACTF.Square).then_inc(*ACT.done(("latent_sq", 2)))
                    nc.scalar.activation(ckv_hi[:, N_META:], ps[:, 2, :], ACTF.Copy,
                                         scale=col("kv_a_norm")).then_inc(*ACT.done(("ckv_hi",)))
                    act.wait_ge(*PE.after("acc", name, "meta"))
                    nc.scalar.activation(ckv_hi[:, 0:N_META], ps[:, 4, 0:N_META], ACTF.Copy,
                                         scale=col("kv_a_norm")).then_inc(*ACT.done(("ckv_hi", "meta")))
                    nc.scalar.activation(ckv_sq[:, 0:N_META], ps[:, 4, 0:N_META],
                                         ACTF.Square).then_inc(*ACT.done(("latent_sq", "meta")))
                elif name == "k_rope":
                    act.wait_ge(*PE.after("acc", name, NT))
                    nc.scalar.activation(kr[:, :, :], ps[:, 5, 0:(NT + 1) * QKR].rearrange("p (t n) -> p t n", n=QKR),
                                         ACTF.Copy).then_inc(*ACT.done(("kr",)))
                elif name.startswith("w_uq"):
                    n = int(name[-1])
                    act.wait_ge(*DVE.after("r", "lat"))
                    act.wait_ge(*DVE.after("conv_lo", 1))
                    for t in range(NT):
                        act.wait_ge(*PE.after("acc", name, t))
                        nc.scalar.activation(q_sb[:, t, 384 * n:384 * n + 384], ps[:, t, 0:384], ACTF.Copy,
                                             scale=ss[:, 2, t:t + 1]).then_inc(*ACT.done(("q_raw", n, t)))
                elif name.startswith("w_ukv"):
                    n = int(name[-1])
                    for t in range(NT + 1):
                        rows = P if t < NT else N_META
                        act.wait_ge(*PE.after("acc", name, t))
                        src = ps[0:rows, t, :].rearrange("p (h n) -> p h n", h=4)
                        dst = k_sb[0:rows, t, 384 * n:384 * n + 384].rearrange("p (h n) -> p h n", h=4)
                        nc.scalar.activation(dst[:, :, 0:QKN], src[:, :, 0:QKN], ACTF.Copy,
                                             scale=ss[0:rows, 2, NT + t:NT + t + 1]).then_inc(*ACT.done(("k_raw", n, t)))
                elif name == "mla_z":
                    for t in range(NT):
                        act.wait_ge(*PE.after("acc", name, t))
                        nc.scalar.activation(z_mla[:, t, :], ps[:, t, :], ACTF.Silu).then_inc(*ACT.done(("z_mla", t)))
                elif name == "ret_vz":
                    for t in range(NT + 1):
                        rows = P if t < NT else N_META
                        act.wait_ge(*PE.after("acc", name, t))
                        nc.scalar.activation(rv[0:rows, t, :], ps[0:rows, t, 0:256], ACTF.Copy).then_inc(*ACT.done(("rv", t)))
                        if t < NT:
                            nc.scalar.activation(z_ret[:, t, :], ps[:, t, 256:512], ACTF.Silu).then_inc(*ACT.done(("z_ret", t)))

                elif name == "small2":
                    act.wait_ge(*PE.after("acc", name, NT - 1))
                    nc.scalar.activation(sm2[:, :, :], ps[:, 5, 0:NT * 88].rearrange("p (t n) -> p t n", n=88),
                                         ACTF.Copy).then_inc(*ACT.done(("sm2",)))
                elif name in ("gla_q", "gla_k"):
                    dst = gq if name == "gla_q" else gk
                    for b in range(GLA_H):
                        act.wait_ge(*PE.after("acc", name, b))
                        nc.scalar.activation(dst[:, b, :], ps[:, b, :], ACTF.Copy).then_inc(*ACT.done((name, b)))
                elif name.startswith(("gla_v", "gla_g")):
                    n = int(name[-1])
                    for t in range(NT):
                        act.wait_ge(*PE.after("acc", name, t))
                        if name.startswith("gla_v"):
                            nc.scalar.activation(gv[:, t, 512 * n:512 * n + 512], ps[:, t, :],
                                                 ACTF.Copy).then_inc(*ACT.done(("gv", n, t)))
                        else:
                            if n or t >= 2:
                                act.wait_ge(*DVE.after("go", *divmod(NT * n + t - 2, NT), 1))
                            nc.scalar.activation(g_silu[:, t % 2, :], ps[:, t, :], ACTF.Silu).then_inc(*ACT.done(("g_silu", n, t)))
                elif name.startswith("gate"):
                    for t in range(NT):
                        act.wait_ge(*DVE.after("gate_sum", int(name[4]), int(name[5]), t))
                        nc.scalar.activation(gate[:, t, :], gate[:, t, :], ACTF.Sigmoid).then_inc(*ACT.done(("gate", int(name[4]), int(name[5]), t)))
                elif name == "idx_q":
                    for b in range(4):
                        act.wait_ge(*PE.after("acc", name, b))
                        nc.scalar.activation(iqT[:, b, :], ps[:, b, :], ACTF.Copy).then_inc(*ACT.done(("iqT", b)))
                elif name.startswith("dsa_q") or name.startswith("mem_q"):
                    n = int(name[-1])
                    tag = name[0:1]
                    for t in range(NT):
                        act.wait_ge(*PE.after("acc", name, t))
                        i = NT * n + t
                        if i >= 2:
                            act.wait_ge(*DVE.after(tag + "q_ss", i - 2))
                        else:
                            act.wait_ge(*DVE.after(tag + "k_ss", 2 + i))
                        nc.scalar.activation(d_sq[:, i % 2, :], ps[:, t, :], ACTF.Square).then_inc(*ACT.done((tag + "q_sq", i)))
                        nc.scalar.activation(dq[:, t, 512 * n:512 * n + 512], ps[:, t, :],
                                             ACTF.Copy).then_inc(*ACT.done(("dq" if tag == "d" else "mq", n, t)))
                elif name == "dsa_kv":
                    for t in range(NT):
                        act.wait_ge(*PE.after("acc", name, t))
                        if t >= 2:
                            act.wait_ge(*DVE.after("dk_ss", t - 2))
                        nc.scalar.activation(d_sq[:, t % 2, 0:256], ps[:, t, 0:256], ACTF.Square).then_inc(*ACT.done(("dk_sq", t)))
                        nc.scalar.activation(dk[:, t, :], ps[:, t, 0:256], ACTF.Copy).then_inc(*ACT.done(("dk", t)))
                        nc.scalar.activation(dv[:, t, :], ps[:, t, 256:512], ACTF.Copy).then_inc(*ACT.done(("dv", t)))
                elif name.startswith("mem_kv"):
                    n = int(name[-1])
                    for t in range(2):
                        act.wait_ge(*PE.after("acc", name, t))
                        if n < 2:
                            if n:
                                act.wait_ge(*DVE.after("mk_ss", t))
                            nc.scalar.activation(d_sq[:, t, :], ps[:, t, :], ACTF.Square).then_inc(*ACT.done(("mk_sq", 2 * n + t)))
                        if (n, t) == (0, 0):
                            act.wait_ge(*DVE.after("merged", 1, 1, NT - 1))
                        dst = (mk if n < 2 else mv)[:, t, 512 * (n % 2):512 * (n % 2) + 512]
                        nc.scalar.activation(dst, ps[:, t, :], ACTF.Copy).then_inc(*ACT.done(("mkv", n, t)))

            def resort():
                for k in range(KC):
                    act.wait_ge(*PE.after("resorted", k))
                    nc.scalar.activation(mix_hi[:, k, :], ps[:, k % 4, :], ACTF.Copy,
                                         scale=col("g_ffn_2", k)).then_inc(*ACT.done(("s_hi", k)))

            def visit(v):
                act.wait_ge(*PE.after("up", v))
                if v >= 2:
                    act.wait_ge(*ACT.after("e_silu", v - 2))
                    act.wait_ge(*DVE.after("hid", v - 2))
                nc.scalar.activation(e_silu[:, v % 2, :], ps[:, v % NT, 0:D_EXP], ACTF.Silu).then_inc(*ACT.done(("e_silu", v)))
                act.wait_ge(*PE.after("turn", v))
                if v:
                    act.wait_ge(*DVE.after("hid_lo", v - 1))
                if v >= NT:
                    act.wait_ge(*ACT.after("hid_hi", v - NT))
                    act.wait_ge(*PE.after("down", v - NT))
                nc.scalar.activation(hid_hi[:, v % NT, :], ps[:, 4, 0:D_EXP], ACTF.Copy).then_inc(*ACT.done(("hid_hi", v)))

            def unsort():
                for s in range(NT):
                    act.wait_ge(*PE.after("permT", s))
                    nc.scalar.activation(permT[:, s, :], ps[:, s % 2, :], ACTF.Copy).then_inc(*ACT.done(("permT", s)))
                for s in range(NT):
                    act.wait_ge(*DVE.after("y", NT * (N_EXP - 1) + s))
                    nc.scalar.activation(y_hi[:, s, :], y_exp[:, s, :], ACTF.Copy).then_inc(*ACT.done(("y_hi", s)))

            def gla_low():
                act.wait_ge(*PE.after("low_t"))
                nc.scalar.activation(low_t[:, :], ps[0:16, 6, :], ACTF.Copy).then_inc(*ACT.done(("low_t",)))

            def gla_decays(h):
                s = h % 2
                act.wait_ge(*PE.after("g_z", h))
                if h:
                    act.wait_ge(*DVE.after("g_la", h - 1))
                nc.scalar.activation(gz[:, :], ps[:, 7, :], ACTF.Identity, bias=col("b_gla_a2_2", h)).then_inc(*ACT.done(("g_z", h)))
                act.wait_ge(*ACT.after("g_z", h))
                if h:
                    act.wait_ge(*ACT.after("g_dec", h - 1))
                nc.scalar.activation(gab[:, :], gz[:, :], ACTF.Abs).then_inc(*ACT.done(("g_ab", h)))
                act.wait_ge(*ACT.after("g_ab", h))
                nc.scalar.activation(gex[:, :], gab[:, :], ACTF.Exp, scale=-1.0).then_inc(*ACT.done(("g_ex", h)))
                act.wait_ge(*ACT.after("g_ex", h))
                nc.scalar.activation(gex[:, :], gex[:, :], ACTF.Ln, bias=1.0).then_inc(*ACT.done(("g_ln", h)))
                act.wait_ge(*DVE.after("g_lc", h))
                if h >= 2:
                    act.wait_ge(*PE.after("g_o", h - 2, NT - 1))
                k = 1.0 / 16
                nc.scalar.activation(g_ke[:, s, :], glc[:, :], ACTF.Exp, scale=k).then_inc(*ACT.done(("g_e3", h)))
                nc.scalar.activation(g_qd[:, s, :], gab[:, :], ACTF.Exp, scale=k).then_inc(*ACT.done(("g_e1", h)))
                nc.scalar.activation(g_ki[:, s, :], gab[:, :], ACTF.Exp, scale=-k).then_inc(*ACT.done(("g_e2", h)))
                nc.scalar.activation(g_dec[:, s, :], gab[:, CHUNK - 1::CHUNK], ACTF.Exp, scale=k).then_inc(*ACT.done(("g_dec", h)))

            def gla_states(h):
                act.wait_ge(*PE.after("g_keT", h))
                nc.scalar.activation(g_keT[:, h % 2, :], ps[:, 6, :], ACTF.Copy).then_inc(*ACT.done(("g_keT", h)))

            def gla_values(h):
                for t in range(NT):
                    act.wait_ge(*PE.after("g_o", h, t))
                    src = ps[:, 4 + t % 2, 0:GLA_DV]
                    nc.scalar.activation(go[:, t, GLA_DV * h:GLA_DV * (h + 1)], src, ACTF.Copy).then_inc(*ACT.done(("g_oc", h, t)))
                    if h or t:
                        act.wait_ge(*ACT.after("g_oss", *divmod(NT * h + t - 1, NT)))
                    at = gla_stat(h, t)
                    nc.scalar.activation(gsq[:, :], src, ACTF.Square,
                                         accum_out=ss[:, 5, at:at + 1]).then_inc(*ACT.done(("g_oss", h, t)))

            def mix(tag):
                for c in range(KC):
                    act.wait_ge(*PE.after("mixT", tag, c))
                    nc.scalar.activation(mix_hi[:, c, :], ps[:, 4 + c % 4, :], ACTF.Copy,
                                         scale=col("gla_norm_2", c % 2) if tag == "gla" else 1.0
                                         ).then_inc(*ACT.done(("mix_hi", tag, c)))

            def idx_key():
                act.wait_ge(*DVE.after("ss0", "idx"))
                for t in range(NT):
                    if t:
                        act.wait_ge(*ACT.after("ik_ss", t - 1))
                    nc.scalar.activation(d_sq[:, 0, 0:IDX_D], sm2[:, t, 16:80], ACTF.Square,
                                         accum_out=ss[:, 0, t:t + 1]).then_inc(*ACT.done(("ik_ss", t)))
                rsqrt_start(("ik",), (ss[:, 1, 0:4], ss[:, 2, 0:4]))
                act.wait_ge(*PE.after("ikT"))
                nc.scalar.activation(ikT[:, :], ps[:, 6, :], ACTF.Copy, scale=col("idx_k_norm_2")).then_inc(*ACT.done(("ikT",)))

            def idx_scores(t):
                n = P * (t + 1)
                for h in range(IDX_H):
                    act.wait_ge(*PE.after("rel", t, h))
                    i = IDX_H * (t - 1) + h
                    if i >= 2:
                        act.wait_ge(*DVE.after("score", *idx_of(i - 2)))
                    nc.scalar.activation(rel[:, h % 2, 0:n], ps[:, 4 + h % 4, 0:n], ACTF.Relu).then_inc(*ACT.done(("rel", t, h)))

            def head_transposed(tag, c, dst, n, gain):
                act.wait_ge(*PE.after(tag, c))
                nc.scalar.activation(dst, ps[:, 4 + c % 4, 0:n], ACTF.Copy, scale=gain).then_inc(*ACT.done((tag, c)))

            def dsa_scale(part):
                a, b = HEAD_STATS["dsa", part]
                rsqrt_start(("dsa", part), (ss[:, 3, a:b], ss[:, 4, a:b]))

            def dsa_prepare(part):
                if part == "k":
                    for c in range(2):
                        head_transposed("dkT", c, dkT[:, c, :], SEQ, col("dsa_k_norm_2"))
                else:
                    n = int(part[1])
                    for c in range(4 * n, 4 * n + 4):
                        head_transposed("dqT", c, dqT[:, c, :], SEQ, col("dsa_q_norm_2"))

            def mix_high(tag, c, bank):
                nc.scalar.activation(mix_hi[:, c, :], ps[:, bank, :], ACTF.Copy).then_inc(*ACT.done(("mix_hi", tag, c)))

            def dsa_scores(j):
                n = P * (j % NT + 1)
                act.wait_ge(*DVE.after("d_nmax", j))
                nc.scalar.activation(d_prob[:, j % 3, 0:n], d_prob[:, j % 3, 0:n], ACTF.Exp, bias=sm[:, 1, j:j + 1],
                                     scale=float(P) ** -0.5, accum_out=sm[:, 2, j:j + 1]).then_inc(*ACT.done(("d_exp", j)))

            def dsa_turn(j):
                n = P * (j % NT + 1)
                act.wait_ge(*PE.after("d_PT", j))
                if j >= 2:
                    act.wait_ge(*PE.after("d_O", j - 2))
                nc.scalar.activation(d_probT[:, j % 2, 0:n], ps[:, 6 if j % 2 else 2, 0:n], ACTF.Copy).then_inc(*ACT.done(("d_PT", j)))

            def dsa_values(j):
                h, t = divmod(j, NT)
                if t == NT - 1:
                    act.wait_ge(*PE.after("d_O", j))
                    mix_high("dsa", h, 7 if h % 2 else 3)

            def mem_scale(part):
                a, b = HEAD_STATS["mem", part]
                rsqrt_start(("mem", part), (ss[:, 3, a:b], ss[:, 4, a:b]))

            def mem_prepare(part):
                if part == "k":
                    for c in range(KC):
                        head_transposed("mkT", c, mkT[:, c, :], MEM, col("mem_k_norm_2", c % 2))
                else:
                    n = int(part[1])
                    for c in range(4 * n, 4 * n + 4):
                        head_transposed("mqT", c, mqT[:, c, :], SEQ, col("mem_q_norm_2", c % 2))

            def mem_scores(j):
                act.wait_ge(*DVE.after("m_nmax", j))
                if j >= 3:
                    act.wait_ge(*PE.after("m_PT", j - 3))
                nc.scalar.activation(m_prob[:, j % 3, :], ps[:, 4 + j % 2, 0:MEM], ACTF.Exp, bias=sm[:, 1, j:j + 1],
                                     scale=float(MEM) ** -0.5, accum_out=sm[:, 2, j:j + 1]).then_inc(*ACT.done(("m_exp", j)))

            def mem_turn(j):
                act.wait_ge(*PE.after("m_PT", j))
                if j >= 2:
                    act.wait_ge(*PE.after("m_O", j - 2))
                nc.scalar.activation(m_probT[:, j % 2, :], ps[:, 6, 0:MEM], ACTF.Copy).then_inc(*ACT.done(("m_PT", j)))

            def mem_values(j):
                h, t = divmod(j, NT)
                if t == NT - 1:
                    act.wait_ge(*PE.after("m_O", j))
                    for c in range(2):
                        mix_high("mem", 2 * h + c, MEM_BANKS[2 * h + c])

            def route(part):
                if part == 0:
                    return
                act.wait_ge(*DVE.after("r_g"))
                nc.scalar.activation(rt[:, 2, :], rt[:, 2, :], ACTF.Exp).then_inc(*ACT.done(("r_eg",)))
                act.wait_ge(*DVE.after("r_d"))
                nc.scalar.activation(rt[:, 9, 0:4], rt[:, 9, 0:4], ACTF.Exp).then_inc(*ACT.done(("r_ed",)))

            def loads(section):
                if section == "mla":
                    load_decay(0)
                elif section == "gla":
                    act.dma_start(w_a2[:, :], w["w_gla_a2_2"][0]).then_inc(gla_in, 16)
                    act.dma_start(scan_mask[:, :], w["c_scan"]).then_inc(gla_in, 16)
                elif section == "mem":
                    for t in range(2):
                        act.dma_start(mem_in[:, t, :], w["mem_2"][0, P * t:P * t + P, :]).then_inc(mem_landed, 16)
                elif section == "experts":
                    act.dma_start(r_bias[:, 0:4], w["b_r1_2"][0].partition_broadcast(P)).then_inc(route_in, 16)
                    act.dma_start(r_bias[:, 4:20], w["b_r2_2"][0].partition_broadcast(P)).then_inc(route_in, 16)
                    act.dma_start(iota[:, :], w["c_iota"].partition_broadcast(P)).then_inc(sort_in, 16)
                    act.dma_start(before_t[:, :], w["c_before"]).then_inc(sort_in, 16)

            def mla_sums():
                for i, (kind, t) in enumerate(HEAD_TILES):
                    rows = P if t < NT else N_META
                    x = q_sb if kind == "q" else k_sb
                    act.wait_ge(*(ACT.after("q_raw", 1, t) if kind == "q" else DVE.after("kr_in", t)))
                    if i >= 2:
                        act.wait_ge(*DVE.after("hss", *HEAD_TILES[i - 2]))
                    nc.scalar.activation(sq[0:rows, i % 2, :], x[0:rows, t, :], ACTF.Square).then_inc(*ACT.done(("hsq", kind, t)))
                rsqrt_start(("head",), (ss[:, 3, 0:72], ss[:, 4, 0:72]))

            def q_transposed(tag, h, width, dst, bank):
                act.wait_ge(*PE.after("qT", tag, h))
                if h >= 2:
                    act.wait_ge(*PE.after(*last_scores(tag, h - 2)))
                nc.scalar.activation(dst[0:width, h % 2, :], ps[0:width, bank, :], ACTF.Copy).then_inc(*ACT.done(("qT", tag, h)))

            def mla_scores(j):
                n = P * (j % NT + 1)
                act.wait_ge(*DVE.after("nmax", "mla", j))
                if j >= 3:
                    act.wait_ge(*PE.after("PT", "mla", j - 3))
                nc.scalar.activation(prob[:, j % 3, 0:N_META + n], psf[:, 5 * SEQ - N_META:5 * SEQ + n], ACTF.Exp,
                                     bias=sm[:, 1, j:j + 1], scale=float(QKH) ** -0.5,
                                     accum_out=sm[:, 2, j:j + 1]).then_inc(*ACT.done(("exp", "mla", j)))

            def mla_turn(j):
                n = P * (j % NT + 1)
                act.wait_ge(*PE.after("PT", "mla", j))
                if j >= 2:
                    act.wait_ge(*PE.after("O", "mla", j - 2))
                nc.scalar.activation(probT[:, j % 2, 0:n], ps[:, 6, 0:n], ACTF.Copy).then_inc(*ACT.done(("PT", "mla", j)))

            def load_decay(h):
                act.dma_start(decay[:, :], w["c_decay"][h]).then_inc(decay_in, 16)
                act.dma_start(decay_m[:, :], w["c_decay_m"][h]).then_inc(decay_in, 16)

            def ret_values(h):
                if h + 1 < RET_H:
                    act.wait_ge(*DVE.after("sd", h, NT - 1))
                    load_decay(h + 1)
                act.wait_ge(*PE.after("rO", h))
                nc.scalar.activation(y_ret[:, :, RET_D * h:RET_D * (h + 1)],
                                     ps[:, 0, 0:NT * RET_D].rearrange("p (t n) -> p t n", t=NT),
                                     ACTF.Copy).then_inc(*ACT.done(("rO", h)))

            def ret_norm():
                act.wait_ge(*ACT.after("rO", RET_H - 1))
                act.wait_ge(*PE.after("rO", RET_H - 1))
                nc.scalar.activation(ysq[:, :, :], y_ret[:, :, :], ACTF.Square).then_inc(*ACT.done(("ysq",)))
                rsqrt_start(("ret",), (ss[:, 3, 0:16], ss[:, 4, 0:16]))

            def mix_one():
                for c in range(6):
                    act.wait_ge(*PE.after("mixT", 2 + c))
                    nc.scalar.activation(mix_hi[:, 2 + c, :], ps[:, 6 + c % 2, :], ACTF.Copy,
                                         scale=1.0 if c < 4 else col("ret_norm")).then_inc(*ACT.done(("mix_hi", 2 + c)))

            steps = {"mla_sums": mla_sums, "mla_scores": mla_scores, "mla_turn": mla_turn, "ret_values": ret_values,
                     "ret_norm": ret_norm, "mix_one": mix_one, "gla_low": gla_low, "gla_decays": gla_decays,
                     "gla_states": gla_states, "gla_values": gla_values, "mix": mix, "idx_key": idx_key,
                     "idx_scores": idx_scores, "dsa_prepare": dsa_prepare, "dsa_scale": dsa_scale, "dsa_scores": dsa_scores,
                     "dsa_turn": dsa_turn, "dsa_values": dsa_values, "mem_prepare": mem_prepare, "mem_scale": mem_scale,
                     "mem_scores": mem_scores, "mem_turn": mem_turn, "mem_values": mem_values, "route": route,
                     "visit": visit, "unsort": unsort}
            act.wait_ge(zeroed, 2)
            load_gains(act, 1)
            for step, *a in order:
                if step == "item" and a[0].startswith("gate"):
                    b, n = int(a[0][4]), int(a[0][5])
                    if b:
                        act.wait_ge(*DVE.after("gate_sum", b - 1, n, NT - 1))
                    else:
                        act.wait_ge(*DVE.after("g_ke", GLA_H - 1))
                    c = D * b + 512 * n
                    act.dma_start(gate_bias[:, n, :], w["b_gate_2"][0, c:c + 512].partition_broadcast(P)).then_inc(bias_in[n], 16)
                if step == "item":
                    split_high(min(expert_unit, first_unit[a[0]] + len(items[a[0]]) + 2))
                    item(*a)
                elif step == "norm":
                    norm(*a)
                elif step == "norm_scale":
                    norm_scale(*a)
                elif step == "conv":
                    for b in range(2):
                        act.wait_ge(*DVE.after("cy", b))
                        nc.scalar.activation(mix_hi[:, b, :], cy[:, b, :], ACTF.Copy).then_inc(*ACT.done(("conv_hi", b)))
                elif step == "latent_sums":
                    rsqrt_start(("lat",), (ss[:, 1, 0:9], ss[:, 2, 0:9]))
                elif step == "weights":
                    split_high(min(len(units), expert_unit + a[0]))
                elif step == "split_x":
                    for t in range(NT):
                        act.wait_ge(*DVE.after("scaled", "ffn", t))
                        nc.scalar.activation(xs_hi[:, t, :], xs[:, t, :], ACTF.Copy).then_inc(*ACT.done(("xs_hi", t)))
                elif step == "resort":
                    resort()
                elif step == "mla_transposes":
                    q_transposed("mla", a[0], QKH, qT, 6)
                elif step == "ret_transposes":
                    q_transposed("ret", a[0], RET_D, rqT, 0)
                elif step == "gla_rstd":
                    a, b = 8 * a[0], 8 * a[0] + 8
                    rsqrt_start(("gla", a // 8), (ss[:, 3, a:b], ss[:, 4, a:b]))
                elif step in steps:
                    steps[step](*a)
                elif step == "barrier":
                    barrier(act, a[0])
                    ACT.section = a[0]
                    loads(a[0])

        @block.vector
        def _(dve):
            def mean(key, v, total, width):
                return dve.tensor_scalar(v, total, 1.0 / width, EPS, ALU.mult, ALU.add).then_inc(*DVE.done(("v", *key)))

            def rsqrt_finish(key, v, y, t):
                dve.wait_ge(*ACT.after("y0", *key))
                dve.scalar_tensor_tensor(t, y, -0.5, y, ALU.mult, ALU.mult).then_inc(*DVE.done(("r1", *key)))
                dve.wait_ge(*DVE.after("r1", *key))
                dve.tensor_tensor(t, t, v, ALU.mult).then_inc(*DVE.done(("r2", *key)))
                dve.wait_ge(*DVE.after("r2", *key))
                dve.scalar_tensor_tensor(y, t, 1.5, y, ALU.add, ALU.mult).then_inc(*DVE.done(("r", *key)))
                dve.wait_ge(*DVE.after("r", *key))

            def norm_scale(name):
                tiles = NORM_TILES[name]
                n = len(tiles)
                if name != "h":
                    dve.memset(ss[:, 0:3, 0:n], 1.0).then_inc(*DVE.done(("ss0", name)))
                for i in range(n):
                    dve.wait_ge(*ACT.after("ss", name, i))
                mean((name,), ss[:, 1, 0:n], ss[:, 0, 0:n], D)
                rsqrt_finish((name,), ss[:, 1, 0:n], ss[:, 2, 0:n], ss[:, 0, 0:n])
                for i, (src, scaled, rows) in enumerate(tiles):
                    dve.tensor_scalar(scaled, src, ss[0:rows, 2, i:i + 1], None, ALU.mult).then_inc(*DVE.done(("scaled", name, i)))

            def norm(name):
                tiles = NORM_TILES[name]
                if ("norm_scale", name) not in order:
                    norm_scale(name)
                n = sum(t[2] == P for t in tiles) * P
                hi, off = norm_dest(name)
                lo = act_lo if hi is act_hi else norm_lo(name)
                for k in range(KC):
                    dve.wait_ge(*ACT.after("hi", name, k))
                    dve.scalar_tensor_tensor(lo[:, k, off:off + n], ps[:, 4 + k % 4, 0:n], col(NORMS[name], k),
                                             hi[:, k, off:off + n].bitcast(F32), ALU.mult,
                                             ALU.subtract).then_inc(*DVE.done(("lo", name, k)))
                if name == "h":
                    dve.wait_ge(*PE.after("T", name, "meta"))
                    g = gains[:, GAINS["ln_w"]:GAINS["ln_w"] + KC].unsqueeze(2).to_broadcast([P, KC, N_META])
                    dve.tensor_tensor(meta_t[:, :, :], ps[:, 3, 0:KC * N_META].rearrange("p (k n) -> p k n", k=KC), g,
                                      ALU.mult).then_inc(*DVE.done(("meta_t", name)))
                    dve.wait_ge(*ACT.after("meta_hi", name))
                    dve.tensor_tensor(act_lo[:, :, 0:N_META], meta_t[:, :, :], act_hi[:, :, 0:N_META].bitcast(F32),
                                      ALU.subtract).then_inc(*DVE.done(("meta_lo", name)))

            def low_part(key, lo, src, hi, gain=1.0):
                return dve.scalar_tensor_tensor(lo, src, gain, hi.bitcast(F32), ALU.mult,
                                                ALU.subtract).then_inc(*DVE.done(key))

            turned = []

            def rope_turn(key, x, out, rows, heads, half, t, cos, sin):
                n = heads * half
                if turned:
                    dve.wait_ge(*DVE.after(*turned[-1], 5))
                turned.append(key)
                tmp = [b[0:rows, 0:n].rearrange("p (h n) -> p h n", h=heads) for b in (t0, t1, t2, t3)]
                c = cos[0:rows, t, :].unsqueeze(1).to_broadcast([rows, heads, half])
                s = sin[0:rows, t, :].unsqueeze(1).to_broadcast([rows, heads, half])
                a, b = x[:, :, 0:half], x[:, :, half:2 * half]
                dve.tensor_tensor(tmp[0], a, c, ALU.mult).then_inc(*DVE.done((*key, 0)))
                dve.tensor_tensor(tmp[1], b, s, ALU.mult).then_inc(*DVE.done((*key, 1)))
                dve.tensor_tensor(tmp[2], a, s, ALU.mult).then_inc(*DVE.done((*key, 2)))
                dve.tensor_tensor(tmp[3], b, c, ALU.mult).then_inc(*DVE.done((*key, 3)))
                dve.wait_ge(*DVE.after(*key, 3))
                dve.tensor_tensor(out[:, :, 0:half], tmp[0], tmp[1], ALU.subtract).then_inc(*DVE.done((*key, 4)))
                dve.tensor_tensor(out[:, :, half:2 * half], tmp[2], tmp[3], ALU.add).then_inc(*DVE.done((*key, 5)))

            def item(name):
                if name == "conv_b":
                    for b in range(2):
                        dve.wait_ge(*PE.after("acc", name, b))
                        dve.wait_ge(*ACT.after("cx", b))
                        dve.tensor_tensor(cu[:, b, N_META:], ps[:, b, :], cx[:, b, N_META:], ALU.mult).then_inc(*DVE.done(("cu", b)))
                    dve.wait_ge(*PE.after("acc", name, "meta"))
                    dve.wait_ge(*ACT.after("cx", "meta"))
                    dve.tensor_tensor(cu[:, :, 0:N_META], ps[:, 4, 0:2 * N_META].rearrange("p (b n) -> p b n", b=2),
                                      cx[:, :, 0:N_META], ALU.mult).then_inc(*DVE.done(("cu", "meta")))
                elif name == "latent":
                    for b in range(2):
                        dve.wait_ge(*ACT.after("cq_hi", b))
                        low_part(("cq_lo", b), cq_lo[:, b, :], ps[:, b, :], cq_hi[:, b, :], col("q_a_norm", b))
                    dve.wait_ge(*ACT.after("ckv_hi"))
                    low_part(("ckv_lo",), ckv_lo[:, N_META:], ps[:, 2, :], ckv_hi[:, N_META:], col("kv_a_norm"))
                    dve.wait_ge(*ACT.after("latent_sq", "meta"))
                    low_part(("ckv_lo", "meta"), ckv_lo[:, 0:N_META], ps[:, 4, 0:N_META], ckv_hi[:, 0:N_META], col("kv_a_norm"))
                elif name.startswith("w_ukv"):
                    n = int(name[-1])
                    for t in range(NT + 1):
                        rows = P if t < NT else N_META
                        dve.wait_ge(*ACT.after("k_raw", n, t))
                        src = ps[0:rows, t, :].rearrange("p (h n) -> p h n", h=4)
                        dst = v_sb[0:rows, t, 256 * n:256 * n + 256].rearrange("p (h n) -> p h n", h=4)
                        dve.tensor_scalar(dst, src[:, :, QKN:P], ss[0:rows, 2, NT + t:NT + t + 1], None,
                                          ALU.mult).then_inc(*DVE.done(("v_raw", n, t)))
                elif name == "ret_qk":
                    dve.wait_ge(rope_in, 48)
                    for t in range(NT + 1):
                        rows = P if t < NT else N_META
                        dve.wait_ge(*PE.after("acc", name, t))
                        rope_turn(("rope_r", t), ps[0:rows, t, :].rearrange("p (h n) -> p h n", h=8),
                                  rqk[0:rows, t, :].rearrange("p (h n) -> p h n", h=8), rows, 8, 32, t, cos_r, sin_r)
                elif name.startswith("w_out"):
                    n = int(name[-1])
                    for t in range(NT):
                        dve.wait_ge(*PE.after("acc", name, t))
                        x = x1[:, t, 512 * n:512 * n + 512]
                        dve.tensor_tensor(x, ps[:, t, :], x, ALU.add).then_inc(*DVE.done(("x", name, t)))

                elif name.startswith("gla_g"):
                    n = int(name[-1])
                    for t in range(NT):
                        dve.wait_ge(*ACT.after("g_silu", n, t))
                        for i in range(2):
                            h = 2 * n + i
                            o = go[:, t, GLA_DV * h:GLA_DV * (h + 1)]
                            dve.scalar_tensor_tensor(o, o, ss[:, 4, gla_stat(h, t):gla_stat(h, t) + 1],
                                                     g_silu[:, t % 2, GLA_DV * i:GLA_DV * (i + 1)], ALU.mult,
                                                     ALU.mult).then_inc(*DVE.done(("go", n, t, i)))
                elif name.startswith("gate"):
                    b, n = int(name[4]), int(name[5])
                    dve.wait_ge(bias_in[n], 16 * (b + 1))
                    for t in range(NT):
                        dve.wait_ge(*PE.after("acc", name, t))
                        if (b, n) != (0, 0):
                            dve.wait_ge(*DVE.after("merged", *((b, 0) if n else (b - 1, 1)), t))
                        dve.tensor_tensor(gate[:, t, :], ps[:, t, :], gate_bias[:, n, :],
                                          ALU.add).then_inc(*DVE.done(("gate_sum", b, n, t)))
                elif name.startswith("w_o"):
                    b, n = int(name[3]), int(name[4])
                    for t in range(NT):
                        dve.wait_ge(*PE.after("acc", name, t))
                        dve.wait_ge(*ACT.after("gate", b, n, t))
                        m = merged[:, t, 512 * n:512 * n + 512]
                        if b == 0:
                            dve.tensor_tensor(m, ps[:, t, :], gate[:, t, :],
                                              ALU.mult).then_inc(*DVE.done(("gated", b, n, t), ("merged", b, n, t)))
                        else:
                            dve.tensor_tensor(gate[:, t, :], ps[:, t, :], gate[:, t, :],
                                              ALU.mult).then_inc(*DVE.done(("gated", b, n, t)))
                            dve.wait_ge(*DVE.after("gated", b, n, t))
                            dve.tensor_tensor(m, m, gate[:, t, :], ALU.add).then_inc(*DVE.done(("merged", b, n, t)))
                elif name.startswith(("dsa_q", "mem_q")):
                    tag, n = name[0:1], int(name[-1])
                    if tag == "d":
                        top_keys(2 + n)
                    for t in range(NT):
                        i = NT * n + t
                        dve.wait_ge(*ACT.after(tag + "q_sq", i))
                        heads = 4 if tag == "d" else 2
                        at = HEAD_STATS["dsa" if tag == "d" else "mem", f"q{n}"][0] + heads * t
                        dve.tensor_reduce(ss[:, 5, at:at + heads], d_sq[:, i % 2, :].rearrange("p (h n) -> p h n", h=heads), X,
                                          ALU.add).then_inc(*DVE.done((tag + "q_ss", i)))
                elif name == "dsa_kv":
                    top_keys(1)
                    for t in range(NT):
                        dve.wait_ge(*ACT.after("dk_sq", t))
                        dve.tensor_reduce(ss[:, 5, 32 + 2 * t:34 + 2 * t],
                                          d_sq[:, t % 2, 0:256].rearrange("p (h n) -> p h n", h=2), X,
                                          ALU.add).then_inc(*DVE.done(("dk_ss", t)))
                elif name in ("mem_kv0", "mem_kv1"):
                    n = int(name[-1])
                    for t in range(2):
                        dve.wait_ge(*ACT.after("mk_sq", 2 * n + t))
                        dve.tensor_reduce(ss[:, 5, 4 * t + 2 * n:4 * t + 2 * n + 2],
                                          d_sq[:, t, :].rearrange("p (h n) -> p h n", h=2), X,
                                          ALU.add).then_inc(*DVE.done(("mk_ss", 2 * n + t)))
                elif name == "router":
                    for i in range(4):
                        dve.memset(rank[:, i:i + 1], 4.0 - i).then_inc(*DVE.done(("rank", i)))
                    dve.wait_ge(*DVE.after("rank", 3))
                    dve.wait_ge(route_in, 32)
                    dve.wait_ge(*PE.after("acc", name, NT - 1))
                    dve.tensor_tensor(rl[:, :, :], ps[:, 5, 0:NT * 20].rearrange("p (t n) -> p t n", n=20),
                                      r_bias[:, :].unsqueeze(1).to_broadcast([P, NT, 20]), ALU.add).then_inc(*DVE.done(("rl",)))

            def gla_decays(h):
                s = h % 2
                if h == 0:
                    dve.wait_ge(gla_in, 32)
                    for b in range(GLA_H):
                        dve.wait_ge(*ACT.after("gla_q", b))
                        dve.wait_ge(*ACT.after("gla_k", b))
                dve.wait_ge(*ACT.after("g_z", h))
                dve.wait_ge(*ACT.after("g_ln", h))
                dve.scalar_tensor_tensor(gz[:, :], gz[:, :], 0.0, gex[:, :], ALU.min, ALU.subtract).then_inc(*DVE.done(("g_la0", h)))
                dve.wait_ge(*DVE.after("g_la0", h))
                dve.tensor_tensor_scan(gab[:, :], scan_mask[:, :], gz[:, :], 0.0, ALU.mult, ALU.add).then_inc(*DVE.done(("g_la", h)))
                dve.wait_ge(*DVE.after("g_la", h))
                cum = gab[:, :].rearrange("p (c n) -> p c n", n=CHUNK)
                dve.tensor_tensor(glc[:, :].rearrange("p (c n) -> p c n", n=CHUNK),
                                  cum[:, :, CHUNK - 1:CHUNK].to_broadcast([P, 8, CHUNK]), cum,
                                  ALU.subtract).then_inc(*DVE.done(("g_lc", h)))
                dve.wait_ge(*ACT.after("g_e3", h))
                dve.tensor_tensor(g_ke[:, s, :], gk[:, h, :], g_ke[:, s, :], ALU.mult).then_inc(*DVE.done(("g_ke", h)))
                dve.wait_ge(*ACT.after("g_e1", h))
                dve.scalar_tensor_tensor(g_qd[:, s, :], gq[:, h, :], float(P) ** -0.5, g_qd[:, s, :], ALU.mult,
                                         ALU.mult).then_inc(*DVE.done(("g_qd", h)))
                dve.wait_ge(*ACT.after("g_e2", h))
                dve.tensor_tensor(g_ki[:, s, :], gk[:, h, :], g_ki[:, s, :], ALU.mult).then_inc(*DVE.done(("g_ki", h)))

            def gla_states(h):
                s = h % 2
                dve.wait_ge(*PE.after("g_att", h))
                dve.tensor_tensor(g_att[:, s, :].rearrange("p (t n) -> p t n", n=P), ps[:, 7, :].rearrange("p (t n) -> p t n", n=P),
                                  gla_mask[:, :].unsqueeze(1).to_broadcast([P, NT, P]), ALU.mult).then_inc(*DVE.done(("g_att", h)))
                for n in range(7):
                    bank, cols = state_bank(n)
                    dve.wait_ge(*PE.after("g_upd", h, bank))
                    if n == 0 and h:
                        dve.wait_ge(*PE.after("g_o", h - 1, NT - 1))
                    upd = ps[:, bank, cols]
                    if n == 0:
                        dve.tensor_copy(state[:, 1, :], upd).then_inc(*DVE.done(("g_state", h, 0)))
                    else:
                        dve.wait_ge(*ACT.after("g_dec", h))
                        dve.wait_ge(*DVE.after("g_state", h, n - 1))
                        dve.scalar_tensor_tensor(state[:, n + 1, :], state[:, n, :], g_dec[:, s, n:n + 1], upd, ALU.mult,
                                                 ALU.add).then_inc(*DVE.done(("g_state", h, n)))

            def gla_rstd(n):
                dve.wait_ge(*ACT.after("g_oss", 2 * n + 1, NT - 1))
                a, b = 8 * n, 8 * n + 8
                mean(("gla", n), ss[:, 3, a:b], ss[:, 5, a:b], GLA_DV)
                rsqrt_finish(("gla", n), ss[:, 3, a:b], ss[:, 4, a:b], ss[:, 0, a:b])

            def mix(tag):
                for c in range(KC):
                    dve.wait_ge(*ACT.after("mix_hi", tag, c))
                    low_part(("mix_lo", tag, c), mix_lo[:, c, :], ps[:, 4 + c % 4, :], mix_hi[:, c, :],
                             col("gla_norm_2", c % 2) if tag == "gla" else 1.0)

            def idx_key():
                dve.memset(ss[:, 0:6, :], 1.0).then_inc(*DVE.done(("ss0", "idx")))
                dve.wait_ge(*ACT.after("ik_ss", NT - 1))
                mean(("ik",), ss[:, 1, 0:4], ss[:, 0, 0:4], IDX_D)
                rsqrt_finish(("ik",), ss[:, 1, 0:4], ss[:, 2, 0:4], ss[:, 0, 0:4])
                for t in range(NT):
                    dve.tensor_scalar(ik2[:, t, 0:IDX_D], sm2[:, t, 16:80], ss[:, 2, t:t + 1], None,
                                      ALU.mult).then_inc(*DVE.done(("ik1", t)))
                    dve.tensor_scalar(ik2[:, t, IDX_D:P], sm2[:, t, 16:80], ss[:, 2, t:t + 1], None,
                                      ALU.mult).then_inc(*DVE.done(("ik2", t)))
                dve.tensor_scalar(sm2[:, :, 80:88], sm2[:, :, 80:88], float(IDX_H * IDX_D) ** -0.5, None,
                                  ALU.mult).then_inc(*DVE.done(("iw",)))
                dve.tensor_copy(d_mask[:, 0:P], dsa_mask[:, :]).then_inc(*DVE.done(("d_mask", 0)))
                dve.wait_ge(*DVE.after("iw"))

            def idx_scores(t):
                n = P * (t + 1)
                acc = work[:, t - 1, 0:n]
                for h in range(IDX_H):
                    dve.wait_ge(*ACT.after("rel", t, h))
                    wt = sm2[:, t, 80 + h:81 + h]
                    if h == 0:
                        dve.tensor_scalar(acc, rel[:, 0, 0:n], wt, None, ALU.mult).then_inc(*DVE.done(("score", t, 0)))
                    else:
                        dve.wait_ge(*DVE.after("score", t, h - 1))
                        dve.scalar_tensor_tensor(acc, rel[:, h % 2, 0:n], wt, acc, ALU.mult, ALU.add).then_inc(*DVE.done(("score", t, h)))
                dve.wait_ge(*DVE.after("score", t, IDX_H - 1))
                dve.tensor_tensor(acc[:, n - P:n], acc[:, n - P:n], dsa_mask[:, :], ALU.add).then_inc(*DVE.done(("picked", t, 0)))

            def top_keys(t):
                n = P * (t + 1)
                acc = work[:, t - 1, 0:n]
                for i in range(TOPK // 8):
                    dve.wait_ge(*DVE.after("picked", t, i))
                    if i == 0 and t > 1:
                        dve.wait_ge(*DVE.after("picked", t - 1, TOPK // 8))
                    dve.max(best8[:, :], acc).then_inc(*DVE.done(("best", t, i)))
                    dve.wait_ge(*DVE.after("best", t, i))
                    dve.match_replace(acc, best8[:, :], acc, PICKED).then_inc(*DVE.done(("picked", t, i + 1)))
                dve.wait_ge(*DVE.after("picked", t, TOPK // 8))
                at = P * (t * (t + 1) // 2)
                dve.tensor_scalar(d_mask[:, at:at + n], acc, 2 * MASKED, MASKED, ALU.is_gt, ALU.mult).then_inc(*DVE.done(("d_mask", t)))

            def scaled_heads(key, x, r, heads):
                x3 = x.rearrange("p (h n) -> p h n", h=heads)
                dve.tensor_tensor(x3, x3, r.unsqueeze(2).to_broadcast([P, heads, x3.shape[2]]),
                                  ALU.mult).then_inc(*DVE.done(key))

            def dsa_scale(part):
                a, b = HEAD_STATS["dsa", part]
                dve.wait_ge(*DVE.after(*(("dk_ss", NT - 1) if part == "k" else ("dq_ss", NT * int(part[1]) + NT - 1))))
                mean(("dsa", part), ss[:, 3, a:b], ss[:, 5, a:b], P)
                rsqrt_finish(("dsa", part), ss[:, 3, a:b], ss[:, 4, a:b], ss[:, 5, a:b])
                for t in range(NT):
                    if part == "k":
                        dve.wait_ge(*ACT.after("dk", t))
                        scaled_heads(("dkn", t), dk[:, t, :], ss[:, 4, a + 2 * t:a + 2 * t + 2], 2)
                    else:
                        n = int(part[1])
                        dve.wait_ge(*ACT.after("dq", n, t))
                        scaled_heads(("dqn", n, t), dq[:, t, 512 * n:512 * n + 512], ss[:, 4, a + 4 * t:a + 4 * t + 4], 4)

            def dsa_max(j):
                t = j % NT
                n, at = P * (t + 1), P * (t * (t + 1) // 2)
                dve.wait_ge(*PE.after("d_S", j))
                if j >= 3:
                    dve.wait_ge(*PE.after("d_PT", j - 3))
                dve.tensor_tensor_reduce(d_prob[:, j % 3, 0:n], ps[:, 4 + j % 2, 0:n], d_mask[:, at:at + n], 1.0, PICKED, ALU.add,
                                         ALU.max, sm[:, 0, j:j + 1]).then_inc(*DVE.done(("d_max", j)))

            def mem_max(j):
                dve.wait_ge(*PE.after("m_S", j))
                dve.tensor_reduce(sm[:, 0, j:j + 1], ps[:, 4 + j % 2, 0:MEM], X, ALU.max).then_inc(*DVE.done(("m_max", j)))

            def softmax_step(tag, j, count, largest, probs, scale):
                if j < count:
                    largest(j)
                if j:
                    dve.wait_ge(*ACT.after(tag + "_exp", j - 1))
                    dve.reciprocal(sm[:, 3, j - 1:j], sm[:, 2, j - 1:j]).then_inc(*DVE.done((tag + "_rsum", j - 1)))
                if j < count:
                    dve.wait_ge(*DVE.after(tag + "_max", j))
                    dve.tensor_scalar(sm[:, 1, j:j + 1], sm[:, 0, j:j + 1], scale, None,
                                      ALU.mult).then_inc(*DVE.done((tag + "_nmax", j)))
                if j:
                    dve.wait_ge(*DVE.after(tag + "_rsum", j - 1))
                    x = probs(j - 1)
                    dve.tensor_scalar(x, x, sm[:, 3, j - 1:j], None, ALU.mult).then_inc(*DVE.done((tag + "_norm", j - 1)))

            def dsa_scores(j):
                softmax_step("d", j, NT * DSA_H, dsa_max, lambda i: d_prob[:, i % 3, 0:P * (i % NT + 1)], -float(P) ** -0.5)

            def dsa_values(j):
                h, t = divmod(j, NT)
                if t == NT - 1:
                    dve.wait_ge(*ACT.after("mix_hi", "dsa", h))
                    low_part(("mix_lo", "dsa", h), mix_lo[:, h, :], ps[:, 7 if h % 2 else 3, :], mix_hi[:, h, :])

            def mem_scale(part):
                a, b = HEAD_STATS["mem", part]
                dve.wait_ge(*DVE.after(*(("mk_ss", 3) if part == "k" else ("mq_ss", NT * int(part[1]) + NT - 1))))
                mean(("mem", part), ss[:, 3, a:b], ss[:, 5, a:b], MEM)
                rsqrt_finish(("mem", part), ss[:, 3, a:b], ss[:, 4, a:b], ss[:, 5, a:b])
                if part == "k":
                    for t in range(2):
                        dve.wait_ge(*ACT.after("mkv", 1, t))
                        scaled_heads(("mkn", t), mk[:, t, :], ss[:, 4, 4 * t:4 * t + 4], 4)
                else:
                    n = int(part[1])
                    for t in range(NT):
                        dve.wait_ge(*ACT.after("mq", n, t))
                        scaled_heads(("mqn", n, t), dq[:, t, 512 * n:512 * n + 512], ss[:, 4, a + 2 * t:a + 2 * t + 2], 2)

            def mem_scores(j):
                softmax_step("m", j, NT * MEM_H, mem_max, lambda i: m_prob[:, i % 3, :], -float(MEM) ** -0.5)

            def mem_values(j):
                h, t = divmod(j, NT)
                if t == NT - 1:
                    for c in range(2):
                        dve.wait_ge(*ACT.after("mix_hi", "mem", 2 * h + c))
                        low_part(("mix_lo", "mem", 2 * h + c), mix_lo[:, 2 * h + c, :], ps[:, MEM_BANKS[2 * h + c], :],
                                 mix_hi[:, 2 * h + c, :])

            def route(part):
                step_at = [0]

                def link(ins, *name):
                    step_at[0] += 1
                    ins.then_inc(*DVE.done(("route", part, step_at[0]), *name))
                    dve.wait_ge(*DVE.after("route", part, step_at[0]))

                def four(row):
                    return rt[:, row, :].rearrange("p (t n) -> p t n", n=4)

                def one(row):
                    return rt[:, row, 0:4].unsqueeze(2).to_broadcast([P, NT, 4])

                def first_best(x, best, key, hot, *name):
                    link(dve.tensor_reduce(rt[:, best, 0:4], x, X, ALU.max))
                    link(dve.tensor_tensor(four(key), x, one(best), ALU.is_equal))
                    link(dve.tensor_tensor(four(key), four(key), rank[:, :].unsqueeze(1).to_broadcast([P, NT, 4]), ALU.mult))
                    link(dve.tensor_reduce(rt[:, 15, 0:4], four(key), X, ALU.max))
                    link(dve.tensor_tensor(four(hot), four(key), one(15), ALU.is_equal), *name)

                g = rl[:, :, 0:4]
                if part == 0:
                    dve.wait_ge(*DVE.after("rl"))
                    return first_best(g, 0, 1, 3, ("hot",))
                for t in range(NT):
                    dve.memset(y_exp[:, t, :], 0.0).then_inc(*DVE.done(("y", t - NT)))
                dve.tensor_tensor(four(2), g, one(0), ALU.subtract).then_inc(*DVE.done(("r_g",)))
                e4 = rl[:, :, 4:20].rearrange("p t (g e) -> p t e g", g=4)
                c4 = combine[:, :, :].rearrange("p t (g e) -> p t e g", g=4)
                hot_g = four(3).unsqueeze(2).to_broadcast([P, NT, 4, 4])
                link(dve.tensor_tensor(c4, e4, hot_g, ALU.mult))
                link(dve.tensor_reduce(four(4), c4, X, ALU.add))
                first_best(four(4), 5, 6, 7)
                link(dve.scalar_tensor_tensor(four(8), four(7), MASKED, four(4), ALU.mult, ALU.add))
                first_best(four(8), 10, 6, 11)
                dve.tensor_tensor(rt[:, 9, 0:4], rt[:, 10, 0:4], rt[:, 5, 0:4], ALU.subtract).then_inc(*DVE.done(("r_d",)))
                dve.wait_ge(*ACT.after("r_ed"))
                link(dve.tensor_scalar(rt[:, 12, 0:4], rt[:, 9, 0:4], 1.0, None, ALU.add))
                dve.wait_ge(*ACT.after("r_eg"))
                link(dve.tensor_reduce(rt[:, 13, 0:4], four(2), X, ALU.add))
                link(dve.tensor_tensor(rt[:, 12, 0:4], rt[:, 12, 0:4], rt[:, 13, 0:4], ALU.mult))
                link(dve.reciprocal(rt[:, 12, 0:4], rt[:, 12, 0:4]))
                link(dve.tensor_tensor(four(11), four(11), one(9), ALU.mult))
                link(dve.tensor_tensor(four(7), four(7), four(11), ALU.add))
                link(dve.tensor_tensor(four(7), four(7), one(12), ALU.mult))
                dve.tensor_tensor(c4, hot_g, four(7).unsqueeze(3).to_broadcast([P, NT, 4, 4]),
                                  ALU.mult).then_inc(*DVE.done(("combine",)))

            def sort():
                step_at = [0]

                def link(ins):
                    step_at[0] += 1
                    ins.then_inc(*DVE.done(("sort", step_at[0])))
                    dve.wait_ge(*DVE.after("sort", step_at[0]))

                def by_tile(row):
                    return so[:, row, :].rearrange("p (g t) -> p t g", g=4)

                def by_group(row):
                    return so[:, row, :].rearrange("p (g t) -> p g t", g=4)

                hot = rt[:, 3, :].rearrange("p (t g) -> p t g", g=4)
                link(dve.memset(so[:, 0, :], 1.0))
                dve.wait_ge(*PE.after("counts"))
                link(dve.tensor_copy(by_tile(1), ps[:, 6, 16:32].rearrange("p (t g) -> p t g", g=4)))
                link(dve.tensor_tensor_scan(so[:, 2, :], so[:, 0, :], so[:, 1, :], 0.0, ALU.mult, ALU.add))
                link(dve.tensor_tensor(so[:, 3, :], so[:, 2, :], so[:, 1, :], ALU.subtract))
                dve.tensor_tensor(by_tile(4), ps[:, 6, 0:16].rearrange("p (t g) -> p t g", g=4), by_tile(3),
                                  ALU.add).then_inc(*DVE.done(("counts",)))
                dve.wait_ge(*DVE.after("counts"))
                link(dve.tensor_tensor(by_tile(4), by_tile(4), hot, ALU.mult))
                link(dve.tensor_reduce(so[:, 5, 0:4], by_tile(4), X, ALU.add))
                dve.wait_ge(sort_in, 32)
                for t in range(NT):
                    dve.tensor_scalar(perm[:, t, :], iota[:, :], so[:, 5, t:t + 1], None,
                                      ALU.is_equal).then_inc(*DVE.done(("perm", t)))
                link(dve.tensor_tensor(by_group(6), by_group(2)[:, :, NT - 1:NT].to_broadcast([P, 4, NT]),
                                       iota[:, 0:SEQ:P].unsqueeze(1).to_broadcast([P, 4, NT]), ALU.is_gt))
                link(dve.tensor_tensor(by_group(7), by_group(3)[:, :, 0:1].to_broadcast([P, 4, NT]),
                                       iota[:, P - 1:SEQ:P].unsqueeze(1).to_broadcast([P, 4, NT]), ALU.is_le))
                link(dve.tensor_tensor(so[:, 6, :], so[:, 6, :], so[:, 7, :], ALU.mult))
                dve.tensor_copy(flags[:, :], so[:, 6, :]).then_inc(*DVE.done(("flags",)))

            def combine_sorted():
                dve.wait_ge(*PE.after("combine_s"))
                dve.tensor_copy(combine_s[:, :, :], ps[:, 6, 0:NT * N_EXP].rearrange("p (t n) -> p t n", n=N_EXP)
                                ).then_inc(*DVE.done(("combine_s",)))
                dve.wait_ge(*DVE.after("combine_s"))

            def resort():
                for k in range(KC):
                    dve.wait_ge(*ACT.after("s_hi", k))
                    low_part(("s_lo", k), mix_lo[:, k, :], ps[:, k % 4, :], mix_hi[:, k, :], col("g_ffn_2", k))

            def flag(v):
                return active[NT * (v // NT // 4) + v % NT]

            def skip(i, v, done, steps):
                dve.tensor_scalar(skipped[0:1, i, v:v + 1], ones[0:1, 0:1], 1.0, None, ALU.mult).then_inc(done[0], steps)

            def add(v):
                e, s = divmod(v, NT)
                dve.wait_ge(*PE.after("down", v))
                dve.wait_ge(*DVE.after("y", v - NT))
                for n in range(2):
                    y = y_exp[:, s, 512 * n:512 * n + 512]
                    op = dve.scalar_tensor_tensor(y, ps[:, 5 + n, :], combine_s[:, s, e:e + 1], y, ALU.mult, ALU.add)
                done = DVE.done(("y", v))
                op.then_inc(*done)
                return done

            def visit(v):
                e, s = divmod(v, NT)
                with dve.If_ne(flag(v), 0):
                    dve.wait_ge(*ACT.after("e_silu", v))
                    if v >= 2:
                        dve.wait_ge(*PE.after("turn", v - 2))
                    dve.tensor_tensor(hid[:, v % 2, :], ps[:, s, D_EXP:2 * D_EXP], e_silu[:, v % 2, :],
                                      ALU.mult).then_inc(*DVE.done(("hid", v)))
                    dve.wait_ge(*ACT.after("hid_hi", v))
                    done = DVE.done(("hid_lo", v))
                    dve.scalar_tensor_tensor(hid_lo[:, s, :], ps[:, 4, 0:D_EXP], 1.0, hid_hi[:, s, :].bitcast(F32),
                                             ALU.mult, ALU.subtract).then_inc(*done)
                    if e % 4:
                        done = add(v - NT)
                with dve.Else():
                    skip(0, v, done, 3 if e % 4 else 2)

            def finish(v):
                with dve.If_ne(flag(v), 0):
                    done = add(v)
                with dve.Else():
                    skip(1, v, done, 1)

            def split_low(upto):
                for g in range(fill[0], upto):
                    if low_by(g) is DVE:
                        hi, lo = split_slot(g)
                        dve.wait_ge(*ACT.after("w_hi", g))
                        dve.tensor_tensor(lo, raw[:, g % RAW_SLOTS, :], hi.bitcast(F32),
                                          ALU.subtract).then_inc(*DVE.done(("w_lo", g)))
                fill[0] = max(fill[0], upto)

            def unsort():
                for s in range(NT):
                    dve.wait_ge(*ACT.after("y_hi", s))
                    dve.tensor_tensor(y_lo[:, s, :], y_exp[:, s, :], y_hi[:, s, :].bitcast(F32),
                                      ALU.subtract).then_inc(*DVE.done(("y_lo", s)))
                for t in range(NT):
                    for n in range(2):
                        dve.wait_ge(*PE.after("unsorted", t, n))
                        x = x1[:, t, 512 * n:512 * n + 512]
                        op = dve.tensor_tensor(x, ps[:, (2 + 2 * t + n) % 8, :], x, ALU.add)
                    op.then_inc(*DVE.done(("x", LAST, t)))

            def conv():
                for b in range(2):
                    y = cy[:, b, :]
                    dve.wait_ge(*DVE.after("cu", b))
                    dve.wait_ge(*DVE.after("cu", "meta"))
                    dve.tensor_scalar(y, cu[:, b, N_META:], col("conv_w", 4 + b), col("conv_b", b), ALU.mult,
                                      ALU.add).then_inc(*DVE.done(("cy2", b)))
                    for j in (1, 0):
                        dve.wait_ge(*DVE.after(f"cy{j + 1}", b))
                        at = N_META - 2 + j
                        dve.scalar_tensor_tensor(y, cu[:, b, at:at + SEQ], col("conv_w", 2 * j + b), y, ALU.mult,
                                                 ALU.add).then_inc(*DVE.done((f"cy{j}", b)))
                    dve.wait_ge(*DVE.after("cy0", b))
                    dve.wait_ge(*ACT.after("cb", b))
                    dve.tensor_tensor(y, y, cb[:, b, :], ALU.mult).then_inc(*DVE.done(("cyb", b)))
                    dve.wait_ge(*DVE.after("cyb", b))
                    dve.wait_ge(*ACT.after("cz", b))
                    dve.tensor_tensor(y, y, cz[:, b, :], ALU.mult).then_inc(*DVE.done(("cy", b)))
                    dve.wait_ge(*ACT.after("conv_hi", b))
                    low_part(("conv_lo", b), mix_lo[:, b, :], y, mix_hi[:, b, :])

            def latent_sums():
                dve.memset(ss[:, 1:3, 0:9], 1.0).then_inc(*DVE.done(("lat0",)))
                dve.wait_ge(*DVE.after("lat0"))
                dve.wait_ge(*PE.after("lat_ss"))
                dve.tensor_scalar(ss[:, 1, 0:4], ps[:, 6, 0:4], 1.0 / 256, EPS, ALU.mult, ALU.add).then_inc(*DVE.done(("lat_q",)))
                dve.tensor_scalar(ss[:, 1, 4:8], ps[:, 6, 4:8], 1.0 / 128, EPS, ALU.mult, ALU.add).then_inc(*DVE.done(("lat_kv",)))
                dve.tensor_scalar(ss[0:N_META, 1, 8:9], ps[0:N_META, 6, 8:9], 1.0 / 128, EPS, ALU.mult,
                                  ALU.add).then_inc(*DVE.done(("lat_v",), ("v", "lat")))
                rsqrt_finish(("lat",), ss[:, 1, 0:9], ss[:, 2, 0:9], ss[:, 0, 0:9])

            def mla_sums():
                dve.memset(ss[:, 3:6, 0:72], 1.0).then_inc(*DVE.done(("head0",)))
                dve.wait_ge(*DVE.after("head0"))
                dve.wait_ge(rope_in, 48)
                dve.wait_ge(*ACT.after("kr"))
                for t in range(NT + 1):
                    rows = P if t < NT else N_META
                    for n in range(2):
                        dve.wait_ge(*ACT.after("k_raw", n, t))
                    k3 = k_sb[0:rows, t, :].rearrange("p (h n) -> p h n", h=MLA_H)
                    dve.tensor_copy(k3[:, :, QKN:QKH], kr[0:rows, t, :].unsqueeze(1).to_broadcast([rows, MLA_H, QKR])
                                    ).then_inc(*DVE.done(("kr_in", t)))
                for i, (kind, t) in enumerate(HEAD_TILES):
                    rows = P if t < NT else N_META
                    dve.wait_ge(*ACT.after("hsq", kind, t))
                    at = (0 if kind == "q" else 32) + 8 * t
                    dve.tensor_reduce(ss[0:rows, 5, at:at + 8], sq[0:rows, i % 2, :].rearrange("p (h n) -> p h n", h=MLA_H), X,
                                      ALU.add).then_inc(*DVE.done(("hss", kind, t)))
                dve.wait_ge(*DVE.after("hss", "k", NT))
                mean(("head",), ss[:, 3, 0:72], ss[:, 5, 0:72], QKH)
                rsqrt_finish(("head",), ss[:, 3, 0:72], ss[:, 4, 0:72], ss[:, 5, 0:72])

            def mla_norm(t):
                rows = P if t < NT else N_META
                for kind, x in (("q", q_sb), ("k", k_sb)):
                    if kind == "q" and t == NT:
                        continue
                    x3 = x[0:rows, t, :].rearrange("p (h n) -> p h n", h=MLA_H)
                    if kind == "q":
                        r = ss[0:rows, 4, 8 * t:8 * t + 8].unsqueeze(2).to_broadcast([rows, MLA_H, QKH])
                        dve.tensor_tensor(x3, x3, r, ALU.mult).then_inc(*DVE.done(("hn1", "q", t)))
                        dve.wait_ge(*DVE.after("hn1", "q", t))
                        dve.tensor_tensor(x3, x3, qk_gain[0:rows, 0, :].unsqueeze(1).to_broadcast([rows, MLA_H, QKH]),
                                          ALU.mult).then_inc(*DVE.done(("hn2", "q", t)))
                        dve.wait_ge(*DVE.after("hn2", "q", t))
                    else:
                        dve.wait_ge(*POOL.after("hn2", "k", t))
                    rope_turn(("rope_m", kind, t), x3[:, :, QKN:QKH], x3[:, :, QKN:QKH], rows, MLA_H, QKR // 2, t, cos_m, sin_m)

            def k_transposed(tag, h, width, dst, bank):
                dve.wait_ge(*PE.after("kT", tag, h))
                if h >= 2:
                    dve.wait_ge(*PE.after(*last_scores(tag, h - 2)))
                dve.tensor_copy(dst[0:width, h % 2, :],
                                psf[0:width, (bank + 1) * SEQ - N_META:(bank + 2) * SEQ]).then_inc(*DVE.done(("kT", tag, h)))

            def mla_scores(j):
                n = P * (j % NT + 1)
                dve.wait_ge(*PE.after("S", "mla", j))
                dve.tensor_reduce(sm[:, 0, j:j + 1], psf[:, 5 * SEQ - N_META:5 * SEQ + n], X,
                                  ALU.max).then_inc(*DVE.done(("max", "mla", j)))
                dve.wait_ge(*DVE.after("max", "mla", j))
                dve.tensor_scalar(sm[:, 1, j:j + 1], sm[:, 0, j:j + 1], -float(QKH) ** -0.5, None,
                                  ALU.mult).then_inc(*DVE.done(("nmax", "mla", j)))

            def mla_turn(j):
                dve.wait_ge(*ACT.after("exp", "mla", j))
                dve.reciprocal(sm[:, 3, j:j + 1], sm[:, 2, j:j + 1]).then_inc(*DVE.done(("rsum", "mla", j)))
                dve.wait_ge(*PE.after("PTm", "mla", j))
                dve.tensor_copy(probT_m[:, j % 2, :], ps[0:N_META, 7, 0:P]).then_inc(*DVE.done(("PTm", "mla", j)))

            def mla_values(j):
                h, t = divmod(j, NT)
                dve.wait_ge(*PE.after("O", "mla", j))
                dve.wait_ge(*DVE.after("rsum", "mla", j))
                dve.wait_ge(*ACT.after("z_mla", t))
                cols = slice(VH * h, VH * (h + 1))
                dve.scalar_tensor_tensor(y_mla[:, t, cols], ps[:, 7, P:P + VH], sm[:, 3, j:j + 1], z_mla[:, t, cols],
                                         ALU.mult, ALU.mult).then_inc(*DVE.done(("y", "mla", j)))

            def ret_scores(h):
                dve.wait_ge(decay_in, 32 * (h + 1))
                dve.wait_ge(*PE.after("rS", h, "meta"))
                if h:
                    dve.wait_ge(*PE.after("rO", h - 1))
                dve.tensor_tensor(sd_m[:, :], ps[0:N_META, 3, :], decay_m[:, :], ALU.mult).then_inc(*DVE.done(("sd", h, "meta")))
                for b in range(NT):
                    dve.wait_ge(*PE.after("rS", h, b))
                    dve.tensor_tensor(sd[:, b, P * b:SEQ], ps[:, b, P * b:SEQ], decay[:, 0:SEQ - P * b],
                                      ALU.mult).then_inc(*DVE.done(("sd", h, b)))

            def ret_norm():
                dve.wait_ge(*ACT.after("ysq"))
                dve.tensor_reduce(ss[:, 5, 0:16], ysq[:, :, :].rearrange("p t (h n) -> p (t h) n", n=RET_D), X,
                                  ALU.add).then_inc(*DVE.done(("yss",)))
                dve.wait_ge(*DVE.after("yss"))
                mean(("ret",), ss[:, 3, 0:16], ss[:, 5, 0:16], RET_D)
                rsqrt_finish(("ret",), ss[:, 3, 0:16], ss[:, 4, 0:16], ss[:, 5, 0:16])
                for t in range(NT):
                    y = y_ret[:, t, :].rearrange("p (h n) -> p h n", h=RET_H)
                    dve.tensor_tensor(y, y, ss[:, 4, 4 * t:4 * t + 4].unsqueeze(2).to_broadcast([P, RET_H, RET_D]),
                                      ALU.mult).then_inc(*DVE.done(("yn", t)))
                    dve.wait_ge(*DVE.after("yn", t))
                    dve.tensor_tensor(y_ret[:, t, :], y_ret[:, t, :], z_ret[:, t, :], ALU.mult).then_inc(*DVE.done(("y_ret", t)))

            def mix_one():
                for c in range(6):
                    dve.wait_ge(*ACT.after("mix_hi", 2 + c))
                    low_part(("mix_lo", 2 + c), mix_lo[:, 2 + c, :], ps[:, 6 + c % 2, :], mix_hi[:, 2 + c, :],
                             1.0 if c < 4 else col("ret_norm"))

            steps = {"item": item, "norm": norm, "norm_scale": norm_scale, "conv": conv, "latent_sums": latent_sums, "mla_sums": mla_sums,
                     "mla_norm": mla_norm, "mla_scores": mla_scores, "mla_turn": mla_turn, "mla_values": mla_values,
                     "ret_scores": ret_scores, "ret_norm": ret_norm, "mix_one": mix_one, "gla_decays": gla_decays,
                     "gla_states": gla_states, "gla_rstd": gla_rstd, "mix": mix, "idx_key": idx_key,
                     "idx_scores": idx_scores, "dsa_scale": dsa_scale, "dsa_scores": dsa_scores,
                     "dsa_values": dsa_values, "mem_scale": mem_scale, "mem_scores": mem_scores,
                     "mem_values": mem_values, "route": route, "sort": sort, "combine_s": combine_sorted, "visit": visit, "finish": finish,
                     "unsort": unsort}
            active = []
            fill = [expert_unit]
            for step, *a in order:
                if step == "constants":
                    dve.memset(ss[:, 0:3, 0:NT + 1], 1.0).then_inc(*DVE.done(("ss0", "h")))
                    dve.wait_ge(*PE.after("gains"))
                    dve.tensor_copy(gains[:, :], ps[:, 7, 0:64]).then_inc(*DVE.done(("gains",)))
                    dve.wait_ge(*DVE.after("gains"))
                elif step == "weights":
                    split_low(min(len(units), expert_unit + a[0]))
                elif step == "resort":
                    active = load_flags(dve, "dve")
                    resort()
                elif step == "mla_transposes":
                    k_transposed("mla", a[0], QKH, kT, 4)
                elif step == "ret_transposes":
                    k_transposed("ret", a[0], RET_D, rkT, 1)
                elif step == "dsa_turn":
                    if a[0] == NT * DSA_H - 1:
                        dsa_scores(a[0] + 1)
                elif step == "mem_turn":
                    if a[0] == NT * MEM_H - 1:
                        mem_scores(a[0] + 1)
                elif step in steps:
                    steps[step](*a)
                elif step == "barrier":
                    barrier(dve, a[0])
                    DVE.section = a[0]

        for engine, p in (("tensor", PE), ("scalar", ACT), ("vector", DVE), ("gpsimd", POOL)):
            known[engine] = p.at
            known[engine + " ends"] = p.count


def constants():
    f = np.float32
    pos = np.arange(L, dtype=f)

    def tables(dim):
        inv = f(1.0) / (f(10000.0) ** (np.arange(0, dim, 2, dtype=f) / f(dim)))
        ang = pos[:, None] * inv[None, :]
        return np.cos(ang).astype(f), np.sin(ang).astype(f)

    def tiles(table):
        n = table.shape[1]
        t = np.zeros((P, NT + 1, n), f)
        for i in range(NT):
            t[:, i] = table[N_META + P * i:N_META + P * (i + 1)]
        t[:N_META, NT] = table[:N_META]
        return t.reshape(P, -1)

    cm, sm = tables(QKR)
    cr, sr = tables(RET_D)
    rope = np.concatenate([tiles(cm), tiles(sm), tiles(cr), tiles(sr)], axis=1)
    log_g = np.log1p(-np.exp2(-5.0 - np.arange(RET_H)))
    m, c = np.arange(P)[:, None], np.arange(SEQ)[None, :]
    seen = (m // CHUNK) <= (c // CHUNK)
    decay = np.stack([np.where(seen, np.exp(g * np.abs(c - m)), 0.0) for g in log_g]) * RET_D ** -0.5
    mm = np.arange(N_META)[:, None]
    decay_m = np.stack([np.exp(g * (c + N_META - mm)) for g in log_g]) * RET_D ** -0.5
    j, i = np.arange(P)[:, None], np.arange(P)[None, :]
    return {
        "c_ident": np.eye(P, dtype=f),
        "c_gla_mask": ((j // CHUNK == i // CHUNK) & (i >= j)).astype(f),
        "c_dsa_mask": np.where(i <= j, 0.0, MASKED).astype(f),
        "c_mask_q": (np.arange(P) < CHUNK).astype(f)[None, :],
        "c_mask_k": np.full((1, CHUNK), MASKED, f),
        "c_rope": rope.astype(f),
        "c_decay": decay.astype(f),
        "c_decay_m": decay_m.astype(f),
        "c_iota": np.arange(SEQ, dtype=f),
        "c_before": (j < i).astype(f),
        "c_scan": np.tile((np.arange(SEQ) % CHUNK != 0).astype(f), (P, 1)),
    }


def kernel(**inputs):
    import concourse.bacc as bacc
    from concourse.bass_utils import run_bass_kernel_spmd

    arrays = {name: np.ascontiguousarray(a) for name, a in inputs.items()}
    arrays.update(constants())

    def build(known):
        nc = bacc.Bacc("TRN2", target_bir_lowering=False, num_devices=1)
        w = {name: nc.dram_tensor(f"in_{name}", a.shape, mybir.dt.from_np(a.dtype), kind="ExternalInput").ap()
             for name, a in arrays.items()}
        out = nc.dram_tensor("out_0", (1, SEQ, D), F32, kind="ExternalOutput").ap()
        program(nc, w, out, known)
        return nc

    known = {}
    build(known)
    nc = build(known)
    r = run_bass_kernel_spmd(nc, [{f"in_{name}": a for name, a in arrays.items()}], core_ids=[0])
    return r.results[0]["out_0"]
```
